# Optimizing a Trainium2 kernel written in Bass

```python
import math
import jax
import jax.numpy as jnp
from jax import lax
import numpy as np
import jax, jax.numpy as jnp

D_MODEL = 1024
BATCH = 1
SEQ = 512
DEPTH = 2

CHUNK = 64
N_MIXERS = 2
CONV_WIDTH = 4
EPS = 1e-6

D_RNN = D_MODEL
LRU_BLOCKS = 8
LRU_BLOCK_W = D_RNN // LRU_BLOCKS
RG_C = 8.0

GDN_HEAD_DIM = 128
GDN_HEADS = max(4, D_MODEL // GDN_HEAD_DIM)
GDN_DK = GDN_HEAD_DIM
GDN_DV = GDN_HEAD_DIM
GDN_HK = GDN_HEADS * GDN_DK
GDN_HV = GDN_HEADS * GDN_DV
GDN_PROJ = 2 * GDN_HK + 2 * GDN_HV + 2 * GDN_HEADS


def rmsnorm(x, g):
    xf = x.astype(jnp.float32)
    y = xf * lax.rsqrt(jnp.mean(xf * xf, axis=-1, keepdims=True) + EPS)
    return (y * g.astype(jnp.float32)).astype(x.dtype)

def l2norm(x):
    return x * lax.rsqrt(jnp.sum(x * x, axis=-1, keepdims=True) + EPS)

def causal_dwconv(x, w):
    k = w.shape[0]
    s = x.shape[1]
    xp = jnp.pad(x, ((0, 0), (k - 1, 0), (0, 0)))
    out = xp[:, 0:s] * w[0]
    for j in range(1, k):
        out = out + xp[:, j:j + s] * w[j]
    return out

def _lin_combine(e1, e2):
    a1, b1 = e1
    a2, b2 = e2
    return a1 * a2, a2 * b1 + b2

def rglru_block(h, in_w, conv_w, conv_b, gate_w, gate_b, lam, out_w):
    bsz, s, _ = h.shape
    proj = h @ in_w
    xb, zg = proj[..., :D_RNN], proj[..., D_RNN:]
    xb = causal_dwconv(xb, conv_w) + conv_b
    xf = xb.astype(jnp.float32)
    xg = xf.reshape(bsz, s, LRU_BLOCKS, LRU_BLOCK_W)
    pre = jnp.einsum('bsni,knij->kbsnj', xg, gate_w.astype(jnp.float32))
    pre = pre.reshape(2, bsz, s, D_RNN) + gate_b.astype(jnp.float32)[:, None, None, :]
    gates = jax.nn.sigmoid(pre)
    r_t, i_t = gates[0], gates[1]
    log_a = -RG_C * r_t * jax.nn.softplus(-lam.astype(jnp.float32))
    a_t = jnp.exp(log_a)
    mult = jnp.sqrt(-jnp.expm1(2.0 * log_a))
    b_t = mult * (i_t * xf)
    _, hseq = lax.associative_scan(_lin_combine, (a_t, b_t), axis=1)
    y = hseq.astype(h.dtype) * jax.nn.silu(zg)
    return y @ out_w

def chunk_gated_delta_rule(q, k, v, g, beta):
    bsz, s, nh, dk = q.shape
    dv = v.shape[-1]
    n = s // CHUNK

    def to_chunks(t):
        return t.reshape(bsz, n, CHUNK, nh, -1).transpose(0, 3, 1, 2, 4)

    q, k, v = to_chunks(q), to_chunks(k), to_chunks(v)
    g = g.reshape(bsz, n, CHUNK, nh).transpose(0, 3, 1, 2)
    beta = beta.reshape(bsz, n, CHUNK, nh).transpose(0, 3, 1, 2)
    g = jnp.cumsum(g, axis=-1)
    idx = jnp.arange(CHUNK)
    causal = idx[:, None] >= idx[None, :]
    strict = idx[:, None] > idx[None, :]
    diff = g[..., :, None] - g[..., None, :]
    decay_mask = jnp.exp(jnp.where(causal, diff, -jnp.inf))
    k_beta = k * beta[..., None]
    v_beta = v * beta[..., None]
    a_mat = jnp.where(strict, jnp.einsum('bhncd,bhnmd->bhncm', k_beta, k) * decay_mask, 0.0)
    eye = jnp.eye(CHUNK, dtype=jnp.float32)
    t_mat = lax.linalg.triangular_solve(a_mat + eye, jnp.broadcast_to(eye, a_mat.shape),
                                        left_side=True, lower=True)
    w = jnp.einsum('bhncm,bhnmd->bhncd', t_mat, k_beta * jnp.exp(g)[..., None])
    u = jnp.einsum('bhncm,bhnmd->bhncd', t_mat, v_beta)
    attn = jnp.where(causal, jnp.einsum('bhncd,bhnmd->bhncm', q, k) * decay_mask, 0.0)
    g_last = g[..., -1]
    q_dec = q * jnp.exp(g)[..., None]
    k_dec = k * jnp.exp(g_last[..., None] - g)[..., None]
    e_last = jnp.exp(g_last)

    def step(state, inp):
        w_c, u_c, attn_c, q_c, k_c, e_c = inp
        v_new = u_c - jnp.einsum('bhcd,bhde->bhce', w_c, state)
        o_c = jnp.einsum('bhcd,bhde->bhce', q_c, state) + jnp.einsum('bhcm,bhme->bhce', attn_c, v_new)
        state = state * e_c[..., None, None] + jnp.einsum('bhcd,bhce->bhde', k_c, v_new)
        return state, o_c

    def lead(t):
        return jnp.moveaxis(t, 2, 0)

    s0 = jnp.zeros((bsz, nh, dk, dv), jnp.float32)
    _, o = lax.scan(step, s0, (lead(w), lead(u), lead(attn), lead(q_dec), lead(k_dec), lead(e_last)))
    return o.transpose(1, 0, 3, 2, 4).reshape(bsz, s, nh, dv)

def gated_deltanet_block(h, in_w, conv_w, a_log, dt_bias, onorm_g, out_w):
    bsz, s, _ = h.shape
    proj = h @ in_w
    o1 = 2 * GDN_HK + GDN_HV
    o2 = o1 + GDN_HV
    qkv = jax.nn.silu(causal_dwconv(proj[..., :o1], conv_w))
    z = proj[..., o1:o2]
    a_in = proj[..., o2:o2 + GDN_HEADS]
    b_in = proj[..., o2 + GDN_HEADS:]
    qkv = qkv.astype(jnp.float32)
    q = qkv[..., :GDN_HK].reshape(bsz, s, GDN_HEADS, GDN_DK)
    k = qkv[..., GDN_HK:2 * GDN_HK].reshape(bsz, s, GDN_HEADS, GDN_DK)
    v = qkv[..., 2 * GDN_HK:].reshape(bsz, s, GDN_HEADS, GDN_DV)
    q = l2norm(q) * (GDN_DK ** -0.5)
    k = l2norm(k)
    beta = jax.nn.sigmoid(b_in.astype(jnp.float32))
    g = -jnp.exp(a_log.astype(jnp.float32)) * jax.nn.softplus(
        a_in.astype(jnp.float32) + dt_bias.astype(jnp.float32))
    o = chunk_gated_delta_rule(q, k, v, g, beta)
    o = o * lax.rsqrt(jnp.mean(o * o, axis=-1, keepdims=True) + EPS) * onorm_g.astype(jnp.float32)
    o = o.astype(h.dtype) * jax.nn.silu(z.reshape(bsz, s, GDN_HEADS, GDN_DV))
    return o.reshape(bsz, s, GDN_HV) @ out_w

def first_inputs(seed: int = 0) -> dict:
    key = jax.random.key(seed)
    ks = jax.random.split(key, 24)
    n_a = (DEPTH + 1) // 2
    n_b = DEPTH // 2
    f32 = jnp.float32
    nrm = lambda k, shp, sc: jax.random.normal(k, shp, f32) * sc
    x = jax.random.normal(ks[0], (BATCH, SEQ, D_MODEL), f32)
    c = jax.random.normal(ks[1], (BATCH, D_MODEL), f32)
    ada_w = nrm(ks[2], (DEPTH, D_MODEL, 3 * D_MODEL), 0.5 * D_MODEL ** -0.5)
    ada_b = nrm(ks[3], (DEPTH, 3 * D_MODEL), 0.02)
    norm_g = 1.0 + nrm(ks[4], (DEPTH, D_MODEL), 0.02)
    final_g = 1.0 + nrm(ks[5], (D_MODEL,), 0.02)
    lru_in_w = nrm(ks[6], (n_a, D_MODEL, 2 * D_RNN), D_MODEL ** -0.5)
    lru_conv_w = nrm(ks[7], (n_a, CONV_WIDTH, D_RNN), CONV_WIDTH ** -0.5)
    lru_conv_b = nrm(ks[8], (n_a, D_RNN), 0.01)
    lru_gate_w = nrm(ks[9], (n_a, 2, LRU_BLOCKS, LRU_BLOCK_W, LRU_BLOCK_W), LRU_BLOCK_W ** -0.5)
    lru_gate_b = nrm(ks[10], (n_a, 2, D_RNN), 0.01)
    a_target = jax.random.uniform(ks[11], (n_a, D_RNN), f32, 0.9, 0.999)
    s_lam = a_target ** (1.0 / RG_C)
    lru_lambda = jnp.log(s_lam) - jnp.log1p(-s_lam)
    lru_out_w = nrm(ks[12], (n_a, D_RNN, D_MODEL), D_RNN ** -0.5)
    gdn_in_w = nrm(ks[13], (n_b, D_MODEL, GDN_PROJ), D_MODEL ** -0.5)
    gdn_conv_w = nrm(ks[14], (n_b, CONV_WIDTH, 2 * GDN_HK + GDN_HV), CONV_WIDTH ** -0.5)
    gdn_a_log = jnp.log(jax.random.uniform(ks[15], (n_b, GDN_HEADS), f32, 1.0, 16.0))
    dt = jnp.exp(jax.random.uniform(ks[16], (n_b, GDN_HEADS), f32, math.log(1e-3), math.log(1e-1)))
    gdn_dt_bias = dt + jnp.log(-jnp.expm1(-dt))
    gdn_onorm_g = 1.0 + nrm(ks[17], (n_b, GDN_DV), 0.02)
    gdn_out_w = nrm(ks[18], (n_b, GDN_HV, D_MODEL), GDN_HV ** -0.5)
    return {"x": x, "c": c, "ada_w": ada_w, "ada_b": ada_b, "norm_g": norm_g, "final_g": final_g,
            "lru_in_w": lru_in_w, "lru_conv_w": lru_conv_w, "lru_conv_b": lru_conv_b,
            "lru_gate_w": lru_gate_w, "lru_gate_b": lru_gate_b, "lru_lambda": lru_lambda,
            "lru_out_w": lru_out_w,
            "gdn_in_w": gdn_in_w, "gdn_conv_w": gdn_conv_w, "gdn_a_log": gdn_a_log,
            "gdn_dt_bias": gdn_dt_bias, "gdn_onorm_g": gdn_onorm_g, "gdn_out_w": gdn_out_w}

def first_block(x, c, ada_w, ada_b, norm_g, final_g,
              lru_in_w, lru_conv_w, lru_conv_b, lru_gate_w, lru_gate_b, lru_lambda, lru_out_w,
              gdn_in_w, gdn_conv_w, gdn_a_log, gdn_dt_bias, gdn_onorm_g, gdn_out_w):
    c_act = jax.nn.silu(c)
    for i in range(DEPTH):
        cond = c_act @ ada_w[i] + ada_b[i]
        shift = cond[:, None, :D_MODEL]
        scale = cond[:, None, D_MODEL:2 * D_MODEL]
        gate = cond[:, None, 2 * D_MODEL:]
        h = rmsnorm(x, norm_g[i]) * (1.0 + scale) + shift
        j = i // N_MIXERS
        if i % N_MIXERS == 0:
            out = rglru_block(h, lru_in_w[j], lru_conv_w[j], lru_conv_b[j], lru_gate_w[j],
                              lru_gate_b[j], lru_lambda[j], lru_out_w[j])
        else:
            out = gated_deltanet_block(h, gdn_in_w[j], gdn_conv_w[j], gdn_a_log[j],
                                       gdn_dt_bias[j], gdn_onorm_g[j], gdn_out_w[j])
        x = x + gate * out
    return rmsnorm(x, final_g)


ROPE_THETA = 10000.0
D_FF = 2816
CONV_K = 4
BLOCK = 128

D_MIX = 2 * D_MODEL
SSD_WIDTH = D_MIX // 2
SSD_HEAD_DIM = 64
SSD_HEADS = SSD_WIDTH // SSD_HEAD_DIM
SSD_GROUPS = 2
SSD_STATE = 128
SSD_CONV_DIM = SSD_WIDTH + 2 * SSD_GROUPS * SSD_STATE
SSD_CHUNK = 128
ML_WIDTH = D_MIX - SSD_WIDTH
ML_HEADS = 4
ML_V_DIM = ML_WIDTH // ML_HEADS
ML_QK_DIM = ML_V_DIM // 2
ML_CHUNK = 128
HY_SPLITS = (SSD_WIDTH, SSD_CONV_DIM, SSD_HEADS, ML_HEADS * ML_QK_DIM, ML_HEADS * ML_QK_DIM,
             ML_WIDTH, ML_WIDTH, ML_HEADS, ML_HEADS)
HY_IN = sum(HY_SPLITS)

ATT_HEAD_DIM = 64
ATT_HEADS = D_MODEL // ATT_HEAD_DIM
IDX_HEADS = ATT_HEADS // 2
IDX_DIM = ATT_HEAD_DIM
TOPK_MAX = 256
SA_SPLITS = (ATT_HEADS * ATT_HEAD_DIM, ATT_HEAD_DIM, ATT_HEAD_DIM, IDX_HEADS * IDX_DIM, IDX_DIM, IDX_HEADS)
SA_IN = sum(SA_SPLITS)

N_EVEN = (DEPTH + 1) // 2
N_ODD = DEPTH // 2


def split_cols(y, sizes):
    bounds, acc = [], 0
    for s in sizes[:-1]:
        acc += s
        bounds.append(acc)
    return jnp.split(y, bounds, axis=-1)

def rms_norm(x, g):
    xf = x.astype(jnp.float32)
    y = xf * lax.rsqrt(jnp.mean(xf * xf, axis=-1, keepdims=True) + EPS) * g.astype(jnp.float32)
    return y.astype(x.dtype)

def swiglu(h, w_gate, w_up, w_down):
    return (jax.nn.silu(h @ w_gate) * (h @ w_up)) @ w_down

def rope_tables(positions, dim):
    inv = ROPE_THETA ** (-jnp.arange(0, dim, 2, dtype=jnp.float32) / dim)
    ang = positions.astype(jnp.float32)[..., None] * inv
    return jnp.cos(ang), jnp.sin(ang)

def apply_rope(x, cos, sin):
    half = x.shape[-1] // 2
    xf = x.astype(jnp.float32)
    x1, x2 = xf[..., :half], xf[..., half:]
    c, s = cos[:, :, None, :], sin[:, :, None, :]
    return jnp.concatenate([x1 * c - x2 * s, x1 * s + x2 * c], axis=-1).astype(x.dtype)

def causal_dwconv_2(u, w, bias):
    L, K = u.shape[1], w.shape[0]
    up = jnp.pad(u, ((0, 0), (K - 1, 0), (0, 0)))
    return sum(up[:, k:k + L] * w[k] for k in range(K)) + bias

def ssd_chunked(x, dt, A, B, C, chunk):
    b, L, H, P = x.shape
    G, N = B.shape[-2:]
    E, nc = H // G, L // chunk
    a = (dt * A).reshape(b, nc, chunk, G, E)
    xd = (x * dt[..., None]).reshape(b, nc, chunk, G, E, P)
    B = B.reshape(b, nc, chunk, G, N)
    C = C.reshape(b, nc, chunk, G, N)
    acs = jnp.cumsum(a, axis=2)
    seg = acs[:, :, :, None] - acs[:, :, None, :]
    mask = jnp.tril(jnp.ones((chunk, chunk), bool))[:, :, None, None]
    Lm = jnp.exp(jnp.where(mask, seg, -jnp.inf))
    CB = jnp.einsum('bctgn,bcsgn->bctsg', C, B)
    y_diag = jnp.einsum('bctsg,bctsge,bcsgep->bctgep', CB, Lm, xd)
    decay_end = jnp.exp(acs[:, :, -1:] - acs)
    s_loc = jnp.einsum('bcsgn,bcsge,bcsgep->bcgepn', B, decay_end, xd)
    chunk_decay = jnp.exp(acs[:, :, -1])

    def step(hc, inp):
        dec, s = inp
        return hc * dec[..., None, None] + s, hc

    h0 = jnp.zeros((b, G, E, P, N), jnp.float32)
    _, h_in = lax.scan(step, h0, (jnp.moveaxis(chunk_decay, 1, 0), jnp.moveaxis(s_loc, 1, 0)))
    h_in = jnp.moveaxis(h_in, 0, 1)
    y_off = jnp.einsum('bctgn,bcgepn,bctge->bctgep', C, h_in, jnp.exp(acs))
    return (y_diag + y_off).reshape(b, L, H, P)

def mlstm_chunked(q, k, v, i_pre, f_pre, chunk):
    b, L, H, dk = q.shape
    dv = v.shape[-1]
    nc = L // chunk
    q = (q.astype(jnp.float32) * dk ** -0.5).reshape(b, nc, chunk, H, dk)
    k = k.astype(jnp.float32).reshape(b, nc, chunk, H, dk)
    v = v.astype(jnp.float32).reshape(b, nc, chunk, H, dv)
    li = i_pre.astype(jnp.float32).reshape(b, nc, chunk, H)
    lf = jax.nn.log_sigmoid(f_pre.astype(jnp.float32)).reshape(b, nc, chunk, H)
    bcs = jnp.cumsum(lf, axis=2)
    b_last = bcs[:, :, -1]
    g = b_last[:, :, None] - bcs + li
    m_loc = jnp.max(g, axis=2)
    wg = jnp.exp(g - m_loc[:, :, None])
    c_loc = jnp.einsum('bcsh,bcshv,bcshk->bchvk', wg, v, k)
    n_loc = jnp.einsum('bcsh,bcshk->bchk', wg, k)

    def step(carry, inp):
        Cs, ns, ms = carry
        bl, cl, nl, ml = inp
        m_new = jnp.maximum(bl + ms, ml)
        a = jnp.exp(bl + ms - m_new)
        gg = jnp.exp(ml - m_new)
        new = (a[..., None, None] * Cs + gg[..., None, None] * cl,
               a[..., None] * ns + gg[..., None] * nl, m_new)
        return new, (Cs, ns, ms)

    init = (jnp.zeros((b, H, dv, dk), jnp.float32), jnp.zeros((b, H, dk), jnp.float32),
            jnp.zeros((b, H), jnp.float32))
    xs = tuple(jnp.moveaxis(t, 1, 0) for t in (b_last, c_loc, n_loc, m_loc))
    _, (c_in, n_in, m_in) = lax.scan(step, init, xs)
    c_in, n_in, m_in = (jnp.moveaxis(t, 0, 1) for t in (c_in, n_in, m_in))
    Dm = bcs[:, :, :, None, :] - bcs[:, :, None, :, :] + li[:, :, None, :, :]
    mask = jnp.tril(jnp.ones((chunk, chunk), bool))[:, :, None]
    Dm = jnp.where(mask, Dm, -jnp.inf)
    inter = bcs + m_in[:, :, None, :]
    m_t = jnp.maximum(jnp.max(Dm, axis=3), inter)
    S = jnp.einsum('bcthk,bcshk->bctsh', q, k) * jnp.exp(Dm - m_t[:, :, :, None, :])
    w_inter = jnp.exp(inter - m_t)
    num = jnp.einsum('bctsh,bcshv->bcthv', S, v) + w_inter[..., None] * jnp.einsum('bcthk,bchvk->bcthv', q, c_in)
    den = jnp.sum(S, axis=3) + w_inter * jnp.einsum('bcthk,bchk->bcth', q, n_in)
    h = num / jnp.maximum(jnp.abs(den), jnp.exp(-m_t))[..., None]
    return h.reshape(b, L, H, dv)

def hybrid_mixer(h, w_in, conv_w, conv_b, dt_bias, a_log, d_skip, ssd_norm,
                 igate_bias, fgate_bias, mlstm_norm, w_out):
    b, L, _ = h.shape
    z, xbc, dt_raw, qm, km, vm, om, ig, fg = split_cols(h @ w_in, HY_SPLITS)
    xbc = jax.nn.silu(causal_dwconv_2(xbc, conv_w, conv_b))
    xs, bm, cm = split_cols(xbc, (SSD_WIDTH, SSD_GROUPS * SSD_STATE, SSD_GROUPS * SSD_STATE))
    xs = xs.reshape(b, L, SSD_HEADS, SSD_HEAD_DIM).astype(jnp.float32)
    dt = jax.nn.softplus(dt_raw.astype(jnp.float32) + dt_bias.astype(jnp.float32))
    A = -jnp.exp(a_log.astype(jnp.float32))
    y = ssd_chunked(xs, dt, A,
                    bm.reshape(b, L, SSD_GROUPS, SSD_STATE).astype(jnp.float32),
                    cm.reshape(b, L, SSD_GROUPS, SSD_STATE).astype(jnp.float32), SSD_CHUNK)
    y = y + xs * d_skip.astype(jnp.float32)[:, None]
    gate = jax.nn.silu(z.astype(jnp.float32)).reshape(b, L, SSD_GROUPS, -1)
    y = rms_norm(y.reshape(b, L, SSD_GROUPS, -1) * gate, ssd_norm.reshape(SSD_GROUPS, -1))
    y = y.reshape(b, L, SSD_WIDTH)
    hm = mlstm_chunked(qm.reshape(b, L, ML_HEADS, ML_QK_DIM), km.reshape(b, L, ML_HEADS, ML_QK_DIM),
                       vm.reshape(b, L, ML_HEADS, ML_V_DIM), ig + igate_bias, fg + fgate_bias, ML_CHUNK)
    hm = rms_norm(hm, mlstm_norm.reshape(ML_HEADS, ML_V_DIM)).reshape(b, L, ML_WIDTH)
    hm = hm * jax.nn.sigmoid(om.astype(jnp.float32))
    return jnp.concatenate([y, hm], axis=-1).astype(h.dtype) @ w_out

def sparse_attention(h, cos, sin, w_in, q_norm, k_norm, w_out, topk):
    b, L, _ = h.shape
    q, k, v, qi, ki, wi = split_cols(h @ w_in, SA_SPLITS)
    q = apply_rope(rms_norm(q.reshape(b, L, ATT_HEADS, ATT_HEAD_DIM), q_norm), cos, sin)
    k = apply_rope(rms_norm(k, k_norm)[:, :, None, :], cos, sin)[:, :, 0]
    qi = apply_rope(qi.reshape(b, L, IDX_HEADS, IDX_DIM), cos, sin)
    ki = apply_rope(ki[:, :, None, :], cos, sin)[:, :, 0]
    kv = jnp.concatenate([k, v], axis=-1)
    nb = L // BLOCK
    key_pos = jnp.arange(L)
    idx_scale = (IDX_HEADS ** -0.5) * (IDX_DIM ** -0.5)
    att_scale = ATT_HEAD_DIM ** -0.5

    def to_blocks(t):
        return jnp.moveaxis(t.reshape(b, nb, BLOCK, *t.shape[2:]), 1, 0)

    def block(args):
        j, qb, qib, wib = args
        q_pos = j * BLOCK + jnp.arange(BLOCK)
        logits = jnp.einsum('bthd,bsd->btsh', qib, ki).astype(jnp.float32)
        score = jnp.einsum('btsh,bth->bts', jax.nn.relu(logits), wib.astype(jnp.float32)) * idx_scale
        causal = key_pos[None, :] <= q_pos[:, None]
        score = jnp.where(causal[None], score, -jnp.inf)
        _, sel = lax.top_k(score, topk)
        valid = sel <= q_pos[None, :, None]
        kv_sel = jax.vmap(lambda kvb, sb: kvb[sb])(kv, sel)
        k_sel, v_sel = kv_sel[..., :ATT_HEAD_DIM], kv_sel[..., ATT_HEAD_DIM:]
        s = jnp.einsum('bthd,btkd->bthk', qb, k_sel).astype(jnp.float32) * att_scale
        s = jnp.where(valid[:, :, None, :], s, -jnp.inf)
        p = jax.nn.softmax(s, axis=-1).astype(v_sel.dtype)
        return jnp.einsum('bthk,btkd->bthd', p, v_sel)

    o = lax.map(block, (jnp.arange(nb), to_blocks(q), to_blocks(qi), to_blocks(wi)))
    o = jnp.moveaxis(o, 0, 1).reshape(b, L, ATT_HEADS * ATT_HEAD_DIM)
    return o @ w_out

def second_inputs(seed: int = 0) -> dict:
    key = jax.random.key(seed)
    ks = jax.random.split(key, 24)
    f32 = jnp.float32

    def nrm(k, shape, scale):
        return jax.random.normal(k, shape, f32) * scale

    def gain(k, shape):
        return 1.0 + 0.02 * jax.random.normal(k, shape, f32)

    x = nrm(ks[0], (BATCH, SEQ, D_MODEL), 1.0)
    positions = (jax.random.randint(ks[1], (BATCH, 1), 0, 4096, jnp.int32)
                 + jnp.arange(SEQ, dtype=jnp.int32)[None, :])
    dt0 = jnp.exp(jax.random.uniform(ks[10], (N_EVEN, SSD_HEADS), f32, math.log(1e-3), math.log(1e-1)))
    return {
        "x": x,
        "positions": positions,
        "ffn_norm": gain(ks[2], (DEPTH, 2, D_MODEL)),
        "ffn_w_gate": nrm(ks[3], (DEPTH, 2, D_MODEL, D_FF), D_MODEL ** -0.5),
        "ffn_w_up": nrm(ks[4], (DEPTH, 2, D_MODEL, D_FF), D_MODEL ** -0.5),
        "ffn_w_down": nrm(ks[5], (DEPTH, 2, D_FF, D_MODEL), D_FF ** -0.5),
        "mix_norm": gain(ks[6], (DEPTH, D_MODEL)),
        "hy_w_in": nrm(ks[7], (N_EVEN, D_MODEL, HY_IN), D_MODEL ** -0.5),
        "hy_conv_w": nrm(ks[8], (N_EVEN, CONV_K, SSD_CONV_DIM), CONV_K ** -0.5),
        "hy_conv_b": nrm(ks[9], (N_EVEN, SSD_CONV_DIM), 0.01),
        "hy_dt_bias": jnp.log(jnp.expm1(dt0)),
        "hy_a_log": jnp.log(jax.random.uniform(ks[11], (N_EVEN, SSD_HEADS), f32, 1.0, 16.0)),
        "hy_d_skip": gain(ks[12], (N_EVEN, SSD_HEADS)),
        "hy_ssd_norm": gain(ks[13], (N_EVEN, SSD_WIDTH)),
        "hy_igate_bias": nrm(ks[14], (N_EVEN, ML_HEADS), 0.1),
        "hy_fgate_bias": jnp.linspace(3.0, 6.0, ML_HEADS, dtype=f32)[None, :] + nrm(ks[15], (N_EVEN, ML_HEADS), 0.1),
        "hy_mlstm_norm": gain(ks[16], (N_EVEN, ML_WIDTH)),
        "hy_w_out": nrm(ks[17], (N_EVEN, D_MIX, D_MODEL), D_MIX ** -0.5),
        "sa_w_in": nrm(ks[18], (N_ODD, D_MODEL, SA_IN), D_MODEL ** -0.5),
        "sa_q_norm": gain(ks[19], (N_ODD, ATT_HEAD_DIM)),
        "sa_k_norm": gain(ks[20], (N_ODD, ATT_HEAD_DIM)),
        "sa_w_out": nrm(ks[21], (N_ODD, ATT_HEADS * ATT_HEAD_DIM, D_MODEL), (ATT_HEADS * ATT_HEAD_DIM) ** -0.5),
    }

def second_block(x, positions, ffn_norm, ffn_w_gate, ffn_w_up, ffn_w_down, mix_norm,
              hy_w_in, hy_conv_w, hy_conv_b, hy_dt_bias, hy_a_log, hy_d_skip, hy_ssd_norm,
              hy_igate_bias, hy_fgate_bias, hy_mlstm_norm, hy_w_out,
              sa_w_in, sa_q_norm, sa_k_norm, sa_w_out):
    cos, sin = rope_tables(positions, ATT_HEAD_DIM)
    topk = min(TOPK_MAX, x.shape[1] // 4)
    for l in range(DEPTH):
        x = x + 0.5 * swiglu(rms_norm(x, ffn_norm[l, 0]), ffn_w_gate[l, 0], ffn_w_up[l, 0], ffn_w_down[l, 0])
        h = rms_norm(x, mix_norm[l])
        if l % 2 == 0:
            e = l // 2
            m = hybrid_mixer(h, hy_w_in[e], hy_conv_w[e], hy_conv_b[e], hy_dt_bias[e], hy_a_log[e],
                             hy_d_skip[e], hy_ssd_norm[e], hy_igate_bias[e], hy_fgate_bias[e],
                             hy_mlstm_norm[e], hy_w_out[e])
        else:
            o = l // 2
            m = sparse_attention(h, cos, sin, sa_w_in[o], sa_q_norm[o], sa_k_norm[o], sa_w_out[o], topk)
        x = x + m
        x = x + 0.5 * swiglu(rms_norm(x, ffn_norm[l, 1]), ffn_w_gate[l, 1], ffn_w_up[l, 1], ffn_w_down[l, 1])
    return x


def setup_inputs(seed=0):
    out = dict(first_inputs(seed))
    for name, value in second_inputs(seed + 1).items():
        if name != "x":
            out[name + "_2"] = value
    return out


def reference(
    x, c, ada_w, ada_b, norm_g, final_g, lru_in_w, lru_conv_w, lru_conv_b, lru_gate_w,
    lru_gate_b, lru_lambda, lru_out_w, gdn_in_w, gdn_conv_w, gdn_a_log, gdn_dt_bias,
    gdn_onorm_g, gdn_out_w, positions_2, ffn_norm_2, ffn_w_gate_2, ffn_w_up_2, ffn_w_down_2,
    mix_norm_2, hy_w_in_2, hy_conv_w_2, hy_conv_b_2, hy_dt_bias_2, hy_a_log_2, hy_d_skip_2,
    hy_ssd_norm_2, hy_igate_bias_2, hy_fgate_bias_2, hy_mlstm_norm_2, hy_w_out_2, sa_w_in_2,
    sa_q_norm_2, sa_k_norm_2, sa_w_out_2,
):
    x = first_block(
        x, c, ada_w, ada_b, norm_g, final_g, lru_in_w, lru_conv_w, lru_conv_b, lru_gate_w,
        lru_gate_b, lru_lambda, lru_out_w, gdn_in_w, gdn_conv_w, gdn_a_log, gdn_dt_bias,
        gdn_onorm_g, gdn_out_w,
    )
    return second_block(
        x, positions_2, ffn_norm_2, ffn_w_gate_2, ffn_w_up_2, ffn_w_down_2, mix_norm_2,
        hy_w_in_2, hy_conv_w_2, hy_conv_b_2, hy_dt_bias_2, hy_a_log_2, hy_d_skip_2,
        hy_ssd_norm_2, hy_igate_bias_2, hy_fgate_bias_2, hy_mlstm_norm_2, hy_w_out_2, sa_w_in_2,
        sa_q_norm_2, sa_k_norm_2, sa_w_out_2,
    )


_drawn_inputs = setup_inputs


def setup_inputs(seed=0):
    import zlib

    import numpy as np

    out = dict(_drawn_inputs(seed))
    spreads = {}
    factors = {'norm_g': 3.439,
     'lru_conv_b': 3.26,
     'lru_gate_b': 8.0,
     'gdn_onorm_g': 6.56,
     'ffn_norm_2': 2.927,
     'hy_conv_b_2': 5.014,
     'hy_d_skip_2': 6.043,
     'hy_ssd_norm_2': 3.684,
     'hy_igate_bias_2': 200.0,
     'hy_mlstm_norm_2': 5.58,
     'sa_q_norm_2': 22.666,
     'sa_k_norm_2': 8.0}
    for name, (base, spread) in spreads.items():
        noise = np.random.default_rng([zlib.crc32(name.encode()), seed]).standard_normal(out[name].shape)
        drawn = base * np.exp(spread * noise) if base else spread * noise
        out[name] = jnp.asarray(drawn.astype(out[name].dtype))
    for name, factor in factors.items():
        out[name] = (out[name] * factor).astype(out[name].dtype)
    return out
```

```python
import concourse.bass as bass
from concourse import mybir
from contextlib import ExitStack

F32 = mybir.dt.float32
F32R = mybir.dt.float32r
I32 = mybir.dt.int32
ALU = mybir.AluOpType
ACT = mybir.ActivationFunctionType
AX = mybir.AxisListType

P = 128
S = 512
D = 1024
DT = D // P
FF = 2816
FT = FF // P
CH = 128
NC = S // CH
EPS = 1e-6
RG_C = 8.0
NEG = -1.0e30
LEVELS = 7
RING = 4
SLAB_K = 8
TOPK = 128
GH = 8
SH, SP_ = 16, 64
MH = 4
AH, AD = 16, 64
IH = 8

LINEARS = [
    ("ada", 48, 1, 8), ("lru_in", 16, 1, 8), ("lru_out", 8, 1, 8),
    ("gdn_in", 33, 1, 8), ("gdn_out", 8, 1, 8),
    ("up0", 24, 1, 8), ("down0", 8, 2, 6), ("up1", 20, 1, 8), ("down1", 8, 2, 5),
    ("hy_in", 45, 1, 8), ("hy_out", 8, 2, 8),
    ("up2", 24, 1, 8), ("down2", 8, 2, 6), ("up3", 20, 1, 8), ("down3", 8, 2, 5),
    ("up4", 24, 1, 8), ("down4", 8, 2, 6), ("up5", 20, 1, 8), ("down5", 8, 2, 5),
    ("sa_in", 15, 1, 8), ("sa_out", 8, 1, 8),
    ("up6", 24, 1, 8), ("down6", 8, 2, 6), ("up7", 20, 1, 8), ("down7", 8, 2, 5),
]
PART = [12, 10]

VECS = [("norm_g", 16), ("final_g", 8), ("ada_b", 48), ("lru_conv_w", 32), ("lru_conv_b", 8),
        ("lru_gate_b", 16), ("lru_lambda", 8), ("gdn_conv_w", 96), ("gdn_onorm_g", 1),
        ("ffn_norm", 32), ("mix_norm", 16), ("hy_conv_w", 48), ("hy_conv_b", 12),
        ("hy_ssd_norm", 8), ("hy_mlstm_norm", 8), ("hy_d_skip", 8), ("sa_q_norm", 1),
        ("sa_k_norm", 1), ("gdn_a_log", 1), ("gdn_dt_bias", 1), ("hy_dt_bias", 1),
        ("hy_a_log", 1), ("hy_igate_bias", 1), ("hy_fgate_bias", 1), ("c", 8)]
VEC_AT = {}
_n = 0
for _name, _k in VECS:
    VEC_AT[_name] = _n
    _n += _k
VEC_N = _n

CONSTS = [("ident", P), ("ones", P), ("half_ones", P), ("rotate", P), ("keep_upper", P),
          ("keep_lower_strict", P), ("keep_lower", P), ("levels", LEVELS * P),
          ("inv_freq", 1), ("eps", 1), ("one", 1)]
CONST_AT = {}
_n = 0
for _name, _k in CONSTS:
    CONST_AT[_name] = _n
    _n += _k
CONST_N = _n


class Steps:

    def __init__(self, name, sem, table, final):
        self.name, self.sem, self.table, self.final, self.n = name, sem, table, final, 0

    def mark(self, *step):
        self.n += 1
        if step:
            if not self.final:
                assert (self.name, *step) not in self.table, step
            self.table[(self.name, *step)] = self.n
        return 1

    def at(self, *step):
        if self.final:
            return self.table[(self.name, *step)]
        return self.table.get((self.name, *step), 1)


def bass_program(nc, a, out, table, final):
    ctx = ExitStack()
    with ctx:
        def sb(name, shape, dt=F32, stack=ctx):
            return stack.enter_context(nc.sbuf_tensor(name, shape, dt))

        def sem(name):
            return ctx.enter_context(nc.semaphore(name))

        X = sb("X", [P, DT, S])
        H = sb("H", [P, DT, S])
        W = sb("W", [P, RING, SLAB_K * P])
        VEC = sb("VEC", [P, VEC_N])
        CST = sb("CST", [P, CONST_N])
        COND = sb("COND", [P, 48])
        GS = sb("GS", [P, 2, DT])
        RT = sb("RT", [P, S])
        PS = [ctx.enter_context(nc.psum_tensor(f"PS{i}", [P, S], F32)) for i in range(8)]
        LB, MB = PS[0:4], PS[4:8]

        def vec(name, j=0, n=1, rows=P):
            return VEC[0:rows, VEC_AT[name] + j:VEC_AT[name] + j + n]

        def cst(name, rows=P, n=P, at=0):
            return CST[0:rows, CONST_AT[name] + at:CONST_AT[name] + at + n]

        ident, ones, half_ones, rotate = cst("ident"), cst("ones"), cst("half_ones"), cst("rotate")
        eps, one = cst("eps", n=1), cst("one", n=1)

        def heads(col, n, width=CH):
            return col.unsqueeze(2).to_broadcast([col.shape[0], n, width])

        def per_head(tile, n):
            return tile.unsqueeze(1).to_broadcast([tile.shape[0], n, tile.shape[1]])

        slab_in = [sem(f"slab_in{i}") for i in range(RING)]
        tile_done = sem("tile_done")
        x_in, vec_in, cst_in = sem("x_in"), sem("vec_in"), sem("cst_in")
        gate_w_in, pos_in = sem("gate_w_in"), sem("pos_in")
        x_ready = sem("x_ready")
        square_ready = sem("square_ready")
        sum_ready = sem("sum_ready")
        root_ready = sem("root_ready")
        inv_ready = sem("inv_ready")
        h_part = sem("h_part")
        h_ready = sem("h_ready")
        silu_ready = sem("silu_ready")
        prod_ready = sem("prod_ready")
        hid_high = sem("hid_high")
        hid_ready = sem("hid_ready")
        w_high = sem("w_high")
        w_ready = sem("w_ready")
        hh_ready = sem("hh_ready")
        hl_even = sem("hl_even")
        hl_odd = sem("hl_odd")
        out_done = sem("out_done")
        V = Steps("vector", sem("vector_step"), table, final)
        A = Steps("scalar", sem("scalar_step"), table, final)
        T = Steps("tensor", sem("tensor_step"), table, final)
        G = Steps("gpsimd", sem("gpsimd_step"), table, final)

        def chain(eng, steps, ins):
            ins.then_inc(steps.sem, steps.mark())
            eng.wait_ge(steps.sem, steps.n)

        TILE0, SLAB0, last_tile = {}, {}, []
        t = 0
        for name, tiles, per, _ in LINEARS:
            TILE0[name], SLAB0[name] = t, len(last_tile)
            for j in range(tiles):
                last_tile += [t + j] * per
            t += tiles
        ADA = 48
        SPLIT_NO = {}
        for name, tiles, per, _ in LINEARS:
            if name.startswith(("up", "down")):
                for j in range(tiles * per):
                    SPLIT_NO[SLAB0[name] + j] = len(SPLIT_NO)

        def bank_of(tile):
            return (tile - ADA) % 4

        def slab_ap(s, k):
            return W[:, s % RING, 0:k * P].rearrange("p (k f) -> p k f", k=k)

        def load_slab(sp, name, j, k):
            s = SLAB0[name] + j
            if s >= RING:
                sp.wait_ge(*slab_left(s - RING))
            sp.dma_start(W[:, s % RING, 0:k * P], a["w_" + name][j]).then_inc(slab_in[s % RING], 16)

        def slab_left(s):
            return (w_ready, SPLIT_NO[s] + 1) if s in SPLIT_NO else (tile_done, last_tile[s] + 1)

        def sync_program(sp):
            for name, tiles, per, k in LINEARS:
                if name.startswith("up"):
                    for j in range(RING):
                        load_slab(sp, name, j, k)
                    with sp.Fori(1, tiles // RING) as i:
                        for j in range(RING):
                            s = SLAB0[name] + j
                            sp.wait_ge(w_ready, i * RING + (SPLIT_NO[s] - RING + 1))
                            sp.dma_start(W[:, s % RING, 0:k * P],
                                         a["w_" + name][bass.ds(i * RING + j, 1)].rearrange("a p n -> (a p) n")
                                         ).then_inc(slab_in[s % RING], 16)
                else:
                    for j in range(tiles * per):
                        load_slab(sp, name, j, k)
            sp.wait_ge(x_ready, 8 * len(RES))
            sp.dma_start(out, X[:, :, :]).then_inc(out_done, 16)
            sp.wait_ge(out_done, 16)

        def freed(tile):
            name = next(n for n, c, _, _ in LINEARS if TILE0[n] <= tile < TILE0[n] + c)
            return FREED[name](tile - TILE0[name])

        def pe_tile(pe, name, j, rhs, ready=None, outs=None):
            _, _, per, k = next(x for x in LINEARS if x[0] == name)
            tile = TILE0[name] + j
            if outs is None:
                if tile - 4 >= ADA:
                    pe.wait_ge(*freed(tile - 4))
                outs = [(LB[bank_of(tile)][:, :], 0, P)]
            for n, (o, c0, c1) in enumerate(outs):
                for q in range(per):
                    s = SLAB0[name] + j * per + q
                    if n == 0:
                        pe.wait_ge(slab_in[s % RING], 16 * (s // RING + 1))
                    w = slab_ap(s, k)
                    for kk in range(k):
                        if ready is not None and n == 0:
                            ready(q * k + kk)
                        last = nc.tensor.matmul(o, w[:, kk, c0:c1], rhs(q * k + kk),
                                                start=(q == 0 and kk == 0),
                                                stop=(q == per - 1 and kk == k - 1))
            last.then_inc(tile_done, 1)

        def act_norm(act, n, between=None):
            for d in range(DT):
                if n == 0:
                    if d == 0:
                        act.wait_ge(x_in, 16)
                else:
                    act.wait_ge(x_ready, DT * NORM_AFTER[n] + d + 1)
                if n == 8 and d == 0:
                    act.wait_ge(tile_done, last_tile[SLAB0["up6"] - 1] + 1)
                nc.scalar.activation(H[:, d, :], X[:, d, :], ACT.Square).then_inc(square_ready, 1)
            if between is not None:
                between()
            act.wait_ge(sum_ready, n + 1)
            nc.scalar.activation(RT[:, :], MB[0][:, :], ACT.Sqrt, bias=eps, scale=1.0 / D
                                 ).then_inc(root_ready, 1)

        def pe_norm(pe, n):
            for d in range(DT):
                pe.wait_ge(square_ready, DT * n + d + 1)
                last = nc.tensor.matmul(MB[0][:, :], ones, H[:, d, :], start=d == 0, stop=d == DT - 1)
            last.then_inc(sum_ready, 1)

        def dve_norm(dve, n, gain, shift=None, dst=None, sig=None):
            dve.wait_ge(root_ready, n + 1)
            nc.vector.reciprocal(RT[:, :], RT[:, :]).then_inc(inv_ready, 1)
            dve.wait_ge(inv_ready, n + 1)
            dst = dst or (lambda d: H[:, d, :])
            for d in range(DT):
                ins = nc.vector.scalar_tensor_tensor(dst(d), X[:, d, :], gain(d), RT[:, :],
                                                     ALU.mult, ALU.mult)
                if shift is None:
                    ins.then_inc(sig or h_ready, 1)
                else:
                    ins.then_inc(h_part, 1)
            if shift is not None:
                for d in range(DT):
                    dve.wait_ge(h_part, DT * n + d + 1)
                    nc.vector.tensor_scalar(dst(d), dst(d), shift(d), None, ALU.add
                                            ).then_inc(h_ready, 1)

        H_NORM = {0: 0, 1: 1, 3: 2, 4: 3, 5: 4, 6: 5, 7: 6, 8: 7}

        def h_wait(pe, n):
            base = DT * H_NORM[n]
            return lambda k: pe.wait_ge(h_ready, base + k + 1)

        def h_tile(k):
            return H[:, k, :]

        ada_done = sem("ada_done")
        act_c = sem("act_c")
        cond_ready = sem("cond_ready")

        def pe_ada(pe):
            pe.wait_ge(act_c, 1)
            for j in range(48):
                pe_tile(pe, "ada", j, lambda k: CA[:, k:k + 1], outs=[(MB[1][:, j:j + 1], 0, P)])

        def act_ada(act):
            act.wait_ge(vec_in, 16)
            act.wait_ge(cst_in, 16)
            nc.scalar.activation(CA[:, :], vec("c", 0, DT), ACT.Silu).then_inc(act_c, 1)

        def dve_ada(dve):
            dve.wait_ge(vec_in, 16)
            dve.wait_ge(tile_done, 48)
            nc.vector.tensor_tensor(COND[:, :], MB[1][:, 0:48], vec("ada_b", 0, 48), ALU.add
                                    ).then_inc(cond_ready, 1)
            dve.wait_ge(cond_ready, 1)
            for l in range(2):
                nc.vector.scalar_tensor_tensor(GS[:, l, :], COND[:, 24 * l + 8:24 * l + 16], 1.0,
                                               vec("norm_g", 8 * l, 8), ALU.add, ALU.mult
                                               ).then_inc(cond_ready, 1)
            dve.wait_ge(cond_ready, 3)

        CA = sb("CA", [P, DT])

        lru = ExitStack()
        XP = sb("XP", [P, 2, S + 3])
        CV = sb("CV", [P, 2, S])
        SQ = sb("SQ", [P, 2, S])
        RN = sb("RN", [P, 2, S])
        LXB = sb("LXB", [P, DT, S], stack=lru)
        LR = sb("LR", [P, DT, S], stack=lru)
        LI_ = sb("LI", [P, DT, S], stack=lru)
        LA = sb("LA", [P, DT, S], stack=lru)
        LM = sb("LM", [P, DT, S], stack=lru)
        LZ = sb("LZ", [P, DT, S], stack=lru)
        GW = sb("GW", [P, 16, P], stack=lru)
        LAM = sb("LAM", [P, DT], stack=lru)
        LAT = sb("LAT", [P, 2, DT], stack=lru)
        lru.close()

        def gate_at(j):
            return j // 2, j % 2

        def pe_lru(pe):
            for j in range(10):
                pe_tile(pe, "lru_in", j, h_tile, h_wait(pe, 0) if j == 0 else None)
            pe.wait_ge(gate_w_in, 16)
            for j in range(16):
                d, g = gate_at(j)
                pe.wait_ge(V.sem, V.at("lru conv", d))
                if j >= 4:
                    pe.wait_ge(A.sem, A.at("lru gate", j - 4))
                nc.tensor.matmul(MB[j % 4][:, :], GW[:, g * 8 + d, :], LXB[:, d, :],
                                 start=True, stop=True).then_inc(T.sem, T.mark("lru gate", j))
            for j in range(10, 16):
                pe_tile(pe, "lru_in", j, h_tile)
            for j in range(8):
                pe_tile(pe, "lru_out", j, lambda k: LXB[:, k, :],
                        (lambda k: pe.wait_ge(V.sem, V.at("lru y", k))) if j == 0 else None)

        def arrived(eng, name, j):
            tile = TILE0[name] + j
            eng.wait_ge(tile_done, tile + 1)
            return LB[bank_of(tile)]

        def act_lru(act):
            chain(act, A, nc.scalar.activation(LAT[:, 0, :], vec("lru_lambda", 0, 8), ACT.Abs))
            chain(act, A, nc.scalar.activation(LAT[:, 0, :], LAT[:, 0, :], ACT.Exp, scale=-1.0))
            nc.scalar.activation(LAT[:, 0, :], LAT[:, 0, :], ACT.Ln, bias=one
                                 ).then_inc(A.sem, A.mark("lambda ln"))
            act.wait_ge(V.sem, V.at("pads"))
            for j in range(8):
                bank = arrived(act, "lru_in", j)
                if j >= 2:
                    act.wait_ge(V.sem, V.at("lru conv", j - 2))
                nc.scalar.activation(XP[:, j % 2, 3:], bank[:, :], ACT.Copy).then_inc(A.sem, A.mark("lru xp", j))
            for j in range(8, 10):
                bank = arrived(act, "lru_in", j)
                nc.scalar.activation(LZ[:, j - 8, :], bank[:, :], ACT.Silu).then_inc(A.sem, A.mark("lru silu", j - 8))
            for j in range(16):
                d, g = gate_at(j)
                act.wait_ge(T.sem, T.at("lru gate", j))
                nc.scalar.activation((LI_ if g else LR)[:, d, :], MB[j % 4][:, :], ACT.Sigmoid,
                                     bias=vec("lru_gate_b", 8 * g + d)
                                     ).then_inc(A.sem, A.mark("lru gate", j))
            act.wait_ge(V.sem, V.at("lambda"))
            act.wait_ge(A.sem, A.at("lru gate", 15))
            for d in range(8):
                nc.scalar.activation(LA[:, d, :], LR[:, d, :], ACT.Exp, scale=LAM[:, d:d + 1]
                                     ).then_inc(A.sem, A.mark("lru a", d))
                nc.scalar.activation(LR[:, d, :], LR[:, d, :], ACT.Tanh, scale=LAM[:, d:d + 1]
                                     ).then_inc(A.sem, A.mark("lru tanh", d))
            for d in range(8):
                act.wait_ge(A.sem, A.at("lru a", d))
                nc.scalar.activation(LM[:, d, :], LA[:, d, :], ACT.Square).then_inc(A.sem, A.mark("lru a2", d))
            for d in range(8):
                act.wait_ge(V.sem, V.at("lru m2", d))
                nc.scalar.activation(LM[:, d, :], LM[:, d, :], ACT.Sqrt, scale=-1.0
                                     ).then_inc(A.sem, A.mark("lru mult", d))
            for j in range(10, 16):
                bank = arrived(act, "lru_in", j)
                nc.scalar.activation(LZ[:, j - 8, :], bank[:, :], ACT.Silu
                                     ).then_inc(A.sem, A.mark("lru silu", j - 8))

        def conv(dve, xp, dst, w, j, stride, bias, step):
            first = nc.vector.tensor_scalar(dst, xp[:, 0:S], vec(w, j), bias, ALU.mult,
                                            ALU.bypass if bias is None else ALU.add) \
                if bias is not None else nc.vector.tensor_scalar(dst, xp[:, 0:S], vec(w, j), None, ALU.mult)
            chain(dve, V, first)
            for t in range(1, 4):
                ins = nc.vector.scalar_tensor_tensor(dst, xp[:, t:t + S], vec(w, t * stride + j), dst,
                                                     ALU.mult, ALU.add)
                if t < 3:
                    chain(dve, V, ins)
                else:
                    ins.then_inc(V.sem, V.mark(*step))

        def dve_lru(dve):
            nc.vector.memset(XP[:, :, 0:3], 0.0).then_inc(V.sem, V.mark("pads"))
            dve.wait_ge(A.sem, A.at("lambda ln"))
            chain(dve, V, nc.vector.tensor_scalar(LAT[:, 1, :], vec("lru_lambda", 0, 8), -1.0, 0.0,
                                                  ALU.mult, ALU.max))
            chain(dve, V, nc.vector.tensor_tensor(LAT[:, 1, :], LAT[:, 1, :], LAT[:, 0, :], ALU.add))
            nc.vector.tensor_scalar(LAM[:, :], LAT[:, 1, :], -RG_C, None, ALU.mult
                                    ).then_inc(V.sem, V.mark("lambda"))
            for j in range(8):
                dve.wait_ge(A.sem, A.at("lru xp", j))
                conv(dve, XP[:, j % 2, :], LXB[:, j, :], "lru_conv_w", j, 8, vec("lru_conv_b", j),
                     ("lru conv", j))
            for d in range(8):
                dve.wait_ge(A.sem, A.at("lru gate", 2 * d + 1))
                dve.wait_ge(V.sem, V.at("lru conv", d))
                nc.vector.tensor_tensor(LI_[:, d, :], LI_[:, d, :], LXB[:, d, :], ALU.mult
                                        ).then_inc(V.sem, V.mark("lru ix", d))
            for d in range(8):
                dve.wait_ge(A.sem, A.at("lru a2", d))
                nc.vector.scalar_tensor_tensor(LM[:, d, :], LM[:, d, :], 1.0, LR[:, d, :],
                                               ALU.add, ALU.mult).then_inc(V.sem, V.mark("lru m2", d))
            for d in range(8):
                dve.wait_ge(A.sem, A.at("lru mult", d))
                dve.wait_ge(V.sem, V.at("lru ix", d))
                chain(dve, V, nc.vector.tensor_tensor(LM[:, d, :], LM[:, d, :], LI_[:, d, :], ALU.mult))
                nc.vector.tensor_tensor_scan(LXB[:, d, :], LA[:, d, :], LM[:, d, :], 0.0,
                                             ALU.mult, ALU.add).then_inc(V.sem, V.mark("lru h", d))
            for d in range(8):
                dve.wait_ge(A.sem, A.at("lru silu", d))
                dve.wait_ge(V.sem, V.at("lru h", d))
                nc.vector.tensor_tensor(LXB[:, d, :], LXB[:, d, :], LZ[:, d, :], ALU.mult
                                        ).then_inc(V.sem, V.mark("lru y", d))
            residual(dve, "lru_out", lambda d: COND[:, 16 + d:17 + d])

        def residual(dve, name, gate):
            for d in range(8):
                bank = arrived(dve, name, d)
                nc.vector.scalar_tensor_tensor(X[:, d, :], bank[:, :], gate(d), X[:, d, :],
                                               ALU.mult, ALU.add).then_inc(x_ready, 1)

        RES = {n: i for i, n in enumerate(
            ["lru_out", "gdn_out", "final", "down0", "down1", "hy_out", "down2", "down3", "down4", "down5",
             "sa_out", "down6", "down7"])}
        NORM_AFTER = {1: RES["lru_out"], 2: RES["gdn_out"], 3: RES["final"], 4: RES["down1"], 5: RES["hy_out"],
                      6: RES["down3"], 7: RES["down5"], 8: RES["sa_out"]}

        ffn = ExitStack()
        HH = sb("HH", [P, DT, S], F32R, stack=ffn)
        HL = sb("HL", [P, DT, S], F32R, stack=ffn)
        DH = sb("DH", [P, PART[0], S], F32R, stack=ffn)
        DL = sb("DL", [P, PART[0], S], F32R, stack=ffn)
        WH = sb("WH", [P, RING, SLAB_K * P], F32R, stack=ffn)
        WL = sb("WL", [P, RING, SLAB_K * P], F32R, stack=ffn)
        FGT = sb("FGT", [P, 2, S], stack=ffn)
        PRD = sb("PRD", [P, 2, S], stack=ffn)
        ffn.close()
        HID0 = [FT * (p // 2) + PART[0] * (p % 2) for p in range(8)]

        def split_high(act, s, k):
            if s >= RING:
                act.wait_ge(tile_done, last_tile[s - RING] + 1)
            act.wait_ge(slab_in[s % RING], 16 * (s // RING + 1))
            nc.scalar.activation(WH[:, s % RING, 0:k * P], W[:, s % RING, 0:k * P], ACT.Copy
                                 ).then_inc(w_high, 1)

        def split_low(pool, s, k):
            pool.wait_ge(w_high, SPLIT_NO[s] + 1)
            nc.gpsimd.tensor_tensor(WL[:, s % RING, 0:k * P], W[:, s % RING, 0:k * P],
                                    WH[:, s % RING, 0:k * P].bitcast(F32), ALU.subtract).then_inc(w_ready, 1)

        def three(o, wh, wl, xh, xl, first, last):
            nc.tensor.matmul(o, wh, xh, start=first, stop=False)
            nc.tensor.matmul(o, wh, xl, start=False, stop=False)
            return nc.tensor.matmul(o, wl, xh, start=False, stop=last)

        def pe_up_tile(pe, name, j, wait_h):
            s = SLAB0[name] + j
            for k in range(DT):
                if wait_h:
                    pe.wait_ge(*((hl_odd, 4 * wait_h - 3 + k // 2) if k % 2 else (hl_even, 4 * wait_h - 3 + k // 2)))
                c = slice(k * P, (k + 1) * P)
                last = three(LB[bank_of(TILE0[name] + j)][:, :], WH[:, s % RING, c], WL[:, s % RING, c],
                             HH[:, k, :], HL[:, k, :], k == 0, k == DT - 1)
            last.then_inc(tile_done, 1)

        def pe_ffn(pe, f):
            for p in (2 * f, 2 * f + 1):
                name = f"up{p}"
                for j in range(RING):
                    pe.wait_ge(*freed(TILE0[name] + j - 4))
                    pe.wait_ge(w_ready, SPLIT_NO[SLAB0[name] + j] + 1)
                    pe_up_tile(pe, name, j, f + 1 if p % 2 == 0 and j == 0 else 0)
                with pe.Fori(1, 2 * PART[p % 2] // RING) as i:
                    for j in range(RING):
                        pe.wait_ge(prod_ready if j % 2 else silu_ready, i * 2 + (HID0[p] + j // 2 - 1))
                        pe.wait_ge(w_ready, i * RING + (SPLIT_NO[SLAB0[name] + j] + 1))
                        pe_up_tile(pe, name, j, 0)
                name = f"down{p}"
                for j in range(8):
                    tile = TILE0[name] + j
                    pe.wait_ge(*freed(tile - 4))
                    for q in range(2):
                        n = PART[p % 2] // 2
                        s = SLAB0[name] + 2 * j + q
                        pe.wait_ge(w_ready, SPLIT_NO[s] + 1)
                        for kk in range(n):
                            k = q * n + kk
                            if j == 0:
                                pe.wait_ge(hid_ready, HID0[p] + k + 1)
                            c = slice(kk * P, (kk + 1) * P)
                            last = three(LB[bank_of(tile)][:, :], WH[:, s % RING, c], WL[:, s % RING, c],
                                         DH[:, k, :], DL[:, k, :], k == 0, k == 2 * n - 1)
                    last.then_inc(tile_done, 1)

        def act_ffn_high(act, n, f):
            act.wait_ge(x_ready, DT * NORM_AFTER[n] + DT)
            for j in range(RING):
                split_high(act, SLAB0[f"up{2 * f}"] + j, DT)

        def act_ffn(act, f):
            for d in range(DT):
                act.wait_ge(h_ready, DT * H_NORM[FFN_NORM[f]] + d + 1)
                nc.scalar.activation(HH[:, d, :], H[:, d, :], ACT.Copy).then_inc(hh_ready, 1)
            for p in (2 * f, 2 * f + 1):
                name = f"up{p}"
                k_down = PART[p % 2] // 2

                def gate(m):
                    if m >= 2:
                        act.wait_ge(prod_ready, HID0[p] + m - 1)
                    bank = arrived(act, name, 2 * m)
                    nc.scalar.activation(FGT[:, m % 2, :], bank[:, :], ACT.Silu).then_inc(silu_ready, 1)

                for m in range(2):
                    gate(m)
                    for j in range(2):
                        split_high(act, SLAB0[name] + 2 * m + j + RING, DT)
                with act.Fori(1, PART[p % 2] // 2 - 1) as i:
                    for m in range(2):
                        act.wait_ge(prod_ready, i * 2 + (HID0[p] + m - 1))
                        act.wait_ge(tile_done, i * 4 + (TILE0[name] + 2 * m + 1))
                        nc.scalar.activation(FGT[:, m, :], LB[bank_of(TILE0[name] + 2 * m)][:, :], ACT.Silu
                                             ).then_inc(silu_ready, 1)
                        for j in range(2):
                            s = SLAB0[name] + 2 * m + j
                            act.wait_ge(tile_done, i * 4 + (TILE0[name] + 2 * m + j + 1))
                            act.wait_ge(slab_in[s % RING], i * 16 + 16 * (s // RING + 2))
                            nc.scalar.activation(WH[:, s % RING, :], W[:, s % RING, :], ACT.Copy
                                                 ).then_inc(w_high, 1)
                for m in range(2):
                    gate(PART[p % 2] - 2 + m)
                    for j in range(2):
                        split_high(act, SLAB0[f"down{p}"] + 2 * m + j, k_down)
                for j in range(4, 16):
                    split_high(act, SLAB0[f"down{p}"] + j, k_down)
                if p % 2 == 0:
                    for j in range(RING):
                        split_high(act, SLAB0[f"up{p + 1}"] + j, DT)

        def pool_ffn(pool, f):
            for j in range(RING):
                split_low(pool, SLAB0[f"up{2 * f}"] + j, DT)
            for d in range(1, DT, 2):
                pool.wait_ge(hh_ready, DT * f + d + 1)
                nc.gpsimd.tensor_tensor(HL[:, d, :], H[:, d, :], HH[:, d, :].bitcast(F32), ALU.subtract
                                        ).then_inc(hl_odd, 1)
            for p in (2 * f, 2 * f + 1):
                name = f"up{p}"
                with pool.Fori(1, 2 * PART[p % 2] // RING) as i:
                    for j in range(RING):
                        s = SLAB0[name] + j
                        pool.wait_ge(w_high, i * RING + (SPLIT_NO[s] + 1))
                        nc.gpsimd.tensor_tensor(WL[:, s % RING, :], W[:, s % RING, :],
                                                WH[:, s % RING, :].bitcast(F32), ALU.subtract
                                                ).then_inc(w_ready, 1)
                for j in range(16):
                    split_low(pool, SLAB0[f"down{p}"] + j, PART[p % 2] // 2)
                if p % 2 == 0:
                    for j in range(RING):
                        split_low(pool, SLAB0[f"up{p + 1}"] + j, DT)

        def dve_ffn(dve, f):
            for d in range(0, DT, 2):
                dve.wait_ge(hh_ready, DT * f + d + 1)
                nc.vector.tensor_tensor(HL[:, d, :], H[:, d, :], HH[:, d, :].bitcast(F32), ALU.subtract
                                        ).then_inc(hl_even, 1)
            for p in (2 * f, 2 * f + 1):
                name = f"up{p}"
                with dve.Fori(0, PART[p % 2] // 2) as i:
                    for m in range(2):
                        def hid(tensor):
                            return tensor[:, bass.ds(i * 2 + m, 1), :].rearrange("p a s -> p (a s)")

                        dve.wait_ge(silu_ready, i * 2 + (HID0[p] + m + 1))
                        dve.wait_ge(tile_done, i * 4 + (TILE0[name] + 2 * m + 2))
                        nc.vector.tensor_tensor(PRD[:, m, :], FGT[:, m, :], LB[bank_of(TILE0[name] + 2 * m + 1)][:, :],
                                                ALU.mult).then_inc(prod_ready, 1)
                        dve.wait_ge(prod_ready, i * 2 + (HID0[p] + m + 1))
                        nc.vector.tensor_copy(hid(DH), PRD[:, m, :]).then_inc(hid_high, 1)
                        dve.wait_ge(hid_high, i * 2 + (HID0[p] + m + 1))
                        nc.vector.tensor_tensor(hid(DL), PRD[:, m, :], hid(DH).bitcast(F32), ALU.subtract
                                                ).then_inc(hid_ready, 1)
                residual(dve, f"down{p}", lambda d: 0.5)

        FFN_NORM = [3, 5, 6, 8]

        def up_freed(p):
            return lambda j: (prod_ready if j % 2 else silu_ready, HID0[p] + j // 2 + 1)

        def res_freed(name):
            return lambda j: (x_ready, 8 * RES[name] + j + 1)

        FREED = {
            "lru_in": lambda j: (A.sem, A.at("lru xp", j) if j < 8 else A.at("lru silu", j - 8)),
            **{f"up{p}": up_freed(p) for p in range(8)},
            **{n: res_freed(n) for n in RES if n != "final"},
        }

        gdn = ExitStack()
        GK = sb("GK", [P, GH, S], stack=gdn)
        GQ = sb("GQ", [P, GH, S], stack=gdn)
        GV = sb("GV", [P, GH, S], stack=gdn)
        GZ = sb("GZ", [P, GH, S], stack=gdn)
        GROW = sb("GROW", [GH, 4, S], stack=gdn)
        GBETA = sb("GBETA", [GH, 2, S], stack=gdn)
        GCOL = sb("GCOL", [P, 3, NC, GH], stack=gdn)
        GSEL = sb("GSEL", [GH, NC, GH], stack=gdn)
        GEL = sb("GEL", [P, NC, GH], stack=gdn)
        GEA = sb("GEA", [GH, 1], stack=gdn)
        gt = [{n: sb(f"G{n}{g}", [P, 4, P], stack=gdn)
               for n in ("TMP", "AT", "AM", "L", "T", "U", "Y", "KT", "QD", "KD", "VB")} for g in range(2)]
        GS_ = sb("GSTATE", [P, GH, P], stack=gdn)
        GVN = [H[:, g, :].rearrange("p (h t) -> p h t", h=4) for g in range(2)]
        gdn.close()
        GO = GQ
        GB = [[MB[b] for b in range(4)], [LB[b] for b in range(4)]]

        def four(bank):
            return bank[:, :].rearrange("p (h t) -> p h t", h=4)

        def fm(tensor, c, g):
            return tensor[:, 4 * g:4 * g + 4, c * CH:(c + 1) * CH]

        GNORM = [(GK, h) for h in range(8)] + [(GQ, h) for h in range(8)]

        def gconv_dst(j):
            return (GK, GQ, GV)[j // 8][:, j % 8, :]

        def pe_gdn(pe):
            ready = h_wait(pe, 1)
            pe_tile(pe, "gdn_in", 0, h_tile, ready,
                    outs=[(MB[1][0:GH, :], 0, GH), (MB[2][0:GH, :], GH, 2 * GH)])
            for j in range(1, 19):
                pe_tile(pe, "gdn_in", j, h_tile)
            for j in range(16):
                pe.wait_ge(A.sem, A.at("gdn sq", j))
                if j < 2:
                    pe.wait_ge(A.sem, A.at("beta"))
                else:
                    pe.wait_ge(A.sem, A.at("gdn root", j - 2))
                nc.tensor.matmul(MB[j % 2 + 2][:, :], ones, SQ[:, j % 2, :], start=True, stop=True
                                 ).then_inc(T.sem, T.mark("gdn sum", j))
            for j in range(19, 33):
                pe_tile(pe, "gdn_in", j, h_tile)
            pe.wait_ge(A.sem, A.at("gdn ed"))
            pe.wait_ge(V.sem, V.at("gdn sel"))
            rows = [GROW[:, 1, :], GBETA[:, 0, :], GROW[:, 3, :]]
            for n, row in enumerate(rows):
                for c in range(NC):
                    nc.tensor.matmul(MB[1][:, (n * NC + c) * GH:(n * NC + c + 1) * GH],
                                     row[:, c * CH:(c + 1) * CH], ident[0:GH, 0:GH], start=True, stop=True)
            nc.tensor.matmul(MB[1][:, 96:128], ones[0:GH, :], GSEL[:, :, :].rearrange("p c h -> p (c h)"),
                             start=True, stop=True).then_inc(T.sem, T.mark("gdn cols"))
            for g in range(2):
                pe.wait_ge(A.sem, A.at("gdn z", 7))
                pe.wait_ge(V.sem, V.at("gdn qk", 15))
            pe.wait_ge(V.sem, V.at("gdn cols"))
            for c in range(NC):
                for g in range(2):
                    B = GB[g]
                    if c:
                        pe.wait_ge(A.sem, A.at("gdn vn", c - 1, g))
                        pe.wait_ge(A.sem, A.at("gdn o", c - 1, g))
                        pe.wait_ge(V.sem, V.at("gdn state", c - 1, g))
                    for n, row in ((0, GROW[:, 1, :]), (1, GROW[:, 2, :]), (2, GBETA[:, 1, :])):
                        for h in range(4):
                            last = nc.tensor.matmul(
                                B[n][:, h * P:(h + 1) * P],
                                ident[0:GH, 4 * g + h:4 * g + h + 1].to_broadcast([GH, P]),
                                row[:, c * CH:(c + 1) * CH], start=True, stop=True)
                    last.then_inc(T.sem, T.mark("gdn rows", c, g))
                    for h in range(4):
                        kc = GK[:, 4 * g + h, c * CH:(c + 1) * CH]
                        last = nc.tensor.matmul(B[3][:, h * P:(h + 1) * P], kc, kc, start=True, stop=True)
                    last.then_inc(T.sem, T.mark("gdn kk", c, g))
                for g in range(2):
                    B = GB[g]
                    pe.wait_ge(V.sem, V.at("gdn tmp", c, g))
                    for h in range(4):
                        last = nc.tensor.matmul(B[0][:, h * P:(h + 1) * P],
                                                GK[:, 4 * g + h, c * CH:(c + 1) * CH],
                                                GQ[:, 4 * g + h, c * CH:(c + 1) * CH], start=True, stop=True)
                    last.then_inc(T.sem, T.mark("gdn qk", c, g))
                    pe.wait_ge(V.sem, V.at("gdn kt", c, g))
                    for n, src in ((1, GK), (2, GV)):
                        for h in range(4):
                            last = nc.tensor.transpose(B[n][:, h * P:(h + 1) * P],
                                                       src[:, 4 * g + h, c * CH:(c + 1) * CH], ident)
                    last.then_inc(T.sem, T.mark("gdn tok", c, g))
                for l in range(LEVELS):
                    for g in range(2):
                        B, b = GB[g], gt[g]
                        pe.wait_ge(G.sem, G.at("gdn l", c, g, l))
                        if l == 0:
                            pe.wait_ge(V.sem, V.at("gdn at", c, g))
                        else:
                            pe.wait_ge(V.sem, V.at("gdn tu", c, g, l - 1))
                        for h in range(4):
                            last = nc.tensor.matmul(B[0][:, h * P:(h + 1) * P], b["L"][:, h, :],
                                                    ident if l == 0 else b["U"][:, h, :], start=True, stop=True)
                        last.then_inc(T.sem, T.mark("gdn y", c, g, l))
                    for g in range(2):
                        B, b = GB[g], gt[g]
                        pe.wait_ge(A.sem, A.at("gdn y", c, g, l))
                        if l == 0:
                            pe.wait_ge(V.sem, V.at("gdn vb", c, g))
                        for h in range(4):
                            last = nc.tensor.matmul(B[1][:, h * P:(h + 1) * P], ident if l == 0 else b["T"][:, h, :],
                                                    b["Y"][:, h, :], start=True, stop=True)
                        for h in range(4 if l < LEVELS - 1 else 0):
                            last = nc.tensor.matmul(B[2][:, h * P:(h + 1) * P], b["Y"][:, h, :],
                                                    ident if l == 0 else b["T"][:, h, :], start=True, stop=True)
                        last.then_inc(T.sem, T.mark("gdn uy", c, g, l))
                if c:
                    for g in range(2):
                        b = gt[g]
                        pe.wait_ge(V.sem, V.at("gdn am", c, g))
                        for h in range(4):
                            last = nc.tensor.matmul(GB[g][3][:, h * P:(h + 1) * P], b["KT"][:, h, :],
                                                    GS_[:, 4 * g + h, :], start=True, stop=True)
                        last.then_inc(T.sem, T.mark("gdn ks", c, g))
                for g in range(2):
                    b = gt[g]
                    pe.wait_ge(V.sem, V.at("gdn tu", c, g, LEVELS - 1))
                    pe.wait_ge(V.sem, V.at("gdn r", c, g) if c else V.at("gdn vb", c, g))
                    for h in range(4):
                        last = nc.tensor.matmul(GB[g][0][:, h * P:(h + 1) * P], b["U"][:, h, :],
                                                b["VB"][:, h, :], start=True, stop=True)
                    last.then_inc(T.sem, T.mark("gdn vn", c, g))
                for g in range(2):
                    b = gt[g]
                    pe.wait_ge(A.sem, A.at("gdn vn", c, g))
                    for h in range(4):
                        if c:
                            nc.tensor.matmul(GB[g][1][:, h * P:(h + 1) * P], GS_[:, 4 * g + h, :],
                                             b["QD"][:, h, :], start=True, stop=False)
                        last = nc.tensor.matmul(GB[g][1][:, h * P:(h + 1) * P], GVN[g][:, h, :],
                                                b["AT"][:, h, :], start=not c, stop=True)
                    last.then_inc(T.sem, T.mark("gdn o", c, g))
                    for h in range(4):
                        last = nc.tensor.matmul(GB[g][2][:, h * P:(h + 1) * P], b["KD"][:, h, :],
                                                GVN[g][:, h, :], start=True, stop=True)
                    last.then_inc(T.sem, T.mark("gdn su", c, g))
            for h in range(GH):
                pe.wait_ge(A.sem, A.at("gdn osq", h))
                if h >= 2:
                    pe.wait_ge(A.sem, A.at("gdn oroot", h - 2))
                nc.tensor.matmul(MB[h % 2][:, :], ones, SQ[:, h % 2, :], start=True, stop=True
                                 ).then_inc(T.sem, T.mark("gdn osum", h))
            for j in range(8):
                pe_tile(pe, "gdn_out", j, lambda k: GO[:, k, :],
                        (lambda k: pe.wait_ge(V.sem, V.at("gdn y", k))) if j == 0 else None)

        def act_gdn(act):
            nc.scalar.activation(GEA[:, :], vec("gdn_a_log", rows=GH), ACT.Exp).then_inc(A.sem, A.mark("gdn ea"))
            act.wait_ge(tile_done, TILE0["gdn_in"] + 1)
            nc.scalar.activation(GBETA[:, 0, :], MB[2][0:GH, :], ACT.Sigmoid).then_inc(A.sem, A.mark("beta"))
            act.wait_ge(V.sem, V.at("gdn u"))
            chain(act, A, nc.scalar.activation(GROW[:, 1, :], GROW[:, 0, :], ACT.Abs))
            chain(act, A, nc.scalar.activation(GROW[:, 1, :], GROW[:, 1, :], ACT.Exp, scale=-1.0))
            nc.scalar.activation(GROW[:, 1, :], GROW[:, 1, :], ACT.Ln, bias=one[0:GH, :]
                                 ).then_inc(A.sem, A.mark("gdn ln"))

            def copy_in(j):
                bank = arrived(act, "gdn_in", j + 1)
                if j >= 2:
                    act.wait_ge(V.sem, V.at("gdn conv", j - 2))
                nc.scalar.activation(XP[:, j % 2, 3:], bank[:, :], ACT.Copy).then_inc(A.sem, A.mark("gdn xp", j))

            def silu(j):
                act.wait_ge(V.sem, V.at("gdn conv", j))
                nc.scalar.activation(gconv_dst(j), CV[:, j % 2, :], ACT.Silu).then_inc(A.sem, A.mark("gdn silu", j))

            copy_in(0)
            for j in range(1, 16):
                copy_in(j)
                silu(j - 1)
            silu(15)
            for j in range(16):
                tensor, h = GNORM[j]
                act.wait_ge(A.sem, A.at("gdn silu", j))
                if j >= 2:
                    act.wait_ge(T.sem, T.at("gdn sum", j - 2))
                nc.scalar.activation(SQ[:, j % 2, :], tensor[:, h, :], ACT.Square).then_inc(A.sem, A.mark("gdn sq", j))
                if j:
                    root(act, j - 1)
            root(act, 15)
            for j in range(16, 24):
                copy_in(j)
                if j > 16:
                    silu(j - 1)
            silu(23)
            for j in range(8):
                bank = arrived(act, "gdn_in", 25 + j)
                nc.scalar.activation(GZ[:, j, :], bank[:, :], ACT.Silu).then_inc(A.sem, A.mark("gdn z", j))
            act.wait_ge(V.sem, V.at("gdn cum"))
            nc.scalar.activation(GROW[:, 2, :], GROW[:, 1, :], ACT.Exp).then_inc(A.sem, A.mark("gdn eg"))
            for c in range(NC):
                nc.scalar.activation(GROW[:, 3, c * CH:(c + 1) * CH], GROW[:, 1, c * CH:(c + 1) * CH], ACT.Exp,
                                     bias=GROW[:, 1, (c + 1) * CH - 1:(c + 1) * CH], scale=-1.0
                                     ).then_inc(A.sem, A.mark("gdn ed") if c == NC - 1 else A.mark())
            for c in range(NC):
                for g in range(2):
                    b = gt[g]
                    for n in ("AT", "AM"):
                        act.wait_ge(G.sem, G.at("gdn at", c, g)) if n == "AT" else \
                            act.wait_ge(V.sem, V.at("gdn amask", c, g))
                        nc.scalar.activation(b[n][:, :, :], b[n][:, :, :], ACT.Exp
                                             ).then_inc(A.sem, A.mark("gdn exp" + n, c, g))
                for l in range(LEVELS):
                    for g in range(2):
                        act.wait_ge(T.sem, T.at("gdn y", c, g, l))
                        nc.scalar.activation(gt[g]["Y"][:, :, :], four(GB[g][0]), ACT.Copy
                                             ).then_inc(A.sem, A.mark("gdn y", c, g, l))
                for g in range(2):
                    act.wait_ge(T.sem, T.at("gdn vn", c, g))
                    nc.scalar.activation(GVN[g], four(GB[g][0]), ACT.Copy).then_inc(A.sem, A.mark("gdn vn", c, g))
                for g in range(2):
                    act.wait_ge(T.sem, T.at("gdn o", c, g))
                    nc.scalar.activation(fm(GO, c, g), four(GB[g][1]), ACT.Copy).then_inc(A.sem, A.mark("gdn o", c, g))
            act.wait_ge(A.sem, A.at("gdn o", NC - 1, 1))
            for h in range(GH):
                if h >= 2:
                    act.wait_ge(T.sem, T.at("gdn osum", h - 2))
                nc.scalar.activation(SQ[:, h % 2, :], GO[:, h, :], ACT.Square).then_inc(A.sem, A.mark("gdn osq", h))
                if h:
                    oroot(act, h - 1)
            oroot(act, 7)

        def root(act, j):
            act.wait_ge(T.sem, T.at("gdn sum", j))
            if j >= 2:
                act.wait_ge(V.sem, V.at("gdn qk", j - 2))
            nc.scalar.activation(RN[:, j % 2, :], MB[j % 2 + 2][:, :], ACT.Sqrt, bias=eps
                                 ).then_inc(A.sem, A.mark("gdn root", j))

        def oroot(act, h):
            act.wait_ge(T.sem, T.at("gdn osum", h))
            if h >= 2:
                act.wait_ge(V.sem, V.at("gdn y", h - 2))
            nc.scalar.activation(RN[:, h % 2, :], MB[h % 2][:, :], ACT.Sqrt, bias=eps, scale=1.0 / P
                                 ).then_inc(A.sem, A.mark("gdn oroot", h))

        def dve_gdn(dve):
            dve.wait_ge(tile_done, TILE0["gdn_in"] + 1)
            nc.vector.tensor_scalar(GROW[:, 0, :], MB[1][0:GH, :], vec("gdn_dt_bias", rows=GH), None, ALU.add
                                    ).then_inc(V.sem, V.mark("gdn u"))
            dve.wait_ge(A.sem, A.at("gdn ln"))
            chain(dve, V, nc.vector.scalar_tensor_tensor(GROW[:, 0, :], GROW[:, 0, :], 0.0, GROW[:, 1, :],
                                                         ALU.max, ALU.add))
            chain(dve, V, nc.vector.tensor_scalar(GROW[:, 0, :], GROW[:, 0, :], GEA[:, :], -1.0,
                                                  ALU.mult, ALU.mult))
            for c in range(NC):
                nc.vector.tensor_tensor_scan(GROW[:, 1, c * CH:(c + 1) * CH], ones[0:GH, :],
                                             GROW[:, 0, c * CH:(c + 1) * CH], 0.0, ALU.mult, ALU.add
                                             ).then_inc(V.sem, V.mark("gdn cum") if c == NC - 1 else V.mark())
            for j in range(16):
                dve.wait_ge(A.sem, A.at("gdn xp", j))
                if j >= 2:
                    dve.wait_ge(A.sem, A.at("gdn silu", j - 2))
                conv(dve, XP[:, j % 2, :], CV[:, j % 2, :], "gdn_conv_w", GCONV[j], 24, None, ("gdn conv", j))
            for j in range(16):
                tensor, h = GNORM[j]
                dve.wait_ge(A.sem, A.at("gdn root", j))
                chain(dve, V, nc.vector.reciprocal(RN[:, j % 2, :], RN[:, j % 2, :]))
                nc.vector.scalar_tensor_tensor(tensor[:, h, :], tensor[:, h, :], 1.0 if j < 8 else P ** -0.5,
                                               RN[:, j % 2, :], ALU.mult, ALU.mult
                                               ).then_inc(V.sem, V.mark("gdn qk", j))
            for j in range(16, 24):
                dve.wait_ge(A.sem, A.at("gdn xp", j))
                dve.wait_ge(A.sem, A.at("gdn silu", j - 2))
                conv(dve, XP[:, j % 2, :], CV[:, j % 2, :], "gdn_conv_w", GCONV[j], 24, None, ("gdn conv", j))
            dve.wait_ge(A.sem, A.at("gdn eg"))
            nc.vector.tensor_tensor(GBETA[:, 1, :], GBETA[:, 0, :], GROW[:, 2, :], ALU.mult).then_inc(V.sem, V.mark())
            nc.vector.tensor_tensor(GSEL[:, :, :], heads(GROW[:, 2, CH - 1::CH], NC, GH),
                                    per_head(ident[0:GH, 0:GH], NC), ALU.mult).then_inc(V.sem, V.mark("gdn sel"))
            dve.wait_ge(T.sem, T.at("gdn cols"))
            nc.vector.tensor_copy(GCOL[:, :, :, :].rearrange("p n c h -> p (n c h)"), MB[1][:, 0:96]
                                  ).then_inc(V.sem, V.mark())
            nc.vector.tensor_copy(GEL[:, :, :].rearrange("p c h -> p (c h)"), MB[1][:, 96:128]
                                  ).then_inc(V.sem, V.mark("gdn cols"))
            dve.wait_ge(V.sem, V.at("gdn cols"))
            for c in range(NC):
                for g in range(2):
                    B, b = GB[g], gt[g]
                    gcol = heads(GCOL[:, 0, c, 4 * g:4 * g + 4], 4)
                    dve.wait_ge(T.sem, T.at("gdn rows", c, g))
                    if c:
                        dve.wait_ge(G.sem, G.at("gdn at", c - 1, g))
                    nc.vector.tensor_tensor(b["TMP"][:, :, :], four(B[0]), gcol, ALU.subtract
                                            ).then_inc(V.sem, V.mark("gdn tmp", c, g))
                    dve.wait_ge(V.sem, V.at("gdn tmp", c, g))
                    nc.vector.scalar_tensor_tensor(b["AM"][:, :, :], b["TMP"][:, :, :], -1.0,
                                                   per_head(cst("keep_lower_strict"), 4), ALU.mult, ALU.add
                                                   ).then_inc(V.sem, V.mark("gdn amask", c, g))
                    nc.vector.tensor_tensor(b["QD"][:, :, :], fm(GQ, c, g), four(B[1]), ALU.mult
                                            ).then_inc(V.sem, V.mark("gdn qd", c, g))
                    nc.vector.tensor_tensor(b["KT"][:, :, :], fm(GK, c, g), four(B[2]), ALU.mult
                                            ).then_inc(V.sem, V.mark("gdn kt", c, g))
                for g in range(2):
                    B, b = GB[g], gt[g]
                    dve.wait_ge(A.sem, A.at("gdn expAM", c, g))
                    dve.wait_ge(T.sem, T.at("gdn kk", c, g))
                    nc.vector.tensor_tensor(b["AM"][:, :, :], b["AM"][:, :, :], four(B[3]), ALU.mult
                                            ).then_inc(V.sem, V.mark("gdn am", c, g))
                    dve.wait_ge(T.sem, T.at("gdn qk", c, g))
                    nc.vector.tensor_tensor(b["AT"][:, :, :], b["AT"][:, :, :], four(B[0]), ALU.mult
                                            ).then_inc(V.sem, V.mark("gdn at", c, g))
                    dve.wait_ge(T.sem, T.at("gdn tok", c, g))
                    nc.vector.tensor_tensor(b["KD"][:, :, :], heads(GCOL[:, 2, c, 4 * g:4 * g + 4], 4),
                                            four(B[1]), ALU.mult).then_inc(V.sem, V.mark("gdn kd", c, g))
                    nc.vector.tensor_tensor(b["VB"][:, :, :], heads(GCOL[:, 1, c, 4 * g:4 * g + 4], 4),
                                            four(B[2]), ALU.mult).then_inc(V.sem, V.mark("gdn vb", c, g))
                for l in range(LEVELS):
                    for g in range(2):
                        B, b = GB[g], gt[g]
                        eye = per_head(ident, 4)
                        dve.wait_ge(T.sem, T.at("gdn uy", c, g, l))
                        ins = nc.vector.tensor_tensor(b["U"][:, :, :], eye if l == 0 else b["U"][:, :, :],
                                                      four(B[1]), ALU.subtract)
                        if l < LEVELS - 1:
                            ins.then_inc(V.sem, V.mark())
                            ins = nc.vector.tensor_tensor(b["T"][:, :, :], eye if l == 0 else b["T"][:, :, :],
                                                          four(B[2]), ALU.subtract)
                        ins.then_inc(V.sem, V.mark("gdn tu", c, g, l))
                if c:
                    for g in range(2):
                        b = gt[g]
                        dve.wait_ge(T.sem, T.at("gdn ks", c, g))
                        nc.vector.tensor_tensor(b["VB"][:, :, :], b["VB"][:, :, :], four(GB[g][3]), ALU.subtract
                                                ).then_inc(V.sem, V.mark("gdn r", c, g))
                for g in range(2):
                    dve.wait_ge(T.sem, T.at("gdn su", c, g))
                    state = GS_[:, 4 * g:4 * g + 4, :]
                    if c == 0:
                        nc.vector.tensor_copy(state, four(GB[g][2])).then_inc(V.sem, V.mark("gdn state", c, g))
                    else:
                        chain(dve, V, nc.vector.tensor_tensor(state, state, heads(GEL[:, c, 4 * g:4 * g + 4], 4),
                                                              ALU.mult))
                        nc.vector.tensor_tensor(state, state, four(GB[g][2]), ALU.add
                                                ).then_inc(V.sem, V.mark("gdn state", c, g))
            for h in range(GH):
                dve.wait_ge(A.sem, A.at("gdn oroot", h))
                chain(dve, V, nc.vector.reciprocal(RN[:, h % 2, :], RN[:, h % 2, :]))
                chain(dve, V, nc.vector.scalar_tensor_tensor(GO[:, h, :], GO[:, h, :], vec("gdn_onorm_g"),
                                                             RN[:, h % 2, :], ALU.mult, ALU.mult))
                nc.vector.tensor_tensor(GO[:, h, :], GO[:, h, :], GZ[:, h, :], ALU.mult
                                        ).then_inc(V.sem, V.mark("gdn y", h))
            residual(dve, "gdn_out", lambda d: COND[:, 40 + d:41 + d])

        def pool_gdn(pool):
            for c in range(NC):
                for g in range(2):
                    b = gt[g]
                    pool.wait_ge(V.sem, V.at("gdn tmp", c, g))
                    if c:
                        pool.wait_ge(T.sem, T.at("gdn o", c - 1, g))
                    nc.gpsimd.tensor_tensor(b["AT"][:, :, :], b["TMP"][:, :, :],
                                            per_head(cst("keep_upper"), 4), ALU.add
                                            ).then_inc(G.sem, G.mark("gdn at", c, g))
                for g in range(2):
                    b = gt[g]
                    pool.wait_ge(V.sem, V.at("gdn am", c, g))
                    nc.gpsimd.tensor_tensor(b["AM"][:, :, :], b["AM"][:, :, :],
                                            heads(GCOL[:, 1, c, 4 * g:4 * g + 4], 4), ALU.mult
                                            ).then_inc(G.sem, G.mark("gdn beta", c, g))
                for l in range(LEVELS):
                    for g in range(2):
                        b = gt[g]
                        if l == 0:
                            pool.wait_ge(G.sem, G.at("gdn beta", c, g))
                        else:
                            pool.wait_ge(T.sem, T.at("gdn y", c, g, l - 1))
                        nc.gpsimd.tensor_tensor(b["L"][:, :, :], b["AM"][:, :, :],
                                                per_head(cst("levels", at=l * P), 4), ALU.mult
                                                ).then_inc(G.sem, G.mark("gdn l", c, g, l))

        GCONV = list(range(8, 16)) + list(range(0, 8)) + list(range(16, 24))
        FREED["gdn_in"] = lambda j: (A.sem, A.at("beta") if j == 0 else
                                     A.at("gdn xp", j - 1) if j <= 24 else A.at("gdn z", j - 25))

        hy = ExitStack()
        YX = sb("YX", [P, 12, S], stack=hy)
        YZ = sb("YZ", [P, 8, S], stack=hy)
        MQ = sb("MQ", [P, MH, S], stack=hy)
        MK = sb("MK", [P, MH, S], stack=hy)
        MV = sb("MV", [P, 2 * MH, S], stack=hy)
        MO = sb("MO", [P, 2 * MH, S], stack=hy)
        YROW = sb("YROW", [SH, 5, S], stack=hy)
        YCOL = sb("YCOL", [P, 3, NC, SH], stack=hy)
        YSEL = sb("YSEL", [SH, NC, SH], stack=hy)
        YEL = sb("YEL", [P, NC, SH], stack=hy)
        YEA = sb("YEA", [SH, 1], stack=hy)
        MROW = sb("MROW", [MH, 7, S], stack=hy)
        MIN = sb("MIN", [MH, NC + 1], stack=hy)
        NCM = sb("NCM", [MH, NC], stack=hy)
        MAC = sb("MAC", [MH, NC], stack=hy)
        MCOL = sb("MCOL", [P, 2, NC, MH], stack=hy)
        MSEL = sb("MSEL", [MH, NC, MH], stack=hy)
        MEL = sb("MEL", [P, NC, MH], stack=hy)
        HF = H[:, :, :].rearrange("p a s -> p (a s)")
        YM = [HF[:, 512 * g:512 * g + 512] for g in range(2)]
        YCD = [HF[:, 1024 + 512 * g:1536 + 512 * g] for g in range(2)]
        YXD = HF[:, 2048:3072]
        YXE = HF[:, 3072:4096]
        YBT = sb("YBT", [P, 2, P], stack=hy)
        MCS = sb("MCS", [P, MH, 3 * P], stack=hy)
        YST = MCS[:, :, :].rearrange("p h v -> p (h v)")[:, 0:SH * SP_]
        MVA = sb("MVA", [P, MH, 3 * P], stack=hy)
        hy.close()
        MS, MQH, MKW, MEM = YM[0], YCD[0], YM[1], YCD[1]

        def h4(ap):
            return ap.rearrange("p (h t) -> p h t", h=4)

        def ck(c):
            return slice(c * CH, (c + 1) * CH)

        def pe_hy(pe):
            pe_tile(pe, "hy_in", 0, h_tile, h_wait(pe, 4),
                    outs=[(MB[1][0:SH, :], 0, 16), (MB[2][0:MH, :], 16, 20), (MB[3][0:MH, :], 20, 24)])
            for j in range(1, 45):
                pe_tile(pe, "hy_in", j, h_tile)
            pe.wait_ge(V.sem, V.at("hy rows"))
            for n, row in enumerate((YROW[:, 1, :], YROW[:, 0, :], YROW[:, 4, :])):
                for c in range(NC):
                    nc.tensor.matmul(MB[1][:, (n * NC + c) * SH:(n * NC + c + 1) * SH],
                                     row[:, ck(c)], ident[0:SH, 0:SH], start=True, stop=True)
            nc.tensor.matmul(MB[1][:, 192:256], ones[0:SH, :], YSEL[:, :, :].rearrange("p c h -> p (c h)"),
                             start=True, stop=True)
            for n, row in enumerate((MROW[:, 3, :], MROW[:, 5, :])):
                for c in range(NC):
                    nc.tensor.matmul(MB[1][:, 256 + (n * NC + c) * MH:256 + (n * NC + c + 1) * MH],
                                     row[:, ck(c)], ident[0:MH, 0:MH], start=True, stop=True)
            nc.tensor.matmul(MB[1][:, 288:304], ones[0:MH, :], MSEL[:, :, :].rearrange("p c h -> p (c h)"),
                             start=True, stop=True).then_inc(T.sem, T.mark("hy cols"))
            pe.wait_ge(V.sem, V.at("hy cols"))
            pe.wait_ge(A.sem, A.at("hy o", 7))
            for c in range(NC):
                if c:
                    pe.wait_ge(V.sem, V.at("ssd y", c - 1, 3))
                    pe.wait_ge(V.sem, V.at("ssd state", c - 1))
                for d in range(8):
                    nc.tensor.transpose(LB[d // 4][:, d % 4 * P:(d % 4 + 1) * P], YX[:, d, ck(c)], ident)
                for g in range(2):
                    nc.tensor.transpose(LB[2][:, g * P:(g + 1) * P], YX[:, 8 + g, ck(c)], ident)
                for g in range(2):
                    last = nc.tensor.matmul(LB[3][:, g * P:(g + 1) * P], YX[:, 8 + g, ck(c)],
                                            YX[:, 10 + g, ck(c)], start=True, stop=True)
                last.then_inc(T.sem, T.mark("ssd tok", c))
                for q in range(4):
                    b0, b1 = MB[2 * (q % 2)], MB[2 * (q % 2) + 1]
                    if q >= 2:
                        pe.wait_ge(V.sem, V.at("ssd cd", c, q - 2))
                    elif c:
                        pe.wait_ge(V.sem, V.at("ssd cd", c - 1, q + 2))
                    for n, row in ((0, YROW[:, 1, :]), (1, YROW[:, 2, :])):
                        for h in range(4):
                            last = nc.tensor.matmul((b0, b1)[n][:, h * P:(h + 1) * P],
                                                    ident[0:SH, 4 * q + h:4 * q + h + 1].to_broadcast([SH, P]),
                                                    row[:, ck(c)], start=True, stop=True)
                    last.then_inc(T.sem, T.mark("ssd rows", c, q))
                    if q:
                        ssd_y(pe, c, q - 1)
                ssd_y(pe, c, 3)
                if c < NC - 1:
                    for g in range(2):
                        last = nc.tensor.matmul(LB[g][:, :], YBT[:, g, :], YXE[:, g * 512:(g + 1) * 512],
                                                start=True, stop=True)
                    last.then_inc(T.sem, T.mark("ssd su", c))
            pe.wait_ge(V.sem, V.at("ssd y", NC - 1, 3))
            for c in range(NC):
                if c:
                    pe.wait_ge(A.sem, A.at("ml em", c - 1))
                    pe.wait_ge(V.sem, V.at("ml h", c - 1))
                    pe.wait_ge(V.sem, V.at("ml state", c - 1, 3))
                for n, row in ((0, MROW[:, 4, :]), (1, MROW[:, 6, :]), (2, MROW[:, 2, :])):
                    for h in range(4):
                        nc.tensor.matmul(MB[n][:, h * P:(h + 1) * P],
                                         ident[0:MH, h:h + 1].to_broadcast([MH, P]), row[:, ck(c)],
                                         start=True, stop=True)
                for h in range(4):
                    last = nc.tensor.matmul(MB[3][:, h * P:(h + 1) * P], MK[:, h, ck(c)], MQ[:, h, ck(c)],
                                            start=True, stop=True)
                last.then_inc(T.sem, T.mark("ml rows", c))
                for h in range(4):
                    nc.tensor.transpose(LB[0][:, h * P:(h + 1) * P], MK[:, h, ck(c)], ident)
                for d in range(8):
                    last = nc.tensor.transpose(LB[1 + d // 4][:, d % 4 * P:(d % 4 + 1) * P], MV[:, d, ck(c)], ident)
                last.then_inc(T.sem, T.mark("ml tok", c))
                pe.wait_ge(V.sem, V.at("ml s", c))
                pe.wait_ge(A.sem, A.at("ml va", c))
                pe.wait_ge(A.sem, A.at("ml em", c))
                for n, bank in enumerate((MB[0], MB[1], MB[2])):
                    for h in range(4):
                        o = bank[:, h * P:(h + 1) * P]
                        last = nc.tensor.matmul(o, MVA[:, h, n * P:(n + 1) * P], MS[:, h * P:(h + 1) * P],
                                                start=True, stop=c == 0)
                        if c:
                            last = nc.tensor.matmul(o, MCS[:, h, n * P:(n + 1) * P], MQH[:, h * P:(h + 1) * P],
                                                    start=False, stop=True)
                last.then_inc(T.sem, T.mark("ml out", c))
                pe.wait_ge(V.sem, V.at("ml kw", c))
                for h in range(4):
                    nc.tensor.matmul((LB[0], LB[1], LB[2], LB[3])[h][:, 0:3 * P], MKW[:, h * P:(h + 1) * P],
                                     MVA[:, h, :], start=True, stop=True).then_inc(T.sem, T.mark("ml su", c, h))
            pe.wait_ge(V.sem, V.at("ml h", NC - 1))
            for j in range(6):
                n = 4 if j < 2 else 2
                for i in range(n):
                    m = hy_norm_at(j) + i
                    pe.wait_ge(A.sem, A.at("hy sq", m))
                    if i == 0 and j >= 2:
                        pe.wait_ge(A.sem, A.at("hy root", j - 2))
                    nc.tensor.matmul(MB[j % 2][:, :], ones, SQ[:, m % 2, :], start=i == 0, stop=i == n - 1
                                     ).then_inc(T.sem, T.mark("hy sum", m))
            for j in range(8):
                pe_tile(pe, "hy_out", j, lambda k: YX[:, k, :] if k < 8 else MV[:, k - 8, :],
                        (lambda k: pe.wait_ge(V.sem, V.at("hy y", k))) if j == 0 else None)

        def hy_norm_at(j):
            return 4 * j if j < 2 else 8 + 2 * (j - 2)

        def ssd_y(pe, c, q):
            bank = (LB[2], LB[3])[q % 2]
            pe.wait_ge(V.sem, V.at("ssd m", c, q))
            pe.wait_ge(V.sem, V.at("ssd cd", c, q))
            pe.wait_ge(V.sem, V.at("ssd xd", c))
            pe.wait_ge(A.sem, A.at("ssd bt", c))
            if q >= 2:
                pe.wait_ge(V.sem, V.at("ssd y", c, q - 2))
            for h in range(4):
                head = 4 * q + h
                o = bank[64 * (h % 2):64 * (h % 2) + 64, 256 + h // 2 * P:256 + (h // 2 + 1) * P]
                last = nc.tensor.matmul(o, YXD[:, head * 64:head * 64 + 64], YM[q % 2][:, h * P:(h + 1) * P],
                                        start=True, stop=c == 0)
                if c:
                    last = nc.tensor.matmul(o, YST[:, head * 64:head * 64 + 64], YCD[q % 2][:, h * P:(h + 1) * P],
                                            start=False, stop=True)
            last.then_inc(T.sem, T.mark("ssd y", c, q))

        def act_hy(act):
            nc.scalar.activation(YEA[:, :], vec("hy_a_log", rows=SH), ACT.Exp).then_inc(A.sem, A.mark("ssd ea"))
            act.wait_ge(V.sem, V.at("hy u"))
            for t, n in ((YROW, "ssd"), (MROW, "ml")):
                chain(act, A, nc.scalar.activation(t[:, 1, :], t[:, 0, :], ACT.Abs))
                chain(act, A, nc.scalar.activation(t[:, 1, :], t[:, 1, :], ACT.Exp, scale=-1.0))
                nc.scalar.activation(t[:, 1, :], t[:, 1, :], ACT.Ln, bias=one[0:t.shape[0], :]
                                     ).then_inc(A.sem, A.mark(n + " ln"))

            def copy_in(j):
                bank = arrived(act, "hy_in", j + 1)
                if j >= 2:
                    act.wait_ge(V.sem, V.at("hy conv", j - 2))
                nc.scalar.activation(XP[:, j % 2, 3:], bank[:, :], ACT.Copy).then_inc(A.sem, A.mark("hy xp", j))

            def silu(j):
                act.wait_ge(V.sem, V.at("hy conv", j))
                nc.scalar.activation(YX[:, j, :], CV[:, j % 2, :], ACT.Silu).then_inc(A.sem, A.mark("hy silu", j))

            copy_in(0)
            for j in range(1, 12):
                copy_in(j)
                silu(j - 1)
            silu(11)
            for j in range(8):
                bank = arrived(act, "hy_in", 13 + j)
                nc.scalar.activation(YZ[:, j, :], bank[:, :], ACT.Silu).then_inc(A.sem, A.mark("hy z", j))
            act.wait_ge(V.sem, V.at("ssd cum"))
            nc.scalar.activation(YROW[:, 2, :], YROW[:, 1, :], ACT.Exp).then_inc(A.sem, A.mark("ssd eg"))
            for c in range(NC):
                nc.scalar.activation(YROW[:, 3, ck(c)], YROW[:, 1, ck(c)], ACT.Exp,
                                     bias=YROW[:, 1, (c + 1) * CH - 1:(c + 1) * CH], scale=-1.0
                                     ).then_inc(A.sem, A.mark("ssd ed") if c == NC - 1 else A.mark())
            act.wait_ge(V.sem, V.at("ml max"))
            for c in range(NC):
                nc.scalar.activation(MROW[:, 5, ck(c)], MROW[:, 3, ck(c)], ACT.Exp, bias=NCM[:, c:c + 1]
                                     ).then_inc(A.sem, A.mark())
                nc.scalar.activation(MROW[:, 6, ck(c)], MROW[:, 4, ck(c)], ACT.Exp, bias=MIN[:, c:c + 1],
                                     scale=-1.0).then_inc(A.sem, A.mark())
                nc.scalar.activation(MAC[:, c:c + 1], NCM[:, c:c + 1], ACT.Exp, bias=MIN[:, c:c + 1]
                                     ).then_inc(A.sem, A.mark())
            nc.scalar.activation(MROW[:, 2, :], MROW[:, 0, :], ACT.Exp, scale=-1.0).then_inc(A.sem, A.mark("ml exps"))
            for j in range(4):
                bank = arrived(act, "hy_in", 21 + j)
                nc.scalar.activation(MQ[:, j, :], bank[:, :], ACT.Copy, scale=P ** -0.5).then_inc(A.sem, A.mark("hy q", j))
            for j in range(4):
                bank = arrived(act, "hy_in", 25 + j)
                nc.scalar.activation(MK[:, j, :], bank[:, :], ACT.Copy).then_inc(A.sem, A.mark("hy k", j))
            for j in range(8):
                bank = arrived(act, "hy_in", 29 + j)
                nc.scalar.activation(MV[:, j, :], bank[:, :], ACT.Copy).then_inc(A.sem, A.mark("hy v", j))
            for j in range(8):
                bank = arrived(act, "hy_in", 37 + j)
                nc.scalar.activation(MO[:, j, :], bank[:, :], ACT.Sigmoid).then_inc(A.sem, A.mark("hy o", j))
            for c in range(NC):
                act.wait_ge(T.sem, T.at("ssd tok", c))
                if c:
                    act.wait_ge(T.sem, T.at("ssd su", c - 1))
                nc.scalar.activation(YBT[:, :, :].rearrange("p g n -> p (g n)"), LB[2][:, 0:256], ACT.Copy
                                     ).then_inc(A.sem, A.mark("ssd bt", c))
                for q in range(4):
                    act.wait_ge(G.sem, G.at("ssd mask", c, q))
                    nc.scalar.activation(YM[q % 2], YM[q % 2], ACT.Exp).then_inc(A.sem, A.mark("ssd exp", c, q))
            for c in range(NC):
                act.wait_ge(T.sem, T.at("ml rows", c))
                if c:
                    act.wait_ge(V.sem, V.at("ml h", c - 1))
                else:
                    act.wait_ge(T.sem, T.at("ssd y", NC - 1, 3))
                nc.scalar.activation(MEM, MB[2][:, :], ACT.Copy).then_inc(A.sem, A.mark("ml em", c))
                act.wait_ge(G.sem, G.at("ml mask", c))
                nc.scalar.activation(MS, MS, ACT.Exp).then_inc(A.sem, A.mark("ml exp", c))
                act.wait_ge(T.sem, T.at("ml tok", c))
                if c:
                    act.wait_ge(T.sem, T.at("ml su", c - 1, 3))
                for n in range(2):
                    nc.scalar.activation(MVA[:, 2 * n:2 * n + 2, 0:2 * P],
                                         LB[1 + n][:, :].rearrange("p (h v) -> p h v", h=2), ACT.Copy
                                         ).then_inc(A.sem, A.mark("ml va", c) if n else A.mark())
            act.wait_ge(V.sem, V.at("ml h", NC - 1))
            act.wait_ge(V.sem, V.at("ssd gated"))
            for j in range(6):
                for i in range(4 if j < 2 else 2):
                    m = hy_norm_at(j) + i
                    if m >= 2:
                        act.wait_ge(T.sem, T.at("hy sum", m - 2))
                    nc.scalar.activation(SQ[:, m % 2, :], YX[:, m, :] if m < 8 else MV[:, m - 8, :], ACT.Square
                                         ).then_inc(A.sem, A.mark("hy sq", m))
                act.wait_ge(T.sem, T.at("hy sum", m))
                if j >= 2:
                    act.wait_ge(V.sem, V.at("hy y", hy_norm_at(j - 1) - 1))
                nc.scalar.activation(RN[:, j % 2, :], MB[j % 2][:, :], ACT.Sqrt, bias=eps,
                                     scale=1.0 / 512 if j < 2 else 1.0 / 256).then_inc(A.sem, A.mark("hy root", j))

        def dve_hy(dve):
            dve.wait_ge(tile_done, TILE0["hy_in"] + 1)
            nc.vector.tensor_scalar(YROW[:, 0, :], MB[1][0:SH, :], vec("hy_dt_bias", rows=SH), None, ALU.add
                                    ).then_inc(V.sem, V.mark())
            nc.vector.tensor_scalar(MROW[:, 6, :], MB[2][0:MH, :], vec("hy_igate_bias", rows=MH), None, ALU.add
                                    ).then_inc(V.sem, V.mark())
            nc.vector.tensor_scalar(MROW[:, 0, :], MB[3][0:MH, :], vec("hy_fgate_bias", rows=MH), -1.0,
                                    ALU.add, ALU.mult).then_inc(V.sem, V.mark("hy u"))
            dve.wait_ge(A.sem, A.at("ssd ln"))
            chain(dve, V, nc.vector.scalar_tensor_tensor(YROW[:, 0, :], YROW[:, 0, :], 0.0, YROW[:, 1, :],
                                                         ALU.max, ALU.add))
            chain(dve, V, nc.vector.tensor_scalar(YROW[:, 2, :], YROW[:, 0, :], YEA[:, :], -1.0,
                                                  ALU.mult, ALU.mult))
            for c in range(NC):
                nc.vector.tensor_tensor_scan(YROW[:, 1, ck(c)], ones[0:SH, :], YROW[:, 2, ck(c)], 0.0,
                                             ALU.mult, ALU.add).then_inc(V.sem, V.mark("ssd cum") if c == NC - 1 else V.mark())
            dve.wait_ge(A.sem, A.at("ml ln"))
            chain(dve, V, nc.vector.scalar_tensor_tensor(MROW[:, 1, :], MROW[:, 0, :], 0.0, MROW[:, 1, :],
                                                         ALU.max, ALU.add))
            chain(dve, V, nc.vector.tensor_scalar(MROW[:, 1, :], MROW[:, 1, :], -1.0, None, ALU.mult))
            for c in range(NC):
                chain(dve, V, nc.vector.tensor_tensor_scan(MROW[:, 2, ck(c)], ones[0:MH, :], MROW[:, 1, ck(c)],
                                                           0.0, ALU.mult, ALU.add))
            chain(dve, V, nc.vector.tensor_tensor(MROW[:, 3, :], MROW[:, 6, :], MROW[:, 2, :], ALU.subtract))
            chain(dve, V, nc.vector.memset(MIN[:, 0:1], 0.0))
            for c in range(NC):
                end = slice((c + 1) * CH - 1, (c + 1) * CH)
                chain(dve, V, nc.vector.tensor_tensor_scan(MROW[:, 4, ck(c)], ones[0:MH, :], MROW[:, 3, ck(c)],
                                                           MIN[:, c:c + 1], ALU.mult, ALU.max))
                chain(dve, V, nc.vector.tensor_tensor(MIN[:, c + 1:c + 2], MROW[:, 4, end], MROW[:, 2, end], ALU.add))
                chain(dve, V, nc.vector.tensor_scalar(NCM[:, c:c + 1], MROW[:, 4, end], -1.0, None, ALU.mult))
            nc.vector.tensor_tensor(MROW[:, 0, :], MROW[:, 4, :], MROW[:, 2, :], ALU.add
                                    ).then_inc(V.sem, V.mark("ml max"))
            for j in range(12):
                dve.wait_ge(A.sem, A.at("hy xp", j))
                if j >= 2:
                    dve.wait_ge(A.sem, A.at("hy silu", j - 2))
                conv(dve, XP[:, j % 2, :], CV[:, j % 2, :], "hy_conv_w", j, 12, vec("hy_conv_b", j), ("hy conv", j))
            nc.vector.memset(MVA[:, :, 2 * P:3 * P], 1.0).then_inc(V.sem, V.mark())
            dve.wait_ge(A.sem, A.at("ssd ed"))
            nc.vector.tensor_tensor(YROW[:, 4, :], YROW[:, 3, :], YROW[:, 0, :], ALU.mult).then_inc(V.sem, V.mark())
            nc.vector.tensor_tensor(YSEL[:, :, :], heads(YROW[:, 2, CH - 1::CH], NC, SH),
                                    per_head(ident[0:SH, 0:SH], NC), ALU.mult).then_inc(V.sem, V.mark())
            dve.wait_ge(A.sem, A.at("ml exps"))
            nc.vector.tensor_tensor(MSEL[:, :, :], heads(MAC[:, :], NC, MH), per_head(ident[0:MH, 0:MH], NC),
                                    ALU.mult).then_inc(V.sem, V.mark("hy rows"))
            dve.wait_ge(T.sem, T.at("hy cols"))
            nc.vector.tensor_copy(YCOL[:, :, :, :].rearrange("p n c h -> p (n c h)"), MB[1][:, 0:192]).then_inc(V.sem, V.mark())
            nc.vector.tensor_copy(YEL[:, :, :].rearrange("p c h -> p (c h)"), MB[1][:, 192:256]).then_inc(V.sem, V.mark())
            nc.vector.tensor_copy(MCOL[:, :, :, :].rearrange("p n c h -> p (n c h)"), MB[1][:, 256:288]).then_inc(V.sem, V.mark())
            nc.vector.tensor_copy(MEL[:, :, :].rearrange("p c h -> p (c h)"), MB[1][:, 288:304]).then_inc(V.sem, V.mark("hy cols"))
            dve.wait_ge(V.sem, V.at("hy cols"))

            def ssd_skip(c, q):
                dve.wait_ge(T.sem, T.at("ssd y", c, q))
                for i in range(2):
                    d = 2 * q + i
                    nc.vector.scalar_tensor_tensor(YX[:, d, ck(c)], YX[:, d, ck(c)], vec("hy_d_skip", d),
                                                   (LB[2], LB[3])[q % 2][:, 256 + i * P:256 + (i + 1) * P],
                                                   ALU.mult, ALU.add).then_inc(V.sem, V.mark("ssd y", c, q) if i else V.mark())

            for c in range(NC):
                dve.wait_ge(T.sem, T.at("ssd tok", c))
                for n, dst in ((1, YXD), (2, YXE)):
                    for b in range(2):
                        nc.vector.tensor_tensor(dst[:, 512 * b:512 * b + 512].rearrange("p (h w) -> p h w", w=SP_),
                                                heads(YCOL[:, n, c, 8 * b:8 * b + 8], 8, SP_),
                                                LB[b][:, :].rearrange("p (h w) -> p h w", w=SP_), ALU.mult
                                                ).then_inc(V.sem, V.mark("ssd xd", c) if (n, b) == (2, 1) else V.mark())
                for q in range(4):
                    b0, b1 = MB[2 * (q % 2)], MB[2 * (q % 2) + 1]
                    dve.wait_ge(T.sem, T.at("ssd rows", c, q))
                    if q >= 2:
                        dve.wait_ge(T.sem, T.at("ssd y", c, q - 2))
                    elif c:
                        dve.wait_ge(T.sem, T.at("ssd y", c - 1, q + 2))
                    nc.vector.tensor_tensor(h4(YM[q % 2]), four(b0), heads(YCOL[:, 0, c, 4 * q:4 * q + 4], 4),
                                            ALU.subtract).then_inc(V.sem, V.mark("ssd diff", c, q))
                    nc.vector.tensor_tensor(h4(YCD[q % 2]), per_head(YX[:, 10 + q // 2, ck(c)], 4), four(b1),
                                            ALU.mult).then_inc(V.sem, V.mark("ssd cd", c, q))
                    if q:
                        ssd_m(dve, c, q - 1)
                        ssd_skip(c, q - 1)
                ssd_m(dve, c, 3)
                ssd_skip(c, 3)
                if c < NC - 1:
                    dve.wait_ge(T.sem, T.at("ssd su", c))
                    if c:
                        chain(dve, V, nc.vector.tensor_tensor(
                            YST.rearrange("p (h w) -> p h w", w=SP_),
                            YST.rearrange("p (h w) -> p h w", w=SP_), heads(YEL[:, c, :], SH, SP_), ALU.mult))
                    for g in range(2):
                        dst = YST[:, 512 * g:512 * g + 512]
                        ins = nc.vector.tensor_tensor(dst, dst, LB[g][:, :], ALU.add) if c else \
                            nc.vector.tensor_copy(dst, LB[g][:, :])
                        ins.then_inc(V.sem, V.mark("ssd state", c) if g else V.mark())
            dve.wait_ge(V.sem, V.at("ssd y", NC - 1, 3))
            for d in range(8):
                nc.vector.tensor_tensor(YX[:, d, :], YX[:, d, :], YZ[:, d, :], ALU.mult
                                        ).then_inc(V.sem, V.mark("ssd gated") if d == 7 else V.mark())
            for c in range(NC):
                dve.wait_ge(T.sem, T.at("ml rows", c))
                if c:
                    dve.wait_ge(T.sem, T.at("ml out", c - 1))
                nc.vector.tensor_tensor(h4(MS), heads(MCOL[:, 0, c, :], 4), four(MB[0]), ALU.subtract
                                        ).then_inc(V.sem, V.mark("ml diff", c))
                nc.vector.tensor_tensor(h4(MQH), MQ[:, :, ck(c)], four(MB[1]), ALU.mult).then_inc(V.sem, V.mark())
                dve.wait_ge(A.sem, A.at("ml exp", c))
                nc.vector.tensor_tensor(MS, MS, MB[3][:, :], ALU.mult).then_inc(V.sem, V.mark("ml s", c))
                dve.wait_ge(T.sem, T.at("ml tok", c))
                if c:
                    dve.wait_ge(T.sem, T.at("ml su", c - 1, 3))
                nc.vector.tensor_tensor(h4(MKW), heads(MCOL[:, 1, c, :], 4), four(LB[0]), ALU.mult
                                        ).then_inc(V.sem, V.mark("ml kw", c))
                dve.wait_ge(T.sem, T.at("ml out", c))
                dve.wait_ge(A.sem, A.at("ml em", c))
                chain(dve, V, nc.vector.scalar_tensor_tensor(MEM, MB[2][:, :], -1.0, MEM, ALU.mult, ALU.max))
                chain(dve, V, nc.vector.tensor_tensor(MEM, MEM, MB[2][:, :], ALU.max))
                chain(dve, V, nc.vector.reciprocal(MEM, MEM))
                for n in range(2):
                    nc.vector.tensor_tensor(MV[:, n::2, ck(c)], h4(MEM), four(MB[n]), ALU.mult
                                            ).then_inc(V.sem, V.mark("ml h", c) if n else V.mark())
                for h in range(4):
                    dve.wait_ge(T.sem, T.at("ml su", c, h))
                    src = (LB[0], LB[1], LB[2], LB[3])[h][:, 0:3 * P]
                    ins = nc.vector.scalar_tensor_tensor(MCS[:, h, :], MCS[:, h, :], MEL[:, c, h:h + 1], src,
                                                         ALU.mult, ALU.add) if c else \
                        nc.vector.tensor_copy(MCS[:, h, :], src)
                    ins.then_inc(V.sem, V.mark("ml state", c, h))
            for j in range(6):
                dve.wait_ge(A.sem, A.at("hy root", j))
                chain(dve, V, nc.vector.reciprocal(RN[:, j % 2, :], RN[:, j % 2, :]))
                for i in range(4 if j < 2 else 2):
                    m = hy_norm_at(j) + i
                    y = YX[:, m, :] if m < 8 else MV[:, m - 8, :]
                    g = vec("hy_ssd_norm", m) if m < 8 else vec("hy_mlstm_norm", m - 8)
                    ins = nc.vector.scalar_tensor_tensor(y, y, g, RN[:, j % 2, :], ALU.mult, ALU.mult)
                    if m < 8:
                        ins.then_inc(V.sem, V.mark("hy y", m))
                    else:
                        chain(dve, V, ins)
                        nc.vector.tensor_tensor(y, y, MO[:, m - 8, :], ALU.mult).then_inc(V.sem, V.mark("hy y", m))
            residual(dve, "hy_out", lambda d: 1.0)

        def ssd_m(dve, c, q):
            dve.wait_ge(A.sem, A.at("ssd exp", c, q))
            nc.vector.tensor_tensor(h4(YM[q % 2]), h4(YM[q % 2]),
                                    per_head(LB[3][:, q // 2 * P:(q // 2 + 1) * P], 4), ALU.mult
                                    ).then_inc(V.sem, V.mark("ssd m", c, q))

        def pool_hy(pool):
            for c in range(NC):
                for q in range(4):
                    pool.wait_ge(V.sem, V.at("ssd diff", c, q))
                    nc.gpsimd.tensor_tensor(h4(YM[q % 2]), h4(YM[q % 2]), per_head(cst("keep_upper"), 4), ALU.add
                                            ).then_inc(G.sem, G.mark("ssd mask", c, q))
            for c in range(NC):
                pool.wait_ge(V.sem, V.at("ml diff", c))
                nc.gpsimd.tensor_tensor(h4(MS), h4(MS), per_head(cst("keep_upper"), 4), ALU.add
                                        ).then_inc(G.sem, G.mark("ml mask", c))

        def hy_freed(j):
            if j == 0:
                return V.sem, V.at("hy u")
            for first, count, name in ((1, 12, "hy xp"), (13, 8, "hy z"), (21, 4, "hy q"), (25, 4, "hy k"),
                                       (29, 8, "hy v"), (37, 8, "hy o")):
                if j < first + count:
                    return A.sem, A.at(name, j - first)

        FREED["hy_in"] = hy_freed


        sa = ExitStack()
        AKI = sb("AKI", [P, S], stack=sa)
        AQI = sb("AQI", [P, IH // 2, S], stack=sa)
        AVW = sb("AVW", [P, S], stack=sa)
        AVT = sb("AVT", [P, NC, AD + IH], stack=sa)
        AK = sb("AK", [P, S], stack=sa)
        AQ = sb("AQ", [P, AH // 2, S], stack=sa)
        POS = sb("POS", [P, S], I32, stack=sa)
        ANG = sb("ANG", [P, 3, S], stack=sa)
        COS = sb("COS", [P, S], stack=sa)
        SIN = sb("SIN", [P, S], stack=sa)
        RAW = sb("RAW", [P, 3, S], stack=sa)
        RTC = sb("RTC", [P, 2, S], stack=sa)
        RTS = sb("RTS", [P, 2, S], stack=sa)
        REL = sb("REL", [P, 4, S], stack=sa)
        ASC = sb("ASC", [P, S], stack=sa)
        AWK = sb("AWK", [P, S], stack=sa)
        AM8 = sb("AM8", [P, 8], stack=sa)
        AMB = sb("AMB", [P, NC, S], stack=sa)
        APR = sb("APR", [P, 3, S], stack=sa)
        APT = sb("APT", [P, 2, S], stack=sa)
        AMX = sb("AMX", [P, 64], stack=sa)
        ANM = sb("ANM", [P, 64], stack=sa)
        ASM = sb("ASM", [P, 64], stack=sa)
        ARS = sb("ARS", [P, 64], stack=sa)
        AOT = sb("AOT", [P, 2, S], stack=sa)
        sa.close()
        AO = H
        ROPE = [(0, AKI[:, :])] + [(1 + i, AQI[:, i, :]) for i in range(4)] + [(6, AK[:, :])] \
            + [(7 + i, AQ[:, i, :]) for i in range(8)]
        UNITS = [(qt, h) for qt in range(NC) for h in range(AH)]

        def pe_sa(pe):
            def rot(i):
                pe.wait_ge(V.sem, V.at("sa normed", i)) if i >= 5 else pe.wait_ge(A.sem, A.at("sa raw", i))
                if i >= 2:
                    pe.wait_ge(V.sem, V.at("sa rs", i - 2))
                nc.tensor.matmul(MB[i % 2][:, :], rotate, RAW[:, i % 3, :], start=True, stop=True
                                 ).then_inc(T.sem, T.mark("sa rot", i))

            def total(i):
                pe.wait_ge(A.sem, A.at("sa sq", i))
                if i >= 7:
                    pe.wait_ge(A.sem, A.at("sa root", i - 2))
                nc.tensor.matmul(MB[2 + i % 2][:, :], half_ones, SQ[:, i % 2, :], start=True, stop=True
                                 ).then_inc(T.sem, T.mark("sa sum", i))

            for j in range(15):
                pe_tile(pe, "sa_in", j, h_tile, h_wait(pe, 7) if j == 0 else None)
                if 1 <= j <= 5:
                    rot(j - 1)
                if j >= 7:
                    total(j - 2)
                if j >= 8:
                    rot(j - 3)
            total(13)
            rot(12)
            rot(13)
            pe.wait_ge(V.sem, V.at("sa rs", 13))
            pe.wait_ge(A.sem, A.at("sa vw"))
            for c in range(NC):
                last = nc.tensor.transpose(MB[0][:, c * P:(c + 1) * P], AVW[:, ck(c)], ident)
            last.then_inc(T.sem, T.mark("sa vt"))
            pe.wait_ge(V.sem, V.at("sa rope", 13))
            pe.wait_ge(V.sem, V.at("sa vt"))
            for qt in range(NC):
                if qt:
                    for h in range(IH):
                        n = (qt - 1) * IH + h
                        if n >= 4:
                            pe.wait_ge(A.sem, A.at("sa relu", n - 4))
                        r = slice(64 * (h % 2), 64 * (h % 2) + 64)
                        nc.tensor.matmul(LB[n % 4][:, 0:(qt + 1) * P], AQI[r, h // 2, ck(qt)],
                                         AKI[r, 0:(qt + 1) * P], start=True, stop=True
                                         ).then_inc(T.sem, T.mark("sa logit", n))
            pe.wait_ge(A.sem, A.at("sa relu", 3 * IH - 1))

            def logits(u):
                qt, h = UNITS[u]
                if u >= 3:
                    pe.wait_ge(V.sem, V.at("sa max", u - 3))
                r = slice(64 * (h % 2), 64 * (h % 2) + 64)
                nc.tensor.matmul(LB[u % 3][:, 0:(qt + 1) * P], AQ[r, h // 2, ck(qt)], AK[r, 0:(qt + 1) * P],
                                 start=True, stop=True).then_inc(T.sem, T.mark("sa s", u))

            def flip(u):
                qt, h = UNITS[u]
                pe.wait_ge(A.sem, A.at("sa exp", u))
                if u >= 2:
                    pe.wait_ge(A.sem, A.at("sa pt", u - 2))
                for k in range(qt + 1):
                    last = nc.tensor.transpose(MB[u % 2][:, k * P:(k + 1) * P], APR[:, u % 3, k * P:(k + 1) * P], ident)
                last.then_inc(T.sem, T.mark("sa flip", u))

            def products(u):
                qt, h = UNITS[u]
                g = u // 8
                pe.wait_ge(A.sem, A.at("sa pt", u))
                if u % 8 == 0 and g >= 2:
                    pe.wait_ge(V.sem, V.at("sa ot", g - 2))
                for k in range(qt + 1):
                    last = nc.tensor.matmul(MB[2 + g % 2][:, u % 8 * AD:(u % 8 + 1) * AD], APT[:, u % 2, k * P:(k + 1) * P],
                                            AVT[:, k, 0:AD], start=k == 0, stop=k == qt)
                last.then_inc(T.sem, T.mark("sa pv", u))

            def back(g):
                pe.wait_ge(V.sem, V.at("sa ot", g))
                if g:
                    pe.wait_ge(A.sem, A.at("sa out", g - 1))
                for i in range(4):
                    last = nc.tensor.transpose(LB[3][:, i * P:(i + 1) * P], AOT[:, g % 2, i * P:(i + 1) * P], ident)
                last.then_inc(T.sem, T.mark("sa back", g))

            for u in range(64 + 6):
                if u < 64:
                    logits(u)
                if 0 <= u - 2 < 64:
                    flip(u - 2)
                if 0 <= u - 3 < 64:
                    products(u - 3)
                if u >= 13 and (u - 13) % 8 == 0:
                    back((u - 13) // 8)
            for j in range(8):
                pe_tile(pe, "sa_out", j, lambda k: AO[:, k, :],
                        (lambda k: pe.wait_ge(A.sem, A.at("sa out", 7))) if j == 0 else None)

        def act_sa(act):
            act.dma_start(POS[:, :], a["pos"]).then_inc(pos_in, 16)
            act.wait_ge(V.sem, V.at("sa angles"))
            nc.scalar.activation(SIN[:, :], ANG[:, 0, :], ACT.Sin).then_inc(A.sem, A.mark())
            nc.scalar.activation(COS[:, :], ANG[:, 1, :], ACT.Sin).then_inc(A.sem, A.mark("sa sincos"))
            rope_of = {j: i for i, (j, _) in enumerate(ROPE)}

            def root(i):
                act.wait_ge(T.sem, T.at("sa sum", i))
                if i >= 7:
                    act.wait_ge(V.sem, V.at("sa normed", i - 2))
                nc.scalar.activation(RN[:, i % 2, :], MB[2 + i % 2][:, :], ACT.Sqrt, bias=eps, scale=1.0 / AD
                                     ).then_inc(A.sem, A.mark("sa root", i))

            for j in range(15):
                bank = arrived(act, "sa_in", j)
                if j == 5:
                    nc.scalar.activation(AVW[:, :], bank[:, :], ACT.Copy).then_inc(A.sem, A.mark("sa vw"))
                    continue
                i = rope_of[j]
                if i >= 3:
                    act.wait_ge(V.sem, V.at("sa rope", i - 3))
                    act.wait_ge(T.sem, T.at("sa rot", i - 3))
                nc.scalar.activation(RAW[:, i % 3, :], bank[:, :], ACT.Copy).then_inc(A.sem, A.mark("sa raw", i))
                if i >= 5:
                    if i >= 7:
                        act.wait_ge(T.sem, T.at("sa sum", i - 2))
                    nc.scalar.activation(SQ[:, i % 2, :], bank[:, :], ACT.Square).then_inc(A.sem, A.mark("sa sq", i))
                    if i >= 6:
                        root(i - 1)
            root(13)
            for qt in range(1, NC):
                for h in range(IH):
                    n = (qt - 1) * IH + h
                    act.wait_ge(T.sem, T.at("sa logit", n))
                    if n >= 4:
                        act.wait_ge(V.sem, V.at("sa score", n - 4))
                    w = (qt + 1) * P
                    nc.scalar.activation(REL[:, n % 4, 0:w], LB[n % 4][:, 0:w], ACT.Relu
                                         ).then_inc(A.sem, A.mark("sa relu", n))

            def pt(u):
                act.wait_ge(T.sem, T.at("sa flip", u))
                if u >= 2:
                    act.wait_ge(T.sem, T.at("sa pv", u - 2))
                w = (UNITS[u][0] + 1) * P
                nc.scalar.activation(APT[:, u % 2, 0:w], MB[u % 2][:, 0:w], ACT.Copy).then_inc(A.sem, A.mark("sa pt", u))

            def out_tiles(g):
                act.wait_ge(T.sem, T.at("sa back", g))
                qt, hg = g // 2, g % 2
                nc.scalar.activation(AO[:, 4 * hg:4 * hg + 4, ck(qt)], four(LB[3]), ACT.Copy
                                     ).then_inc(A.sem, A.mark("sa out", g))

            for u in range(64 + 6):
                if u < 64:
                    w = (UNITS[u][0] + 1) * P
                    act.wait_ge(V.sem, V.at("sa negmax", u))
                    nc.scalar.activation(APR[:, u % 3, 0:w], APR[:, u % 3, 0:w], ACT.Exp, bias=ANM[:, u:u + 1],
                                         scale=AD ** -0.5, accum_out=ASM[:, u:u + 1]
                                         ).then_inc(A.sem, A.mark("sa exp", u))
                if 0 <= u - 2 < 64:
                    pt(u - 2)
                if u >= 13 and (u - 13) % 8 == 0:
                    out_tiles((u - 13) // 8)

        def dve_sa(dve):
            two_pi = 6.283185307179586
            c0, c1 = 6.28125, 0.0019350051879882812
            c2 = two_pi - c0 - c1
            magic = 12582912.0
            dve.wait_ge(pos_in, 16)
            chain(dve, V, nc.vector.tensor_copy(ANG[:, 0, :], POS[:, :]))
            chain(dve, V, nc.vector.tensor_scalar(ANG[:, 0, :], ANG[:, 0, :], cst("inv_freq", n=1), None, ALU.mult))
            chain(dve, V, nc.vector.tensor_scalar(ANG[:, 1, :], ANG[:, 0, :], 1.0 / two_pi, magic, ALU.mult, ALU.add))
            chain(dve, V, nc.vector.tensor_scalar(ANG[:, 1, :], ANG[:, 1, :], magic, None, ALU.subtract))
            for n, cc in enumerate((c0, c1, c2)):
                chain(dve, V, nc.vector.scalar_tensor_tensor(ANG[:, 0, :], ANG[:, 1, :], -cc, ANG[:, 0, :],
                                                             ALU.mult, ALU.add))
            pi = 3.1415925
            chain(dve, V, nc.vector.tensor_scalar(ANG[:, 1, :], ANG[:, 0, :], two_pi / 4, None, ALU.add))
            chain(dve, V, nc.vector.tensor_scalar(ANG[:, 2, :], ANG[:, 1, :], pi, -two_pi, ALU.is_gt, ALU.mult))
            chain(dve, V, nc.vector.tensor_tensor(ANG[:, 1, :], ANG[:, 1, :], ANG[:, 2, :], ALU.add))
            nc.vector.tensor_scalar(ANG[:, 0:2, :], ANG[:, 0:2, :], pi, -pi, ALU.min, ALU.max
                                    ).then_inc(V.sem, V.mark("sa angles"))
            dve.wait_ge(A.sem, A.at("sa sincos"))

            def norm(i):
                dve.wait_ge(A.sem, A.at("sa root", i))
                chain(dve, V, nc.vector.reciprocal(RN[:, i % 2, :], RN[:, i % 2, :]))
                nc.vector.scalar_tensor_tensor(RAW[:, i % 3, :], RAW[:, i % 3, :],
                                               vec("sa_k_norm" if i == 5 else "sa_q_norm"), RN[:, i % 2, :],
                                               ALU.mult, ALU.mult).then_inc(V.sem, V.mark("sa normed", i))

            def rope(i):
                if i >= 5:
                    dve.wait_ge(V.sem, V.at("sa normed", i))
                else:
                    dve.wait_ge(A.sem, A.at("sa raw", i))
                nc.vector.tensor_tensor(RTC[:, i % 2, :], RAW[:, i % 3, :], COS[:, :], ALU.mult).then_inc(V.sem, V.mark())
                dve.wait_ge(T.sem, T.at("sa rot", i))
                nc.vector.tensor_tensor(RTS[:, i % 2, :], SIN[:, :], MB[i % 2][:, :], ALU.mult
                                        ).then_inc(V.sem, V.mark("sa rs", i))
                dve.wait_ge(V.sem, V.at("sa rs", i))
                nc.vector.tensor_tensor(ROPE[i][1], RTC[:, i % 2, :], RTS[:, i % 2, :], ALU.add
                                        ).then_inc(V.sem, V.mark("sa rope", i))

            for i in range(5):
                rope(i)
            norm(5)
            for i in range(6, 14):
                norm(i)
                rope(i - 1)
            rope(13)
            dve.wait_ge(T.sem, T.at("sa vt"))
            nc.vector.tensor_copy(AVT[:, :, :], MB[0][:, :].rearrange("p (c f) -> p c f", c=NC)[:, :, 0:AD + IH]
                                  ).then_inc(V.sem, V.mark("sa vt"))
            nc.vector.tensor_copy(AMB[:, 0, 0:P], cst("keep_lower")).then_inc(V.sem, V.mark("sa mask", 0))
            dve.wait_ge(V.sem, V.at("sa vt"))
            for qt in range(1, NC):
                w = (qt + 1) * P
                for h in range(IH):
                    n = (qt - 1) * IH + h
                    dve.wait_ge(A.sem, A.at("sa relu", n))
                    wi = AVT[:, qt, AD + h:AD + h + 1]
                    if h == 0:
                        ins = nc.vector.tensor_scalar(ASC[:, 0:w], REL[:, n % 4, 0:w], wi, None, ALU.mult)
                    else:
                        dve.wait_ge(V.sem, V.at("sa score", n - 1))
                        ins = nc.vector.scalar_tensor_tensor(ASC[:, 0:w], REL[:, n % 4, 0:w], wi, ASC[:, 0:w],
                                                             ALU.mult, ALU.add)
                    ins.then_inc(V.sem, V.mark("sa score", n))
                dve.wait_ge(V.sem, V.at("sa score", n))
                chain(dve, V, nc.vector.tensor_scalar(ASC[:, 0:w], ASC[:, 0:w], (IH * AD) ** -0.5, None, ALU.mult))
                chain(dve, V, nc.vector.tensor_tensor(ASC[:, qt * P:w], ASC[:, qt * P:w], cst("keep_lower"), ALU.add))
                for r in range(TOPK // 8):
                    src = AWK if r else ASC
                    chain(dve, V, nc.vector.max(AM8[:, :], src[:, 0:w]))
                    chain(dve, V, nc.vector.match_replace(AWK[:, 0:w], AM8[:, :], src[:, 0:w], -3.0e38))
                chain(dve, V, nc.vector.tensor_tensor(AMB[:, qt, 0:w], AWK[:, 0:w], ASC[:, 0:w], ALU.is_equal))
                nc.vector.tensor_scalar(AMB[:, qt, 0:w], AMB[:, qt, 0:w], NEG, None, ALU.mult
                                        ).then_inc(V.sem, V.mark("sa mask", qt))
            def scale_out(g):
                dve.wait_ge(T.sem, T.at("sa pv", 8 * g + 7))
                dve.wait_ge(A.sem, A.at("sa exp", 8 * g + 7))
                if g >= 2:
                    dve.wait_ge(T.sem, T.at("sa back", g - 2))
                chain(dve, V, nc.vector.reciprocal(ARS[:, 8 * g:8 * g + 8], ASM[:, 8 * g:8 * g + 8]))
                nc.vector.tensor_tensor(AOT[:, g % 2, :].rearrange("p (h w) -> p h w", w=AD),
                                        heads(ARS[:, 8 * g:8 * g + 8], 8, AD),
                                        MB[2 + g % 2][:, :].rearrange("p (h w) -> p h w", w=AD), ALU.mult
                                        ).then_inc(V.sem, V.mark("sa ot", g))

            for u in range(64 + 5):
                if u < 64:
                    qt, h = UNITS[u]
                    w = (qt + 1) * P
                    dve.wait_ge(T.sem, T.at("sa s", u))
                    dve.wait_ge(V.sem, V.at("sa mask", qt))
                    if u >= 3:
                        dve.wait_ge(T.sem, T.at("sa flip", u - 3))
                    nc.vector.tensor_tensor_reduce(out=APR[:, u % 3, 0:w], in0=LB[u % 3][:, 0:w], in1=AMB[:, qt, 0:w],
                                                   scale=1.0, scalar=-3.0e38, op0=ALU.add, op1=ALU.max,
                                                   accum_out=AMX[:, u:u + 1]).then_inc(V.sem, V.mark("sa max", u))
                    dve.wait_ge(V.sem, V.at("sa max", u))
                    nc.vector.tensor_scalar(ANM[:, u:u + 1], AMX[:, u:u + 1], -(AD ** -0.5), None, ALU.mult
                                            ).then_inc(V.sem, V.mark("sa negmax", u))
                if u >= 11 and (u - 11) % 8 == 0:
                    scale_out((u - 11) // 8)
            residual(dve, "sa_out", lambda d: 1.0)

        FREED["sa_in"] = lambda j: (A.sem, A.at("sa vw") if j == 5 else
                                    A.at("sa sq" if j > 5 else "sa raw", j if j < 5 else j - 1))

        block = ctx.enter_context(nc.Block())

        @block.sync
        def _(sp):
            sync_program(sp)

        @block.gpsimd
        def _(pool):
            pool_gdn(pool)
            pool_ffn(pool, 0)
            pool_hy(pool)
            pool_ffn(pool, 1)
            pool_ffn(pool, 2)
            pool_ffn(pool, 3)

        @block.scalar
        def _(act):
            act.dma_start(VEC[:, :], a["vec"]).then_inc(vec_in, 16)
            act.dma_start(CST[:, :], a["cst"]).then_inc(cst_in, 16)
            act.dma_start(X[:, :, :], a["x"]).then_inc(x_in, 16)
            act.dma_start(GW[:, :, :], a["gate_w"]).then_inc(gate_w_in, 16)
            act_ada(act)
            act_norm(act, 0)
            act_lru(act)
            act_norm(act, 1)
            act_gdn(act)
            act_norm(act, 2)
            act_norm(act, 3, lambda: act_ffn_high(act, 3, 0))
            act_ffn(act, 0)
            act_norm(act, 4)
            act_hy(act)
            act_norm(act, 5, lambda: act_ffn_high(act, 5, 1))
            act_ffn(act, 1)
            act_norm(act, 6, lambda: act_ffn_high(act, 6, 2))
            act_ffn(act, 2)
            act_norm(act, 7)
            act_sa(act)
            act_norm(act, 8, lambda: act_ffn_high(act, 8, 3))
            act_ffn(act, 3)

        @block.vector
        def _(dve):
            dve_ada(dve)
            dve_norm(dve, 0, lambda d: GS[:, 0, d:d + 1], lambda d: COND[:, d:d + 1])
            dve_lru(dve)
            dve_norm(dve, 1, lambda d: GS[:, 1, d:d + 1], lambda d: COND[:, 24 + d:25 + d])
            dve_gdn(dve)
            dve_norm(dve, 2, lambda d: vec("final_g", d), dst=lambda d: X[:, d, :], sig=x_ready)
            dve_norm(dve, 3, lambda d: vec("ffn_norm", d))
            dve_ffn(dve, 0)
            dve_norm(dve, 4, lambda d: vec("mix_norm", d))
            dve_hy(dve)
            dve_norm(dve, 5, lambda d: vec("ffn_norm", 8 + d))
            dve_ffn(dve, 1)
            dve_norm(dve, 6, lambda d: vec("ffn_norm", 16 + d))
            dve_ffn(dve, 2)
            dve_norm(dve, 7, lambda d: vec("mix_norm", 8 + d))
            dve_sa(dve)
            dve_norm(dve, 8, lambda d: vec("ffn_norm", 24 + d))
            dve_ffn(dve, 3)

        @block.tensor
        def _(pe):
            pe.wait_ge(cst_in, 16)
            pe_ada(pe)
            pe_norm(pe, 0)
            pe_lru(pe)
            pe_norm(pe, 1)
            pe_gdn(pe)
            pe_norm(pe, 2)
            pe_norm(pe, 3)
            pe_ffn(pe, 0)
            pe_norm(pe, 4)
            pe_hy(pe)
            pe_norm(pe, 5)
            pe_ffn(pe, 1)
            pe_norm(pe, 6)
            pe_ffn(pe, 2)
            pe_norm(pe, 7)
            pe_sa(pe)
            pe_norm(pe, 8)
            pe_ffn(pe, 3)


def host_constants():
    import numpy as np
    cst = np.zeros((P, CONST_N), np.float32)

    def put(name, value):
        value = np.asarray(value, np.float32)
        cst[:, CONST_AT[name]:CONST_AT[name] + value.shape[1]] = value

    r = np.arange(P)
    put("ident", np.eye(P))
    put("ones", np.ones((P, P)))
    put("half_ones", (r[:, None] // 64) == (r[None, :] // 64))
    rot = np.zeros((P, P))
    for m in range(P):
        if m % 64 < 32:
            rot[m + 32, m] = -1.0
        else:
            rot[m - 32, m] = 1.0
    put("rotate", rot)
    put("keep_upper", np.where(r[:, None] <= r[None, :], 0.0, NEG))
    put("keep_lower_strict", np.where(r[:, None] > r[None, :], 0.0, NEG))
    put("keep_lower", np.where(r[:, None] >= r[None, :], 0.0, NEG))
    lev = [((r[:, None] >> l) == (r[None, :] >> l) + 1) & (((r[None, :] >> l) & 1) == 0) for l in range(LEVELS)]
    put("levels", np.concatenate(lev, 1))
    inv = np.float32(10000.0) ** (-np.arange(0, 64, 2, dtype=np.float32) / np.float32(64))
    put("inv_freq", inv[r % 32][:, None])
    put("eps", np.full((P, 1), EPS))
    put("one", np.ones((P, 1)))
    return cst


def kernel(**inputs):
    import numpy as np
    import concourse.bacc as bacc
    from concourse import mybir as mb
    from concourse.bass_utils import run_bass_kernel_spmd

    x = {k: np.asarray(v) for k, v in inputs.items()}

    def slabs(w, parts, k, per=1):
        out = np.zeros((len(parts) * per, P, k, P), w.dtype)
        w = w.reshape(per, k, P, w.shape[1])
        for t, runs in enumerate(parts):
            for c, n, at in runs:
                out[t * per:(t + 1) * per, :, :, at:at + n] = w[:, :, :, c:c + n].transpose(0, 2, 1, 3)
        return out.reshape(len(parts) * per, P, k * P)

    def tiles(first, n):
        return [[(first + P * t, P, 0)] for t in range(n)]

    arrays = {}
    arrays["w_ada"] = np.concatenate([slabs(x["ada_w"][l], tiles(0, 24), 8) for l in range(2)])
    arrays["w_lru_in"] = slabs(x["lru_in_w"][0], tiles(0, 16), 8)
    arrays["w_lru_out"] = slabs(x["lru_out_w"][0], tiles(0, 8), 8)
    arrays["w_gdn_in"] = slabs(x["gdn_in_w"][0], [[(4096, 16, 0)]] + tiles(1024, 8) + tiles(0, 8)
                               + tiles(2048, 8) + tiles(3072, 8), 8)
    arrays["w_gdn_out"] = slabs(x["gdn_out_w"][0], tiles(0, 8), 8)
    for p in range(8):
        f, first, n = p // 2, PART[0] * (p % 2), PART[p % 2]
        gate = slabs(x["ffn_w_gate_2"][f // 2, f % 2], tiles(P * first, n), 8)
        up = slabs(x["ffn_w_up_2"][f // 2, f % 2], tiles(P * first, n), 8)
        arrays[f"w_up{p}"] = np.stack([gate, up], 1).reshape(2 * n, P, 8 * P)
        arrays[f"w_down{p}"] = slabs(x["ffn_w_down_2"][f // 2, f % 2][P * first:P * (first + n)],
                                     tiles(0, 8), n // 2, 2)
    arrays["w_hy_in"] = slabs(x["hy_w_in_2"][0], [[(2560, 16, 0), (5648, 8, 16)]] + tiles(1024, 12) + tiles(0, 8)
                              + tiles(2576, 4) + tiles(3088, 4) + tiles(3600, 8) + tiles(4624, 8), 8)
    arrays["w_hy_out"] = slabs(x["hy_w_out_2"][0], tiles(0, 8), 8, 2)
    arrays["w_sa_in"] = slabs(x["sa_w_in_2"][0], [[(1664, 64, 0), (1664, 64, 64)]] + tiles(1152, 4)
                              + [[(1088, 64, 0), (1728, 8, 64)]] + [[(1024, 64, 0), (1024, 64, 64)]]
                              + tiles(0, 8), 8)
    arrays["w_sa_out"] = slabs(x["sa_w_out_2"][0], tiles(0, 8), 8)
    arrays["gate_w"] = np.ascontiguousarray(
        x["lru_gate_w"][0].transpose(2, 0, 1, 3).reshape(P, 16, P))
    arrays["x"] = np.ascontiguousarray(x["x"][0].T.reshape(DT, P, S).transpose(1, 0, 2))
    arrays["pos"] = np.ascontiguousarray(np.broadcast_to(x["positions_2"], (P, S)))

    def cols(v):
        return v.reshape(-1, P).T

    v = np.zeros((P, VEC_N), np.float32)

    def put(name, value, rows=P):
        v[0:rows, VEC_AT[name]:VEC_AT[name] + value.shape[1]] = value

    put("norm_g", cols(x["norm_g"]))
    put("final_g", cols(x["final_g"]))
    put("ada_b", cols(x["ada_b"]))
    put("lru_conv_w", cols(x["lru_conv_w"]))
    put("lru_conv_b", cols(x["lru_conv_b"]))
    put("lru_gate_b", cols(x["lru_gate_b"]))
    put("lru_lambda", cols(x["lru_lambda"]))
    put("gdn_conv_w", cols(x["gdn_conv_w"]))
    put("gdn_onorm_g", cols(x["gdn_onorm_g"]))
    put("ffn_norm", cols(x["ffn_norm_2"]))
    put("mix_norm", cols(x["mix_norm_2"]))
    put("hy_conv_w", cols(x["hy_conv_w_2"]))
    put("hy_conv_b", cols(x["hy_conv_b_2"]))
    put("hy_ssd_norm", cols(x["hy_ssd_norm_2"]))
    put("hy_mlstm_norm", cols(x["hy_mlstm_norm_2"]))
    put("hy_d_skip", cols(np.repeat(x["hy_d_skip_2"][0], SP_)))
    put("sa_q_norm", np.tile(x["sa_q_norm_2"][0], 2)[:, None])
    put("sa_k_norm", np.tile(x["sa_k_norm_2"][0], 2)[:, None])
    put("gdn_a_log", x["gdn_a_log"].T, GH)
    put("gdn_dt_bias", x["gdn_dt_bias"].T, GH)
    put("hy_dt_bias", x["hy_dt_bias_2"].T, SH)
    put("hy_a_log", x["hy_a_log_2"].T, SH)
    put("hy_igate_bias", x["hy_igate_bias_2"].T, MH)
    put("hy_fgate_bias", x["hy_fgate_bias_2"].T, MH)
    put("c", cols(x["c"]))
    arrays["vec"] = v
    arrays["cst"] = host_constants()

    def build(table, final):
        nc = bacc.Bacc("TRN2", target_bir_lowering=False, num_devices=1)
        ins = {n: nc.dram_tensor(f"in_{n}", t.shape, mb.dt.from_np(t.dtype), kind="ExternalInput").ap()
               for n, t in arrays.items()}
        out = nc.dram_tensor("out_0", (P, DT, S), mb.dt.float32, kind="ExternalOutput").ap()
        bass_program(nc, ins, out, table, final)
        return nc

    table = {}
    build(table, False)
    nc = build(table, True)
    r = run_bass_kernel_spmd(nc, [{f"in_{n}": t for n, t in arrays.items()}], core_ids=[0])
    y = r.results[0]["out_0"]
    return np.ascontiguousarray(y.transpose(1, 0, 2).reshape(D, S).T)[None]
```

```python
import concourse.bass as bass
from concourse import mybir
from contextlib import ExitStack

F32 = mybir.dt.float32
F32R = mybir.dt.float32r
I32 = mybir.dt.int32
ALU = mybir.AluOpType
ACT = mybir.ActivationFunctionType
AX = mybir.AxisListType

P = 128
S = 512
D = 1024
DT = D // P
FF = 2816
FT = FF // P
CH = 128
NC = S // CH
EPS = 1e-6
RG_C = 8.0
NEG = -1.0e30
LEVELS = 7
RING = 4
SLAB_K = 8
TOPK = 128
GH = 8
SH, SP_ = 16, 64
MH = 4
AH, AD = 16, 64
IH = 8

LINEARS = [
    ("ada", 24, 1, 8), ("lru_in", 16, 1, 8), ("lru_out", 8, 1, 8),
    ("gdn_in", 33, 1, 8), ("gdn_out", 8, 1, 8),
    ("up0", 24, 1, 8), ("down0", 8, 2, 6), ("up1", 20, 1, 8), ("down1", 8, 2, 5),
    ("hy_in", 45, 1, 8), ("hy_out", 8, 2, 8),
    ("up2", 24, 1, 8), ("down2", 8, 2, 6), ("up3", 20, 1, 8), ("down3", 8, 2, 5),
    ("up4", 24, 1, 8), ("down4", 8, 2, 6), ("up5", 20, 1, 8), ("down5", 8, 2, 5),
    ("sa_in", 15, 1, 8), ("sa_out", 8, 1, 8),
    ("up6", 24, 1, 8), ("down6", 8, 2, 6), ("up7", 20, 1, 8), ("down7", 8, 2, 5),
]
PART = [12, 10]

VECS = [("norm_g", 16), ("final_g", 8), ("ada_b", 48), ("lru_conv_w", 32), ("lru_conv_b", 8),
        ("lru_gate_b", 16), ("lru_lambda", 8), ("gdn_conv_w", 96), ("gdn_onorm_g", 1),
        ("ffn_norm", 32), ("mix_norm", 16), ("hy_conv_w", 48), ("hy_conv_b", 12),
        ("hy_ssd_norm", 8), ("hy_mlstm_norm", 8), ("hy_d_skip", 8), ("sa_q_norm", 1),
        ("sa_k_norm", 1), ("gdn_a_log", 1), ("gdn_dt_bias", 1), ("hy_dt_bias", 1),
        ("hy_a_log", 1), ("hy_igate_bias", 1), ("hy_fgate_bias", 1), ("c", 8)]
VEC_AT = {}
_n = 0
for _name, _k in VECS:
    VEC_AT[_name] = _n
    _n += _k
VEC_N = _n

CONSTS = [("ident", P), ("ones", P), ("half_ones", P), ("rotate", P), ("keep_upper", P),
          ("keep_lower_strict", P), ("keep_lower", P), ("levels", LEVELS * P),
          ("inv_freq", 1), ("eps", 1), ("one", 1)]
CONST_AT = {}
_n = 0
for _name, _k in CONSTS:
    CONST_AT[_name] = _n
    _n += _k
CONST_N = _n


class Steps:

    def __init__(self, name, sem, table, final):
        self.name, self.sem, self.table, self.final, self.n = name, sem, table, final, 0

    def mark(self, *step):
        self.n += 1
        if step:
            if not self.final:
                assert (self.name, *step) not in self.table, step
            self.table[(self.name, *step)] = self.n
        return 1

    def at(self, *step):
        if self.final:
            return self.table[(self.name, *step)]
        return self.table.get((self.name, *step), 1)


def bass_program(nc, a, out, table, final):
    ctx = ExitStack()
    with ctx:
        def sb(name, shape, dt=F32, stack=ctx):
            return stack.enter_context(nc.sbuf_tensor(name, shape, dt))

        def sem(name):
            return ctx.enter_context(nc.semaphore(name))

        def twins(name, shape, stack=ctx):
            with ExitStack() as part:
                parts = sb(name + "_PART", shape, F32R, stack=part)
            return sb(name, shape, stack=stack), parts

        X = sb("X", [P, DT, S])
        H, HL = twins("H", [P, DT, S])
        W, WIL = twins("W", [P, RING, SLAB_K * P])
        HHF, HH = twins("HH", [P, DT, S])
        WH = sb("WH", [P, RING, SLAB_K * P], F32R)
        VEC = sb("VEC", [P, VEC_N])
        CST = sb("CST", [P, CONST_N])
        COND = sb("COND", [P, 48])
        GS = sb("GS", [P, 2, DT])
        RT = sb("RT", [P, S])
        PS = [ctx.enter_context(nc.psum_tensor(f"PS{i}", [P, S], F32)) for i in range(8)]
        LB, MB = PS[0:4], PS[4:8]

        def vec(name, j=0, n=1, rows=P):
            return VEC[0:rows, VEC_AT[name] + j:VEC_AT[name] + j + n]

        def cst(name, rows=P, n=P, at=0):
            return CST[0:rows, CONST_AT[name] + at:CONST_AT[name] + at + n]

        ident, ones, half_ones, rotate = cst("ident"), cst("ones"), cst("half_ones"), cst("rotate")
        eps, one = cst("eps", n=1), cst("one", n=1)

        def heads(col, n, width=CH):
            return col.unsqueeze(2).to_broadcast([col.shape[0], n, width])

        def per_head(tile, n):
            return tile.unsqueeze(1).to_broadcast([tile.shape[0], n, tile.shape[1]])

        slab_in = [sem(f"slab_in{i}") for i in range(RING)]
        tile_done = sem("tile_done")
        x_in, vec_in, cst_in = sem("x_in"), sem("vec_in"), sem("cst_in")
        gate_w_in, pos_in = sem("gate_w_in"), sem("pos_in")
        x_ready = sem("x_ready")
        square_ready = sem("square_ready")
        sum_ready = sem("sum_ready")
        root_ready = sem("root_ready")
        inv_ready = sem("inv_ready")
        h_part = sem("h_part")
        h_ready = sem("h_ready")
        silu_ready = sem("silu_ready")
        prod_ready = sem("prod_ready")
        hid_high = sem("hid_high")
        hid_ready = sem("hid_ready")
        w_high = sem("w_high")
        w_ready = sem("w_ready")
        mix_high = sem("mix_high")
        mix_ready = sem("mix_ready")
        hh_ready = sem("hh_ready")
        hl_even = sem("hl_even")
        hl_odd = sem("hl_odd")
        out_done = sem("out_done")
        V = Steps("vector", sem("vector_step"), table, final)
        A = Steps("scalar", sem("scalar_step"), table, final)
        T = Steps("tensor", sem("tensor_step"), table, final)
        G = Steps("gpsimd", sem("gpsimd_step"), table, final)

        def chain(eng, steps, ins):
            ins.then_inc(steps.sem, steps.mark())
            eng.wait_ge(steps.sem, steps.n)

        TILE0, SLAB0, last_tile = {}, {}, []
        t = 0
        for name, tiles, per, _ in LINEARS:
            TILE0[name], SLAB0[name] = t, len(last_tile)
            if name == "ada":
                last_tile += [None] * tiles
                continue
            for j in range(tiles):
                last_tile += [t + j] * per
            t += tiles
        SPLIT_NO, MIX_NO = {}, {}
        for name, tiles, per, _ in LINEARS[1:]:
            numbers = SPLIT_NO if name.startswith(("up", "down")) else MIX_NO
            for j in range(tiles * per):
                numbers[SLAB0[name] + j] = len(numbers)

        def bank_of(tile):
            return tile % 4

        def load_slab(sp, name, j, k):
            s = SLAB0[name] + j
            if s >= RING:
                sp.wait_ge(*slab_left(s - RING))
            sp.dma_start(W[:, s % RING, 0:k * P], a["w_" + name][j]).then_inc(slab_in[s % RING], 16)

        def slab_left(s):
            if last_tile[s] is None:
                return ada_used, s + 1
            return (w_ready, SPLIT_NO[s] + 1) if s in SPLIT_NO else (tile_done, last_tile[s] + 1)

        def load_ada2(sp, n):
            if n >= 2:
                sp.wait_ge(ada2_used, n - 1)
            sp.dma_start(W2[:, n % 2, :], a["w_ada2"][n]).then_inc(ada2_in[n % 2], 16)

        def sync_program(sp):
            for name, tiles, per, k in LINEARS:
                if name.startswith("up"):
                    for j in range(RING):
                        load_slab(sp, name, j, k)
                    with sp.Fori(1, tiles // RING) as i:
                        for j in range(RING):
                            s = SLAB0[name] + j
                            sp.wait_ge(w_ready, i * RING + (SPLIT_NO[s] - RING + 1))
                            sp.dma_start(W[:, s % RING, 0:k * P],
                                         a["w_" + name][bass.ds(i * RING + j, 1)].rearrange("a p n -> (a p) n")
                                         ).then_inc(slab_in[s % RING], 16)
                else:
                    for j in range(tiles * per):
                        load_slab(sp, name, j, k)
                        if name == "lru_in" and j >= RING:
                            load_ada2(sp, 2 * (j - RING))
                            load_ada2(sp, 2 * (j - RING) + 1)
            sp.wait_ge(x_ready, 8 * len(RES))
            sp.dma_start(out, X[:, :, :]).then_inc(out_done, 16)
            sp.wait_ge(out_done, 16)

        def three(o, wh, wl, xh, xl, first, last):
            nc.tensor.matmul(o, wh, xh, start=first, stop=False)
            nc.tensor.matmul(o, wh, xl, start=False, stop=False)
            return nc.tensor.matmul(o, wl, xh, start=False, stop=last)

        def mix_split(pool, name, first=0, count=None):
            _, tiles, per, k = next(x for x in LINEARS if x[0] == name)
            for j in range(first, tiles * per if count is None else first + count):
                s = SLAB0[name] + j
                if last_tile[s - RING] is not None:
                    pool.wait_ge(tile_done, last_tile[s - RING] + 1)
                pool.wait_ge(slab_in[s % RING], 16 * (s // RING + 1))
                w, wh = W[:, s % RING, 0:k * P], WH[:, s % RING, 0:k * P]
                nc.gpsimd.tensor_tensor(wh, w, one.to_broadcast([P, k * P]), ALU.mult).then_inc(mix_high, 1)
                pool.wait_ge(mix_high, MIX_NO[s] + 1)
                nc.gpsimd.tensor_tensor(WIL[:, s % RING, 0:k * P], w, wh.bitcast(F32), ALU.subtract).then_inc(mix_ready, 1)

        SETS = ["lru_in", "lru_out", "gdn_in", "gdn_out", "ffn0", "hy_in", "hy_out", "hy_out2",
                "ffn1", "ffn2", "sa_in", "ffn3"]

        def x_high(act, x, hi):
            nc.scalar.activation(hi, x, ACT.Copy).then_inc(hh_ready, 1)

        def x_low(eng, name, k, x, lo, hi):
            eng.wait_ge(hh_ready, DT * SETS.index(name) + k + 1)
            (nc.gpsimd if k % 2 else nc.vector).tensor_tensor(
                lo, x, hi.bitcast(F32), ALU.subtract).then_inc(hl_odd if k % 2 else hl_even, 1)

        def x_wait(pe, name):
            base = DT // 2 * SETS.index(name)
            return lambda k: pe.wait_ge(hl_odd if k % 2 else hl_even, base + k // 2 + 1)

        def act_h_high(act, name, n):
            for d in range(DT):
                act.wait_ge(h_ready, DT * H_NORM[n] + d + 1)
                x_high(act, H[:, d, :], HH[:, d, :])

        def h_low(eng, name, odd):
            for d in range(odd, DT, 2):
                x_low(eng, name, d, H[:, d, :], HL[:, d, :], HH[:, d, :])

        def pool_in(pool, name):
            mix_split(pool, name, 0, RING)
            h_low(pool, name, 1)
            mix_split(pool, name, RING)

        def freed(tile):
            name = next(n for n, c, _, _ in LINEARS if n != "ada" and TILE0[n] <= tile < TILE0[n] + c)
            return FREED[name](tile - TILE0[name])

        def pe_tile(pe, name, j, rhs, ready=None, outs=None):
            _, _, per, k = next(x for x in LINEARS if x[0] == name)
            tile = TILE0[name] + j
            if outs is None:
                if tile >= 4:
                    pe.wait_ge(*freed(tile - 4))
                outs = [(LB[bank_of(tile)][:, :], 0, P)]
            for n, (o, c0, c1) in enumerate(outs):
                for q in range(per):
                    s = SLAB0[name] + j * per + q
                    if n == 0:
                        pe.wait_ge(mix_ready, MIX_NO[s] + 1)
                    wl = WIL[:, s % RING, 0:k * P].rearrange("p (k f) -> p k f", k=k)
                    wh = WH[:, s % RING, 0:k * P].rearrange("p (k f) -> p k f", k=k)
                    for kk in range(k):
                        if ready is not None and n == 0:
                            ready(q * k + kk)
                        xh, xl = rhs(q * k + kk)
                        last = three(o, wh[:, kk, c0:c1], wl[:, kk, c0:c1], xh, xl,
                                     q == 0 and kk == 0, q == per - 1 and kk == k - 1)
            last.then_inc(tile_done, 1)

        def act_norm(act, n, between=None):
            for d in range(DT):
                if n == 0:
                    if d == 0:
                        act.wait_ge(x_in, 16)
                else:
                    act.wait_ge(x_ready, DT * NORM_AFTER[n] + d + 1)
                if n == 8 and d == 0:
                    act.wait_ge(tile_done, last_tile[SLAB0["up6"] - 1] + 1)
                nc.scalar.activation(H[:, d, :], X[:, d, :], ACT.Square).then_inc(square_ready, 1)
            if between is not None:
                between()
            act.wait_ge(sum_ready, n + 1)
            nc.scalar.activation(RT[:, :], MB[0][:, :], ACT.Sqrt, bias=eps, scale=1.0 / D
                                 ).then_inc(root_ready, 1)

        def pe_norm(pe, n):
            for d in range(DT):
                pe.wait_ge(square_ready, DT * n + d + 1)
                last = nc.tensor.matmul(MB[0][:, :], ones, H[:, d, :], start=d == 0, stop=d == DT - 1)
            last.then_inc(sum_ready, 1)

        def dve_norm(dve, n, gain, shift=None, dst=None, sig=None):
            dve.wait_ge(root_ready, n + 1)
            nc.vector.reciprocal(RT[:, :], RT[:, :]).then_inc(inv_ready, 1)
            dve.wait_ge(inv_ready, n + 1)
            dst = dst or (lambda d: H[:, d, :])
            for d in range(DT):
                ins = nc.vector.scalar_tensor_tensor(dst(d), X[:, d, :], gain(d), RT[:, :],
                                                     ALU.mult, ALU.mult)
                if shift is None:
                    ins.then_inc(sig or h_ready, 1)
                else:
                    ins.then_inc(h_part, 1)
            if shift is not None:
                for d in range(DT):
                    dve.wait_ge(h_part, DT * n + d + 1)
                    nc.vector.tensor_scalar(dst(d), dst(d), shift(d), None, ALU.add
                                            ).then_inc(h_ready, 1)

        H_NORM = {0: 0, 1: 1, 3: 2, 4: 3, 5: 4, 6: 5, 7: 6, 8: 7}

        def h_tile(k):
            return HH[:, k, :], HL[:, k, :]

        act_c = sem("act_c")
        ada_used = sem("ada_used")
        ada2_in = [sem("ada2_in0"), sem("ada2_in1")]
        ada2_used = sem("ada2_used")
        cond_sum = sem("cond_sum")
        cond_ready = sem("cond_ready")
        ADA_N = SLAB_K * P

        def ada_add(eng, acc, w, k):
            return eng.tensor_scalar(acc, w, CA[:, k:k + 1], None, ALU.mult) if k == 0 else \
                eng.scalar_tensor_tensor(acc, w, CA[:, k:k + 1], acc, ALU.mult, ALU.add)

        def pe_ada_columns(acc, g, col):
            for j in range(ADA_N // P):
                last = nc.tensor.matmul(MB[1][:, col + j:col + j + 1], acc[:, g, j * P:(j + 1) * P],
                                        ones[:, 0:1], start=True, stop=True)
            last.then_inc(cond_sum, 1)

        def pe_ada(pe):
            for g in range(3):
                pe.wait_ge(ada_used, DT * (g + 1))
                pe_ada_columns(ACC1, g, 8 * g)

        def pe_ada2(pe):
            pe.wait_ge(ada2_used, 3 * DT)
            for g in range(3):
                pe_ada_columns(ACC2, g, 8 * g)

        def act_ada(act):
            act.wait_ge(vec_in, 16)
            act.wait_ge(cst_in, 16)
            nc.scalar.activation(CA[:, :], vec("c", 0, DT), ACT.Silu).then_inc(act_c, 1)

        def cond(dve, l):
            dve.wait_ge(cond_sum, 3 * (l + 1))
            nc.vector.tensor_tensor(COND[:, 24 * l:24 * l + 24], MB[1][:, 0:24], vec("ada_b", 24 * l, 24), ALU.add
                                    ).then_inc(cond_ready, 1)
            dve.wait_ge(cond_ready, 2 * l + 1)
            nc.vector.scalar_tensor_tensor(GS[:, l, :], COND[:, 24 * l + 8:24 * l + 16], 1.0,
                                           vec("norm_g", 8 * l, 8), ALU.add, ALU.mult).then_inc(cond_ready, 1)
            dve.wait_ge(cond_ready, 2 * l + 2)

        def dve_ada(dve):
            dve.wait_ge(vec_in, 16)
            dve.wait_ge(cst_in, 16)
            dve.wait_ge(act_c, 1)
            for s in range(3 * DT):
                g, k = s // DT, s % DT
                dve.wait_ge(slab_in[s % RING], 16 * (s // RING + 1))
                if k:
                    dve.wait_ge(ada_used, s)
                ada_add(nc.vector, ACC1[:, g, :], W[:, s % RING, :], k).then_inc(ada_used, 1)
            cond(dve, 0)

        def dve_ada2(dve, pair):
            for s in (2 * pair, 2 * pair + 1):
                g, k = s // DT, s % DT
                dve.wait_ge(ada2_in[s % 2], 16 * (s // 2 + 1))
                if k:
                    dve.wait_ge(ada2_used, s)
                ada_add(nc.vector, ACC2[:, g, :], W2[:, s % 2, :], k).then_inc(ada2_used, 1)

        CA = sb("CA", [P, DT])

        lru = ExitStack()
        XP = sb("XP", [P, 2, S + 3])
        CV = sb("CV", [P, 2, S])
        SQ = sb("SQ", [P, 2, S])
        RN = sb("RN", [P, 2, S])
        LXB, LXL = twins("LXB", [P, DT, S], lru)
        LR = sb("LR", [P, 4, S], stack=lru)
        LI_ = sb("LI", [P, 4, S], stack=lru)
        LA = sb("LA", [P, 4, S], stack=lru)
        LM = sb("LM", [P, 4, S], stack=lru)
        LZ = sb("LZ", [P, DT, S], stack=lru)
        GW = sb("GW", [P, 16, P], stack=lru)
        LAM = sb("LAM", [P, DT], stack=lru)
        LAT = sb("LAT", [P, 2, DT], stack=lru)
        ACC2 = sb("ACC2", [P, 3, ADA_N], stack=lru)
        W2 = sb("W2", [P, 2, ADA_N], stack=lru)
        ACC1 = LZ[:, 0:3 * ADA_N // S, :].rearrange("p a s -> p (a s)").rearrange("p (g n) -> p g n", g=3)
        lru.close()

        def gate_at(j):
            return j // 2, j % 2

        def pe_lru(pe):
            def gates(first):
                for j in range(first, first + 8):
                    d, g = gate_at(j)
                    pe.wait_ge(V.sem, V.at("lru conv", d))
                    if j >= 4:
                        pe.wait_ge(A.sem, A.at("lru gate", j - 4))
                    nc.tensor.matmul(MB[j % 4][:, :], GW[:, g * 8 + d, :], LXB[:, d, :],
                                     start=True, stop=True).then_inc(T.sem, T.mark("lru gate", j))

            for j in range(6):
                pe_tile(pe, "lru_in", j, h_tile, x_wait(pe, "lru_in") if j == 0 else None)
            pe.wait_ge(gate_w_in, 16)
            gates(0)
            for j in range(6, 10):
                pe_tile(pe, "lru_in", j, h_tile)
            gates(8)
            for j in range(10, 16):
                pe_tile(pe, "lru_in", j, h_tile)
            pe.wait_ge(A.sem, A.at("lru gate", 15))
            pe_ada2(pe)
            for j in range(8):
                pe_tile(pe, "lru_out", j, lambda k: (HH[:, k, :], LXL[:, k, :]),
                        x_wait(pe, "lru_out") if j == 0 else None)

        def arrived(eng, name, j):
            tile = TILE0[name] + j
            eng.wait_ge(tile_done, tile + 1)
            return LB[bank_of(tile)]

        def act_lru(act):
            chain(act, A, nc.scalar.activation(LAT[:, 0, :], vec("lru_lambda", 0, 8), ACT.Abs))
            chain(act, A, nc.scalar.activation(LAT[:, 0, :], LAT[:, 0, :], ACT.Exp, scale=-1.0))
            nc.scalar.activation(LAT[:, 0, :], LAT[:, 0, :], ACT.Ln, bias=one
                                 ).then_inc(A.sem, A.mark("lambda ln"))
            act.wait_ge(V.sem, V.at("pads"))
            def xp(j):
                bank = arrived(act, "lru_in", j)
                if j >= 2:
                    act.wait_ge(V.sem, V.at("lru conv", j - 2))
                nc.scalar.activation(XP[:, j % 2, 3:], bank[:, :], ACT.Copy).then_inc(A.sem, A.mark("lru xp", j))

            def silu_z(j):
                bank = arrived(act, "lru_in", 8 + j)
                nc.scalar.activation(LZ[:, j, :], bank[:, :], ACT.Silu).then_inc(A.sem, A.mark("lru silu", j))

            def gates(first):
                for j in range(first, first + 8):
                    d, g = gate_at(j)
                    act.wait_ge(T.sem, T.at("lru gate", j))
                    if d >= 4:
                        act.wait_ge(V.sem, V.at("lru b", d - 4))
                    nc.scalar.activation((LI_ if g else LR)[:, d % 4, :], MB[j % 4][:, :], ACT.Sigmoid,
                                         bias=vec("lru_gate_b", 8 * g + d)
                                         ).then_inc(A.sem, A.mark("lru gate", j))

            def decays(first):
                act.wait_ge(A.sem, A.at("lru gate", 2 * first + 7))
                for d in range(first, first + 4):
                    if d >= 4:
                        act.wait_ge(V.sem, V.at("lru h", d - 4))
                    nc.scalar.activation(LA[:, d % 4, :], LR[:, d % 4, :], ACT.Exp, scale=LAM[:, d:d + 1]
                                         ).then_inc(A.sem, A.mark("lru a", d))
                    nc.scalar.activation(LR[:, d % 4, :], LR[:, d % 4, :], ACT.Tanh, scale=LAM[:, d:d + 1]
                                         ).then_inc(A.sem, A.mark("lru tanh", d))
                for d in range(first, first + 4):
                    act.wait_ge(A.sem, A.at("lru a", d))
                    nc.scalar.activation(LM[:, d % 4, :], LA[:, d % 4, :], ACT.Square
                                         ).then_inc(A.sem, A.mark("lru a2", d))

            def mults(first):
                for d in range(first, first + 4):
                    act.wait_ge(V.sem, V.at("lru m2", d))
                    nc.scalar.activation(LM[:, d % 4, :], LM[:, d % 4, :], ACT.Sqrt, scale=-1.0
                                         ).then_inc(A.sem, A.mark("lru mult", d))

            for j in range(6):
                xp(j)
            gates(0)
            xp(6)
            act.wait_ge(V.sem, V.at("lambda"))
            decays(0)
            xp(7)
            mults(0)
            silu_z(0)
            silu_z(1)
            gates(8)
            silu_z(2)
            decays(4)
            silu_z(3)
            mults(4)
            for j in range(4, 8):
                silu_z(j)
            for d in range(8):
                act.wait_ge(V.sem, V.at("lru y", d))
                x_high(act, LXB[:, d, :], HH[:, d, :])

        def conv(dve, xp, dst, w, j, stride, bias, step):
            first = nc.vector.tensor_scalar(dst, xp[:, 0:S], vec(w, j), bias, ALU.mult,
                                            ALU.bypass if bias is None else ALU.add) \
                if bias is not None else nc.vector.tensor_scalar(dst, xp[:, 0:S], vec(w, j), None, ALU.mult)
            chain(dve, V, first)
            for t in range(1, 4):
                ins = nc.vector.scalar_tensor_tensor(dst, xp[:, t:t + S], vec(w, t * stride + j), dst,
                                                     ALU.mult, ALU.add)
                if t < 3:
                    chain(dve, V, ins)
                else:
                    ins.then_inc(V.sem, V.mark(*step))

        def dve_lru(dve):
            nc.vector.memset(XP[:, :, 0:3], 0.0).then_inc(V.sem, V.mark("pads"))
            dve.wait_ge(A.sem, A.at("lambda ln"))
            chain(dve, V, nc.vector.tensor_scalar(LAT[:, 1, :], vec("lru_lambda", 0, 8), -1.0, 0.0,
                                                  ALU.mult, ALU.max))
            chain(dve, V, nc.vector.tensor_tensor(LAT[:, 1, :], LAT[:, 1, :], LAT[:, 0, :], ALU.add))
            nc.vector.tensor_scalar(LAM[:, :], LAT[:, 1, :], -RG_C, None, ALU.mult
                                    ).then_inc(V.sem, V.mark("lambda"))
            for j in range(8):
                dve.wait_ge(A.sem, A.at("lru xp", j))
                conv(dve, XP[:, j % 2, :], LXB[:, j, :], "lru_conv_w", j, 8, vec("lru_conv_b", j),
                     ("lru conv", j))
                dve_ada2(dve, j)
            for first in (0, 4):
                for d in range(first, first + 4):
                    dve.wait_ge(A.sem, A.at("lru gate", 2 * d + 1))
                    dve.wait_ge(V.sem, V.at("lru conv", d))
                    nc.vector.tensor_tensor(LI_[:, d % 4, :], LI_[:, d % 4, :], LXB[:, d, :], ALU.mult
                                            ).then_inc(V.sem, V.mark("lru ix", d))
                for d in range(first, first + 4):
                    dve.wait_ge(A.sem, A.at("lru a2", d))
                    nc.vector.scalar_tensor_tensor(LM[:, d % 4, :], LM[:, d % 4, :], 1.0, LR[:, d % 4, :],
                                                   ALU.add, ALU.mult).then_inc(V.sem, V.mark("lru m2", d))
                dve_ada2(dve, 8 + first // 2)
                for d in range(first, first + 4):
                    dve.wait_ge(A.sem, A.at("lru mult", d))
                    dve.wait_ge(V.sem, V.at("lru ix", d))
                    nc.vector.tensor_tensor(LM[:, d % 4, :], LM[:, d % 4, :], LI_[:, d % 4, :], ALU.mult
                                            ).then_inc(V.sem, V.mark("lru b", d))
                for d in range(first, first + 4):
                    dve.wait_ge(V.sem, V.at("lru b", d))
                    nc.vector.tensor_tensor_scan(LXB[:, d, :], LA[:, d % 4, :], LM[:, d % 4, :], 0.0,
                                                 ALU.mult, ALU.add).then_inc(V.sem, V.mark("lru h", d))
                dve_ada2(dve, 9 + first // 2)
            for d in range(8):
                dve.wait_ge(A.sem, A.at("lru silu", d))
                dve.wait_ge(V.sem, V.at("lru h", d))
                nc.vector.tensor_tensor(LXB[:, d, :], LXB[:, d, :], LZ[:, d, :], ALU.mult
                                        ).then_inc(V.sem, V.mark("lru y", d))
                if d % 2:
                    x_low(dve, "lru_out", d - 1, LXB[:, d - 1, :], LXL[:, d - 1, :], HH[:, d - 1, :])
            residual(dve, "lru_out", lambda d: COND[:, 16 + d:17 + d])

        def pool_lru(pool):
            pool.wait_ge(cst_in, 16)
            pool_in(pool, "lru_in")
            mix_split(pool, "lru_out", 0, RING)
            for d in range(1, DT, 2):
                x_low(pool, "lru_out", d, LXB[:, d, :], LXL[:, d, :], HH[:, d, :])
            mix_split(pool, "lru_out", RING)

        def residual(dve, name, gate):
            for d in range(8):
                bank = arrived(dve, name, d)
                nc.vector.scalar_tensor_tensor(X[:, d, :], bank[:, :], gate(d), X[:, d, :],
                                               ALU.mult, ALU.add).then_inc(x_ready, 1)

        RES = {n: i for i, n in enumerate(
            ["lru_out", "gdn_out", "final", "down0", "down1", "hy_out", "down2", "down3", "down4", "down5",
             "sa_out", "down6", "down7"])}
        NORM_AFTER = {1: RES["lru_out"], 2: RES["gdn_out"], 3: RES["final"], 4: RES["down1"], 5: RES["hy_out"],
                      6: RES["down3"], 7: RES["down5"], 8: RES["sa_out"]}

        ffn = ExitStack()
        DH = sb("DH", [P, PART[0], S], F32R, stack=ffn)
        DL = sb("DL", [P, PART[0], S], F32R, stack=ffn)
        WL = sb("WL", [P, RING, SLAB_K * P], F32R, stack=ffn)
        FGT = sb("FGT", [P, 2, S], stack=ffn)
        PRD = sb("PRD", [P, 2, S], stack=ffn)
        ffn.close()
        HID0 = [FT * (p // 2) + PART[0] * (p % 2) for p in range(8)]

        def split_high(act, s, k):
            if s >= RING:
                act.wait_ge(tile_done, last_tile[s - RING] + 1)
            act.wait_ge(slab_in[s % RING], 16 * (s // RING + 1))
            nc.scalar.activation(WH[:, s % RING, 0:k * P], W[:, s % RING, 0:k * P], ACT.Copy
                                 ).then_inc(w_high, 1)

        def split_low(pool, s, k):
            pool.wait_ge(w_high, SPLIT_NO[s] + 1)
            nc.gpsimd.tensor_tensor(WL[:, s % RING, 0:k * P], W[:, s % RING, 0:k * P],
                                    WH[:, s % RING, 0:k * P].bitcast(F32), ALU.subtract).then_inc(w_ready, 1)

        def pe_up_tile(pe, name, j, wait_h):
            s = SLAB0[name] + j
            for k in range(DT):
                if wait_h:
                    x_wait(pe, wait_h)(k)
                c = slice(k * P, (k + 1) * P)
                last = three(LB[bank_of(TILE0[name] + j)][:, :], WH[:, s % RING, c], WL[:, s % RING, c],
                             *h_tile(k), k == 0, k == DT - 1)
            last.then_inc(tile_done, 1)

        def pe_ffn(pe, f):
            for p in (2 * f, 2 * f + 1):
                name = f"up{p}"
                for j in range(RING):
                    pe.wait_ge(*freed(TILE0[name] + j - 4))
                    pe.wait_ge(w_ready, SPLIT_NO[SLAB0[name] + j] + 1)
                    pe_up_tile(pe, name, j, f"ffn{f}" if p % 2 == 0 and j == 0 else None)
                with pe.Fori(1, 2 * PART[p % 2] // RING) as i:
                    for j in range(RING):
                        pe.wait_ge(prod_ready if j % 2 else silu_ready, i * 2 + (HID0[p] + j // 2 - 1))
                        pe.wait_ge(w_ready, i * RING + (SPLIT_NO[SLAB0[name] + j] + 1))
                        pe_up_tile(pe, name, j, None)
                name = f"down{p}"
                for j in range(8):
                    tile = TILE0[name] + j
                    pe.wait_ge(*freed(tile - 4))
                    for q in range(2):
                        n = PART[p % 2] // 2
                        s = SLAB0[name] + 2 * j + q
                        pe.wait_ge(w_ready, SPLIT_NO[s] + 1)
                        for kk in range(n):
                            k = q * n + kk
                            if j == 0:
                                pe.wait_ge(hid_ready, HID0[p] + k + 1)
                            c = slice(kk * P, (kk + 1) * P)
                            last = three(LB[bank_of(tile)][:, :], WH[:, s % RING, c], WL[:, s % RING, c],
                                         DH[:, k, :], DL[:, k, :], k == 0, k == 2 * n - 1)
                    last.then_inc(tile_done, 1)

        def act_ffn_high(act, n, f):
            act.wait_ge(x_ready, DT * NORM_AFTER[n] + DT)
            for j in range(RING):
                split_high(act, SLAB0[f"up{2 * f}"] + j, DT)

        def act_ffn(act, f):
            act_h_high(act, f"ffn{f}", FFN_NORM[f])
            for p in (2 * f, 2 * f + 1):
                name = f"up{p}"
                k_down = PART[p % 2] // 2

                def gate(m):
                    if m >= 2:
                        act.wait_ge(prod_ready, HID0[p] + m - 1)
                    bank = arrived(act, name, 2 * m)
                    nc.scalar.activation(FGT[:, m % 2, :], bank[:, :], ACT.Silu).then_inc(silu_ready, 1)

                for m in range(2):
                    gate(m)
                    for j in range(2):
                        split_high(act, SLAB0[name] + 2 * m + j + RING, DT)
                with act.Fori(1, PART[p % 2] // 2 - 1) as i:
                    for m in range(2):
                        act.wait_ge(prod_ready, i * 2 + (HID0[p] + m - 1))
                        act.wait_ge(tile_done, i * 4 + (TILE0[name] + 2 * m + 1))
                        nc.scalar.activation(FGT[:, m, :], LB[bank_of(TILE0[name] + 2 * m)][:, :], ACT.Silu
                                             ).then_inc(silu_ready, 1)
                        for j in range(2):
                            s = SLAB0[name] + 2 * m + j
                            act.wait_ge(tile_done, i * 4 + (TILE0[name] + 2 * m + j + 1))
                            act.wait_ge(slab_in[s % RING], i * 16 + 16 * (s // RING + 2))
                            nc.scalar.activation(WH[:, s % RING, :], W[:, s % RING, :], ACT.Copy
                                                 ).then_inc(w_high, 1)
                for m in range(2):
                    gate(PART[p % 2] - 2 + m)
                    for j in range(2):
                        split_high(act, SLAB0[f"down{p}"] + 2 * m + j, k_down)
                for j in range(4, 16):
                    split_high(act, SLAB0[f"down{p}"] + j, k_down)
                if p % 2 == 0:
                    for j in range(RING):
                        split_high(act, SLAB0[f"up{p + 1}"] + j, DT)

        def pool_ffn(pool, f):
            for j in range(RING):
                split_low(pool, SLAB0[f"up{2 * f}"] + j, DT)
            h_low(pool, f"ffn{f}", 1)
            for p in (2 * f, 2 * f + 1):
                name = f"up{p}"
                with pool.Fori(1, 2 * PART[p % 2] // RING) as i:
                    for j in range(RING):
                        s = SLAB0[name] + j
                        pool.wait_ge(w_high, i * RING + (SPLIT_NO[s] + 1))
                        nc.gpsimd.tensor_tensor(WL[:, s % RING, :], W[:, s % RING, :],
                                                WH[:, s % RING, :].bitcast(F32), ALU.subtract
                                                ).then_inc(w_ready, 1)
                for j in range(16):
                    split_low(pool, SLAB0[f"down{p}"] + j, PART[p % 2] // 2)
                if p % 2 == 0:
                    for j in range(RING):
                        split_low(pool, SLAB0[f"up{p + 1}"] + j, DT)

        def dve_ffn(dve, f):
            h_low(dve, f"ffn{f}", 0)
            for p in (2 * f, 2 * f + 1):
                name = f"up{p}"
                with dve.Fori(0, PART[p % 2] // 2) as i:
                    for m in range(2):
                        def hid(tensor):
                            return tensor[:, bass.ds(i * 2 + m, 1), :].rearrange("p a s -> p (a s)")

                        dve.wait_ge(silu_ready, i * 2 + (HID0[p] + m + 1))
                        dve.wait_ge(tile_done, i * 4 + (TILE0[name] + 2 * m + 2))
                        nc.vector.tensor_tensor(PRD[:, m, :], FGT[:, m, :], LB[bank_of(TILE0[name] + 2 * m + 1)][:, :],
                                                ALU.mult).then_inc(prod_ready, 1)
                        dve.wait_ge(prod_ready, i * 2 + (HID0[p] + m + 1))
                        nc.vector.tensor_copy(hid(DH), PRD[:, m, :]).then_inc(hid_high, 1)
                        dve.wait_ge(hid_high, i * 2 + (HID0[p] + m + 1))
                        nc.vector.tensor_tensor(hid(DL), PRD[:, m, :], hid(DH).bitcast(F32), ALU.subtract
                                                ).then_inc(hid_ready, 1)
                residual(dve, f"down{p}", lambda d: 0.5)

        FFN_NORM = [3, 5, 6, 8]

        def up_freed(p):
            return lambda j: (prod_ready if j % 2 else silu_ready, HID0[p] + j // 2 + 1)

        def res_freed(name):
            return lambda j: (x_ready, 8 * RES[name] + j + 1)

        FREED = {
            "lru_in": lambda j: (A.sem, A.at("lru xp", j) if j < 8 else A.at("lru silu", j - 8)),
            **{f"up{p}": up_freed(p) for p in range(8)},
            **{n: res_freed(n) for n in RES if n != "final"},
        }

        gdn = ExitStack()
        GK = sb("GK", [P, GH, S], stack=gdn)
        GQ, GOL = twins("GQ", [P, GH, S], gdn)
        GV = sb("GV", [P, GH, S], stack=gdn)
        GZ = sb("GZ", [P, GH, S], stack=gdn)
        GROWS = sb("GROWS", [P, 4, S], stack=gdn)
        GROW = GROWS[0:GH]
        GBETAS = sb("GBETAS", [P, 2, S], stack=gdn)
        GBETA = GBETAS[0:GH]
        GCOL = sb("GCOL", [P, 3, NC, GH], stack=gdn)
        GSEL = sb("GSEL", [GH, NC, GH], stack=gdn)
        GEL = sb("GEL", [P, NC, GH], stack=gdn)
        GEA = sb("GEA", [GH, 1], stack=gdn)
        gt = [{n: sb(f"G{n}{g}", [P, 4, P], stack=gdn) for n in ("KT", "QD", "KD", "VB")} for g in range(2)]
        for g in range(2):
            for i, n in enumerate(("T", "U", "Y", "L")):
                gt[g][n] = HHF[:, 4 * g + i, :].rearrange("p (h t) -> p h t", h=4)
            for i, n in enumerate(("TMP", "AT", "AM")):
                gt[g][n] = H[:, 2 + 3 * g + i, :].rearrange("p (h t) -> p h t", h=4)
        GS_ = sb("GSTATE", [P, GH, P], stack=gdn)
        GVN = [H[:, g, :].rearrange("p (h t) -> p h t", h=4) for g in range(2)]
        gdn.close()
        GO = GQ
        GB = [[MB[b] for b in range(4)], [LB[b] for b in range(4)]]

        def four(bank):
            return bank[:, :].rearrange("p (h t) -> p h t", h=4)

        def fm(tensor, c, g):
            return tensor[:, 4 * g:4 * g + 4, c * CH:(c + 1) * CH]

        GNORM = [(GK, h) for h in range(8)] + [(GQ, h) for h in range(8)]

        def gconv_dst(j):
            return (GK, GQ, GV)[j // 8][:, j % 8, :]

        def pe_gdn(pe):
            pe_tile(pe, "gdn_in", 0, h_tile, x_wait(pe, "gdn_in"),
                    outs=[(MB[1][0:GH, :], 0, GH), (MB[2][0:GH, :], GH, 2 * GH)])
            for j in range(1, 19):
                pe_tile(pe, "gdn_in", j, h_tile)
            for j in range(16):
                pe.wait_ge(A.sem, A.at("gdn sq", j))
                if j < 2:
                    pe.wait_ge(A.sem, A.at("beta"))
                else:
                    pe.wait_ge(A.sem, A.at("gdn root", j - 2))
                nc.tensor.matmul(MB[j % 2 + 2][:, :], ones, SQ[:, j % 2, :], start=True, stop=True
                                 ).then_inc(T.sem, T.mark("gdn sum", j))
            for j in range(19, 33):
                pe_tile(pe, "gdn_in", j, h_tile)
            pe.wait_ge(A.sem, A.at("gdn ed"))
            pe.wait_ge(V.sem, V.at("gdn sel"))
            rows = [GROW[:, 1, :], GBETA[:, 0, :], GROW[:, 3, :]]
            for n, row in enumerate(rows):
                for c in range(NC):
                    nc.tensor.matmul(MB[1][:, (n * NC + c) * GH:(n * NC + c + 1) * GH],
                                     row[:, c * CH:(c + 1) * CH], ident[0:GH, 0:GH], start=True, stop=True)
            nc.tensor.matmul(MB[1][:, 96:128], ones[0:GH, :], GSEL[:, :, :].rearrange("p c h -> p (c h)"),
                             start=True, stop=True).then_inc(T.sem, T.mark("gdn cols"))
            for g in range(2):
                pe.wait_ge(A.sem, A.at("gdn z", 7))
                pe.wait_ge(V.sem, V.at("gdn qk", 15))
            pe.wait_ge(V.sem, V.at("gdn cols"))
            for c in range(NC):
                for g in range(2):
                    B = GB[g]
                    if c:
                        pe.wait_ge(A.sem, A.at("gdn vn", c - 1, g))
                        pe.wait_ge(A.sem, A.at("gdn o", c - 1, g))
                        pe.wait_ge(V.sem, V.at("gdn state", c - 1, g))
                    for n, row in ((0, GROWS[:, 1, :]), (1, GROWS[:, 2, :]), (2, GBETAS[:, 1, :])):
                        for h in range(4):
                            last = nc.tensor.matmul(
                                B[n][:, h * P:(h + 1) * P],
                                ident[:, 4 * g + h:4 * g + h + 1].to_broadcast([P, P]),
                                row[:, c * CH:(c + 1) * CH], start=True, stop=True)
                    last.then_inc(T.sem, T.mark("gdn rows", c, g))
                    for h in range(4):
                        kc = GK[:, 4 * g + h, c * CH:(c + 1) * CH]
                        last = nc.tensor.matmul(B[3][:, h * P:(h + 1) * P], kc, kc, start=True, stop=True)
                    last.then_inc(T.sem, T.mark("gdn kk", c, g))
                for g in range(2):
                    B = GB[g]
                    pe.wait_ge(V.sem, V.at("gdn tmp", c, g))
                    for h in range(4):
                        last = nc.tensor.matmul(B[0][:, h * P:(h + 1) * P],
                                                GK[:, 4 * g + h, c * CH:(c + 1) * CH],
                                                GQ[:, 4 * g + h, c * CH:(c + 1) * CH], start=True, stop=True)
                    last.then_inc(T.sem, T.mark("gdn qk", c, g))
                    pe.wait_ge(V.sem, V.at("gdn kt", c, g))
                    for n, src in ((1, GK), (2, GV)):
                        for h in range(4):
                            last = nc.tensor.transpose(B[n][:, h * P:(h + 1) * P],
                                                       src[:, 4 * g + h, c * CH:(c + 1) * CH], ident)
                    last.then_inc(T.sem, T.mark("gdn tok", c, g))
                for l in range(LEVELS):
                    if l == 1 and c:
                        gdn_osum(pe, c - 1)
                    for g in range(2):
                        B, b = GB[g], gt[g]
                        pe.wait_ge(G.sem, G.at("gdn l", c, g, l))
                        if l == 0:
                            pe.wait_ge(V.sem, V.at("gdn at", c, g))
                        else:
                            pe.wait_ge(V.sem, V.at("gdn tu", c, g, l - 1))
                        for h in range(4):
                            last = nc.tensor.matmul(B[0][:, h * P:(h + 1) * P], b["L"][:, h, :],
                                                    ident if l == 0 else b["U"][:, h, :], start=True, stop=True)
                        last.then_inc(T.sem, T.mark("gdn y", c, g, l))
                    for g in range(2 if l else 0):
                        B, b = GB[g], gt[g]
                        pe.wait_ge(A.sem, A.at("gdn y", c, g, l))
                        for h in range(4):
                            last = nc.tensor.matmul(B[1][:, h * P:(h + 1) * P], b["T"][:, h, :],
                                                    b["Y"][:, h, :], start=True, stop=True)
                        for h in range(4 if l < LEVELS - 1 else 0):
                            last = nc.tensor.matmul(B[2][:, h * P:(h + 1) * P], b["Y"][:, h, :],
                                                    b["T"][:, h, :], start=True, stop=True)
                        last.then_inc(T.sem, T.mark("gdn uy", c, g, l))
                if c:
                    for g in range(2):
                        b = gt[g]
                        pe.wait_ge(A.sem, A.at("gdn oroot", c - 1, g))
                        for h in range(4):
                            last = nc.tensor.matmul(GB[g][3][:, h * P:(h + 1) * P], b["KT"][:, h, :],
                                                    GS_[:, 4 * g + h, :], start=True, stop=True)
                        last.then_inc(T.sem, T.mark("gdn ks", c, g))
                for g in range(2):
                    b = gt[g]
                    pe.wait_ge(V.sem, V.at("gdn tu", c, g, LEVELS - 1))
                    pe.wait_ge(V.sem, V.at("gdn r", c, g) if c else V.at("gdn vb", c, g))
                    for h in range(4):
                        last = nc.tensor.matmul(GB[g][0][:, h * P:(h + 1) * P], b["U"][:, h, :],
                                                b["VB"][:, h, :], start=True, stop=True)
                    last.then_inc(T.sem, T.mark("gdn vn", c, g))
                for g in range(2):
                    b = gt[g]
                    pe.wait_ge(A.sem, A.at("gdn vn", c, g))
                    for h in range(4):
                        if c:
                            nc.tensor.matmul(GB[g][1][:, h * P:(h + 1) * P], GS_[:, 4 * g + h, :],
                                             b["QD"][:, h, :], start=True, stop=False)
                        last = nc.tensor.matmul(GB[g][1][:, h * P:(h + 1) * P], GVN[g][:, h, :],
                                                b["AT"][:, h, :], start=not c, stop=True)
                    last.then_inc(T.sem, T.mark("gdn o", c, g))
                    for h in range(4):
                        last = nc.tensor.matmul(GB[g][2][:, h * P:(h + 1) * P], b["KD"][:, h, :],
                                                GVN[g][:, h, :], start=True, stop=True)
                    last.then_inc(T.sem, T.mark("gdn su", c, g))
            gdn_osum(pe, NC - 1)
            for j in range(8):
                pe_tile(pe, "gdn_out", j, lambda k: (HH[:, k, :], GOL[:, k, :]),
                        x_wait(pe, "gdn_out") if j == 0 else None)

        def gdn_osum(pe, c):
            for g in range(2):
                pe.wait_ge(A.sem, A.at("gdn osq", c, g))
                pe.wait_ge(V.sem, V.at("gdn am", c + 1, g) if c < NC - 1 else V.at("gdn r", c, g))
                nc.tensor.matmul(GB[g][3][:, :], ones, SQ[:, g, :], start=True, stop=True
                                 ).then_inc(T.sem, T.mark("gdn osum", c, g))

        def act_gdn(act):
            nc.scalar.activation(GEA[:, :], vec("gdn_a_log", rows=GH), ACT.Exp).then_inc(A.sem, A.mark("gdn ea"))
            act.wait_ge(V.sem, V.at("gdn zero"))
            act.wait_ge(tile_done, TILE0["gdn_in"] + 1)
            nc.scalar.activation(GBETA[:, 0, :], MB[2][0:GH, :], ACT.Sigmoid).then_inc(A.sem, A.mark("beta"))
            act.wait_ge(V.sem, V.at("gdn u"))
            chain(act, A, nc.scalar.activation(GROW[:, 1, :], GROW[:, 0, :], ACT.Abs))
            chain(act, A, nc.scalar.activation(GROW[:, 1, :], GROW[:, 1, :], ACT.Exp, scale=-1.0))
            nc.scalar.activation(GROW[:, 1, :], GROW[:, 1, :], ACT.Ln, bias=one[0:GH, :]
                                 ).then_inc(A.sem, A.mark("gdn ln"))

            def copy_in(j):
                bank = arrived(act, "gdn_in", j + 1)
                if j >= 2:
                    act.wait_ge(V.sem, V.at("gdn conv", j - 2))
                nc.scalar.activation(XP[:, j % 2, 3:], bank[:, :], ACT.Copy).then_inc(A.sem, A.mark("gdn xp", j))

            def silu(j):
                act.wait_ge(V.sem, V.at("gdn conv", j))
                nc.scalar.activation(gconv_dst(j), CV[:, j % 2, :], ACT.Silu).then_inc(A.sem, A.mark("gdn silu", j))

            copy_in(0)
            for j in range(1, 16):
                copy_in(j)
                silu(j - 1)
            silu(15)
            for j in range(16):
                tensor, h = GNORM[j]
                act.wait_ge(A.sem, A.at("gdn silu", j))
                if j >= 2:
                    act.wait_ge(T.sem, T.at("gdn sum", j - 2))
                nc.scalar.activation(SQ[:, j % 2, :], tensor[:, h, :], ACT.Square).then_inc(A.sem, A.mark("gdn sq", j))
                if j:
                    root(act, j - 1)
            root(act, 15)
            for j in range(16, 24):
                copy_in(j)
                if j > 16:
                    silu(j - 1)
            silu(23)
            for j in range(8):
                bank = arrived(act, "gdn_in", 25 + j)
                nc.scalar.activation(GZ[:, j, :], bank[:, :], ACT.Silu).then_inc(A.sem, A.mark("gdn z", j))
            act.wait_ge(V.sem, V.at("gdn cum"))
            nc.scalar.activation(GROW[:, 2, :], GROW[:, 1, :], ACT.Exp).then_inc(A.sem, A.mark("gdn eg"))
            for c in range(NC):
                nc.scalar.activation(GROW[:, 3, c * CH:(c + 1) * CH], GROW[:, 1, c * CH:(c + 1) * CH], ACT.Exp,
                                     bias=GROW[:, 1, (c + 1) * CH - 1:(c + 1) * CH], scale=-1.0
                                     ).then_inc(A.sem, A.mark("gdn ed") if c == NC - 1 else A.mark())
            for c in range(NC):
                for g in range(2):
                    b = gt[g]
                    for n in ("AT", "AM"):
                        act.wait_ge(G.sem, G.at("gdn at", c, g)) if n == "AT" else \
                            act.wait_ge(V.sem, V.at("gdn amask", c, g))
                        nc.scalar.activation(b[n][:, :, :], b[n][:, :, :], ACT.Exp
                                             ).then_inc(A.sem, A.mark("gdn exp" + n, c, g))
                if c:
                    osq(act, c - 1)
                for l in range(1, LEVELS):
                    if l == 2 and c:
                        oroot(act, c - 1)
                    for g in range(2):
                        act.wait_ge(T.sem, T.at("gdn y", c, g, l))
                        nc.scalar.activation(gt[g]["Y"][:, :, :], four(GB[g][0]), ACT.Copy
                                             ).then_inc(A.sem, A.mark("gdn y", c, g, l))
                for g in range(2):
                    act.wait_ge(T.sem, T.at("gdn vn", c, g))
                    nc.scalar.activation(GVN[g], four(GB[g][0]), ACT.Copy).then_inc(A.sem, A.mark("gdn vn", c, g))
                for g in range(2):
                    act.wait_ge(T.sem, T.at("gdn o", c, g))
                    nc.scalar.activation(fm(GO, c, g), four(GB[g][1]), ACT.Copy).then_inc(A.sem, A.mark("gdn o", c, g))
            osq(act, NC - 1)
            oroot(act, NC - 1)
            for h in range(GH):
                act.wait_ge(G.sem, G.at("gdn y", NC - 1, h // 4))
                x_high(act, GO[:, h, :], HH[:, h, :])

        def osq(act, c):
            for g in range(2):
                act.wait_ge(A.sem, A.at("gdn o", c, g))
                if c:
                    act.wait_ge(T.sem, T.at("gdn osum", c - 1, g))
                nc.scalar.activation(SQ[:, g, :].rearrange("p (h t) -> p h t", h=4), fm(GO, c, g), ACT.Square
                                     ).then_inc(A.sem, A.mark("gdn osq", c, g))

        def root(act, j):
            act.wait_ge(T.sem, T.at("gdn sum", j))
            if j >= 2:
                act.wait_ge(V.sem, V.at("gdn qk", j - 2))
            nc.scalar.activation(RN[:, j % 2, :], MB[j % 2 + 2][:, :], ACT.Sqrt, bias=eps
                                 ).then_inc(A.sem, A.mark("gdn root", j))

        def oroot(act, c):
            for g in range(2):
                act.wait_ge(T.sem, T.at("gdn osum", c, g))
                if c:
                    act.wait_ge(V.sem, V.at("gdn on", c - 1, g))
                nc.scalar.activation(RN[:, g, :], GB[g][3][:, :], ACT.Sqrt, bias=eps, scale=1.0 / P
                                     ).then_inc(A.sem, A.mark("gdn oroot", c, g))

        def dve_gdn(dve):
            nc.vector.memset(GROWS[:, :, :], 0.0).then_inc(V.sem, V.mark())
            nc.vector.memset(GBETAS[:, :, :], 0.0).then_inc(V.sem, V.mark("gdn zero"))
            dve.wait_ge(V.sem, V.at("gdn zero"))
            dve.wait_ge(tile_done, TILE0["gdn_in"] + 1)
            nc.vector.tensor_scalar(GROW[:, 0, :], MB[1][0:GH, :], vec("gdn_dt_bias", rows=GH), None, ALU.add
                                    ).then_inc(V.sem, V.mark("gdn u"))
            dve.wait_ge(A.sem, A.at("gdn ln"))
            chain(dve, V, nc.vector.scalar_tensor_tensor(GROW[:, 0, :], GROW[:, 0, :], 0.0, GROW[:, 1, :],
                                                         ALU.max, ALU.add))
            chain(dve, V, nc.vector.tensor_scalar(GROW[:, 0, :], GROW[:, 0, :], GEA[:, :], -1.0,
                                                  ALU.mult, ALU.mult))
            for c in range(NC):
                nc.vector.tensor_tensor_scan(GROW[:, 1, c * CH:(c + 1) * CH], ones[0:GH, :],
                                             GROW[:, 0, c * CH:(c + 1) * CH], 0.0, ALU.mult, ALU.add
                                             ).then_inc(V.sem, V.mark("gdn cum") if c == NC - 1 else V.mark())
            for j in range(16):
                dve.wait_ge(A.sem, A.at("gdn xp", j))
                if j >= 2:
                    dve.wait_ge(A.sem, A.at("gdn silu", j - 2))
                conv(dve, XP[:, j % 2, :], CV[:, j % 2, :], "gdn_conv_w", GCONV[j], 24, None, ("gdn conv", j))
            for j in range(16):
                tensor, h = GNORM[j]
                dve.wait_ge(A.sem, A.at("gdn root", j))
                chain(dve, V, nc.vector.reciprocal(RN[:, j % 2, :], RN[:, j % 2, :]))
                nc.vector.scalar_tensor_tensor(tensor[:, h, :], tensor[:, h, :], 1.0 if j < 8 else P ** -0.5,
                                               RN[:, j % 2, :], ALU.mult, ALU.mult
                                               ).then_inc(V.sem, V.mark("gdn qk", j))
            for j in range(16, 24):
                dve.wait_ge(A.sem, A.at("gdn xp", j))
                dve.wait_ge(A.sem, A.at("gdn silu", j - 2))
                conv(dve, XP[:, j % 2, :], CV[:, j % 2, :], "gdn_conv_w", GCONV[j], 24, None, ("gdn conv", j))
            dve.wait_ge(A.sem, A.at("gdn eg"))
            nc.vector.tensor_tensor(GBETA[:, 1, :], GBETA[:, 0, :], GROW[:, 2, :], ALU.mult).then_inc(V.sem, V.mark())
            nc.vector.tensor_tensor(GSEL[:, :, :], heads(GROW[:, 2, CH - 1::CH], NC, GH),
                                    per_head(ident[0:GH, 0:GH], NC), ALU.mult).then_inc(V.sem, V.mark("gdn sel"))
            dve.wait_ge(T.sem, T.at("gdn cols"))
            nc.vector.tensor_copy(GCOL[:, :, :, :].rearrange("p n c h -> p (n c h)"), MB[1][:, 0:96]
                                  ).then_inc(V.sem, V.mark())
            nc.vector.tensor_copy(GEL[:, :, :].rearrange("p c h -> p (c h)"), MB[1][:, 96:128]
                                  ).then_inc(V.sem, V.mark("gdn cols"))
            dve.wait_ge(V.sem, V.at("gdn cols"))
            for c in range(NC):
                for g in range(2):
                    B, b = GB[g], gt[g]
                    gcol = heads(GCOL[:, 0, c, 4 * g:4 * g + 4], 4)
                    dve.wait_ge(T.sem, T.at("gdn rows", c, g))
                    if c:
                        dve.wait_ge(G.sem, G.at("gdn at", c - 1, g))
                    nc.vector.tensor_tensor(b["TMP"][:, :, :], four(B[0]), gcol, ALU.subtract
                                            ).then_inc(V.sem, V.mark("gdn tmp", c, g))
                    dve.wait_ge(V.sem, V.at("gdn tmp", c, g))
                    nc.vector.scalar_tensor_tensor(b["AM"][:, :, :], b["TMP"][:, :, :], -1.0,
                                                   per_head(cst("keep_lower_strict"), 4), ALU.mult, ALU.add
                                                   ).then_inc(V.sem, V.mark("gdn amask", c, g))
                    nc.vector.tensor_tensor(b["QD"][:, :, :], fm(GQ, c, g), four(B[1]), ALU.mult
                                            ).then_inc(V.sem, V.mark("gdn qd", c, g))
                    nc.vector.tensor_tensor(b["KT"][:, :, :], fm(GK, c, g), four(B[2]), ALU.mult
                                            ).then_inc(V.sem, V.mark("gdn kt", c, g))
                for g in range(2):
                    B, b = GB[g], gt[g]
                    dve.wait_ge(A.sem, A.at("gdn expAM", c, g))
                    dve.wait_ge(T.sem, T.at("gdn kk", c, g))
                    nc.vector.tensor_tensor(b["AM"][:, :, :], b["AM"][:, :, :], four(B[3]), ALU.mult
                                            ).then_inc(V.sem, V.mark("gdn am", c, g))
                    dve.wait_ge(T.sem, T.at("gdn qk", c, g))
                    nc.vector.tensor_tensor(b["AT"][:, :, :], b["AT"][:, :, :], four(B[0]), ALU.mult
                                            ).then_inc(V.sem, V.mark("gdn at", c, g))
                    dve.wait_ge(T.sem, T.at("gdn tok", c, g))
                    nc.vector.tensor_tensor(b["KD"][:, :, :], heads(GCOL[:, 2, c, 4 * g:4 * g + 4], 4),
                                            four(B[1]), ALU.mult).then_inc(V.sem, V.mark("gdn kd", c, g))
                    nc.vector.tensor_tensor(b["VB"][:, :, :], heads(GCOL[:, 1, c, 4 * g:4 * g + 4], 4),
                                            four(B[2]), ALU.mult).then_inc(V.sem, V.mark("gdn vb", c, g))
                for g in range(2):
                    B, b = GB[g], gt[g]
                    dve.wait_ge(T.sem, T.at("gdn y", c, g, 0))
                    for dst, src in ((b["U"], four(B[0])), (b["T"], b["L"][:, :, :])):
                        nc.vector.tensor_tensor(dst[:, :, :], per_head(ident, 4), src, ALU.subtract
                                                ).then_inc(V.sem, V.mark("gdn tu", c, g, 0) if dst is b["T"] else V.mark())
                for l in range(1, LEVELS):
                    for g in range(2):
                        B, b = GB[g], gt[g]
                        dve.wait_ge(T.sem, T.at("gdn uy", c, g, l))
                        ins = nc.vector.tensor_tensor(b["U"][:, :, :], b["U"][:, :, :], four(B[1]), ALU.subtract)
                        if l < LEVELS - 1:
                            ins.then_inc(V.sem, V.mark())
                            ins = nc.vector.tensor_tensor(b["T"][:, :, :], b["T"][:, :, :], four(B[2]), ALU.subtract)
                        ins.then_inc(V.sem, V.mark("gdn tu", c, g, l))
                    if c and 2 <= l < 6:
                        gdn_onorm(dve, c - 1, (l - 2) // 2, l % 2)
                if c:
                    for g in range(2):
                        b = gt[g]
                        dve.wait_ge(T.sem, T.at("gdn ks", c, g))
                        nc.vector.tensor_tensor(b["VB"][:, :, :], b["VB"][:, :, :], four(GB[g][3]), ALU.subtract
                                                ).then_inc(V.sem, V.mark("gdn r", c, g))
                for g in range(2):
                    dve.wait_ge(T.sem, T.at("gdn su", c, g))
                    state = GS_[:, 4 * g:4 * g + 4, :]
                    if c == 0:
                        nc.vector.tensor_copy(state, four(GB[g][2])).then_inc(V.sem, V.mark("gdn state", c, g))
                    else:
                        chain(dve, V, nc.vector.tensor_tensor(state, state, heads(GEL[:, c, 4 * g:4 * g + 4], 4),
                                                              ALU.mult))
                        nc.vector.tensor_tensor(state, state, four(GB[g][2]), ALU.add
                                                ).then_inc(V.sem, V.mark("gdn state", c, g))
            for g in range(2):
                for half in range(2):
                    gdn_onorm(dve, NC - 1, g, half)
            for h in range(0, GH, 2):
                x_low(dve, "gdn_out", h, GO[:, h, :], GOL[:, h, :], HH[:, h, :])
            residual(dve, "gdn_out", lambda d: COND[:, 40 + d:41 + d])

        def gdn_onorm(dve, c, g, half):
            dve.wait_ge(A.sem, A.at("gdn oroot", c, g))
            r = RN[:, g, 2 * P * half:2 * P * (half + 1)]
            chain(dve, V, nc.vector.reciprocal(r, r))
            if half:
                nc.vector.scalar_tensor_tensor(fm(GO, c, g), fm(GO, c, g), vec("gdn_onorm_g"),
                                               RN[:, g, :].rearrange("p (h t) -> p h t", h=4), ALU.mult, ALU.mult
                                               ).then_inc(V.sem, V.mark("gdn on", c, g))

        def gdn_gate(pool, c, g):
            pool.wait_ge(V.sem, V.at("gdn on", c, g))
            nc.gpsimd.tensor_tensor(fm(GO, c, g), fm(GO, c, g), fm(GZ, c, g), ALU.mult
                                    ).then_inc(G.sem, G.mark("gdn y", c, g))

        def pool_gdn(pool):
            pool_in(pool, "gdn_in")
            mix_split(pool, "gdn_out", 0, RING)
            for c in range(NC):
                for g in range(2):
                    b = gt[g]
                    pool.wait_ge(V.sem, V.at("gdn tmp", c, g))
                    if c:
                        pool.wait_ge(T.sem, T.at("gdn o", c - 1, g))
                    nc.gpsimd.tensor_tensor(b["AT"][:, :, :], b["TMP"][:, :, :],
                                            per_head(cst("keep_upper"), 4), ALU.add
                                            ).then_inc(G.sem, G.mark("gdn at", c, g))
                for g in range(2):
                    b = gt[g]
                    pool.wait_ge(V.sem, V.at("gdn am", c, g))
                    nc.gpsimd.tensor_tensor(b["AM"][:, :, :], b["AM"][:, :, :],
                                            heads(GCOL[:, 1, c, 4 * g:4 * g + 4], 4), ALU.mult
                                            ).then_inc(G.sem, G.mark("gdn beta", c, g))
                for l in range(LEVELS):
                    for g in range(2):
                        b = gt[g]
                        if l == 0:
                            pool.wait_ge(G.sem, G.at("gdn beta", c, g))
                        else:
                            pool.wait_ge(T.sem, T.at("gdn y", c, g, l - 1))
                        if l == 1:
                            pool.wait_ge(V.sem, V.at("gdn tu", c, g, 0))
                        nc.gpsimd.tensor_tensor(b["L"][:, :, :], b["AM"][:, :, :],
                                                per_head(cst("levels", at=l * P), 4), ALU.mult
                                                ).then_inc(G.sem, G.mark("gdn l", c, g, l))
                    if c and l in (4, 6):
                        gdn_gate(pool, c - 1, l // 2 - 2)
            for g in range(2):
                gdn_gate(pool, NC - 1, g)
            for h in range(1, DT, 2):
                x_low(pool, "gdn_out", h, GO[:, h, :], GOL[:, h, :], HH[:, h, :])
            mix_split(pool, "gdn_out", RING)

        GCONV = list(range(8, 16)) + list(range(0, 8)) + list(range(16, 24))
        FREED["gdn_in"] = lambda j: (A.sem, A.at("beta") if j == 0 else
                                     A.at("gdn xp", j - 1) if j <= 24 else A.at("gdn z", j - 25))

        hy = ExitStack()
        YX, YXL = twins("YX", [P, 12, S], hy)
        YZ, YZH = twins("YZ", [P, 8, S], hy)
        MQ = sb("MQ", [P, MH, S], stack=hy)
        MK = sb("MK", [P, MH, S], stack=hy)
        MV, MVL = twins("MV", [P, 2 * MH, S], hy)
        MO = sb("MO", [P, 2 * MH, S], stack=hy)
        ROWS = sb("ROWS", [P, 3, S], stack=hy)
        YCOL = sb("YCOL", [P, 3, NC, SH], stack=hy)
        YSEL = sb("YSEL", [SH, NC, SH], stack=hy)
        YEL = sb("YEL", [P, NC, SH], stack=hy)
        YEA = sb("YEA", [SH, 1], stack=hy)
        MR = slice(32, 32 + MH)
        MIN = sb("MIN", [P, NC + 1], stack=hy)[MR, :]
        NCM = sb("NCM", [P, NC], stack=hy)[MR, :]
        MAC = sb("MAC", [P, NC], stack=hy)[MR, :]
        MCOL = sb("MCOL", [P, 2, NC, MH], stack=hy)
        MSEL = sb("MSEL", [P, NC, MH], stack=hy)[MR, :, :]
        MEL = sb("MEL", [P, NC, MH], stack=hy)
        HF = H[:, :, :].rearrange("p a s -> p (a s)")
        YM = [HF[:, 512 * g:512 * g + 512] for g in range(2)]
        YCD = [HF[:, 1024 + 512 * g:1536 + 512 * g] for g in range(2)]
        YXD = HF[:, 2048:3072]
        YXE = HF[:, 3072:4096]
        HHQ = HHF[:, :, :].rearrange("p a s -> p (a s)")
        YBT = HHQ[:, 0:2 * P].rearrange("p (g n) -> p g n", g=2)
        MCS = HHQ[:, 512:512 + 12 * P].rearrange("p (h v) -> p h v", h=MH)
        YST = HHQ[:, 512:512 + SH * SP_]
        MVA = HHQ[:, 2048:2048 + 12 * P].rearrange("p (h v) -> p h v", h=MH)
        hy.close()
        MS, MQH, MKW, MEM = YM[0], YCD[0], YM[1], YCD[1]

        def row(i):
            return ROWS[:, i, :] if i < 3 else (SQ if i < 5 else RN)[:, (i - 3) % 2, :]

        def yrow(i):
            return row(i)[0:SH, :]

        def mrow(i):
            return row(i)[MR, :]

        def hy_y(k):
            return (YX[:, k, :], YXL[:, k, :], HH[:, k, :]) if k < 8 else \
                (MV[:, k - 8, :], MVL[:, k - 8, :], YZH[:, k - 8, :])

        def h4(ap):
            return ap.rearrange("p (h t) -> p h t", h=4)

        def ck(c):
            return slice(c * CH, (c + 1) * CH)

        def pe_hy(pe):
            pe_tile(pe, "hy_in", 0, h_tile, x_wait(pe, "hy_in"),
                    outs=[(MB[1][0:SH, :], 0, 16), (MB[2][0:MR.stop, :], 16, 16 + MR.stop),
                          (MB[3][0:MR.stop, :], 16 + MR.stop, 16 + 2 * MR.stop)])
            for j in range(1, 45):
                pe_tile(pe, "hy_in", j, h_tile)
            pe.wait_ge(V.sem, V.at("hy rows"))
            for n, r in enumerate((yrow(1), yrow(0), yrow(4))):
                for c in range(NC):
                    nc.tensor.matmul(MB[1][:, (n * NC + c) * SH:(n * NC + c + 1) * SH],
                                     r[:, ck(c)], ident[0:SH, 0:SH], start=True, stop=True)
            nc.tensor.matmul(MB[1][:, 192:256], ones[0:SH, :], YSEL[:, :, :].rearrange("p c h -> p (c h)"),
                             start=True, stop=True)
            for n, r in enumerate((mrow(3), mrow(5))):
                for c in range(NC):
                    nc.tensor.matmul(MB[2][:, (n * NC + c) * MH:(n * NC + c + 1) * MH],
                                     r[:, ck(c)], ident[MR, MR], start=True, stop=True)
            nc.tensor.matmul(MB[2][:, 32:48], ones[MR, :], MSEL[:, :, :].rearrange("p c h -> p (c h)"),
                             start=True, stop=True).then_inc(T.sem, T.mark("hy cols"))
            pe.wait_ge(V.sem, V.at("hy cols"))
            pe.wait_ge(A.sem, A.at("hy o", 7))
            for c in range(NC):
                if c:
                    pe.wait_ge(V.sem, V.at("ssd y", c - 1, 3))
                    pe.wait_ge(V.sem, V.at("ssd state", c - 1))
                for d in range(8):
                    nc.tensor.transpose(LB[d // 4][:, d % 4 * P:(d % 4 + 1) * P], YX[:, d, ck(c)], ident)
                for g in range(2):
                    nc.tensor.transpose(LB[2][:, g * P:(g + 1) * P], YX[:, 8 + g, ck(c)], ident)
                for g in range(2):
                    last = nc.tensor.matmul(LB[3][:, g * P:(g + 1) * P], YX[:, 8 + g, ck(c)],
                                            YX[:, 10 + g, ck(c)], start=True, stop=True)
                last.then_inc(T.sem, T.mark("ssd tok", c))
                for q in range(4):
                    b0, b1 = MB[2 * (q % 2)], MB[2 * (q % 2) + 1]
                    if q >= 2:
                        pe.wait_ge(V.sem, V.at("ssd cd", c, q - 2))
                    elif c:
                        pe.wait_ge(V.sem, V.at("ssd cd", c - 1, q + 2))
                    for n, r in ((0, row(1)), (1, row(2))):
                        for h in range(4):
                            last = nc.tensor.matmul((b0, b1)[n][:, h * P:(h + 1) * P],
                                                    ident[:, 4 * q + h:4 * q + h + 1].to_broadcast([P, P]),
                                                    r[:, ck(c)], start=True, stop=True)
                    last.then_inc(T.sem, T.mark("ssd rows", c, q))
                    if q:
                        ssd_y(pe, c, q - 1)
                ssd_y(pe, c, 3)
                if c < NC - 1:
                    for g in range(2):
                        last = nc.tensor.matmul(LB[g][:, :], YBT[:, g, :], YXE[:, g * 512:(g + 1) * 512],
                                                start=True, stop=True)
                    last.then_inc(T.sem, T.mark("ssd su", c))
            pe.wait_ge(V.sem, V.at("ssd y", NC - 1, 3))
            for c in range(NC):
                if c:
                    pe.wait_ge(A.sem, A.at("ml em", c - 1))
                    pe.wait_ge(V.sem, V.at("ml h", c - 1))
                    pe.wait_ge(V.sem, V.at("ml state", c - 1, 3))
                for n, r in ((0, row(4)), (1, row(6)), (2, row(2))):
                    for h in range(4):
                        nc.tensor.matmul(MB[n][:, h * P:(h + 1) * P],
                                         ident[:, 32 + h:33 + h].to_broadcast([P, P]), r[:, ck(c)],
                                         start=True, stop=True)
                for h in range(4):
                    last = nc.tensor.matmul(MB[3][:, h * P:(h + 1) * P], MK[:, h, ck(c)], MQ[:, h, ck(c)],
                                            start=True, stop=True)
                last.then_inc(T.sem, T.mark("ml rows", c))
                for h in range(4):
                    nc.tensor.transpose(LB[0][:, h * P:(h + 1) * P], MK[:, h, ck(c)], ident)
                for d in range(8):
                    last = nc.tensor.transpose(LB[1 + d // 4][:, d % 4 * P:(d % 4 + 1) * P], MV[:, d, ck(c)], ident)
                last.then_inc(T.sem, T.mark("ml tok", c))
                pe.wait_ge(V.sem, V.at("ml s", c))
                pe.wait_ge(A.sem, A.at("ml va", c))
                pe.wait_ge(A.sem, A.at("ml em", c))
                for n, bank in enumerate((MB[0], MB[1], MB[2])):
                    for h in range(4):
                        o = bank[:, h * P:(h + 1) * P]
                        last = nc.tensor.matmul(o, MVA[:, h, n * P:(n + 1) * P], MS[:, h * P:(h + 1) * P],
                                                start=True, stop=c == 0)
                        if c:
                            last = nc.tensor.matmul(o, MCS[:, h, n * P:(n + 1) * P], MQH[:, h * P:(h + 1) * P],
                                                    start=False, stop=True)
                last.then_inc(T.sem, T.mark("ml out", c))
                pe.wait_ge(V.sem, V.at("ml kw", c))
                for h in range(4):
                    nc.tensor.matmul((LB[0], LB[1], LB[2], LB[3])[h][:, 0:3 * P], MKW[:, h * P:(h + 1) * P],
                                     MVA[:, h, :], start=True, stop=True).then_inc(T.sem, T.mark("ml su", c, h))
            pe.wait_ge(V.sem, V.at("ml h", NC - 1))
            for j in range(6):
                n = 4 if j < 2 else 2
                for i in range(n):
                    m = hy_norm_at(j) + i
                    pe.wait_ge(A.sem, A.at("hy sq", m))
                    if i == 0 and j >= 2:
                        pe.wait_ge(A.sem, A.at("hy root", j - 2))
                    nc.tensor.matmul(MB[j % 2][:, :], ones, SQ[:, m % 2, :], start=i == 0, stop=i == n - 1
                                     ).then_inc(T.sem, T.mark("hy sum", m))
            for j in range(8):
                pe_tile(pe, "hy_out", j, lambda k: (hy_y(k)[2], hy_y(k)[1]),
                        x_wait(pe, "hy_out") if j == 0 else None)

        def hy_norm_at(j):
            return 4 * j if j < 2 else 8 + 2 * (j - 2)

        def ssd_y(pe, c, q):
            bank = (LB[2], LB[3])[q % 2]
            pe.wait_ge(V.sem, V.at("ssd m", c, q))
            pe.wait_ge(V.sem, V.at("ssd cd", c, q))
            pe.wait_ge(V.sem, V.at("ssd xd", c))
            pe.wait_ge(A.sem, A.at("ssd bt", c))
            if q >= 2:
                pe.wait_ge(V.sem, V.at("ssd y", c, q - 2))
            for h in range(4):
                head = 4 * q + h
                o = bank[64 * (h % 2):64 * (h % 2) + 64, 256 + h // 2 * P:256 + (h // 2 + 1) * P]
                last = nc.tensor.matmul(o, YXD[:, head * 64:head * 64 + 64], YM[q % 2][:, h * P:(h + 1) * P],
                                        start=True, stop=c == 0)
                if c:
                    last = nc.tensor.matmul(o, YST[:, head * 64:head * 64 + 64], YCD[q % 2][:, h * P:(h + 1) * P],
                                            start=False, stop=True)
            last.then_inc(T.sem, T.mark("ssd y", c, q))

        def act_hy(act):
            nc.scalar.activation(YEA[:, :], vec("hy_a_log", rows=SH), ACT.Exp).then_inc(A.sem, A.mark("ssd ea"))
            act.wait_ge(V.sem, V.at("hy u"))
            for t, n, r in ((yrow, "ssd", slice(0, SH)), (mrow, "ml", MR)):
                chain(act, A, nc.scalar.activation(t(1), t(0), ACT.Abs))
                chain(act, A, nc.scalar.activation(t(1), t(1), ACT.Exp, scale=-1.0))
                nc.scalar.activation(t(1), t(1), ACT.Ln, bias=one[r, :]
                                     ).then_inc(A.sem, A.mark(n + " ln"))

            def copy_in(j):
                bank = arrived(act, "hy_in", j + 1)
                if j >= 2:
                    act.wait_ge(V.sem, V.at("hy conv", j - 2))
                nc.scalar.activation(XP[:, j % 2, 3:], bank[:, :], ACT.Copy).then_inc(A.sem, A.mark("hy xp", j))

            def silu(j):
                act.wait_ge(V.sem, V.at("hy conv", j))
                nc.scalar.activation(YX[:, j, :], CV[:, j % 2, :], ACT.Silu).then_inc(A.sem, A.mark("hy silu", j))

            copy_in(0)
            for j in range(1, 12):
                copy_in(j)
                silu(j - 1)
            silu(11)
            for j in range(8):
                bank = arrived(act, "hy_in", 13 + j)
                nc.scalar.activation(YZ[:, j, :], bank[:, :], ACT.Silu).then_inc(A.sem, A.mark("hy z", j))
            act.wait_ge(V.sem, V.at("ssd cum"))
            nc.scalar.activation(yrow(2)[:, :], yrow(1)[:, :], ACT.Exp).then_inc(A.sem, A.mark("ssd eg"))
            for c in range(NC):
                nc.scalar.activation(yrow(3)[:, ck(c)], yrow(1)[:, ck(c)], ACT.Exp,
                                     bias=yrow(1)[:, (c + 1) * CH - 1:(c + 1) * CH], scale=-1.0
                                     ).then_inc(A.sem, A.mark("ssd ed") if c == NC - 1 else A.mark())
            act.wait_ge(V.sem, V.at("ml max"))
            for c in range(NC):
                nc.scalar.activation(mrow(5)[:, ck(c)], mrow(3)[:, ck(c)], ACT.Exp, bias=NCM[:, c:c + 1]
                                     ).then_inc(A.sem, A.mark())
                nc.scalar.activation(mrow(6)[:, ck(c)], mrow(4)[:, ck(c)], ACT.Exp, bias=MIN[:, c:c + 1],
                                     scale=-1.0).then_inc(A.sem, A.mark())
                nc.scalar.activation(MAC[:, c:c + 1], NCM[:, c:c + 1], ACT.Exp, bias=MIN[:, c:c + 1]
                                     ).then_inc(A.sem, A.mark())
            nc.scalar.activation(mrow(2)[:, :], mrow(0)[:, :], ACT.Exp, scale=-1.0).then_inc(A.sem, A.mark("ml exps"))
            for j in range(4):
                bank = arrived(act, "hy_in", 21 + j)
                nc.scalar.activation(MQ[:, j, :], bank[:, :], ACT.Copy, scale=P ** -0.5).then_inc(A.sem, A.mark("hy q", j))
            for j in range(4):
                bank = arrived(act, "hy_in", 25 + j)
                nc.scalar.activation(MK[:, j, :], bank[:, :], ACT.Copy).then_inc(A.sem, A.mark("hy k", j))
            for j in range(8):
                bank = arrived(act, "hy_in", 29 + j)
                nc.scalar.activation(MV[:, j, :], bank[:, :], ACT.Copy).then_inc(A.sem, A.mark("hy v", j))
            for j in range(8):
                bank = arrived(act, "hy_in", 37 + j)
                nc.scalar.activation(MO[:, j, :], bank[:, :], ACT.Sigmoid).then_inc(A.sem, A.mark("hy o", j))
            for c in range(NC):
                act.wait_ge(T.sem, T.at("ssd tok", c))
                if c:
                    act.wait_ge(T.sem, T.at("ssd su", c - 1))
                nc.scalar.activation(YBT[:, :, :].rearrange("p g n -> p (g n)"), LB[2][:, 0:256], ACT.Copy
                                     ).then_inc(A.sem, A.mark("ssd bt", c))
                for q in range(4):
                    act.wait_ge(G.sem, G.at("ssd mask", c, q))
                    nc.scalar.activation(YM[q % 2], YM[q % 2], ACT.Exp).then_inc(A.sem, A.mark("ssd exp", c, q))
            for c in range(NC):
                act.wait_ge(T.sem, T.at("ml rows", c))
                if c:
                    act.wait_ge(V.sem, V.at("ml h", c - 1))
                else:
                    act.wait_ge(T.sem, T.at("ssd y", NC - 1, 3))
                nc.scalar.activation(MEM, MB[2][:, :], ACT.Copy).then_inc(A.sem, A.mark("ml em", c))
                act.wait_ge(G.sem, G.at("ml mask", c))
                nc.scalar.activation(MS, MS, ACT.Exp).then_inc(A.sem, A.mark("ml exp", c))
                act.wait_ge(T.sem, T.at("ml tok", c))
                if c:
                    act.wait_ge(T.sem, T.at("ml su", c - 1, 3))
                for n in range(2):
                    nc.scalar.activation(MVA[:, 2 * n:2 * n + 2, 0:2 * P],
                                         LB[1 + n][:, :].rearrange("p (h v) -> p h v", h=2), ACT.Copy
                                         ).then_inc(A.sem, A.mark("ml va", c) if n else A.mark())
            act.wait_ge(V.sem, V.at("ml h", NC - 1))
            act.wait_ge(V.sem, V.at("ssd gated"))

            def y_highs(j):
                for m in range(hy_norm_at(j), hy_norm_at(j) + (4 if j < 2 else 2)):
                    act.wait_ge(V.sem, V.at("hy y", m))
                    x_high(act, hy_y(m)[0], hy_y(m)[2])

            for j in range(6):
                for i in range(4 if j < 2 else 2):
                    m = hy_norm_at(j) + i
                    if m >= 2:
                        act.wait_ge(T.sem, T.at("hy sum", m - 2))
                    nc.scalar.activation(SQ[:, m % 2, :], YX[:, m, :] if m < 8 else MV[:, m - 8, :], ACT.Square
                                         ).then_inc(A.sem, A.mark("hy sq", m))
                act.wait_ge(T.sem, T.at("hy sum", m))
                if j >= 2:
                    act.wait_ge(V.sem, V.at("hy y", hy_norm_at(j - 1) - 1))
                nc.scalar.activation(RN[:, j % 2, :], MB[j % 2][:, :], ACT.Sqrt, bias=eps,
                                     scale=1.0 / 512 if j < 2 else 1.0 / 256).then_inc(A.sem, A.mark("hy root", j))
                if j:
                    y_highs(j - 1)
            y_highs(5)

        def dve_hy(dve):
            for t in (ROWS, SQ, RN):
                nc.vector.memset(t[:, :, :], 0.0).then_inc(V.sem, V.mark("hy zero") if t is RN else V.mark())
            dve.wait_ge(V.sem, V.at("hy zero"))
            dve.wait_ge(tile_done, TILE0["hy_in"] + 1)
            nc.vector.tensor_scalar(yrow(0)[:, :], MB[1][0:SH, :], vec("hy_dt_bias", rows=SH), None, ALU.add
                                    ).then_inc(V.sem, V.mark())
            nc.vector.tensor_scalar(mrow(6)[:, :], MB[2][MR, :], vec("hy_igate_bias")[MR, :], None, ALU.add
                                    ).then_inc(V.sem, V.mark())
            nc.vector.tensor_scalar(mrow(0)[:, :], MB[3][MR, :], vec("hy_fgate_bias")[MR, :], -1.0,
                                    ALU.add, ALU.mult).then_inc(V.sem, V.mark("hy u"))
            dve.wait_ge(A.sem, A.at("ssd ln"))
            chain(dve, V, nc.vector.scalar_tensor_tensor(yrow(0)[:, :], yrow(0)[:, :], 0.0, yrow(1)[:, :],
                                                         ALU.max, ALU.add))
            chain(dve, V, nc.vector.tensor_scalar(yrow(2)[:, :], yrow(0)[:, :], YEA[:, :], -1.0,
                                                  ALU.mult, ALU.mult))
            for c in range(NC):
                nc.vector.tensor_tensor_scan(yrow(1)[:, ck(c)], ones[0:SH, :], yrow(2)[:, ck(c)], 0.0,
                                             ALU.mult, ALU.add).then_inc(V.sem, V.mark("ssd cum") if c == NC - 1 else V.mark())
            dve.wait_ge(A.sem, A.at("ml ln"))
            chain(dve, V, nc.vector.scalar_tensor_tensor(mrow(1)[:, :], mrow(0)[:, :], 0.0, mrow(1)[:, :],
                                                         ALU.max, ALU.add))
            chain(dve, V, nc.vector.tensor_scalar(mrow(1)[:, :], mrow(1)[:, :], -1.0, None, ALU.mult))
            for c in range(NC):
                chain(dve, V, nc.vector.tensor_tensor_scan(mrow(2)[:, ck(c)], ones[MR, :], mrow(1)[:, ck(c)],
                                                           0.0, ALU.mult, ALU.add))
            chain(dve, V, nc.vector.tensor_tensor(mrow(3)[:, :], mrow(6)[:, :], mrow(2)[:, :], ALU.subtract))
            chain(dve, V, nc.vector.memset(MIN[:, 0:1], 0.0))
            for c in range(NC):
                end = slice((c + 1) * CH - 1, (c + 1) * CH)
                chain(dve, V, nc.vector.tensor_tensor_scan(mrow(4)[:, ck(c)], ones[MR, :], mrow(3)[:, ck(c)],
                                                           MIN[:, c:c + 1], ALU.mult, ALU.max))
                chain(dve, V, nc.vector.tensor_tensor(MIN[:, c + 1:c + 2], mrow(4)[:, end], mrow(2)[:, end], ALU.add))
                chain(dve, V, nc.vector.tensor_scalar(NCM[:, c:c + 1], mrow(4)[:, end], -1.0, None, ALU.mult))
            chain(dve, V, nc.vector.tensor_tensor(mrow(0), mrow(4), mrow(2), ALU.add))
            nc.vector.tensor_scalar(mrow(0), mrow(0), -88.0, None, ALU.max).then_inc(V.sem, V.mark("ml max"))
            for j in range(12):
                dve.wait_ge(A.sem, A.at("hy xp", j))
                if j >= 2:
                    dve.wait_ge(A.sem, A.at("hy silu", j - 2))
                conv(dve, XP[:, j % 2, :], CV[:, j % 2, :], "hy_conv_w", j, 12, vec("hy_conv_b", j), ("hy conv", j))
            dve.wait_ge(A.sem, A.at("ssd ed"))
            nc.vector.tensor_tensor(yrow(4)[:, :], yrow(3)[:, :], yrow(0)[:, :], ALU.mult).then_inc(V.sem, V.mark())
            nc.vector.tensor_tensor(YSEL[:, :, :], heads(yrow(2)[:, CH - 1::CH], NC, SH),
                                    per_head(ident[0:SH, 0:SH], NC), ALU.mult).then_inc(V.sem, V.mark())
            dve.wait_ge(A.sem, A.at("ml exps"))
            nc.vector.tensor_tensor(MSEL[:, :, :], heads(MAC[:, :], NC, MH), per_head(ident[MR, MR], NC),
                                    ALU.mult).then_inc(V.sem, V.mark("hy rows"))
            dve.wait_ge(T.sem, T.at("hy cols"))
            nc.vector.memset(MVA[:, :, 2 * P:3 * P], 1.0).then_inc(V.sem, V.mark())
            nc.vector.tensor_copy(YCOL[:, :, :, :].rearrange("p n c h -> p (n c h)"), MB[1][:, 0:192]).then_inc(V.sem, V.mark())
            nc.vector.tensor_copy(YEL[:, :, :].rearrange("p c h -> p (c h)"), MB[1][:, 192:256]).then_inc(V.sem, V.mark())
            nc.vector.tensor_copy(MCOL[:, :, :, :].rearrange("p n c h -> p (n c h)"), MB[2][:, 0:32]).then_inc(V.sem, V.mark())
            nc.vector.tensor_copy(MEL[:, :, :].rearrange("p c h -> p (c h)"), MB[2][:, 32:48]).then_inc(V.sem, V.mark("hy cols"))
            dve.wait_ge(V.sem, V.at("hy cols"))

            def ssd_skip(c, q):
                dve.wait_ge(T.sem, T.at("ssd y", c, q))
                for i in range(2):
                    d = 2 * q + i
                    nc.vector.scalar_tensor_tensor(YX[:, d, ck(c)], YX[:, d, ck(c)], vec("hy_d_skip", d),
                                                   (LB[2], LB[3])[q % 2][:, 256 + i * P:256 + (i + 1) * P],
                                                   ALU.mult, ALU.add).then_inc(V.sem, V.mark("ssd y", c, q) if i else V.mark())

            for c in range(NC):
                dve.wait_ge(T.sem, T.at("ssd tok", c))
                for n, dst in ((1, YXD), (2, YXE)):
                    for b in range(2):
                        nc.vector.tensor_tensor(dst[:, 512 * b:512 * b + 512].rearrange("p (h w) -> p h w", w=SP_),
                                                heads(YCOL[:, n, c, 8 * b:8 * b + 8], 8, SP_),
                                                LB[b][:, :].rearrange("p (h w) -> p h w", w=SP_), ALU.mult
                                                ).then_inc(V.sem, V.mark("ssd xd", c) if (n, b) == (2, 1) else V.mark())
                for q in range(4):
                    b0, b1 = MB[2 * (q % 2)], MB[2 * (q % 2) + 1]
                    dve.wait_ge(T.sem, T.at("ssd rows", c, q))
                    if q >= 2:
                        dve.wait_ge(T.sem, T.at("ssd y", c, q - 2))
                    elif c:
                        dve.wait_ge(T.sem, T.at("ssd y", c - 1, q + 2))
                    nc.vector.tensor_tensor(h4(YM[q % 2]), four(b0), heads(YCOL[:, 0, c, 4 * q:4 * q + 4], 4),
                                            ALU.subtract).then_inc(V.sem, V.mark("ssd diff", c, q))
                    nc.vector.tensor_tensor(h4(YCD[q % 2]), per_head(YX[:, 10 + q // 2, ck(c)], 4), four(b1),
                                            ALU.mult).then_inc(V.sem, V.mark("ssd cd", c, q))
                    if q:
                        ssd_m(dve, c, q - 1)
                        ssd_skip(c, q - 1)
                ssd_m(dve, c, 3)
                ssd_skip(c, 3)
                if c < NC - 1:
                    dve.wait_ge(T.sem, T.at("ssd su", c))
                    if c:
                        chain(dve, V, nc.vector.tensor_tensor(
                            YST.rearrange("p (h w) -> p h w", w=SP_),
                            YST.rearrange("p (h w) -> p h w", w=SP_), heads(YEL[:, c, :], SH, SP_), ALU.mult))
                    for g in range(2):
                        dst = YST[:, 512 * g:512 * g + 512]
                        ins = nc.vector.tensor_tensor(dst, dst, LB[g][:, :], ALU.add) if c else \
                            nc.vector.tensor_copy(dst, LB[g][:, :])
                        ins.then_inc(V.sem, V.mark("ssd state", c) if g else V.mark())
            dve.wait_ge(V.sem, V.at("ssd y", NC - 1, 3))
            for d in range(8):
                nc.vector.tensor_tensor(YX[:, d, :], YX[:, d, :], YZ[:, d, :], ALU.mult
                                        ).then_inc(V.sem, V.mark("ssd gated") if d == 7 else V.mark())
            for c in range(NC):
                dve.wait_ge(T.sem, T.at("ml rows", c))
                if c:
                    dve.wait_ge(T.sem, T.at("ml out", c - 1))
                nc.vector.tensor_tensor(h4(MS), heads(MCOL[:, 0, c, :], 4), four(MB[0]), ALU.subtract
                                        ).then_inc(V.sem, V.mark("ml diff", c))
                nc.vector.tensor_tensor(h4(MQH), MQ[:, :, ck(c)], four(MB[1]), ALU.mult).then_inc(V.sem, V.mark())
                dve.wait_ge(A.sem, A.at("ml exp", c))
                nc.vector.tensor_tensor(MS, MS, MB[3][:, :], ALU.mult).then_inc(V.sem, V.mark("ml s", c))
                dve.wait_ge(T.sem, T.at("ml tok", c))
                if c:
                    dve.wait_ge(T.sem, T.at("ml su", c - 1, 3))
                nc.vector.tensor_tensor(h4(MKW), heads(MCOL[:, 1, c, :], 4), four(LB[0]), ALU.mult
                                        ).then_inc(V.sem, V.mark("ml kw", c))
                dve.wait_ge(T.sem, T.at("ml out", c))
                dve.wait_ge(A.sem, A.at("ml em", c))
                chain(dve, V, nc.vector.scalar_tensor_tensor(MEM, MB[2][:, :], -1.0, MEM, ALU.mult, ALU.max))
                chain(dve, V, nc.vector.tensor_tensor(MEM, MEM, MB[2][:, :], ALU.max))
                chain(dve, V, nc.vector.reciprocal(MEM, MEM))
                for n in range(2):
                    nc.vector.tensor_tensor(MV[:, n::2, ck(c)], h4(MEM), four(MB[n]), ALU.mult
                                            ).then_inc(V.sem, V.mark("ml h", c) if n else V.mark())
                for h in range(4):
                    dve.wait_ge(T.sem, T.at("ml su", c, h))
                    src = (LB[0], LB[1], LB[2], LB[3])[h][:, 0:3 * P]
                    ins = nc.vector.scalar_tensor_tensor(MCS[:, h, :], MCS[:, h, :], MEL[:, c, h:h + 1], src,
                                                         ALU.mult, ALU.add) if c else \
                        nc.vector.tensor_copy(MCS[:, h, :], src)
                    ins.then_inc(V.sem, V.mark("ml state", c, h))

            def y_lows(j):
                for m in range(hy_norm_at(j), hy_norm_at(j) + (4 if j < 2 else 2), 2):
                    x_low(dve, "hy_out", m, *hy_y(m))

            for j in range(6):
                dve.wait_ge(A.sem, A.at("hy root", j))
                chain(dve, V, nc.vector.reciprocal(RN[:, j % 2, :], RN[:, j % 2, :]))
                for i in range(4 if j < 2 else 2):
                    m = hy_norm_at(j) + i
                    y = YX[:, m, :] if m < 8 else MV[:, m - 8, :]
                    g = vec("hy_ssd_norm", m) if m < 8 else vec("hy_mlstm_norm", m - 8)
                    ins = nc.vector.scalar_tensor_tensor(y, y, g, RN[:, j % 2, :], ALU.mult, ALU.mult)
                    if m < 8:
                        ins.then_inc(V.sem, V.mark("hy y", m))
                    else:
                        chain(dve, V, ins)
                        nc.vector.tensor_tensor(y, y, MO[:, m - 8, :], ALU.mult).then_inc(V.sem, V.mark("hy y", m))
                if j:
                    y_lows(j - 1)
            y_lows(5)
            residual(dve, "hy_out", lambda d: 1.0)

        def ssd_m(dve, c, q):
            dve.wait_ge(A.sem, A.at("ssd exp", c, q))
            nc.vector.tensor_tensor(h4(YM[q % 2]), h4(YM[q % 2]),
                                    per_head(LB[3][:, q // 2 * P:(q // 2 + 1) * P], 4), ALU.mult
                                    ).then_inc(V.sem, V.mark("ssd m", c, q))

        def pool_hy(pool):
            pool_in(pool, "hy_in")
            mix_split(pool, "hy_out", 0, RING)
            for c in range(NC):
                for q in range(4):
                    pool.wait_ge(V.sem, V.at("ssd diff", c, q))
                    nc.gpsimd.tensor_tensor(h4(YM[q % 2]), h4(YM[q % 2]), per_head(cst("keep_upper"), 4), ALU.add
                                            ).then_inc(G.sem, G.mark("ssd mask", c, q))
            for c in range(NC):
                pool.wait_ge(V.sem, V.at("ml diff", c))
                nc.gpsimd.tensor_tensor(h4(MS), h4(MS), per_head(cst("keep_upper"), 4), ALU.add
                                        ).then_inc(G.sem, G.mark("ml mask", c))
            for m in range(1, 2 * DT, 2):
                x_low(pool, "hy_out", m, *hy_y(m))
            mix_split(pool, "hy_out", RING)

        def hy_freed(j):
            if j == 0:
                return V.sem, V.at("hy u")
            for first, count, name in ((1, 12, "hy xp"), (13, 8, "hy z"), (21, 4, "hy q"), (25, 4, "hy k"),
                                       (29, 8, "hy v"), (37, 8, "hy o")):
                if j < first + count:
                    return A.sem, A.at(name, j - first)

        FREED["hy_in"] = hy_freed


        sa = ExitStack()
        AKI = sb("AKI", [P, 2, S], stack=sa)
        AQI = sb("AQI", [P, IH // 2, S], stack=sa)
        AVW = sb("AVW", [P, S], stack=sa)
        AVT = sb("AVT", [P, NC, AD + IH], stack=sa)
        AK = sb("AK", [P, 2, S], stack=sa)
        AQ = sb("AQ", [P, AH // 2, S], stack=sa)
        POS = sb("POS", [P, S], I32, stack=sa)
        ANG = sb("ANG", [P, 3, S], stack=sa)
        COS = sb("COS", [P, S], stack=sa)
        SIN = sb("SIN", [P, S], stack=sa)
        RAW = sb("RAW", [P, 3, S], stack=sa)
        RTC = sb("RTC", [P, 2, S], stack=sa)
        RTS = sb("RTS", [P, 2, S], stack=sa)
        REL = sb("REL", [P, 4, S], stack=sa)
        ASC = sb("ASC", [P, S], stack=sa)
        AWK = sb("AWK", [P, S], stack=sa)
        AM8 = sb("AM8", [P, 8], stack=sa)
        AMB = sb("AMB", [P, NC, S], stack=sa)
        APR = sb("APR", [P, 3, S], stack=sa)
        APT = sb("APT", [P, 2, S], stack=sa)
        AMX = sb("AMX", [P, 64], stack=sa)
        ANM = sb("ANM", [P, 64], stack=sa)
        ASM = sb("ASM", [P, 64], stack=sa)
        ARS = sb("ARS", [P, 64], stack=sa)
        AOT = sb("AOT", [P, 2, S], stack=sa)
        sa.close()
        AO = H
        ROPE = [(0, AKI)] + [(1 + i, AQI[:, i, :]) for i in range(4)] + [(6, AK)] \
            + [(7 + i, AQ[:, i, :]) for i in range(8)]
        UNITS = [(qt, h) for qt in range(NC) for h in range(AH)]

        def pe_sa(pe):
            def rot(i):
                pe.wait_ge(V.sem, V.at("sa normed", i)) if i >= 5 else pe.wait_ge(A.sem, A.at("sa raw", i))
                if i >= 2:
                    pe.wait_ge(V.sem, V.at("sa rs", i - 2))
                nc.tensor.matmul(MB[i % 2][:, :], rotate, RAW[:, i % 3, :], start=True, stop=True
                                 ).then_inc(T.sem, T.mark("sa rot", i))

            def total(i):
                pe.wait_ge(A.sem, A.at("sa sq", i))
                if i >= 7:
                    pe.wait_ge(A.sem, A.at("sa root", i - 2))
                nc.tensor.matmul(MB[2 + i % 2][:, :], half_ones, SQ[:, i % 2, :], start=True, stop=True
                                 ).then_inc(T.sem, T.mark("sa sum", i))

            for j in range(15):
                pe_tile(pe, "sa_in", j, h_tile, x_wait(pe, "sa_in") if j == 0 else None)
                if 1 <= j <= 5:
                    rot(j - 1)
                if j >= 7:
                    total(j - 2)
                if j >= 8:
                    rot(j - 3)
            total(13)
            rot(12)
            rot(13)
            pe.wait_ge(V.sem, V.at("sa rs", 13))
            pe.wait_ge(A.sem, A.at("sa vw"))
            for c in range(NC):
                last = nc.tensor.transpose(MB[0][:, c * P:(c + 1) * P], AVW[:, ck(c)], ident)
            last.then_inc(T.sem, T.mark("sa vt"))
            pe.wait_ge(V.sem, V.at("sa rope", 13))
            pe.wait_ge(V.sem, V.at("sa vt"))
            for qt in range(NC):
                if qt:
                    for h in range(IH):
                        n = (qt - 1) * IH + h
                        if n >= 4:
                            pe.wait_ge(A.sem, A.at("sa relu", n - 4))
                        nc.tensor.matmul(LB[n % 4][:, 0:(qt + 1) * P], AQI[:, h // 2, ck(qt)],
                                         AKI[:, h % 2, 0:(qt + 1) * P], start=True, stop=True
                                         ).then_inc(T.sem, T.mark("sa logit", n))
            pe.wait_ge(A.sem, A.at("sa relu", 3 * IH - 1))

            def logits(u):
                qt, h = UNITS[u]
                if u >= 3:
                    pe.wait_ge(V.sem, V.at("sa max", u - 3))
                nc.tensor.matmul(LB[u % 3][:, 0:(qt + 1) * P], AQ[:, h // 2, ck(qt)], AK[:, h % 2, 0:(qt + 1) * P],
                                 start=True, stop=True).then_inc(T.sem, T.mark("sa s", u))

            def flip(u):
                qt, h = UNITS[u]
                pe.wait_ge(A.sem, A.at("sa exp", u))
                if u >= 2:
                    pe.wait_ge(A.sem, A.at("sa pt", u - 2))
                for k in range(qt + 1):
                    last = nc.tensor.transpose(MB[u % 2][:, k * P:(k + 1) * P], APR[:, u % 3, k * P:(k + 1) * P], ident)
                last.then_inc(T.sem, T.mark("sa flip", u))

            def products(u):
                qt, h = UNITS[u]
                g = u // 8
                pe.wait_ge(A.sem, A.at("sa pt", u))
                if u % 8 == 0 and g >= 2:
                    pe.wait_ge(V.sem, V.at("sa ot", g - 2))
                for k in range(qt + 1):
                    last = nc.tensor.matmul(MB[2 + g % 2][:, u % 8 * AD:(u % 8 + 1) * AD], APT[:, u % 2, k * P:(k + 1) * P],
                                            AVT[:, k, 0:AD], start=k == 0, stop=k == qt)
                last.then_inc(T.sem, T.mark("sa pv", u))

            def back(g):
                pe.wait_ge(V.sem, V.at("sa ot", g))
                if g:
                    pe.wait_ge(A.sem, A.at("sa out", g - 1))
                for i in range(4):
                    last = nc.tensor.transpose(LB[3][:, i * P:(i + 1) * P], AOT[:, g % 2, i * P:(i + 1) * P], ident)
                last.then_inc(T.sem, T.mark("sa back", g))

            for u in range(64 + 6):
                if u < 64:
                    logits(u)
                if 0 <= u - 2 < 64:
                    flip(u - 2)
                if 0 <= u - 3 < 64:
                    products(u - 3)
                if u >= 13 and (u - 13) % 8 == 0:
                    back((u - 13) // 8)
            for j in range(8):
                pe_tile(pe, "sa_out", j, h_tile,
                        (lambda k: pe.wait_ge(G.sem, G.at("sa low", 7))) if j == 0 else None)

        def act_sa(act):
            act.dma_start(POS[:, :], a["pos"]).then_inc(pos_in, 16)
            act.wait_ge(V.sem, V.at("sa angles"))
            nc.scalar.activation(SIN[:, :], ANG[:, 0, :], ACT.Sin).then_inc(A.sem, A.mark())
            nc.scalar.activation(COS[:, :], ANG[:, 1, :], ACT.Sin).then_inc(A.sem, A.mark("sa sincos"))
            rope_of = {j: i for i, (j, _) in enumerate(ROPE)}

            def root(i):
                act.wait_ge(T.sem, T.at("sa sum", i))
                if i >= 7:
                    act.wait_ge(V.sem, V.at("sa normed", i - 2))
                nc.scalar.activation(RN[:, i % 2, :], MB[2 + i % 2][:, :], ACT.Sqrt, bias=eps, scale=1.0 / AD
                                     ).then_inc(A.sem, A.mark("sa root", i))

            for j in range(15):
                bank = arrived(act, "sa_in", j)
                if j == 5:
                    nc.scalar.activation(AVW[:, :], bank[:, :], ACT.Copy).then_inc(A.sem, A.mark("sa vw"))
                    continue
                i = rope_of[j]
                if i >= 3:
                    act.wait_ge(V.sem, V.at("sa rope", i - 3))
                    act.wait_ge(T.sem, T.at("sa rot", i - 3))
                nc.scalar.activation(RAW[:, i % 3, :], bank[:, :], ACT.Copy).then_inc(A.sem, A.mark("sa raw", i))
                if i >= 5:
                    if i >= 7:
                        act.wait_ge(T.sem, T.at("sa sum", i - 2))
                    nc.scalar.activation(SQ[:, i % 2, :], bank[:, :], ACT.Square).then_inc(A.sem, A.mark("sa sq", i))
                    if i >= 6:
                        root(i - 1)
            root(13)
            for qt in range(1, NC):
                for h in range(IH):
                    n = (qt - 1) * IH + h
                    act.wait_ge(T.sem, T.at("sa logit", n))
                    if n >= 4:
                        act.wait_ge(V.sem, V.at("sa score", n - 4))
                    w = (qt + 1) * P
                    nc.scalar.activation(REL[:, n % 4, 0:w], LB[n % 4][:, 0:w], ACT.Relu
                                         ).then_inc(A.sem, A.mark("sa relu", n))

            def pt(u):
                act.wait_ge(T.sem, T.at("sa flip", u))
                if u >= 2:
                    act.wait_ge(T.sem, T.at("sa pv", u - 2))
                w = (UNITS[u][0] + 1) * P
                nc.scalar.activation(APT[:, u % 2, 0:w], MB[u % 2][:, 0:w], ACT.Copy).then_inc(A.sem, A.mark("sa pt", u))

            def out_tiles(g):
                act.wait_ge(T.sem, T.at("sa back", g))
                qt, hg = g // 2, g % 2
                nc.scalar.activation(AO[:, 4 * hg:4 * hg + 4, ck(qt)], four(LB[3]), ACT.Copy
                                     ).then_inc(A.sem, A.mark())
                nc.scalar.activation(HH[:, 4 * hg:4 * hg + 4, ck(qt)], four(LB[3]), ACT.Copy
                                     ).then_inc(A.sem, A.mark("sa out", g))

            for u in range(64 + 6):
                if u < 64:
                    w = (UNITS[u][0] + 1) * P
                    act.wait_ge(V.sem, V.at("sa negmax", u))
                    nc.scalar.activation(APR[:, u % 3, 0:w], APR[:, u % 3, 0:w], ACT.Exp, bias=ANM[:, u:u + 1],
                                         scale=AD ** -0.5, accum_out=ASM[:, u:u + 1]
                                         ).then_inc(A.sem, A.mark("sa exp", u))
                if 0 <= u - 2 < 64:
                    pt(u - 2)
                if u >= 13 and (u - 13) % 8 == 0:
                    out_tiles((u - 13) // 8)

        def dve_sa(dve):
            two_pi = 6.283185307179586
            c0, c1 = 6.28125, 0.0019350051879882812
            c2 = two_pi - c0 - c1
            magic = 12582912.0
            for t in (AKI, AK):
                for half in range(2):
                    nc.vector.memset(t[64 * (1 - half):64 * (2 - half), half, :], 0.0).then_inc(V.sem, V.mark())
            dve.wait_ge(pos_in, 16)
            chain(dve, V, nc.vector.tensor_copy(ANG[:, 0, :], POS[:, :]))
            chain(dve, V, nc.vector.tensor_scalar(ANG[:, 0, :], ANG[:, 0, :], cst("inv_freq", n=1), None, ALU.mult))
            chain(dve, V, nc.vector.tensor_scalar(ANG[:, 1, :], ANG[:, 0, :], 1.0 / two_pi, magic, ALU.mult, ALU.add))
            chain(dve, V, nc.vector.tensor_scalar(ANG[:, 1, :], ANG[:, 1, :], magic, None, ALU.subtract))
            for n, cc in enumerate((c0, c1, c2)):
                chain(dve, V, nc.vector.scalar_tensor_tensor(ANG[:, 0, :], ANG[:, 1, :], -cc, ANG[:, 0, :],
                                                             ALU.mult, ALU.add))
            pi = 3.1415925
            chain(dve, V, nc.vector.tensor_scalar(ANG[:, 1, :], ANG[:, 0, :], two_pi / 4, None, ALU.add))
            chain(dve, V, nc.vector.tensor_scalar(ANG[:, 2, :], ANG[:, 1, :], pi, -two_pi, ALU.is_gt, ALU.mult))
            chain(dve, V, nc.vector.tensor_tensor(ANG[:, 1, :], ANG[:, 1, :], ANG[:, 2, :], ALU.add))
            nc.vector.tensor_scalar(ANG[:, 0:2, :], ANG[:, 0:2, :], pi, -pi, ALU.min, ALU.max
                                    ).then_inc(V.sem, V.mark("sa angles"))
            dve.wait_ge(A.sem, A.at("sa sincos"))

            def norm(i):
                dve.wait_ge(A.sem, A.at("sa root", i))
                chain(dve, V, nc.vector.reciprocal(RN[:, i % 2, :], RN[:, i % 2, :]))
                nc.vector.scalar_tensor_tensor(RAW[:, i % 3, :], RAW[:, i % 3, :],
                                               vec("sa_k_norm" if i == 5 else "sa_q_norm"), RN[:, i % 2, :],
                                               ALU.mult, ALU.mult).then_inc(V.sem, V.mark("sa normed", i))

            def rope(i):
                if i >= 5:
                    dve.wait_ge(V.sem, V.at("sa normed", i))
                else:
                    dve.wait_ge(A.sem, A.at("sa raw", i))
                nc.vector.tensor_tensor(RTC[:, i % 2, :], RAW[:, i % 3, :], COS[:, :], ALU.mult).then_inc(V.sem, V.mark())
                dve.wait_ge(T.sem, T.at("sa rot", i))
                nc.vector.tensor_tensor(RTS[:, i % 2, :], SIN[:, :], MB[i % 2][:, :], ALU.mult
                                        ).then_inc(V.sem, V.mark("sa rs", i))
                dve.wait_ge(V.sem, V.at("sa rs", i))
                if i in (0, 5):
                    for half in range(2):
                        r = slice(64 * half, 64 * half + 64)
                        nc.vector.tensor_tensor(ROPE[i][1][r, half, :], RTC[r, i % 2, :], RTS[r, i % 2, :], ALU.add
                                                ).then_inc(V.sem, V.mark("sa rope", i) if half else V.mark())
                else:
                    nc.vector.tensor_tensor(ROPE[i][1], RTC[:, i % 2, :], RTS[:, i % 2, :], ALU.add
                                            ).then_inc(V.sem, V.mark("sa rope", i))

            for i in range(5):
                rope(i)
            norm(5)
            for i in range(6, 14):
                norm(i)
                rope(i - 1)
            rope(13)
            dve.wait_ge(T.sem, T.at("sa vt"))
            nc.vector.tensor_copy(AVT[:, :, :], MB[0][:, :].rearrange("p (c f) -> p c f", c=NC)[:, :, 0:AD + IH]
                                  ).then_inc(V.sem, V.mark("sa vt"))
            nc.vector.tensor_copy(AMB[:, 0, 0:P], cst("keep_lower")).then_inc(V.sem, V.mark("sa mask", 0))
            dve.wait_ge(V.sem, V.at("sa vt"))
            for qt in range(1, NC):
                w = (qt + 1) * P
                for h in range(IH):
                    n = (qt - 1) * IH + h
                    dve.wait_ge(A.sem, A.at("sa relu", n))
                    wi = AVT[:, qt, AD + h:AD + h + 1]
                    if h == 0:
                        ins = nc.vector.tensor_scalar(ASC[:, 0:w], REL[:, n % 4, 0:w], wi, None, ALU.mult)
                    else:
                        dve.wait_ge(V.sem, V.at("sa score", n - 1))
                        ins = nc.vector.scalar_tensor_tensor(ASC[:, 0:w], REL[:, n % 4, 0:w], wi, ASC[:, 0:w],
                                                             ALU.mult, ALU.add)
                    ins.then_inc(V.sem, V.mark("sa score", n))
                dve.wait_ge(V.sem, V.at("sa score", n))
                chain(dve, V, nc.vector.tensor_scalar(ASC[:, 0:w], ASC[:, 0:w], (IH * AD) ** -0.5, None, ALU.mult))
                chain(dve, V, nc.vector.tensor_tensor(ASC[:, qt * P:w], ASC[:, qt * P:w], cst("keep_lower"), ALU.add))
                for r in range(TOPK // 8):
                    src = AWK if r else ASC
                    chain(dve, V, nc.vector.max(AM8[:, :], src[:, 0:w]))
                    chain(dve, V, nc.vector.match_replace(AWK[:, 0:w], AM8[:, :], src[:, 0:w], -3.0e38))
                chain(dve, V, nc.vector.tensor_tensor(AMB[:, qt, 0:w], AWK[:, 0:w], ASC[:, 0:w], ALU.is_equal))
                nc.vector.tensor_scalar(AMB[:, qt, 0:w], AMB[:, qt, 0:w], NEG, None, ALU.mult
                                        ).then_inc(V.sem, V.mark("sa mask", qt))
            def scale_out(g):
                dve.wait_ge(T.sem, T.at("sa pv", 8 * g + 7))
                dve.wait_ge(A.sem, A.at("sa exp", 8 * g + 7))
                if g >= 2:
                    dve.wait_ge(T.sem, T.at("sa back", g - 2))
                chain(dve, V, nc.vector.reciprocal(ARS[:, 8 * g:8 * g + 8], ASM[:, 8 * g:8 * g + 8]))
                nc.vector.tensor_tensor(AOT[:, g % 2, :].rearrange("p (h w) -> p h w", w=AD),
                                        heads(ARS[:, 8 * g:8 * g + 8], 8, AD),
                                        MB[2 + g % 2][:, :].rearrange("p (h w) -> p h w", w=AD), ALU.mult
                                        ).then_inc(V.sem, V.mark("sa ot", g))

            for u in range(64 + 5):
                if u < 64:
                    qt, h = UNITS[u]
                    w = (qt + 1) * P
                    dve.wait_ge(T.sem, T.at("sa s", u))
                    dve.wait_ge(V.sem, V.at("sa mask", qt))
                    if u >= 3:
                        dve.wait_ge(T.sem, T.at("sa flip", u - 3))
                    nc.vector.tensor_tensor_reduce(out=APR[:, u % 3, 0:w], in0=LB[u % 3][:, 0:w], in1=AMB[:, qt, 0:w],
                                                   scale=1.0, scalar=-3.0e38, op0=ALU.add, op1=ALU.max,
                                                   accum_out=AMX[:, u:u + 1]).then_inc(V.sem, V.mark("sa max", u))
                    dve.wait_ge(V.sem, V.at("sa max", u))
                    nc.vector.tensor_scalar(ANM[:, u:u + 1], AMX[:, u:u + 1], -(AD ** -0.5), None, ALU.mult
                                            ).then_inc(V.sem, V.mark("sa negmax", u))
                if u >= 11 and (u - 11) % 8 == 0:
                    scale_out((u - 11) // 8)
            residual(dve, "sa_out", lambda d: 1.0)

        def pool_sa(pool):
            pool_in(pool, "sa_in")
            mix_split(pool, "sa_out", 0, RING)
            for g in range(8):
                pool.wait_ge(A.sem, A.at("sa out", g))
                at = slice(4 * (g % 2), 4 * (g % 2) + 4)
                nc.gpsimd.tensor_tensor(HL[:, at, ck(g // 2)], AO[:, at, ck(g // 2)],
                                        HH[:, at, ck(g // 2)].bitcast(F32), ALU.subtract
                                        ).then_inc(G.sem, G.mark("sa low", g))
            mix_split(pool, "sa_out", RING)

        FREED["sa_in"] = lambda j: (A.sem, A.at("sa vw") if j == 5 else
                                    A.at("sa sq" if j > 5 else "sa raw", j if j < 5 else j - 1))

        block = ctx.enter_context(nc.Block())

        @block.sync
        def _(sp):
            sync_program(sp)

        @block.gpsimd
        def _(pool):
            pool_lru(pool)
            pool_gdn(pool)
            pool_ffn(pool, 0)
            pool_hy(pool)
            pool_ffn(pool, 1)
            pool_ffn(pool, 2)
            pool_sa(pool)
            pool_ffn(pool, 3)

        @block.scalar
        def _(act):
            act.dma_start(VEC[:, :], a["vec"]).then_inc(vec_in, 16)
            act.dma_start(CST[:, :], a["cst"]).then_inc(cst_in, 16)
            act.dma_start(X[:, :, :], a["x"]).then_inc(x_in, 16)
            act.dma_start(GW[:, :, :], a["gate_w"]).then_inc(gate_w_in, 16)
            act_ada(act)
            act_norm(act, 0)
            act_h_high(act, "lru_in", 0)
            act_lru(act)
            act_norm(act, 1)
            act_h_high(act, "gdn_in", 1)
            act_gdn(act)
            act_norm(act, 2)
            act_norm(act, 3, lambda: act_ffn_high(act, 3, 0))
            act_ffn(act, 0)
            act_norm(act, 4)
            act_h_high(act, "hy_in", 4)
            act_hy(act)
            act_norm(act, 5, lambda: act_ffn_high(act, 5, 1))
            act_ffn(act, 1)
            act_norm(act, 6, lambda: act_ffn_high(act, 6, 2))
            act_ffn(act, 2)
            act_norm(act, 7)
            act_h_high(act, "sa_in", 7)
            act_sa(act)
            act_norm(act, 8, lambda: act_ffn_high(act, 8, 3))
            act_ffn(act, 3)

        @block.vector
        def _(dve):
            dve_ada(dve)
            dve_norm(dve, 0, lambda d: GS[:, 0, d:d + 1], lambda d: COND[:, d:d + 1])
            h_low(dve, "lru_in", 0)
            dve_lru(dve)
            cond(dve, 1)
            dve_norm(dve, 1, lambda d: GS[:, 1, d:d + 1], lambda d: COND[:, 24 + d:25 + d])
            h_low(dve, "gdn_in", 0)
            dve_gdn(dve)
            dve_norm(dve, 2, lambda d: vec("final_g", d), dst=lambda d: X[:, d, :], sig=x_ready)
            dve_norm(dve, 3, lambda d: vec("ffn_norm", d))
            dve_ffn(dve, 0)
            dve_norm(dve, 4, lambda d: vec("mix_norm", d))
            h_low(dve, "hy_in", 0)
            dve_hy(dve)
            dve_norm(dve, 5, lambda d: vec("ffn_norm", 8 + d))
            dve_ffn(dve, 1)
            dve_norm(dve, 6, lambda d: vec("ffn_norm", 16 + d))
            dve_ffn(dve, 2)
            dve_norm(dve, 7, lambda d: vec("mix_norm", 8 + d))
            h_low(dve, "sa_in", 0)
            dve_sa(dve)
            dve_norm(dve, 8, lambda d: vec("ffn_norm", 24 + d))
            dve_ffn(dve, 3)

        @block.tensor
        def _(pe):
            pe.wait_ge(cst_in, 16)
            pe_norm(pe, 0)
            pe_ada(pe)
            pe_lru(pe)
            pe_norm(pe, 1)
            pe_gdn(pe)
            pe_norm(pe, 2)
            pe_norm(pe, 3)
            pe_ffn(pe, 0)
            pe_norm(pe, 4)
            pe_hy(pe)
            pe_norm(pe, 5)
            pe_ffn(pe, 1)
            pe_norm(pe, 6)
            pe_ffn(pe, 2)
            pe_norm(pe, 7)
            pe_sa(pe)
            pe_norm(pe, 8)
            pe_ffn(pe, 3)


def host_constants():
    import numpy as np
    cst = np.zeros((P, CONST_N), np.float32)

    def put(name, value):
        value = np.asarray(value, np.float32)
        cst[:, CONST_AT[name]:CONST_AT[name] + value.shape[1]] = value

    r = np.arange(P)
    put("ident", np.eye(P))
    put("ones", np.ones((P, P)))
    put("half_ones", (r[:, None] // 64) == (r[None, :] // 64))
    rot = np.zeros((P, P))
    for m in range(P):
        if m % 64 < 32:
            rot[m + 32, m] = -1.0
        else:
            rot[m - 32, m] = 1.0
    put("rotate", rot)
    put("keep_upper", np.where(r[:, None] <= r[None, :], 0.0, NEG))
    put("keep_lower_strict", np.where(r[:, None] > r[None, :], 0.0, NEG))
    put("keep_lower", np.where(r[:, None] >= r[None, :], 0.0, NEG))
    lev = [((r[:, None] >> l) == (r[None, :] >> l) + 1) & (((r[None, :] >> l) & 1) == 0) for l in range(LEVELS)]
    put("levels", np.concatenate(lev, 1))
    inv = np.float32(10000.0) ** (-np.arange(0, 64, 2, dtype=np.float32) / np.float32(64))
    put("inv_freq", inv[r % 32][:, None])
    put("eps", np.full((P, 1), EPS))
    put("one", np.ones((P, 1)))
    return cst


def kernel(**inputs):
    import numpy as np
    import concourse.bacc as bacc
    from concourse import mybir as mb
    from concourse.bass_utils import run_bass_kernel_spmd

    x = {k: np.asarray(v) for k, v in inputs.items()}

    def slabs(w, parts, k, per=1):
        out = np.zeros((len(parts) * per, P, k, P), w.dtype)
        w = w.reshape(per, k, P, w.shape[1])
        for t, runs in enumerate(parts):
            for c, n, at in runs:
                out[t * per:(t + 1) * per, :, :, at:at + n] = w[:, :, :, c:c + n].transpose(0, 2, 1, 3)
        return out.reshape(len(parts) * per, P, k * P)

    def tiles(first, n):
        return [[(first + P * t, P, 0)] for t in range(n)]

    arrays = {}
    for l, name in enumerate(("w_ada", "w_ada2")):
        arrays[name] = np.ascontiguousarray(
            x["ada_w"][l].reshape(DT, P, 3, SLAB_K * P).transpose(2, 0, 1, 3)).reshape(3 * DT, P, SLAB_K * P)
    arrays["w_lru_in"] = slabs(x["lru_in_w"][0], tiles(0, 16), 8)
    arrays["w_lru_out"] = slabs(x["lru_out_w"][0], tiles(0, 8), 8)
    arrays["w_gdn_in"] = slabs(x["gdn_in_w"][0], [[(4096, 16, 0)]] + tiles(1024, 8) + tiles(0, 8)
                               + tiles(2048, 8) + tiles(3072, 8), 8)
    arrays["w_gdn_out"] = slabs(x["gdn_out_w"][0], tiles(0, 8), 8)
    for p in range(8):
        f, first, n = p // 2, PART[0] * (p % 2), PART[p % 2]
        gate = slabs(x["ffn_w_gate_2"][f // 2, f % 2], tiles(P * first, n), 8)
        up = slabs(x["ffn_w_up_2"][f // 2, f % 2], tiles(P * first, n), 8)
        arrays[f"w_up{p}"] = np.stack([gate, up], 1).reshape(2 * n, P, 8 * P)
        arrays[f"w_down{p}"] = slabs(x["ffn_w_down_2"][f // 2, f % 2][P * first:P * (first + n)],
                                     tiles(0, 8), n // 2, 2)
    arrays["w_hy_in"] = slabs(x["hy_w_in_2"][0], [[(2560, 16, 0), (5648, 4, 16 + 32), (5652, 4, 16 + 36 + 32)]] + tiles(1024, 12) + tiles(0, 8)
                              + tiles(2576, 4) + tiles(3088, 4) + tiles(3600, 8) + tiles(4624, 8), 8)
    arrays["w_hy_out"] = slabs(x["hy_w_out_2"][0], tiles(0, 8), 8, 2)
    arrays["w_sa_in"] = slabs(x["sa_w_in_2"][0], [[(1664, 64, 0), (1664, 64, 64)]] + tiles(1152, 4)
                              + [[(1088, 64, 0), (1728, 8, 64)]] + [[(1024, 64, 0), (1024, 64, 64)]]
                              + tiles(0, 8), 8)
    arrays["w_sa_out"] = slabs(x["sa_w_out_2"][0], tiles(0, 8), 8)
    arrays["gate_w"] = np.ascontiguousarray(
        x["lru_gate_w"][0].transpose(2, 0, 1, 3).reshape(P, 16, P))
    arrays["x"] = np.ascontiguousarray(x["x"][0].T.reshape(DT, P, S).transpose(1, 0, 2))
    arrays["pos"] = np.ascontiguousarray(np.broadcast_to(x["positions_2"], (P, S)))

    def cols(v):
        return v.reshape(-1, P).T

    v = np.zeros((P, VEC_N), np.float32)

    def put(name, value, rows=P, first=0):
        v[first:first + rows, VEC_AT[name]:VEC_AT[name] + value.shape[1]] = value

    put("norm_g", cols(x["norm_g"]))
    put("final_g", cols(x["final_g"]))
    put("ada_b", cols(x["ada_b"]))
    put("lru_conv_w", cols(x["lru_conv_w"]))
    put("lru_conv_b", cols(x["lru_conv_b"]))
    put("lru_gate_b", cols(x["lru_gate_b"]))
    put("lru_lambda", cols(x["lru_lambda"]))
    put("gdn_conv_w", cols(x["gdn_conv_w"]))
    put("gdn_onorm_g", cols(x["gdn_onorm_g"]))
    put("ffn_norm", cols(x["ffn_norm_2"]))
    put("mix_norm", cols(x["mix_norm_2"]))
    put("hy_conv_w", cols(x["hy_conv_w_2"]))
    put("hy_conv_b", cols(x["hy_conv_b_2"]))
    put("hy_ssd_norm", cols(x["hy_ssd_norm_2"]))
    put("hy_mlstm_norm", cols(x["hy_mlstm_norm_2"]))
    put("hy_d_skip", cols(np.repeat(x["hy_d_skip_2"][0], SP_)))
    put("sa_q_norm", np.tile(x["sa_q_norm_2"][0], 2)[:, None])
    put("sa_k_norm", np.tile(x["sa_k_norm_2"][0], 2)[:, None])
    put("gdn_a_log", x["gdn_a_log"].T, GH)
    put("gdn_dt_bias", x["gdn_dt_bias"].T, GH)
    put("hy_dt_bias", x["hy_dt_bias_2"].T, SH)
    put("hy_a_log", x["hy_a_log_2"].T, SH)
    put("hy_igate_bias", x["hy_igate_bias_2"].T, MH, 32)
    put("hy_fgate_bias", x["hy_fgate_bias_2"].T, MH, 32)
    put("c", cols(x["c"]))
    arrays["vec"] = v
    arrays["cst"] = host_constants()

    def build(table, final):
        nc = bacc.Bacc("TRN2", target_bir_lowering=False, num_devices=1)
        ins = {n: nc.dram_tensor(f"in_{n}", t.shape, mb.dt.from_np(t.dtype), kind="ExternalInput").ap()
               for n, t in arrays.items()}
        out = nc.dram_tensor("out_0", (P, DT, S), mb.dt.float32, kind="ExternalOutput").ap()
        bass_program(nc, ins, out, table, final)
        return nc

    table = {}
    build(table, False)
    nc = build(table, True)
    r = run_bass_kernel_spmd(nc, [{f"in_{n}": t for n, t in arrays.items()}], core_ids=[0])
    y = r.results[0]["out_0"]
    return np.ascontiguousarray(y.transpose(1, 0, 2).reshape(D, S).T)[None]
```

```python
import concourse.bass as bass
from concourse import mybir
from contextlib import ExitStack

F32 = mybir.dt.float32
F32R = mybir.dt.float32r
I32 = mybir.dt.int32
ALU = mybir.AluOpType
ACT = mybir.ActivationFunctionType
AX = mybir.AxisListType

P = 128
S = 512
D = 1024
DT = D // P
FF = 2816
FT = FF // P
CH = 128
NC = S // CH
EPS = 1e-6
RG_C = 8.0
NEG = -1.0e30
LEVELS = 7
RING = 4
SLAB_K = 8
TOPK = 128
GH = 8
SH, SP_ = 16, 64
MH = 4
AH, AD = 16, 64
IH = 8

LINEARS = [
    ("ada", 16, 1, 8), ("lru_in", 16, 1, 8), ("lru_out", 8, 1, 8),
    ("gdn_in", 33, 1, 8), ("gdn_out", 8, 1, 8),
    ("up0", 24, 1, 8), ("down0", 8, 2, 6), ("up1", 20, 1, 8), ("down1", 8, 2, 5),
    ("hy_in", 45, 1, 8), ("hy_out", 8, 2, 8),
    ("up2", 24, 1, 8), ("down2", 8, 2, 6), ("up3", 20, 1, 8), ("down3", 8, 2, 5),
    ("up4", 24, 1, 8), ("down4", 8, 2, 6), ("up5", 20, 1, 8), ("down5", 8, 2, 5),
    ("sa_in", 15, 1, 8), ("sa_out", 8, 1, 8),
    ("up6", 24, 1, 8), ("down6", 8, 2, 6), ("up7", 20, 1, 8), ("down7", 8, 2, 5),
]
PART = [12, 10]

VECS = [("norm_g", 16), ("final_g", 8), ("ada_b", 48), ("lru_conv_w", 32), ("lru_conv_b", 8),
        ("lru_gate_b", 16), ("lru_lambda", 8), ("gdn_conv_w", 96), ("gdn_onorm_g", 1),
        ("ffn_norm", 32), ("mix_norm", 16), ("hy_conv_w", 48), ("hy_conv_b", 12),
        ("hy_ssd_norm", 8), ("hy_mlstm_norm", 8), ("hy_d_skip", 8), ("sa_q_norm", 1),
        ("sa_k_norm", 1), ("gdn_a_log", 1), ("gdn_dt_bias", 1), ("hy_dt_bias", 1),
        ("hy_a_log", 1), ("hy_igate_bias", 1), ("hy_fgate_bias", 1), ("c", 8)]
VEC_AT = {}
_n = 0
for _name, _k in VECS:
    VEC_AT[_name] = _n
    _n += _k
VEC_N = _n

CONSTS = [("ident", P), ("ones", P), ("half_ones", P), ("rotate", P), ("keep_upper", P),
          ("upper", P), ("keep_lower", P), ("levels", LEVELS * P),
          ("inv_freq", 1), ("eps", 1), ("one", 1)]
CONST_AT = {}
_n = 0
for _name, _k in CONSTS:
    CONST_AT[_name] = _n
    _n += _k
CONST_N = _n


class Steps:

    def __init__(self, name, sem, table, final):
        self.name, self.sem, self.table, self.final, self.n = name, sem, table, final, 0

    def mark(self, *step):
        self.n += 1
        if step:
            if not self.final:
                assert (self.name, *step) not in self.table, step
            self.table[(self.name, *step)] = self.n
        return 1

    def at(self, *step):
        if self.final:
            return self.table[(self.name, *step)]
        return self.table.get((self.name, *step), 1)


def bass_program(nc, a, out, table, final):
    ctx = ExitStack()
    with ctx:
        def sb(name, shape, dt=F32, stack=ctx):
            return stack.enter_context(nc.sbuf_tensor(name, shape, dt))

        def sem(name):
            return ctx.enter_context(nc.semaphore(name))

        def twins(name, shape, stack=ctx):
            with ExitStack() as part:
                parts = sb(name + "_PART", shape, F32R, stack=part)
            return sb(name, shape, stack=stack), parts

        X = sb("X", [P, DT, S])
        H, HL = twins("H", [P, DT, S])
        W, WIL = twins("W", [P, RING, SLAB_K * P])
        HHF, HH = twins("HH", [P, DT, S])
        WH = sb("WH", [P, RING, SLAB_K * P], F32R)
        VEC = sb("VEC", [P, VEC_N])
        CST = sb("CST", [P, CONST_N])
        COND = sb("COND", [P, 48])
        GS = sb("GS", [P, 2, DT])
        RT = sb("RT", [P, S])
        PS = [ctx.enter_context(nc.psum_tensor(f"PS{i}", [P, S], F32)) for i in range(8)]
        LB, MB = PS[0:4], PS[4:8]

        def vec(name, j=0, n=1, rows=P):
            return VEC[0:rows, VEC_AT[name] + j:VEC_AT[name] + j + n]

        def cst(name, rows=P, n=P, at=0):
            return CST[0:rows, CONST_AT[name] + at:CONST_AT[name] + at + n]

        ident, ones, half_ones, rotate = cst("ident"), cst("ones"), cst("half_ones"), cst("rotate")
        eps, one = cst("eps", n=1), cst("one", n=1)

        def heads(col, n, width=CH):
            return col.unsqueeze(2).to_broadcast([col.shape[0], n, width])

        def per_head(tile, n):
            return tile.unsqueeze(1).to_broadcast([tile.shape[0], n, tile.shape[1]])

        slab_in = [sem(f"slab_in{i}") for i in range(RING)]
        tile_done = sem("tile_done")
        x_in, vec_in, cst_in = sem("x_in"), sem("vec_in"), sem("cst_in")
        gate_w_in, pos_in = sem("gate_w_in"), sem("pos_in")
        x_ready = sem("x_ready")
        square_ready = sem("square_ready")
        sum_ready = sem("sum_ready")
        root_ready = sem("root_ready")
        inv_ready = sem("inv_ready")
        h_part = sem("h_part")
        h_ready = sem("h_ready")
        silu_ready = sem("silu_ready")
        prod_ready = sem("prod_ready")
        hid_high = sem("hid_high")
        hid_ready = sem("hid_ready")
        w_high = sem("w_high")
        w_ready = sem("w_ready")
        mix_high = sem("mix_high")
        mix_ready = sem("mix_ready")
        hh_ready = sem("hh_ready")
        hl_even = sem("hl_even")
        hl_odd = sem("hl_odd")
        out_done = sem("out_done")
        V = Steps("vector", sem("vector_step"), table, final)
        A = Steps("scalar", sem("scalar_step"), table, final)
        T = Steps("tensor", sem("tensor_step"), table, final)
        G = Steps("gpsimd", sem("gpsimd_step"), table, final)

        def chain(eng, steps, ins):
            ins.then_inc(steps.sem, steps.mark())
            eng.wait_ge(steps.sem, steps.n)

        TILE0, SLAB0, last_tile = {}, {}, []
        t = 0
        for name, tiles, per, _ in LINEARS:
            TILE0[name], SLAB0[name] = t, len(last_tile)
            if name == "ada":
                last_tile += [None] * tiles
                continue
            for j in range(tiles):
                last_tile += [t + j] * per
            t += tiles
        SPLIT_NO, MIX_NO = {}, {}
        for name, tiles, per, _ in LINEARS[1:]:
            numbers = SPLIT_NO if name.startswith(("up", "down")) else MIX_NO
            for j in range(tiles * per):
                numbers[SLAB0[name] + j] = len(numbers)

        def bank_of(tile):
            return tile % 4

        def load_slab(sp, name, j, k):
            s = SLAB0[name] + j
            if s >= RING:
                sp.wait_ge(*slab_left(s - RING))
            sp.dma_start(W[:, s % RING, 0:k * P], a["w_" + name][j]).then_inc(slab_in[s % RING], 16)

        def slab_left(s):
            if last_tile[s] is None:
                return ada_used, s + 1
            return (w_ready, SPLIT_NO[s] + 1) if s in SPLIT_NO else (tile_done, last_tile[s] + 1)

        def load_ada2(sp, pair):
            for n in (2 * pair, 2 * pair + 1):
                if n >= 2:
                    sp.wait_ge(ada2_used, n - 1)
                sp.dma_start(W2[:, n % 2, :], a["w_ada2"][n]).then_inc(ada2_in[n % 2], 16)

        def sync_program(sp):
            for name, tiles, per, k in LINEARS:
                if name.startswith("up"):
                    for j in range(RING):
                        load_slab(sp, name, j, k)
                    with sp.Fori(1, tiles // RING) as i:
                        for j in range(RING):
                            s = SLAB0[name] + j
                            sp.wait_ge(w_ready, i * RING + (SPLIT_NO[s] - RING + 1))
                            sp.dma_start(W[:, s % RING, 0:k * P],
                                         a["w_" + name][bass.ds(i * RING + j, 1)].rearrange("a p n -> (a p) n")
                                         ).then_inc(slab_in[s % RING], 16)
                else:
                    for j in range(tiles * per):
                        load_slab(sp, name, j, k)
                        if name == "lru_in" and j >= RING:
                            load_ada2(sp, j - RING)
                        if name == "lru_out" and 3 <= j < 7:
                            load_ada2(sp, 12 + j - 3)
            for d in range(DT):
                sp.wait_ge(x_ready, DT * (len(RES) - 1) + d + 1)
                sp.dma_start(out[:, d, :], X[:, d, :]).then_inc(out_done, 16)
            sp.wait_ge(out_done, 16 * DT)

        def three(o, wh, wl, xh, xl, first, last):
            nc.tensor.matmul(o, wh, xh, start=first, stop=False)
            nc.tensor.matmul(o, wh, xl, start=False, stop=False)
            return nc.tensor.matmul(o, wl, xh, start=False, stop=last)

        def mix_split(pool, name, first=0, count=None):
            _, tiles, per, k = next(x for x in LINEARS if x[0] == name)
            for j in range(first, tiles * per if count is None else first + count):
                s = SLAB0[name] + j
                if last_tile[s - RING] is not None:
                    pool.wait_ge(tile_done, last_tile[s - RING] + 1)
                pool.wait_ge(slab_in[s % RING], 16 * (s // RING + 1))
                w, wh = W[:, s % RING, 0:k * P], WH[:, s % RING, 0:k * P]
                nc.gpsimd.tensor_tensor(wh, w, one.to_broadcast([P, k * P]), ALU.mult).then_inc(mix_high, 1)
                pool.wait_ge(mix_high, MIX_NO[s] + 1)
                nc.gpsimd.tensor_tensor(WIL[:, s % RING, 0:k * P], w, wh.bitcast(F32), ALU.subtract).then_inc(mix_ready, 1)

        SETS = ["lru_in", "lru_out", "gdn_in", "gdn_out", "ffn0", "hy_in", "hy_out", "hy_out2",
                "ffn1", "ffn2", "sa_in", "ffn3"]

        def x_high(act, x, hi):
            nc.scalar.activation(hi, x, ACT.Copy).then_inc(hh_ready, 1)

        def x_low(eng, name, k, x, lo, hi):
            eng.wait_ge(hh_ready, DT * SETS.index(name) + k + 1)
            (nc.gpsimd if k % 2 else nc.vector).tensor_tensor(
                lo, x, hi.bitcast(F32), ALU.subtract).then_inc(hl_odd if k % 2 else hl_even, 1)

        def x_wait(pe, name):
            base = DT // 2 * SETS.index(name)
            return lambda k: pe.wait_ge(hl_odd if k % 2 else hl_even, base + k // 2 + 1)

        def act_h_high(act, name, n):
            for d in range(DT):
                act.wait_ge(h_ready, DT * H_NORM[n] + d + 1)
                x_high(act, H[:, d, :], HH[:, d, :])

        INPUT_OF = {0: "lru_in", 1: "gdn_in", 3: "ffn0", 4: "hy_in", 5: "ffn1", 6: "ffn2", 7: "sa_in", 8: "ffn3"}

        def h_low(eng, name, d):
            x_low(eng, name, d, H[:, d, :], HL[:, d, :], HH[:, d, :])

        def pool_h_low(pool, name):
            for d in range(1, DT, 2):
                h_low(pool, name, d)

        def pool_in(pool, name, first=RING):
            mix_split(pool, name, 0, first)
            pool_h_low(pool, name)
            mix_split(pool, name, first)

        def freed(tile):
            name = next(n for n, c, _, _ in LINEARS if n != "ada" and TILE0[n] <= tile < TILE0[n] + c)
            return FREED[name](tile - TILE0[name])

        def pe_tile(pe, name, j, rhs, ready=None, outs=None):
            _, _, per, k = next(x for x in LINEARS if x[0] == name)
            tile = TILE0[name] + j
            if outs is None:
                if tile >= 4:
                    pe.wait_ge(*freed(tile - 4))
                outs = [(LB[bank_of(tile)][:, :], 0, P)]
            for n, (o, c0, c1) in enumerate(outs):
                for q in range(per):
                    s = SLAB0[name] + j * per + q
                    if n == 0:
                        pe.wait_ge(mix_ready, MIX_NO[s] + 1)
                    wl = WIL[:, s % RING, 0:k * P].rearrange("p (k f) -> p k f", k=k)
                    wh = WH[:, s % RING, 0:k * P].rearrange("p (k f) -> p k f", k=k)
                    for kk in range(k):
                        if ready is not None and n == 0:
                            ready(q * k + kk)
                        xh, xl = rhs(q * k + kk)
                        last = three(o, wh[:, kk, c0:c1], wl[:, kk, c0:c1], xh, xl,
                                     q == 0 and kk == 0, q == per - 1 and kk == k - 1)
            last.then_inc(tile_done, 1)

        def act_norm(act, n, between=None):
            for d in range(DT):
                if n == 0:
                    if d == 0:
                        act.wait_ge(x_in, 16)
                else:
                    act.wait_ge(x_ready, DT * NORM_AFTER[n] + d + 1)
                if n == 8 and d == 0:
                    act.wait_ge(tile_done, last_tile[SLAB0["up6"] - 1] + 1)
                nc.scalar.activation(H[:, d, :], X[:, d, :], ACT.Square).then_inc(square_ready, 1)
            if between is not None:
                between()
            act.wait_ge(sum_ready, n + 1)
            nc.scalar.activation(RT[:, :], MB[0][:, :], ACT.Sqrt, bias=eps, scale=1.0 / D
                                 ).then_inc(root_ready, 1)

        def pe_norm(pe, n):
            for d in range(DT):
                pe.wait_ge(square_ready, DT * n + d + 1)
                last = nc.tensor.matmul(MB[0][:, :], ones, H[:, d, :], start=d == 0, stop=d == DT - 1)
            last.then_inc(sum_ready, 1)

        def dve_inverse(dve, n):
            dve.wait_ge(root_ready, n + 1)
            nc.vector.reciprocal(RT[:, :], RT[:, :]).then_inc(inv_ready, 1)

        def dve_norm(dve, n, gain, shift=None, dst=None, sig=None):
            if n:
                dve_inverse(dve, n)
            dve.wait_ge(inv_ready, n + 1)
            dst = dst or (lambda d: H[:, d, :])

            def add_shift(d):
                dve.wait_ge(h_part, DT * n + d + 1)
                nc.vector.tensor_scalar(dst(d), dst(d), shift(d), None, ALU.add).then_inc(h_ready, 1)

            for d in range(DT):
                ins = nc.vector.scalar_tensor_tensor(dst(d), X[:, d, :], gain(d), RT[:, :],
                                                     ALU.mult, ALU.mult)
                if shift is None:
                    ins.then_inc(sig or h_ready, 1)
                else:
                    ins.then_inc(h_part, 1)
                    if d:
                        add_shift(d - 1)
                if n in INPUT_OF and d >= 2 and d % 2 == 0:
                    h_low(dve, INPUT_OF[n], d - 2)
            if shift is not None:
                add_shift(DT - 1)
            if n in INPUT_OF:
                h_low(dve, INPUT_OF[n], DT - 2)

        H_NORM = {0: 0, 1: 1, 3: 2, 4: 3, 5: 4, 6: 5, 7: 6, 8: 7}

        def h_tile(k):
            return HH[:, k, :], HL[:, k, :]

        act_c = sem("act_c")
        ada_used = sem("ada_used")
        ada2_in = [sem("ada2_in0"), sem("ada2_in1")]
        ada2_used = sem("ada2_used")
        cond_sum = sem("cond_sum")
        cond_ready = sem("cond_ready")
        ADA_N = SLAB_K * P

        def ada_add(eng, acc, w, k):
            return eng.tensor_scalar(acc, w, CA[:, k:k + 1], None, ALU.mult) if k == 0 else \
                eng.scalar_tensor_tensor(acc, w, CA[:, k:k + 1], acc, ALU.mult, ALU.add)

        def pe_ada_columns(acc, g, col):
            for j in range(ADA_N // P):
                last = nc.tensor.matmul(MB[1][:, col + j:col + j + 1], acc[:, g, j * P:(j + 1) * P],
                                        ones[:, 0:1], start=True, stop=True)
            last.then_inc(cond_sum, 1)

        def pe_ada(pe):
            for g in range(2):
                pe.wait_ge(ada_used, DT * (g + 1))
                pe_ada_columns(ACC1, g, 8 * g)

        def pe_ada2(pe, first, last):
            pe.wait_ge(ada2_used, DT * last)
            for g in range(first, last):
                pe_ada_columns(ACC2, g, 8 * g)

        def act_ada(act):
            act.wait_ge(vec_in, 16)
            act.wait_ge(cst_in, 16)
            nc.scalar.activation(CA[:, :], vec("c", 0, DT), ACT.Silu).then_inc(act_c, 1)

        cond_steps = [0]

        def cond(dve, groups, col, n, layer):
            def step(ins):
                ins.then_inc(cond_ready, 1)
                cond_steps[0] += 1
                dve.wait_ge(cond_ready, cond_steps[0])

            dve.wait_ge(cond_sum, groups)
            at = 0 if col in (0, 16) else 24
            step(nc.vector.tensor_tensor(COND[:, col:col + n], MB[1][:, at:at + n], vec("ada_b", col, n), ALU.add))
            if layer is not None:
                step(nc.vector.scalar_tensor_tensor(GS[:, layer, :], COND[:, 24 * layer + 8:24 * layer + 16], 1.0,
                                                    vec("norm_g", 8 * layer, 8), ALU.add, ALU.mult))

        def dve_ada(dve):
            dve.wait_ge(vec_in, 16)
            dve.wait_ge(cst_in, 16)
            dve.wait_ge(act_c, 1)
            for s in range(2 * DT):
                g, k = s // DT, s % DT
                dve.wait_ge(slab_in[s % RING], 16 * (s // RING + 1))
                if k:
                    dve.wait_ge(ada_used, s)
                ada_add(nc.vector, ACC1[:, g, :], W[:, s % RING, :], k).then_inc(ada_used, 1)
            dve_inverse(dve, 0)
            cond(dve, 2, 0, 16, 0)

        def dve_ada2(dve, pair):
            for s in (2 * pair, 2 * pair + 1):
                g, k = s // DT, s % DT
                dve.wait_ge(ada2_in[s % 2], 16 * (s // 2 + 1))
                if k:
                    dve.wait_ge(ada2_used, s)
                ada_add(nc.vector, ACC2[:, g, :], W2[:, s % 2, :], k).then_inc(ada2_used, 1)

        CA = sb("CA", [P, DT])

        lru = ExitStack()
        XP = sb("XP", [P, 2, S + 3])
        CV = sb("CV", [P, 2, S])
        SQ = sb("SQ", [P, 2, S])
        RN = sb("RN", [P, 2, S])
        LXB, LXL = twins("LXB", [P, DT, S], lru)
        LR = sb("LR", [P, 4, S], stack=lru)
        LI_ = sb("LI", [P, 4, S], stack=lru)
        LA = sb("LA", [P, 4, S], stack=lru)
        LM = sb("LM", [P, 4, S], stack=lru)
        LZ = sb("LZ", [P, DT, S], stack=lru)
        GW = sb("GW", [P, 16, P], stack=lru)
        LAM = sb("LAM", [P, DT], stack=lru)
        LAT = sb("LAT", [P, 2, DT], stack=lru)
        ACC2 = sb("ACC2", [P, 4, ADA_N], stack=lru)
        W2 = sb("W2", [P, 2, ADA_N], stack=lru)
        ACC1 = LZ[:, 0:2 * ADA_N // S, :].rearrange("p a s -> p (a s)").rearrange("p (g n) -> p g n", g=2)
        lru.close()

        def gate_at(j):
            return j // 2, j % 2

        def pe_lru(pe):
            def gates(first):
                for j in range(first, first + 8):
                    d, g = gate_at(j)
                    pe.wait_ge(V.sem, V.at("lru conv", d))
                    if j >= 4:
                        pe.wait_ge(A.sem, A.at("lru gate", j - 4))
                    nc.tensor.matmul(MB[j % 4][:, :], GW[:, g * 8 + d, :], LXB[:, d, :],
                                     start=True, stop=True).then_inc(T.sem, T.mark("lru gate", j))

            for j in range(6):
                pe_tile(pe, "lru_in", j, h_tile, x_wait(pe, "lru_in") if j == 0 else None)
            pe.wait_ge(gate_w_in, 16)
            gates(0)
            for j in range(6, 10):
                pe_tile(pe, "lru_in", j, h_tile)
            gates(8)
            for j in range(10, 16):
                pe_tile(pe, "lru_in", j, h_tile)
            pe.wait_ge(A.sem, A.at("lru gate", 15))
            pe_ada2(pe, 0, 3)
            for j in range(8):
                pe_tile(pe, "lru_out", j, lambda k: (HH[:, k, :], LXL[:, k, :]),
                        x_wait(pe, "lru_out") if j == 0 else None)
            pe_ada2(pe, 3, 4)

        def arrived(eng, name, j):
            tile = TILE0[name] + j
            eng.wait_ge(tile_done, tile + 1)
            return LB[bank_of(tile)]

        def act_lru(act):
            chain(act, A, nc.scalar.activation(LAT[:, 0, :], vec("lru_lambda", 0, 8), ACT.Abs))
            chain(act, A, nc.scalar.activation(LAT[:, 0, :], LAT[:, 0, :], ACT.Exp, scale=-1.0))
            nc.scalar.activation(LAT[:, 0, :], LAT[:, 0, :], ACT.Ln, bias=one
                                 ).then_inc(A.sem, A.mark("lambda ln"))
            act.wait_ge(V.sem, V.at("pads"))
            def xp(j):
                bank = arrived(act, "lru_in", j)
                if j >= 2:
                    act.wait_ge(V.sem, V.at("lru conv", j - 2))
                nc.scalar.activation(XP[:, j % 2, 3:], bank[:, :], ACT.Copy).then_inc(A.sem, A.mark("lru xp", j))

            def silu_z(j):
                bank = arrived(act, "lru_in", 8 + j)
                nc.scalar.activation(LZ[:, j, :], bank[:, :], ACT.Silu).then_inc(A.sem, A.mark("lru silu", j))

            def gates(first):
                for j in range(first, first + 8):
                    d, g = gate_at(j)
                    act.wait_ge(T.sem, T.at("lru gate", j))
                    if d >= 4:
                        act.wait_ge(V.sem, V.at("lru b", d - 4))
                    nc.scalar.activation((LI_ if g else LR)[:, d % 4, :], MB[j % 4][:, :], ACT.Sigmoid,
                                         bias=vec("lru_gate_b", 8 * g + d)
                                         ).then_inc(A.sem, A.mark("lru gate", j))

            def decays(first):
                act.wait_ge(A.sem, A.at("lru gate", 2 * first + 7))
                for d in range(first, first + 4):
                    if d >= 4:
                        act.wait_ge(V.sem, V.at("lru h", d - 4))
                    nc.scalar.activation(LA[:, d % 4, :], LR[:, d % 4, :], ACT.Exp, scale=LAM[:, d:d + 1]
                                         ).then_inc(A.sem, A.mark("lru a", d))
                    nc.scalar.activation(LR[:, d % 4, :], LR[:, d % 4, :], ACT.Tanh, scale=LAM[:, d:d + 1]
                                         ).then_inc(A.sem, A.mark("lru tanh", d))
                for d in range(first, first + 4):
                    act.wait_ge(A.sem, A.at("lru a", d))
                    nc.scalar.activation(LM[:, d % 4, :], LA[:, d % 4, :], ACT.Square
                                         ).then_inc(A.sem, A.mark("lru a2", d))

            def mults(first):
                for d in range(first, first + 4):
                    act.wait_ge(V.sem, V.at("lru m2", d))
                    nc.scalar.activation(LM[:, d % 4, :], LM[:, d % 4, :], ACT.Sqrt, scale=-1.0
                                         ).then_inc(A.sem, A.mark("lru mult", d))

            for j in range(6):
                xp(j)
            gates(0)
            xp(6)
            act.wait_ge(V.sem, V.at("lambda"))
            decays(0)
            xp(7)
            mults(0)
            silu_z(0)
            silu_z(1)
            gates(8)
            silu_z(2)
            decays(4)
            silu_z(3)
            mults(4)
            for j in range(4, 8):
                silu_z(j)
            for d in range(8):
                act.wait_ge(V.sem, V.at("lru y", d))
                x_high(act, LXB[:, d, :], HH[:, d, :])

        def conv(dve, xp, dst, w, j, stride, bias, step):
            first = nc.vector.tensor_scalar(dst, xp[:, 0:S], vec(w, j), bias, ALU.mult,
                                            ALU.bypass if bias is None else ALU.add) \
                if bias is not None else nc.vector.tensor_scalar(dst, xp[:, 0:S], vec(w, j), None, ALU.mult)
            chain(dve, V, first)
            for t in range(1, 4):
                ins = nc.vector.scalar_tensor_tensor(dst, xp[:, t:t + S], vec(w, t * stride + j), dst,
                                                     ALU.mult, ALU.add)
                if t < 3:
                    chain(dve, V, ins)
                else:
                    ins.then_inc(V.sem, V.mark(*step))

        def dve_lru(dve):
            nc.vector.memset(XP[:, :, 0:3], 0.0).then_inc(V.sem, V.mark("pads"))
            dve.wait_ge(A.sem, A.at("lambda ln"))
            chain(dve, V, nc.vector.tensor_scalar(LAT[:, 1, :], vec("lru_lambda", 0, 8), -1.0, 0.0,
                                                  ALU.mult, ALU.max))
            chain(dve, V, nc.vector.tensor_tensor(LAT[:, 1, :], LAT[:, 1, :], LAT[:, 0, :], ALU.add))
            nc.vector.tensor_scalar(LAM[:, :], LAT[:, 1, :], -RG_C, None, ALU.mult
                                    ).then_inc(V.sem, V.mark("lambda"))
            for j in range(8):
                dve.wait_ge(A.sem, A.at("lru xp", j))
                conv(dve, XP[:, j % 2, :], LXB[:, j, :], "lru_conv_w", j, 8, vec("lru_conv_b", j),
                     ("lru conv", j))
                dve_ada2(dve, j)
            for first in (0, 4):
                for d in range(first, first + 4):
                    dve.wait_ge(A.sem, A.at("lru gate", 2 * d + 1))
                    dve.wait_ge(V.sem, V.at("lru conv", d))
                    nc.vector.tensor_tensor(LI_[:, d % 4, :], LI_[:, d % 4, :], LXB[:, d, :], ALU.mult
                                            ).then_inc(V.sem, V.mark("lru ix", d))
                for d in range(first, first + 4):
                    dve.wait_ge(A.sem, A.at("lru a2", d))
                    nc.vector.scalar_tensor_tensor(LM[:, d % 4, :], LM[:, d % 4, :], 1.0, LR[:, d % 4, :],
                                                   ALU.add, ALU.mult).then_inc(V.sem, V.mark("lru m2", d))
                dve_ada2(dve, 8 + first // 2)
                for d in range(first, first + 4):
                    dve.wait_ge(A.sem, A.at("lru mult", d))
                    dve.wait_ge(V.sem, V.at("lru ix", d))
                    nc.vector.tensor_tensor(LM[:, d % 4, :], LM[:, d % 4, :], LI_[:, d % 4, :], ALU.mult
                                            ).then_inc(V.sem, V.mark("lru b", d))
                for d in range(first, first + 4):
                    dve.wait_ge(V.sem, V.at("lru b", d))
                    nc.vector.tensor_tensor_scan(LXB[:, d, :], LA[:, d % 4, :], LM[:, d % 4, :], 0.0,
                                                 ALU.mult, ALU.add).then_inc(V.sem, V.mark("lru h", d))
                dve_ada2(dve, 9 + first // 2)
            for d in range(8):
                dve.wait_ge(A.sem, A.at("lru silu", d))
                dve.wait_ge(V.sem, V.at("lru h", d))
                nc.vector.tensor_tensor(LXB[:, d, :], LXB[:, d, :], LZ[:, d, :], ALU.mult
                                        ).then_inc(V.sem, V.mark("lru y", d))
                if d % 2:
                    x_low(dve, "lru_out", d - 1, LXB[:, d - 1, :], LXL[:, d - 1, :], HH[:, d - 1, :])
            cond(dve, 5, 16, 24, 1)
            residual(dve, "lru_out", lambda d: COND[:, 16 + d:17 + d],
                     lambda d: dve_ada2(dve, 12 + d) if d < 4 else None)
            cond(dve, 6, 40, 8, None)

        def pool_lru(pool):
            pool.wait_ge(cst_in, 16)
            pool_in(pool, "lru_in", 2)
            mix_split(pool, "lru_out", 0, RING)
            for d in range(1, DT, 2):
                x_low(pool, "lru_out", d, LXB[:, d, :], LXL[:, d, :], HH[:, d, :])
            mix_split(pool, "lru_out", RING)

        def residual(dve, name, gate, between=None):
            for d in range(8):
                if between is not None:
                    between(d)
                bank = arrived(dve, name, d)
                nc.vector.scalar_tensor_tensor(X[:, d, :], bank[:, :], gate(d), X[:, d, :],
                                               ALU.mult, ALU.add).then_inc(x_ready, 1)

        RES = {n: i for i, n in enumerate(
            ["lru_out", "gdn_out", "final", "down0", "down1", "hy_out", "down2", "down3", "down4", "down5",
             "sa_out", "down6", "down7"])}
        NORM_AFTER = {1: RES["lru_out"], 2: RES["gdn_out"], 3: RES["final"], 4: RES["down1"], 5: RES["hy_out"],
                      6: RES["down3"], 7: RES["down5"], 8: RES["sa_out"]}

        ffn = ExitStack()
        DH = sb("DH", [P, PART[0], S], F32R, stack=ffn)
        DL = sb("DL", [P, PART[0], S], F32R, stack=ffn)
        WL = sb("WL", [P, RING, SLAB_K * P], F32R, stack=ffn)
        FGT = sb("FGT", [P, 2, S], stack=ffn)
        PRD = sb("PRD", [P, 2, S], stack=ffn)
        ffn.close()
        HID0 = [FT * (p // 2) + PART[0] * (p % 2) for p in range(8)]

        def split_high(act, s, k):
            if s >= RING:
                act.wait_ge(tile_done, last_tile[s - RING] + 1)
            act.wait_ge(slab_in[s % RING], 16 * (s // RING + 1))
            nc.scalar.activation(WH[:, s % RING, 0:k * P], W[:, s % RING, 0:k * P], ACT.Copy
                                 ).then_inc(w_high, 1)

        def split_low(pool, s, k):
            pool.wait_ge(w_high, SPLIT_NO[s] + 1)
            nc.gpsimd.tensor_tensor(WL[:, s % RING, 0:k * P], W[:, s % RING, 0:k * P],
                                    WH[:, s % RING, 0:k * P].bitcast(F32), ALU.subtract).then_inc(w_ready, 1)

        def pe_up_tile(pe, name, j, wait_h):
            s = SLAB0[name] + j
            for k in range(DT):
                if wait_h:
                    x_wait(pe, wait_h)(k)
                c = slice(k * P, (k + 1) * P)
                last = three(LB[bank_of(TILE0[name] + j)][:, :], WH[:, s % RING, c], WL[:, s % RING, c],
                             *h_tile(k), k == 0, k == DT - 1)
            last.then_inc(tile_done, 1)

        def pe_ffn(pe, f):
            for p in (2 * f, 2 * f + 1):
                name = f"up{p}"
                for j in range(RING):
                    pe.wait_ge(*freed(TILE0[name] + j - 4))
                    pe.wait_ge(w_ready, SPLIT_NO[SLAB0[name] + j] + 1)
                    pe_up_tile(pe, name, j, f"ffn{f}" if p % 2 == 0 and j == 0 else None)
                with pe.Fori(1, 2 * PART[p % 2] // RING) as i:
                    for j in range(RING):
                        pe.wait_ge(prod_ready if j % 2 else silu_ready, i * 2 + (HID0[p] + j // 2 - 1))
                        pe.wait_ge(w_ready, i * RING + (SPLIT_NO[SLAB0[name] + j] + 1))
                        pe_up_tile(pe, name, j, None)
                name = f"down{p}"
                for j in range(8):
                    tile = TILE0[name] + j
                    pe.wait_ge(*freed(tile - 4))
                    for q in range(2):
                        n = PART[p % 2] // 2
                        s = SLAB0[name] + 2 * j + q
                        pe.wait_ge(w_ready, SPLIT_NO[s] + 1)
                        for kk in range(n):
                            k = q * n + kk
                            if j == 0:
                                pe.wait_ge(hid_ready, HID0[p] + k + 1)
                            c = slice(kk * P, (kk + 1) * P)
                            last = three(LB[bank_of(tile)][:, :], WH[:, s % RING, c], WL[:, s % RING, c],
                                         DH[:, k, :], DL[:, k, :], k == 0, k == 2 * n - 1)
                    last.then_inc(tile_done, 1)

        def act_ffn_high(act, n, f):
            act.wait_ge(x_ready, DT * NORM_AFTER[n] + DT)
            for j in range(RING):
                split_high(act, SLAB0[f"up{2 * f}"] + j, DT)

        def act_ffn(act, f):
            act_h_high(act, f"ffn{f}", FFN_NORM[f])
            for p in (2 * f, 2 * f + 1):
                name = f"up{p}"
                k_down = PART[p % 2] // 2

                def gate(m):
                    if m >= 2:
                        act.wait_ge(prod_ready, HID0[p] + m - 1)
                    bank = arrived(act, name, 2 * m)
                    nc.scalar.activation(FGT[:, m % 2, :], bank[:, :], ACT.Silu).then_inc(silu_ready, 1)

                for m in range(2):
                    gate(m)
                    for j in range(2):
                        split_high(act, SLAB0[name] + 2 * m + j + RING, DT)
                with act.Fori(1, PART[p % 2] // 2 - 1) as i:
                    for m in range(2):
                        act.wait_ge(prod_ready, i * 2 + (HID0[p] + m - 1))
                        act.wait_ge(tile_done, i * 4 + (TILE0[name] + 2 * m + 1))
                        nc.scalar.activation(FGT[:, m, :], LB[bank_of(TILE0[name] + 2 * m)][:, :], ACT.Silu
                                             ).then_inc(silu_ready, 1)
                        for j in range(2):
                            s = SLAB0[name] + 2 * m + j
                            act.wait_ge(tile_done, i * 4 + (TILE0[name] + 2 * m + j + 1))
                            act.wait_ge(slab_in[s % RING], i * 16 + 16 * (s // RING + 2))
                            nc.scalar.activation(WH[:, s % RING, :], W[:, s % RING, :], ACT.Copy
                                                 ).then_inc(w_high, 1)
                for m in range(2):
                    gate(PART[p % 2] - 2 + m)
                    for j in range(2):
                        split_high(act, SLAB0[f"down{p}"] + 2 * m + j, k_down)
                for j in range(4, 16):
                    split_high(act, SLAB0[f"down{p}"] + j, k_down)
                if p % 2 == 0:
                    for j in range(RING):
                        split_high(act, SLAB0[f"up{p + 1}"] + j, DT)

        def pool_ffn(pool, f):
            for j in range(RING):
                split_low(pool, SLAB0[f"up{2 * f}"] + j, DT)
            pool_h_low(pool, f"ffn{f}")
            for p in (2 * f, 2 * f + 1):
                name = f"up{p}"
                with pool.Fori(1, 2 * PART[p % 2] // RING) as i:
                    for j in range(RING):
                        s = SLAB0[name] + j
                        pool.wait_ge(w_high, i * RING + (SPLIT_NO[s] + 1))
                        nc.gpsimd.tensor_tensor(WL[:, s % RING, :], W[:, s % RING, :],
                                                WH[:, s % RING, :].bitcast(F32), ALU.subtract
                                                ).then_inc(w_ready, 1)
                for j in range(16):
                    split_low(pool, SLAB0[f"down{p}"] + j, PART[p % 2] // 2)
                if p % 2 == 0:
                    for j in range(RING):
                        split_low(pool, SLAB0[f"up{p + 1}"] + j, DT)

        def dve_ffn(dve, f):
            for p in (2 * f, 2 * f + 1):
                name = f"up{p}"
                with dve.Fori(0, PART[p % 2] // 2) as i:
                    for m in range(2):
                        def hid(tensor):
                            return tensor[:, bass.ds(i * 2 + m, 1), :].rearrange("p a s -> p (a s)")

                        dve.wait_ge(silu_ready, i * 2 + (HID0[p] + m + 1))
                        dve.wait_ge(tile_done, i * 4 + (TILE0[name] + 2 * m + 2))
                        nc.vector.tensor_tensor(PRD[:, m, :], FGT[:, m, :], LB[bank_of(TILE0[name] + 2 * m + 1)][:, :],
                                                ALU.mult).then_inc(prod_ready, 1)
                        dve.wait_ge(prod_ready, i * 2 + (HID0[p] + m + 1))
                        nc.vector.tensor_copy(hid(DH), PRD[:, m, :]).then_inc(hid_high, 1)
                        dve.wait_ge(hid_high, i * 2 + (HID0[p] + m + 1))
                        nc.vector.tensor_tensor(hid(DL), PRD[:, m, :], hid(DH).bitcast(F32), ALU.subtract
                                                ).then_inc(hid_ready, 1)
                residual(dve, f"down{p}", lambda d: 0.5)

        FFN_NORM = [3, 5, 6, 8]

        def up_freed(p):
            return lambda j: (prod_ready if j % 2 else silu_ready, HID0[p] + j // 2 + 1)

        def res_freed(name):
            return lambda j: (x_ready, 8 * RES[name] + j + 1)

        FREED = {
            "lru_in": lambda j: (A.sem, A.at("lru xp", j) if j < 8 else A.at("lru silu", j - 8)),
            **{f"up{p}": up_freed(p) for p in range(8)},
            **{n: res_freed(n) for n in RES if n != "final"},
        }

        gdn = ExitStack()
        GK = sb("GK", [P, GH, S], stack=gdn)
        GQ, GOL = twins("GQ", [P, GH, S], gdn)
        GV = sb("GV", [P, GH, S], stack=gdn)
        GZ = sb("GZ", [P, GH, S], stack=gdn)
        GROWS = sb("GROWS", [P, 4, S], stack=gdn)
        GROW = GROWS[0:GH]
        GBETAS = sb("GBETAS", [P, 2, S], stack=gdn)
        GBETA = GBETAS[0:GH]
        GCOL = sb("GCOL", [P, 3, NC, GH], stack=gdn)
        GSEL = sb("GSEL", [GH, NC, GH], stack=gdn)
        GEL = sb("GEL", [P, NC, GH], stack=gdn)
        GEA = sb("GEA", [GH, 1], stack=gdn)
        gt = [{n: sb(f"G{n}{g}", [P, 4, P], stack=gdn) for n in ("KT", "QD", "KD", "VB")} for g in range(2)]
        for g in range(2):
            for i, n in enumerate(("T", "U", "Y", "L")):
                gt[g][n] = HHF[:, 4 * g + i, :].rearrange("p (h t) -> p h t", h=4)
            for i, n in enumerate(("AT", "AM")):
                gt[g][n] = H[:, 2 + 2 * g + i, :].rearrange("p (h t) -> p h t", h=4)
        GS_ = sb("GSTATE", [P, GH, P], stack=gdn)
        GVN = [H[:, g, :].rearrange("p (h t) -> p h t", h=4) for g in range(2)]
        gdn.close()
        GO = GQ
        GB = [[MB[b] for b in range(4)], [LB[b] for b in range(4)]]

        def four(bank):
            return bank[:, :].rearrange("p (h t) -> p h t", h=4)

        def fm(tensor, c, g):
            return tensor[:, 4 * g:4 * g + 4, c * CH:(c + 1) * CH]

        GNORM = [(GK, h) for h in range(8)] + [(GQ, h) for h in range(8)]

        def gconv_dst(j):
            return (GK, GQ, GV)[j // 8][:, j % 8, :]

        def pe_gdn(pe):
            pe_tile(pe, "gdn_in", 0, h_tile, x_wait(pe, "gdn_in"),
                    outs=[(MB[1][0:GH, :], 0, GH), (MB[2][0:GH, :], GH, 2 * GH)])
            for j in range(1, 33):
                pe_tile(pe, "gdn_in", j, h_tile)
                if j >= 4 and j % 2 == 0:
                    gdn_sum(pe, j // 2 - 2)
                if j == 30:
                    gdn_cols(pe)
            gdn_sum(pe, 15)
            for g in range(2):
                pe.wait_ge(A.sem, A.at("gdn z", 7))
                pe.wait_ge(V.sem, V.at("gdn qk", 15))
            pe.wait_ge(V.sem, V.at("gdn cols"))
            for c in range(NC):
                for g in range(2):
                    B = GB[g]
                    if c:
                        pe.wait_ge(A.sem, A.at("gdn vn", c - 1, g))
                        pe.wait_ge(A.sem, A.at("gdn o", c - 1, g))
                        pe.wait_ge(V.sem, V.at("gdn state", c - 1, g))
                    for n, row in ((0, GROWS[:, 1, :]), (1, GROWS[:, 2, :]), (2, GBETAS[:, 1, :])):
                        for h in range(4):
                            last = nc.tensor.matmul(
                                B[n][:, h * P:(h + 1) * P],
                                ident[:, 4 * g + h:4 * g + h + 1].to_broadcast([P, P]),
                                row[:, c * CH:(c + 1) * CH], start=True, stop=True)
                    last.then_inc(T.sem, T.mark("gdn rows", c, g))
                    for h in range(4):
                        kc = GK[:, 4 * g + h, c * CH:(c + 1) * CH]
                        last = nc.tensor.matmul(B[3][:, h * P:(h + 1) * P], kc, kc, start=True, stop=True)
                    last.then_inc(T.sem, T.mark("gdn kk", c, g))
                for g in range(2):
                    B = GB[g]
                    pe.wait_ge(V.sem, V.at("gdn argAT", c, g))
                    for h in range(4):
                        last = nc.tensor.matmul(B[0][:, h * P:(h + 1) * P],
                                                GK[:, 4 * g + h, c * CH:(c + 1) * CH],
                                                GQ[:, 4 * g + h, c * CH:(c + 1) * CH], start=True, stop=True)
                    last.then_inc(T.sem, T.mark("gdn qk", c, g))
                for g in range(2):
                    pe.wait_ge(G.sem, G.at("gdn l", c, g, 0))
                    for h in range(4):
                        last = nc.tensor.transpose(GB[g][3][:, h * P:(h + 1) * P], gt[g]["L"][:, h, :], ident)
                    last.then_inc(T.sem, T.mark("gdn y", c, g, 0))
                for g in range(2):
                    B = GB[g]
                    pe.wait_ge(V.sem, V.at("gdn kt", c, g))
                    for n, src in ((1, GK), (2, GV)):
                        for h in range(4):
                            last = nc.tensor.transpose(B[n][:, h * P:(h + 1) * P],
                                                       src[:, 4 * g + h, c * CH:(c + 1) * CH], ident)
                    last.then_inc(T.sem, T.mark("gdn tok", c, g))
                for l in range(1, LEVELS):
                    if l == 1 and c:
                        gdn_osum(pe, c - 1)
                    for g in range(2):
                        B, b = GB[g], gt[g]
                        pe.wait_ge(G.sem, G.at("gdn l", c, g, l))
                        pe.wait_ge(V.sem, V.at("gdn tu", c, g, l - 1))
                        if l == 1:
                            pe.wait_ge(V.sem, V.at("gdn at", c, g))
                        for h in range(4):
                            last = nc.tensor.matmul(B[0][:, h * P:(h + 1) * P], b["L"][:, h, :],
                                                    b["U"][:, h, :], start=True, stop=True)
                        last.then_inc(T.sem, T.mark("gdn y", c, g, l))
                    for g in range(2):
                        B, b = GB[g], gt[g]
                        pe.wait_ge(A.sem, A.at("gdn y", c, g, l))
                        if l == 1:
                            pe.wait_ge(V.sem, V.at("gdn vb", c, g))
                        for h in range(4):
                            last = nc.tensor.matmul(B[1][:, h * P:(h + 1) * P], b["T"][:, h, :],
                                                    b["Y"][:, h, :], start=True, stop=True)
                        for h in range(4 if l < LEVELS - 1 else 0):
                            last = nc.tensor.matmul(B[2][:, h * P:(h + 1) * P], b["Y"][:, h, :],
                                                    b["T"][:, h, :], start=True, stop=True)
                        last.then_inc(T.sem, T.mark("gdn uy", c, g, l))
                if c:
                    for g in range(2):
                        b = gt[g]
                        pe.wait_ge(A.sem, A.at("gdn oroot", c - 1, g))
                        for h in range(4):
                            last = nc.tensor.matmul(GB[g][3][:, h * P:(h + 1) * P], b["KT"][:, h, :],
                                                    GS_[:, 4 * g + h, :], start=True, stop=True)
                        last.then_inc(T.sem, T.mark("gdn ks", c, g))
                for g in range(2):
                    b = gt[g]
                    pe.wait_ge(V.sem, V.at("gdn tu", c, g, LEVELS - 1))
                    pe.wait_ge(V.sem, V.at("gdn r", c, g) if c else V.at("gdn vb", c, g))
                    for h in range(4):
                        last = nc.tensor.matmul(GB[g][0][:, h * P:(h + 1) * P], b["U"][:, h, :],
                                                b["VB"][:, h, :], start=True, stop=True)
                    last.then_inc(T.sem, T.mark("gdn vn", c, g))
                for g in range(2):
                    b = gt[g]
                    pe.wait_ge(A.sem, A.at("gdn vn", c, g))
                    pe.wait_ge(G.sem, G.at("gdn causal", c, g))
                    for h in range(4):
                        if c:
                            nc.tensor.matmul(GB[g][1][:, h * P:(h + 1) * P], GS_[:, 4 * g + h, :],
                                             b["QD"][:, h, :], start=True, stop=False)
                        last = nc.tensor.matmul(GB[g][1][:, h * P:(h + 1) * P], GVN[g][:, h, :],
                                                b["AT"][:, h, :], start=not c, stop=True)
                    last.then_inc(T.sem, T.mark("gdn o", c, g))
                    if c == NC - 1:
                        continue
                    for h in range(4):
                        last = nc.tensor.matmul(GB[g][2][:, h * P:(h + 1) * P], b["KD"][:, h, :],
                                                GVN[g][:, h, :], start=True, stop=True)
                    last.then_inc(T.sem, T.mark("gdn su", c, g))
            gdn_osum(pe, NC - 1)
            for j in range(8):
                pe_tile(pe, "gdn_out", j, lambda k: (HH[:, k, :], GOL[:, k, :]),
                        x_wait(pe, "gdn_out") if j == 0 else None)

        def gdn_sum(pe, i):
            pe.wait_ge(A.sem, A.at("gdn sq", i))
            if i < 2:
                pe.wait_ge(A.sem, A.at("beta"))
            else:
                pe.wait_ge(A.sem, A.at("gdn root", i - 2))
            nc.tensor.matmul(MB[i % 2 + 2][:, :], ones, SQ[:, i % 2, :], start=True, stop=True
                             ).then_inc(T.sem, T.mark("gdn sum", i))

        def gdn_cols(pe):
            pe.wait_ge(A.sem, A.at("gdn ed"))
            pe.wait_ge(V.sem, V.at("gdn sel"))
            rows = [GROW[:, 1, :], GBETA[:, 0, :], GROW[:, 3, :]]
            for n, row in enumerate(rows):
                for c in range(NC):
                    nc.tensor.matmul(MB[1][:, (n * NC + c) * GH:(n * NC + c + 1) * GH],
                                     row[:, c * CH:(c + 1) * CH], ident[0:GH, 0:GH], start=True, stop=True)
            nc.tensor.matmul(MB[1][:, 96:128], ones[0:GH, :], GSEL[:, :, :].rearrange("p c h -> p (c h)"),
                             start=True, stop=True).then_inc(T.sem, T.mark("gdn cols"))

        def gdn_osum(pe, c):
            for g in range(2):
                pe.wait_ge(A.sem, A.at("gdn osq", c, g))
                pe.wait_ge(V.sem, V.at("gdn tu", c + 1, g, 0) if c < NC - 1 else V.at("gdn r", c, g))
                nc.tensor.matmul(GB[g][3][:, :], ones, SQ[:, g, :], start=True, stop=True
                                 ).then_inc(T.sem, T.mark("gdn osum", c, g))

        def act_gdn(act):
            nc.scalar.activation(GEA[:, :], vec("gdn_a_log", rows=GH), ACT.Exp).then_inc(A.sem, A.mark("gdn ea"))
            act.wait_ge(V.sem, V.at("gdn zero"))
            act.wait_ge(tile_done, TILE0["gdn_in"] + 1)
            nc.scalar.activation(GBETA[:, 0, :], MB[2][0:GH, :], ACT.Sigmoid).then_inc(A.sem, A.mark("beta"))
            act.wait_ge(V.sem, V.at("gdn u"))
            chain(act, A, nc.scalar.activation(GROW[:, 1, :], GROW[:, 0, :], ACT.Abs))
            chain(act, A, nc.scalar.activation(GROW[:, 1, :], GROW[:, 1, :], ACT.Exp, scale=-1.0))
            nc.scalar.activation(GROW[:, 1, :], GROW[:, 1, :], ACT.Ln, bias=one[0:GH, :]
                                 ).then_inc(A.sem, A.mark("gdn ln"))

            def copy_in(j):
                bank = arrived(act, "gdn_in", j + 1)
                if j >= 2:
                    act.wait_ge(V.sem, V.at("gdn conv", j - 2))
                nc.scalar.activation(XP[:, j % 2, 3:], bank[:, :], ACT.Copy).then_inc(A.sem, A.mark("gdn xp", j))

            def silu(j):
                act.wait_ge(V.sem, V.at("gdn conv", j))
                nc.scalar.activation(gconv_dst(j), CV[:, j % 2, :], ACT.Silu).then_inc(A.sem, A.mark("gdn silu", j))

            def sq(i):
                tensor, h = GNORM[i]
                act.wait_ge(A.sem, A.at("gdn silu", i))
                if i >= 2:
                    act.wait_ge(T.sem, T.at("gdn sum", i - 2))
                nc.scalar.activation(SQ[:, i % 2, :], tensor[:, h, :], ACT.Square).then_inc(A.sem, A.mark("gdn sq", i))

            for j in range(36):
                if j < 24:
                    copy_in(j)
                if 0 < j <= 24:
                    silu(j - 1)
                if 24 <= j < 32:
                    bank = arrived(act, "gdn_in", j + 1)
                    nc.scalar.activation(GZ[:, j - 24, :], bank[:, :], ACT.Silu).then_inc(A.sem, A.mark("gdn z", j - 24))
                if j % 2 and j < 32:
                    sq(j // 2)
                if j >= 4 and j % 2 == 0:
                    root(act, j // 2 - 2)
                if j == 12:
                    act.wait_ge(V.sem, V.at("gdn cum"))
                    nc.scalar.activation(GROW[:, 2, :], GROW[:, 1, :], ACT.Exp).then_inc(A.sem, A.mark("gdn eg"))
                    for c in range(NC):
                        nc.scalar.activation(GROW[:, 3, c * CH:(c + 1) * CH], GROW[:, 1, c * CH:(c + 1) * CH], ACT.Exp,
                                             bias=GROW[:, 1, (c + 1) * CH - 1:(c + 1) * CH], scale=-1.0
                                             ).then_inc(A.sem, A.mark("gdn ed") if c == NC - 1 else A.mark())
            for c in range(NC):
                for n, sign in (("AM", -1.0), ("AT", 1.0)):
                    for g in range(2):
                        act.wait_ge(V.sem, V.at("gdn arg" + n, c, g))
                        nc.scalar.activation(gt[g][n][:, :, :], gt[g][n][:, :, :], ACT.Exp, scale=sign
                                             ).then_inc(A.sem, A.mark("gdn exp" + n, c, g))
                if c:
                    osq(act, c - 1)
                for l in range(1, LEVELS):
                    if l == 2 and c:
                        oroot(act, c - 1)
                    for g in range(2):
                        act.wait_ge(T.sem, T.at("gdn y", c, g, l))
                        nc.scalar.activation(gt[g]["Y"][:, :, :], four(GB[g][0]), ACT.Copy
                                             ).then_inc(A.sem, A.mark("gdn y", c, g, l))
                for g in range(2):
                    act.wait_ge(T.sem, T.at("gdn vn", c, g))
                    nc.scalar.activation(GVN[g], four(GB[g][0]), ACT.Copy).then_inc(A.sem, A.mark("gdn vn", c, g))
                for g in range(2):
                    act.wait_ge(T.sem, T.at("gdn o", c, g))
                    nc.scalar.activation(fm(GO, c, g), four(GB[g][1]), ACT.Copy).then_inc(A.sem, A.mark("gdn o", c, g))
            osq(act, NC - 1)
            oroot(act, NC - 1)
            for h in range(GH):
                act.wait_ge(G.sem, G.at("gdn y", NC - 1, h // 4))
                x_high(act, GO[:, h, :], HH[:, h, :])

        def osq(act, c):
            for g in range(2):
                act.wait_ge(A.sem, A.at("gdn o", c, g))
                if c:
                    act.wait_ge(T.sem, T.at("gdn osum", c - 1, g))
                nc.scalar.activation(SQ[:, g, :].rearrange("p (h t) -> p h t", h=4), fm(GO, c, g), ACT.Square
                                     ).then_inc(A.sem, A.mark("gdn osq", c, g))

        def root(act, j):
            act.wait_ge(T.sem, T.at("gdn sum", j))
            if j >= 2:
                act.wait_ge(V.sem, V.at("gdn qk", j - 2))
            nc.scalar.activation(RN[:, j % 2, :], MB[j % 2 + 2][:, :], ACT.Sqrt, bias=eps
                                 ).then_inc(A.sem, A.mark("gdn root", j))

        def oroot(act, c):
            for g in range(2):
                act.wait_ge(T.sem, T.at("gdn osum", c, g))
                if c:
                    act.wait_ge(V.sem, V.at("gdn on", c - 1, g))
                nc.scalar.activation(RN[:, g, :], GB[g][3][:, :], ACT.Sqrt, bias=eps, scale=1.0 / P
                                     ).then_inc(A.sem, A.mark("gdn oroot", c, g))

        def dve_gdn(dve):
            nc.vector.memset(GROWS[:, :, :], 0.0).then_inc(V.sem, V.mark())
            nc.vector.memset(GBETAS[:, :, :], 0.0).then_inc(V.sem, V.mark("gdn zero"))
            dve.wait_ge(V.sem, V.at("gdn zero"))
            dve.wait_ge(tile_done, TILE0["gdn_in"] + 1)
            nc.vector.tensor_scalar(GROW[:, 0, :], MB[1][0:GH, :], vec("gdn_dt_bias", rows=GH), None, ALU.add
                                    ).then_inc(V.sem, V.mark("gdn u"))
            dve.wait_ge(A.sem, A.at("gdn ln"))
            chain(dve, V, nc.vector.scalar_tensor_tensor(GROW[:, 0, :], GROW[:, 0, :], 0.0, GROW[:, 1, :],
                                                         ALU.max, ALU.add))
            chain(dve, V, nc.vector.tensor_scalar(GROW[:, 0, :], GROW[:, 0, :], GEA[:, :], -1.0,
                                                  ALU.mult, ALU.mult))
            for c in range(NC):
                nc.vector.tensor_tensor_scan(GROW[:, 1, c * CH:(c + 1) * CH], ones[0:GH, :],
                                             GROW[:, 0, c * CH:(c + 1) * CH], 0.0, ALU.mult, ALU.add
                                             ).then_inc(V.sem, V.mark("gdn cum") if c == NC - 1 else V.mark())
            for j in range(36):
                if j < 24:
                    dve.wait_ge(A.sem, A.at("gdn xp", j))
                    if j >= 2:
                        dve.wait_ge(A.sem, A.at("gdn silu", j - 2))
                    conv(dve, XP[:, j % 2, :], CV[:, j % 2, :], "gdn_conv_w", GCONV[j], 24, None, ("gdn conv", j))
                if j >= 4 and j % 2 == 0:
                    i = j // 2 - 2
                    tensor, h = GNORM[i]
                    dve.wait_ge(A.sem, A.at("gdn root", i))
                    chain(dve, V, nc.vector.reciprocal(RN[:, i % 2, :], RN[:, i % 2, :]))
                    nc.vector.scalar_tensor_tensor(tensor[:, h, :], tensor[:, h, :], 1.0 if i < 8 else P ** -0.5,
                                                   RN[:, i % 2, :], ALU.mult, ALU.mult
                                                   ).then_inc(V.sem, V.mark("gdn qk", i))
                if j == 16:
                    dve.wait_ge(A.sem, A.at("gdn eg"))
                    nc.vector.tensor_tensor(GBETA[:, 1, :], GBETA[:, 0, :], GROW[:, 2, :], ALU.mult
                                            ).then_inc(V.sem, V.mark())
                    nc.vector.tensor_tensor(GSEL[:, :, :], heads(GROW[:, 2, CH - 1::CH], NC, GH),
                                            per_head(ident[0:GH, 0:GH], NC), ALU.mult
                                            ).then_inc(V.sem, V.mark("gdn sel"))
            dve.wait_ge(T.sem, T.at("gdn cols"))
            nc.vector.tensor_copy(GCOL[:, :, :, :].rearrange("p n c h -> p (n c h)"), MB[1][:, 0:96]
                                  ).then_inc(V.sem, V.mark())
            nc.vector.tensor_copy(GEL[:, :, :].rearrange("p c h -> p (c h)"), MB[1][:, 96:128]
                                  ).then_inc(V.sem, V.mark("gdn cols"))
            dve.wait_ge(V.sem, V.at("gdn cols"))
            for c in range(NC):
                for g in range(2):
                    B, b = GB[g], gt[g]
                    dve.wait_ge(T.sem, T.at("gdn rows", c, g))
                    if c:
                        dve.wait_ge(T.sem, T.at("gdn o", c - 1, g))
                        dve.wait_ge(G.sem, G.at("gdn l", c - 1, g, LEVELS - 1))
                    for n, op in (("AM", ALU.max), ("AT", ALU.min)):
                        for h in range(4):
                            nc.vector.tensor_scalar(b[n][:, h, :], four(B[0])[:, h, :],
                                                    GCOL[:, 0, c, 4 * g + h:4 * g + h + 1], 0.0, ALU.subtract, op
                                                    ).then_inc(V.sem, V.mark("gdn arg" + n, c, g) if h == 3 else V.mark())
                for g in range(2):
                    B, b = GB[g], gt[g]
                    dve.wait_ge(A.sem, A.at("gdn expAM", c, g))
                    dve.wait_ge(T.sem, T.at("gdn kk", c, g))
                    for h in range(4):
                        nc.vector.scalar_tensor_tensor(b["AM"][:, h, :], b["AM"][:, h, :],
                                                       GCOL[:, 1, c, 4 * g + h:4 * g + h + 1], four(B[3])[:, h, :],
                                                       ALU.mult, ALU.mult
                                                       ).then_inc(V.sem, V.mark("gdn am", c, g) if h == 3 else V.mark())
                for g in range(2):
                    B, b = GB[g], gt[g]
                    nc.vector.tensor_tensor(b["KT"][:, :, :], fm(GK, c, g), four(B[2]), ALU.mult).then_inc(V.sem, V.mark())
                    nc.vector.tensor_tensor(b["QD"][:, :, :], fm(GQ, c, g), four(B[1]), ALU.mult
                                            ).then_inc(V.sem, V.mark("gdn kt", c, g))
                for g in range(2):
                    B, b = GB[g], gt[g]
                    dve.wait_ge(T.sem, T.at("gdn y", c, g, 0))
                    for dst, src in ((b["U"], four(B[3])), (b["T"], b["L"][:, :, :])):
                        nc.vector.tensor_tensor(dst[:, :, :], per_head(ident, 4), src, ALU.subtract
                                                ).then_inc(V.sem, V.mark("gdn tu", c, g, 0) if dst is b["T"] else V.mark())
                for g in range(2):
                    B, b = GB[g], gt[g]
                    dve.wait_ge(T.sem, T.at("gdn qk", c, g))
                    dve.wait_ge(A.sem, A.at("gdn expAT", c, g))
                    nc.vector.tensor_tensor(b["AT"][:, :, :], b["AT"][:, :, :], four(B[0]), ALU.mult
                                            ).then_inc(V.sem, V.mark("gdn at", c, g))
                for g in range(2):
                    B, b = GB[g], gt[g]
                    dve.wait_ge(T.sem, T.at("gdn tok", c, g))
                    nc.vector.tensor_tensor(b["KD"][:, :, :], heads(GCOL[:, 2, c, 4 * g:4 * g + 4], 4),
                                            four(B[1]), ALU.mult).then_inc(V.sem, V.mark("gdn kd", c, g))
                    nc.vector.tensor_tensor(b["VB"][:, :, :], heads(GCOL[:, 1, c, 4 * g:4 * g + 4], 4),
                                            four(B[2]), ALU.mult).then_inc(V.sem, V.mark("gdn vb", c, g))
                for l in range(1, LEVELS):
                    for g in range(2):
                        B, b = GB[g], gt[g]
                        dve.wait_ge(T.sem, T.at("gdn uy", c, g, l))
                        ins = nc.vector.tensor_tensor(b["U"][:, :, :], b["U"][:, :, :], four(B[1]), ALU.subtract)
                        if l < LEVELS - 1:
                            ins.then_inc(V.sem, V.mark())
                            ins = nc.vector.tensor_tensor(b["T"][:, :, :], b["T"][:, :, :], four(B[2]), ALU.subtract)
                        ins.then_inc(V.sem, V.mark("gdn tu", c, g, l))
                    if c and 2 <= l < 6:
                        gdn_onorm(dve, c - 1, (l - 2) // 2, l % 2)
                if c:
                    for g in range(2):
                        b = gt[g]
                        dve.wait_ge(T.sem, T.at("gdn ks", c, g))
                        nc.vector.tensor_tensor(b["VB"][:, :, :], b["VB"][:, :, :], four(GB[g][3]), ALU.subtract
                                                ).then_inc(V.sem, V.mark("gdn r", c, g))
                for g in range(2 if c < NC - 1 else 0):
                    dve.wait_ge(T.sem, T.at("gdn su", c, g))
                    state = GS_[:, 4 * g:4 * g + 4, :]
                    if c == 0:
                        nc.vector.tensor_copy(state, four(GB[g][2])).then_inc(V.sem, V.mark("gdn state", c, g))
                    else:
                        chain(dve, V, nc.vector.tensor_tensor(state, state, heads(GEL[:, c, 4 * g:4 * g + 4], 4),
                                                              ALU.mult))
                        nc.vector.tensor_tensor(state, state, four(GB[g][2]), ALU.add
                                                ).then_inc(V.sem, V.mark("gdn state", c, g))
            for g in range(2):
                for half in range(2):
                    gdn_onorm(dve, NC - 1, g, half)
            for h in range(0, GH, 2):
                x_low(dve, "gdn_out", h, GO[:, h, :], GOL[:, h, :], HH[:, h, :])
            residual(dve, "gdn_out", lambda d: COND[:, 40 + d:41 + d])

        def gdn_onorm(dve, c, g, half):
            dve.wait_ge(A.sem, A.at("gdn oroot", c, g))
            r = RN[:, g, 2 * P * half:2 * P * (half + 1)]
            chain(dve, V, nc.vector.reciprocal(r, r))
            if half:
                nc.vector.scalar_tensor_tensor(fm(GO, c, g), fm(GO, c, g), vec("gdn_onorm_g"),
                                               RN[:, g, :].rearrange("p (h t) -> p h t", h=4), ALU.mult, ALU.mult
                                               ).then_inc(V.sem, V.mark("gdn on", c, g))

        def gdn_gate(pool, c, g):
            pool.wait_ge(V.sem, V.at("gdn on", c, g))
            nc.gpsimd.tensor_tensor(fm(GO, c, g), fm(GO, c, g), fm(GZ, c, g), ALU.mult
                                    ).then_inc(G.sem, G.mark("gdn y", c, g))

        def pool_gdn(pool):
            pool_in(pool, "gdn_in")
            mix_split(pool, "gdn_out", 0, RING)
            for c in range(NC):
                for l in range(LEVELS):
                    for g in range(2):
                        b = gt[g]
                        if l == 0:
                            pool.wait_ge(V.sem, V.at("gdn am", c, g))
                        else:
                            pool.wait_ge(T.sem, T.at("gdn y", c, g, l - 1))
                        if l == 1:
                            pool.wait_ge(V.sem, V.at("gdn tu", c, g, 0))
                        nc.gpsimd.tensor_tensor(b["L"][:, :, :], b["AM"][:, :, :],
                                                per_head(cst("levels", at=l * P), 4), ALU.mult
                                                ).then_inc(G.sem, G.mark("gdn l", c, g, l))
                    if l == 1:
                        for g in range(2):
                            b = gt[g]
                            pool.wait_ge(V.sem, V.at("gdn at", c, g))
                            nc.gpsimd.tensor_tensor(b["AT"][:, :, :], b["AT"][:, :, :], per_head(cst("upper"), 4),
                                                    ALU.mult).then_inc(G.sem, G.mark("gdn causal", c, g))
                    if c and l in (4, 6):
                        gdn_gate(pool, c - 1, l // 2 - 2)
            for g in range(2):
                gdn_gate(pool, NC - 1, g)
            for h in range(1, DT, 2):
                x_low(pool, "gdn_out", h, GO[:, h, :], GOL[:, h, :], HH[:, h, :])
            mix_split(pool, "gdn_out", RING)

        GCONV = list(range(8, 16)) + list(range(0, 8)) + list(range(16, 24))
        FREED["gdn_in"] = lambda j: (A.sem, A.at("beta") if j == 0 else
                                     A.at("gdn xp", j - 1) if j <= 24 else A.at("gdn z", j - 25))

        hy = ExitStack()
        YX, YXL = twins("YX", [P, 12, S], hy)
        YZ, YZH = twins("YZ", [P, 8, S], hy)
        MQ = sb("MQ", [P, MH, S], stack=hy)
        MK = sb("MK", [P, MH, S], stack=hy)
        MV, MVL = twins("MV", [P, 2 * MH, S], hy)
        MO = sb("MO", [P, 2 * MH, S], stack=hy)
        ROWS = sb("ROWS", [P, 3, S], stack=hy)
        YCOL = sb("YCOL", [P, 3, NC, SH], stack=hy)
        YSEL = sb("YSEL", [SH, NC, SH], stack=hy)
        YEL = sb("YEL", [P, NC, SH], stack=hy)
        YEA = sb("YEA", [SH, 1], stack=hy)
        MR = slice(32, 32 + MH)
        MIN = sb("MIN", [P, NC + 1], stack=hy)[MR, :]
        NCM = sb("NCM", [P, NC], stack=hy)[MR, :]
        MAC = sb("MAC", [P, NC], stack=hy)[MR, :]
        MCOL = sb("MCOL", [P, 2, NC, MH], stack=hy)
        MSEL = sb("MSEL", [P, NC, MH], stack=hy)[MR, :, :]
        MEL = sb("MEL", [P, NC, MH], stack=hy)
        HF = H[:, :, :].rearrange("p a s -> p (a s)")
        YM = [HF[:, 512 * g:512 * g + 512] for g in range(2)]
        YCD = [HF[:, 1024 + 512 * g:1536 + 512 * g] for g in range(2)]
        YXD = HF[:, 2048:3072]
        YXE = HF[:, 3072:4096]
        HHQ = HHF[:, :, :].rearrange("p a s -> p (a s)")
        YBT = HHQ[:, 0:2 * P].rearrange("p (g n) -> p g n", g=2)
        MCS = HHQ[:, 512:512 + 12 * P].rearrange("p (h v) -> p h v", h=MH)
        YST = HHQ[:, 512:512 + SH * SP_]
        YCB = HHQ[:, 3584:3584 + 2 * P].rearrange("p (g t) -> p g t", g=2)
        MVA = HHQ[:, 2048:2048 + 12 * P].rearrange("p (h v) -> p h v", h=MH)
        hy.close()
        MS, MQH, MKW, MEM = YM[0], YCD[0], YM[1], YCD[1]

        def row(i):
            return ROWS[:, i, :] if i < 3 else (SQ if i < 5 else RN)[:, (i - 3) % 2, :]

        def yrow(i):
            return row(i)[0:SH, :]

        def mrow(i):
            return row(i)[MR, :]

        def hy_y(k):
            return (YX[:, k, :], YXL[:, k, :], HH[:, k, :]) if k < 8 else \
                (MV[:, k - 8, :], MVL[:, k - 8, :], YZH[:, k - 8, :])

        def h4(ap):
            return ap.rearrange("p (h t) -> p h t", h=4)

        def ck(c):
            return slice(c * CH, (c + 1) * CH)

        def pe_hy(pe):
            pe_tile(pe, "hy_in", 0, h_tile, x_wait(pe, "hy_in"),
                    outs=[(MB[1][0:SH, :], 0, 16), (MB[2][0:MR.stop, :], 16, 16 + MR.stop),
                          (MB[3][0:MR.stop, :], 16 + MR.stop, 16 + 2 * MR.stop)])
            for j in range(1, 45):
                pe_tile(pe, "hy_in", j, h_tile)
            pe.wait_ge(V.sem, V.at("hy rows"))
            for n, r in enumerate((yrow(1), yrow(0), yrow(4))):
                for c in range(NC):
                    nc.tensor.matmul(MB[1][:, (n * NC + c) * SH:(n * NC + c + 1) * SH],
                                     r[:, ck(c)], ident[0:SH, 0:SH], start=True, stop=True)
            nc.tensor.matmul(MB[1][:, 192:256], ones[0:SH, :], YSEL[:, :, :].rearrange("p c h -> p (c h)"),
                             start=True, stop=True)
            for n, r in enumerate((mrow(3), mrow(5))):
                for c in range(NC):
                    nc.tensor.matmul(MB[2][:, (n * NC + c) * MH:(n * NC + c + 1) * MH],
                                     r[:, ck(c)], ident[MR, MR], start=True, stop=True)
            nc.tensor.matmul(MB[2][:, 32:48], ones[MR, :], MSEL[:, :, :].rearrange("p c h -> p (c h)"),
                             start=True, stop=True).then_inc(T.sem, T.mark("hy cols"))
            pe.wait_ge(V.sem, V.at("hy cols"))
            pe.wait_ge(A.sem, A.at("hy o", 7))
            ssd_rows(pe, 0, 0)
            for c in range(NC):
                if c:
                    pe.wait_ge(V.sem, V.at("ssd y", c - 1, 3))
                    pe.wait_ge(V.sem, V.at("ssd state", c - 1))
                for d in range(8):
                    nc.tensor.transpose(LB[d // 4][:, d % 4 * P:(d % 4 + 1) * P], YX[:, d, ck(c)], ident)
                for g in range(2):
                    nc.tensor.transpose(LB[2][:, g * P:(g + 1) * P], YX[:, 8 + g, ck(c)], ident)
                for g in range(2):
                    last = nc.tensor.matmul(LB[3][:, g * P:(g + 1) * P], YX[:, 8 + g, ck(c)],
                                            YX[:, 10 + g, ck(c)], start=True, stop=True)
                last.then_inc(T.sem, T.mark("ssd tok", c))
                for q in range(1, 4):
                    ssd_rows(pe, c, q)
                    ssd_y(pe, c, q - 1)
                if c < NC - 1:
                    for g in range(2):
                        last = nc.tensor.matmul(LB[g][:, :], YBT[:, g, :], YXE[:, g * 512:(g + 1) * 512],
                                                start=True, stop=True)
                    last.then_inc(T.sem, T.mark("ssd su", c))
                ssd_y(pe, c, 3)
                if c < NC - 1:
                    ssd_rows(pe, c + 1, 0)
            pe.wait_ge(V.sem, V.at("ssd y", NC - 1, 3))
            for c in range(NC):
                if c:
                    pe.wait_ge(V.sem, V.at("ml state", c - 1, 3))
                for n, r in ((0, row(4)), (1, row(6)), (2, row(2))):
                    for h in range(4):
                        nc.tensor.matmul(LB[n][:, h * P:(h + 1) * P],
                                         ident[:, 32 + h:33 + h].to_broadcast([P, P]), r[:, ck(c)],
                                         start=True, stop=True)
                for h in range(4):
                    last = nc.tensor.matmul(LB[3][:, h * P:(h + 1) * P], MK[:, h, ck(c)], MQ[:, h, ck(c)],
                                            start=True, stop=True)
                last.then_inc(T.sem, T.mark("ml rows", c))
                if c:
                    pe.wait_ge(V.sem, V.at("ml h", c - 1))
                for h in range(4):
                    nc.tensor.transpose(MB[0][:, h * P:(h + 1) * P], MK[:, h, ck(c)], ident)
                for d in range(8):
                    last = nc.tensor.transpose(MB[1 + d // 4][:, d % 4 * P:(d % 4 + 1) * P], MV[:, d, ck(c)], ident)
                last.then_inc(T.sem, T.mark("ml tok", c))
                pe.wait_ge(V.sem, V.at("ml s", c))
                pe.wait_ge(V.sem, V.at("ml kw", c))
                pe.wait_ge(A.sem, A.at("ml va", c))
                pe.wait_ge(A.sem, A.at("ml em", c))
                for h in range(4 if c < NC - 1 else 0):
                    nc.tensor.matmul(LB[h][:, 0:3 * P], MKW[:, h * P:(h + 1) * P],
                                     MVA[:, h, :], start=True, stop=True).then_inc(T.sem, T.mark("ml su", c, h))
                for n, bank in enumerate((MB[0], MB[1], MB[2])):
                    for h in range(4):
                        o = bank[:, h * P:(h + 1) * P]
                        last = nc.tensor.matmul(o, MVA[:, h, n * P:(n + 1) * P], MS[:, h * P:(h + 1) * P],
                                                start=True, stop=c == 0)
                        if c:
                            last = nc.tensor.matmul(o, MCS[:, h, n * P:(n + 1) * P], MQH[:, h * P:(h + 1) * P],
                                                    start=False, stop=True)
                last.then_inc(T.sem, T.mark("ml out", c))
            pe.wait_ge(V.sem, V.at("ml h", NC - 1))
            for j in range(6):
                n = 4 if j < 2 else 2
                for i in range(n):
                    m = hy_norm_at(j) + i
                    pe.wait_ge(A.sem, A.at("hy sq", m))
                    if i == 0 and j >= 2:
                        pe.wait_ge(A.sem, A.at("hy root", j - 2))
                    nc.tensor.matmul(MB[j % 2][:, :], ones, SQ[:, m % 2, :], start=i == 0, stop=i == n - 1
                                     ).then_inc(T.sem, T.mark("hy sum", m))
            for j in range(8):
                pe_tile(pe, "hy_out", j, lambda k: (hy_y(k)[2], hy_y(k)[1]),
                        x_wait(pe, "hy_out") if j == 0 else None)

        def hy_norm_at(j):
            return 4 * j if j < 2 else 8 + 2 * (j - 2)

        def ssd_rows(pe, c, q):
            b0, b1 = MB[2 * (q % 2)], MB[2 * (q % 2) + 1]
            if q >= 2:
                pe.wait_ge(V.sem, V.at("ssd cd", c, q - 2))
            elif c:
                pe.wait_ge(V.sem, V.at("ssd cd", c - 1, q + 2))
            for bank, r in ((b0, row(1)), (b1, row(2))):
                for h in range(4):
                    last = nc.tensor.matmul(bank[:, h * P:(h + 1) * P],
                                            ident[:, 4 * q + h:4 * q + h + 1].to_broadcast([P, P]),
                                            r[:, ck(c)], start=True, stop=True)
            last.then_inc(T.sem, T.mark("ssd rows", c, q))

        def ssd_y(pe, c, q):
            bank = (LB[2], LB[3])[q % 2]
            pe.wait_ge(V.sem, V.at("ssd m", c, q))
            pe.wait_ge(V.sem, V.at("ssd cd", c, q))
            pe.wait_ge(V.sem, V.at("ssd xd", c))
            pe.wait_ge(A.sem, A.at("ssd bt", c))
            if q >= 2:
                pe.wait_ge(V.sem, V.at("ssd y", c, q - 2))
            for h in range(4):
                head = 4 * q + h
                o = bank[64 * (h % 2):64 * (h % 2) + 64, 256 + h // 2 * P:256 + (h // 2 + 1) * P]
                last = nc.tensor.matmul(o, YXD[:, head * 64:head * 64 + 64], YM[q % 2][:, h * P:(h + 1) * P],
                                        start=True, stop=c == 0)
                if c:
                    last = nc.tensor.matmul(o, YST[:, head * 64:head * 64 + 64], YCD[q % 2][:, h * P:(h + 1) * P],
                                            start=False, stop=True)
            last.then_inc(T.sem, T.mark("ssd y", c, q))

        def act_hy(act):
            nc.scalar.activation(YEA[:, :], vec("hy_a_log", rows=SH), ACT.Exp).then_inc(A.sem, A.mark("ssd ea"))
            act.wait_ge(V.sem, V.at("hy u"))
            for t, n, r in ((yrow, "ssd", slice(0, SH)), (mrow, "ml", MR)):
                chain(act, A, nc.scalar.activation(t(1), t(0), ACT.Abs))
                chain(act, A, nc.scalar.activation(t(1), t(1), ACT.Exp, scale=-1.0))
                nc.scalar.activation(t(1), t(1), ACT.Ln, bias=one[r, :]
                                     ).then_inc(A.sem, A.mark(n + " ln"))

            def copy_in(j):
                bank = arrived(act, "hy_in", j + 1)
                if j >= 2:
                    act.wait_ge(V.sem, V.at("hy conv", j - 2))
                nc.scalar.activation(XP[:, j % 2, 3:], bank[:, :], ACT.Copy).then_inc(A.sem, A.mark("hy xp", j))

            def silu(j):
                act.wait_ge(V.sem, V.at("hy conv", j))
                nc.scalar.activation(YX[:, j, :], CV[:, j % 2, :], ACT.Silu).then_inc(A.sem, A.mark("hy silu", j))

            copy_in(0)
            for j in range(1, 12):
                copy_in(j)
                silu(j - 1)
            silu(11)
            for j in range(8):
                bank = arrived(act, "hy_in", 13 + j)
                nc.scalar.activation(YZ[:, j, :], bank[:, :], ACT.Silu).then_inc(A.sem, A.mark("hy z", j))
            act.wait_ge(V.sem, V.at("ssd cum"))
            nc.scalar.activation(yrow(2)[:, :], yrow(1)[:, :], ACT.Exp).then_inc(A.sem, A.mark("ssd eg"))
            for c in range(NC):
                nc.scalar.activation(yrow(3)[:, ck(c)], yrow(1)[:, ck(c)], ACT.Exp,
                                     bias=yrow(1)[:, (c + 1) * CH - 1:(c + 1) * CH], scale=-1.0
                                     ).then_inc(A.sem, A.mark("ssd ed") if c == NC - 1 else A.mark())
            act.wait_ge(V.sem, V.at("ml max"))
            for c in range(NC):
                nc.scalar.activation(mrow(5)[:, ck(c)], mrow(3)[:, ck(c)], ACT.Exp, bias=NCM[:, c:c + 1]
                                     ).then_inc(A.sem, A.mark())
                nc.scalar.activation(mrow(6)[:, ck(c)], mrow(4)[:, ck(c)], ACT.Exp, bias=MIN[:, c:c + 1],
                                     scale=-1.0).then_inc(A.sem, A.mark())
                nc.scalar.activation(MAC[:, c:c + 1], NCM[:, c:c + 1], ACT.Exp, bias=MIN[:, c:c + 1]
                                     ).then_inc(A.sem, A.mark())
            nc.scalar.activation(mrow(2)[:, :], mrow(0)[:, :], ACT.Exp, scale=-1.0).then_inc(A.sem, A.mark("ml exps"))
            for j in range(4):
                bank = arrived(act, "hy_in", 21 + j)
                nc.scalar.activation(MQ[:, j, :], bank[:, :], ACT.Copy, scale=P ** -0.5).then_inc(A.sem, A.mark("hy q", j))
            for j in range(4):
                bank = arrived(act, "hy_in", 25 + j)
                nc.scalar.activation(MK[:, j, :], bank[:, :], ACT.Copy).then_inc(A.sem, A.mark("hy k", j))
            for j in range(8):
                bank = arrived(act, "hy_in", 29 + j)
                nc.scalar.activation(MV[:, j, :], bank[:, :], ACT.Copy).then_inc(A.sem, A.mark("hy v", j))
            for j in range(8):
                bank = arrived(act, "hy_in", 37 + j)
                nc.scalar.activation(MO[:, j, :], bank[:, :], ACT.Sigmoid).then_inc(A.sem, A.mark("hy o", j))
            for c in range(NC):
                act.wait_ge(T.sem, T.at("ssd tok", c))
                if c:
                    act.wait_ge(T.sem, T.at("ssd su", c - 1))
                nc.scalar.activation(YBT[:, :, :].rearrange("p g n -> p (g n)"), LB[2][:, 0:256], ACT.Copy
                                     ).then_inc(A.sem, A.mark("ssd bt", c))
                for q in range(4):
                    act.wait_ge(V.sem, V.at("ssd diff", c, q))
                    nc.scalar.activation(YM[q % 2], YM[q % 2], ACT.Exp).then_inc(A.sem, A.mark("ssd exp", c, q))
            for c in range(NC):
                act.wait_ge(T.sem, T.at("ml rows", c))
                act.wait_ge(G.sem, G.at("ml mask", c))
                nc.scalar.activation(MS, MS, ACT.Exp).then_inc(A.sem, A.mark("ml exp", c))
                if c:
                    act.wait_ge(V.sem, V.at("ml h", c - 1))
                else:
                    act.wait_ge(T.sem, T.at("ssd y", NC - 1, 3))
                nc.scalar.activation(MEM, LB[2][:, :], ACT.Copy).then_inc(A.sem, A.mark("ml em", c))
                act.wait_ge(T.sem, T.at("ml tok", c))
                if c:
                    act.wait_ge(T.sem, T.at("ml out", c - 1))
                for n in range(2):
                    nc.scalar.activation(MVA[:, 2 * n:2 * n + 2, 0:2 * P],
                                         MB[1 + n][:, :].rearrange("p (h v) -> p h v", h=2), ACT.Copy
                                         ).then_inc(A.sem, A.mark("ml va", c) if n else A.mark())
            act.wait_ge(V.sem, V.at("ml h", NC - 1))
            act.wait_ge(V.sem, V.at("ssd gated"))

            def y_highs(j):
                for m in range(hy_norm_at(j), hy_norm_at(j) + (4 if j < 2 else 2)):
                    act.wait_ge(V.sem, V.at("hy y", m))
                    x_high(act, hy_y(m)[0], hy_y(m)[2])

            for j in range(6):
                for i in range(4 if j < 2 else 2):
                    m = hy_norm_at(j) + i
                    if m >= 2:
                        act.wait_ge(T.sem, T.at("hy sum", m - 2))
                    nc.scalar.activation(SQ[:, m % 2, :], YX[:, m, :] if m < 8 else MV[:, m - 8, :], ACT.Square
                                         ).then_inc(A.sem, A.mark("hy sq", m))
                act.wait_ge(T.sem, T.at("hy sum", m))
                if j >= 2:
                    act.wait_ge(V.sem, V.at("hy y", hy_norm_at(j - 1) - 1))
                nc.scalar.activation(RN[:, j % 2, :], MB[j % 2][:, :], ACT.Sqrt, bias=eps,
                                     scale=1.0 / 512 if j < 2 else 1.0 / 256).then_inc(A.sem, A.mark("hy root", j))
                if j:
                    y_highs(j - 1)
            y_highs(5)

        def dve_hy(dve):
            for t in (ROWS, SQ, RN):
                nc.vector.memset(t[:, :, :], 0.0).then_inc(V.sem, V.mark("hy zero") if t is RN else V.mark())
            dve.wait_ge(V.sem, V.at("hy zero"))
            dve.wait_ge(tile_done, TILE0["hy_in"] + 1)
            nc.vector.tensor_scalar(yrow(0)[:, :], MB[1][0:SH, :], vec("hy_dt_bias", rows=SH), None, ALU.add
                                    ).then_inc(V.sem, V.mark())
            nc.vector.tensor_scalar(mrow(6)[:, :], MB[2][MR, :], vec("hy_igate_bias")[MR, :], None, ALU.add
                                    ).then_inc(V.sem, V.mark())
            nc.vector.tensor_scalar(mrow(0)[:, :], MB[3][MR, :], vec("hy_fgate_bias")[MR, :], -1.0,
                                    ALU.add, ALU.mult).then_inc(V.sem, V.mark("hy u"))
            dve.wait_ge(A.sem, A.at("ssd ln"))
            chain(dve, V, nc.vector.scalar_tensor_tensor(yrow(0)[:, :], yrow(0)[:, :], 0.0, yrow(1)[:, :],
                                                         ALU.max, ALU.add))
            chain(dve, V, nc.vector.tensor_scalar(yrow(2)[:, :], yrow(0)[:, :], YEA[:, :], -1.0,
                                                  ALU.mult, ALU.mult))
            for c in range(NC):
                nc.vector.tensor_tensor_scan(yrow(1)[:, ck(c)], ones[0:SH, :], yrow(2)[:, ck(c)], 0.0,
                                             ALU.mult, ALU.add).then_inc(V.sem, V.mark("ssd cum") if c == NC - 1 else V.mark())
            dve.wait_ge(A.sem, A.at("ml ln"))
            chain(dve, V, nc.vector.scalar_tensor_tensor(mrow(1)[:, :], mrow(0)[:, :], 0.0, mrow(1)[:, :],
                                                         ALU.max, ALU.add))
            chain(dve, V, nc.vector.tensor_scalar(mrow(1)[:, :], mrow(1)[:, :], -1.0, None, ALU.mult))
            for c in range(NC):
                chain(dve, V, nc.vector.tensor_tensor_scan(mrow(2)[:, ck(c)], ones[MR, :], mrow(1)[:, ck(c)],
                                                           0.0, ALU.mult, ALU.add))
            chain(dve, V, nc.vector.tensor_tensor(mrow(3)[:, :], mrow(6)[:, :], mrow(2)[:, :], ALU.subtract))
            chain(dve, V, nc.vector.memset(MIN[:, 0:1], 0.0))
            for c in range(NC):
                end = slice((c + 1) * CH - 1, (c + 1) * CH)
                chain(dve, V, nc.vector.tensor_tensor_scan(mrow(4)[:, ck(c)], ones[MR, :], mrow(3)[:, ck(c)],
                                                           MIN[:, c:c + 1], ALU.mult, ALU.max))
                chain(dve, V, nc.vector.tensor_tensor(MIN[:, c + 1:c + 2], mrow(4)[:, end], mrow(2)[:, end], ALU.add))
                chain(dve, V, nc.vector.tensor_scalar(NCM[:, c:c + 1], mrow(4)[:, end], -1.0, None, ALU.mult))
            chain(dve, V, nc.vector.tensor_tensor(mrow(0), mrow(4), mrow(2), ALU.add))
            nc.vector.tensor_scalar(mrow(0), mrow(0), -88.0, None, ALU.max).then_inc(V.sem, V.mark("ml max"))
            for j in range(12):
                dve.wait_ge(A.sem, A.at("hy xp", j))
                if j >= 2:
                    dve.wait_ge(A.sem, A.at("hy silu", j - 2))
                conv(dve, XP[:, j % 2, :], CV[:, j % 2, :], "hy_conv_w", j, 12, vec("hy_conv_b", j), ("hy conv", j))
            dve.wait_ge(A.sem, A.at("ssd ed"))
            nc.vector.tensor_tensor(yrow(4)[:, :], yrow(3)[:, :], yrow(0)[:, :], ALU.mult).then_inc(V.sem, V.mark())
            nc.vector.tensor_tensor(YSEL[:, :, :], heads(yrow(2)[:, CH - 1::CH], NC, SH),
                                    per_head(ident[0:SH, 0:SH], NC), ALU.mult).then_inc(V.sem, V.mark())
            dve.wait_ge(A.sem, A.at("ml exps"))
            nc.vector.tensor_tensor(MSEL[:, :, :], heads(MAC[:, :], NC, MH), per_head(ident[MR, MR], NC),
                                    ALU.mult).then_inc(V.sem, V.mark("hy rows"))
            dve.wait_ge(T.sem, T.at("hy cols"))
            nc.vector.memset(MVA[:, :, 2 * P:3 * P], 1.0).then_inc(V.sem, V.mark())
            nc.vector.tensor_copy(YCOL[:, :, :, :].rearrange("p n c h -> p (n c h)"), MB[1][:, 0:192]).then_inc(V.sem, V.mark())
            nc.vector.tensor_copy(YEL[:, :, :].rearrange("p c h -> p (c h)"), MB[1][:, 192:256]).then_inc(V.sem, V.mark())
            nc.vector.tensor_copy(MCOL[:, :, :, :].rearrange("p n c h -> p (n c h)"), MB[2][:, 0:32]).then_inc(V.sem, V.mark())
            nc.vector.tensor_copy(MEL[:, :, :].rearrange("p c h -> p (c h)"), MB[2][:, 32:48]).then_inc(V.sem, V.mark("hy cols"))
            dve.wait_ge(V.sem, V.at("hy cols"))

            def ssd_skip(c, q):
                dve.wait_ge(T.sem, T.at("ssd y", c, q))
                for i in range(2):
                    d = 2 * q + i
                    nc.vector.scalar_tensor_tensor(YX[:, d, ck(c)], YX[:, d, ck(c)], vec("hy_d_skip", d),
                                                   (LB[2], LB[3])[q % 2][:, 256 + i * P:256 + (i + 1) * P],
                                                   ALU.mult, ALU.add).then_inc(V.sem, V.mark("ssd y", c, q) if i else V.mark())

            def decays(c, q):
                b0, b1 = MB[2 * (q % 2)], MB[2 * (q % 2) + 1]
                dve.wait_ge(T.sem, T.at("ssd rows", c, q))
                if q >= 2:
                    dve.wait_ge(T.sem, T.at("ssd y", c, q - 2))
                elif c:
                    dve.wait_ge(T.sem, T.at("ssd y", c - 1, q + 2))
                for h in range(4):
                    nc.vector.tensor_scalar(h4(YM[q % 2])[:, h, :], four(b0)[:, h, :],
                                            YCOL[:, 0, c, 4 * q + h:4 * q + h + 1], 0.0, ALU.subtract, ALU.min
                                            ).then_inc(V.sem, V.mark("ssd diff", c, q) if h == 3 else V.mark())
                nc.vector.tensor_tensor(h4(YCD[q % 2]), per_head(YX[:, 10 + q // 2, ck(c)], 4), four(b1),
                                        ALU.mult).then_inc(V.sem, V.mark("ssd cd", c, q))

            for c in range(NC):
                decays(c, 0)
                dve.wait_ge(T.sem, T.at("ssd tok", c))
                nc.vector.tensor_tensor(YCB, per_head(cst("upper"), 2), LB[3][:, 0:2 * P].rearrange("p (g t) -> p g t", g=2),
                                        ALU.mult).then_inc(V.sem, V.mark("ssd cb", c))
                for n, dst in ((1, YXD), (2, YXE)):
                    for b in range(2):
                        nc.vector.tensor_tensor(dst[:, 512 * b:512 * b + 512].rearrange("p (h w) -> p h w", w=SP_),
                                                heads(YCOL[:, n, c, 8 * b:8 * b + 8], 8, SP_),
                                                LB[b][:, :].rearrange("p (h w) -> p h w", w=SP_), ALU.mult
                                                ).then_inc(V.sem, V.mark("ssd xd", c) if (n, b) == (2, 1) else V.mark())
                for q in range(1, 4):
                    ssd_m(dve, c, q - 1)
                    decays(c, q)
                    ssd_skip(c, q - 1)
                ssd_m(dve, c, 3)
                ssd_skip(c, 3)
                if c < NC - 1:
                    dve.wait_ge(T.sem, T.at("ssd su", c))
                    if c:
                        chain(dve, V, nc.vector.tensor_tensor(
                            YST.rearrange("p (h w) -> p h w", w=SP_),
                            YST.rearrange("p (h w) -> p h w", w=SP_), heads(YEL[:, c, :], SH, SP_), ALU.mult))
                    for g in range(2):
                        dst = YST[:, 512 * g:512 * g + 512]
                        ins = nc.vector.tensor_tensor(dst, dst, LB[g][:, :], ALU.add) if c else \
                            nc.vector.tensor_copy(dst, LB[g][:, :])
                        ins.then_inc(V.sem, V.mark("ssd state", c) if g else V.mark())
            dve.wait_ge(V.sem, V.at("ssd y", NC - 1, 3))
            for d in range(8):
                nc.vector.tensor_tensor(YX[:, d, :], YX[:, d, :], YZ[:, d, :], ALU.mult
                                        ).then_inc(V.sem, V.mark("ssd gated") if d == 7 else V.mark())
            for c in range(NC):
                dve.wait_ge(T.sem, T.at("ml rows", c))
                if c:
                    dve.wait_ge(T.sem, T.at("ml out", c - 1))
                nc.vector.tensor_tensor(h4(MS), heads(MCOL[:, 0, c, :], 4), four(LB[0]), ALU.subtract
                                        ).then_inc(V.sem, V.mark("ml diff", c))
                nc.vector.tensor_tensor(h4(MQH), MQ[:, :, ck(c)], four(LB[1]), ALU.mult).then_inc(V.sem, V.mark())
                dve.wait_ge(A.sem, A.at("ml exp", c))
                nc.vector.tensor_tensor(MS, MS, LB[3][:, :], ALU.mult).then_inc(V.sem, V.mark("ml s", c))
                dve.wait_ge(T.sem, T.at("ml tok", c))
                if c:
                    dve.wait_ge(T.sem, T.at("ml su", c - 1, 3))
                nc.vector.tensor_tensor(h4(MKW), heads(MCOL[:, 1, c, :], 4), four(MB[0]), ALU.mult
                                        ).then_inc(V.sem, V.mark("ml kw", c))
                dve.wait_ge(T.sem, T.at("ml out", c))
                for h in range(4 if c < NC - 1 else 0):
                    dve.wait_ge(T.sem, T.at("ml su", c, h))
                    src = LB[h][:, 0:3 * P]
                    ins = nc.vector.scalar_tensor_tensor(MCS[:, h, :], MCS[:, h, :], MEL[:, c, h:h + 1], src,
                                                         ALU.mult, ALU.add) if c else \
                        nc.vector.tensor_copy(MCS[:, h, :], src)
                    ins.then_inc(V.sem, V.mark("ml state", c, h))
                dve.wait_ge(A.sem, A.at("ml em", c))
                chain(dve, V, nc.vector.scalar_tensor_tensor(MEM, MB[2][:, :], -1.0, MEM, ALU.mult, ALU.max))
                chain(dve, V, nc.vector.tensor_tensor(MEM, MEM, MB[2][:, :], ALU.max))
                chain(dve, V, nc.vector.reciprocal(MEM, MEM))
                for n in range(2):
                    nc.vector.tensor_tensor(MV[:, n::2, ck(c)], h4(MEM), four(MB[n]), ALU.mult
                                            ).then_inc(V.sem, V.mark("ml h", c) if n else V.mark())

            def y_lows(j):
                for m in range(hy_norm_at(j), hy_norm_at(j) + (4 if j < 2 else 2), 2):
                    x_low(dve, "hy_out", m, *hy_y(m))

            for j in range(6):
                dve.wait_ge(A.sem, A.at("hy root", j))
                chain(dve, V, nc.vector.reciprocal(RN[:, j % 2, :], RN[:, j % 2, :]))
                for i in range(4 if j < 2 else 2):
                    m = hy_norm_at(j) + i
                    y = YX[:, m, :] if m < 8 else MV[:, m - 8, :]
                    g = vec("hy_ssd_norm", m) if m < 8 else vec("hy_mlstm_norm", m - 8)
                    ins = nc.vector.scalar_tensor_tensor(y, y, g, RN[:, j % 2, :], ALU.mult, ALU.mult)
                    if m < 8:
                        ins.then_inc(V.sem, V.mark("hy y", m))
                    else:
                        chain(dve, V, ins)
                        nc.vector.tensor_tensor(y, y, MO[:, m - 8, :], ALU.mult).then_inc(V.sem, V.mark("hy y", m))
                if j:
                    y_lows(j - 1)
            y_lows(5)
            residual(dve, "hy_out", lambda d: 1.0)

        def ssd_m(dve, c, q):
            dve.wait_ge(A.sem, A.at("ssd exp", c, q))
            dve.wait_ge(V.sem, V.at("ssd cb", c))
            nc.vector.tensor_tensor(h4(YM[q % 2]), h4(YM[q % 2]), per_head(YCB[:, q // 2, :], 4), ALU.mult).then_inc(V.sem, V.mark("ssd m", c, q))

        def pool_hy(pool):
            pool_in(pool, "hy_in")
            mix_split(pool, "hy_out", 0, RING)
            for c in range(NC):
                pool.wait_ge(V.sem, V.at("ml diff", c))
                nc.gpsimd.tensor_tensor(h4(MS), h4(MS), per_head(cst("keep_upper"), 4), ALU.add
                                        ).then_inc(G.sem, G.mark("ml mask", c))
            for m in range(1, 2 * DT, 2):
                x_low(pool, "hy_out", m, *hy_y(m))
            mix_split(pool, "hy_out", RING)

        def hy_freed(j):
            if j == 0:
                return V.sem, V.at("hy u")
            for first, count, name in ((1, 12, "hy xp"), (13, 8, "hy z"), (21, 4, "hy q"), (25, 4, "hy k"),
                                       (29, 8, "hy v"), (37, 8, "hy o")):
                if j < first + count:
                    return A.sem, A.at(name, j - first)

        FREED["hy_in"] = hy_freed


        sa = ExitStack()
        AKI = sb("AKI", [P, 2, S], stack=sa)
        AQI = sb("AQI", [P, IH // 2, S], stack=sa)
        AVW = sb("AVW", [P, S], stack=sa)
        AVT = sb("AVT", [P, NC, AD + IH], stack=sa)
        AK = sb("AK", [P, 2, S], stack=sa)
        AQ = sb("AQ", [P, AH // 2, S], stack=sa)
        POS = sb("POS", [P, S], I32, stack=sa)
        ANG = sb("ANG", [P, 3, S], stack=sa)
        COS = sb("COS", [P, S], stack=sa)
        SIN = sb("SIN", [P, S], stack=sa)
        RAW = sb("RAW", [P, 3, S], stack=sa)
        RTC = sb("RTC", [P, 2, S], stack=sa)
        RTS = sb("RTS", [P, 2, S], stack=sa)
        REL = sb("REL", [P, 4, S], stack=sa)
        ASC = sb("ASC", [P, S], stack=sa)
        AWK = sb("AWK", [P, S], stack=sa)
        AM8 = sb("AM8", [P, 8], stack=sa)
        AMB = sb("AMB", [P, NC, S], stack=sa)
        APR = sb("APR", [P, 3, S], stack=sa)
        APT = sb("APT", [P, 2, S], stack=sa)
        AMX = sb("AMX", [P, 64], stack=sa)
        ANM = sb("ANM", [P, 64], stack=sa)
        ASM = sb("ASM", [P, 64], stack=sa)
        ARS = sb("ARS", [P, 64], stack=sa)
        AOT = sb("AOT", [P, 2, S], stack=sa)
        ARQ = sb("ARQ", [P, 3, 64], stack=sa)
        sa.close()
        ROT = AOT
        KR = APT[:, 1, :]
        RELS = [REL[:, i, :] for i in range(4)] + [APR[:, i, :] for i in range(3)] + [APT[:, 0, :]]
        AO = H
        ROPE = [(0, AKI)] + [(1 + i, AQI[:, i, :]) for i in range(4)] + [(6, AK)] \
            + [(7 + i, AQ[:, i, :]) for i in range(8)]
        UNITS = [(qt, h) for qt in range(NC) for h in range(AH)]

        LOGITS_AFTER = {6: 1, 8: 2, 12: 3}

        def pe_sa(pe):
            def rot(i):
                pe.wait_ge(A.sem, A.at("sa raw", i))
                if i >= 6:
                    pe.wait_ge(A.sem, A.at("sa rotated", i - 1))
                elif 2 <= i < 5:
                    pe.wait_ge(V.sem, V.at("sa rs", i - 2))
                nc.tensor.matmul((MB[i % 2] if i < 5 else MB[2])[:, :], rotate, RAW[:, i % 3, :], start=True, stop=True
                                 ).then_inc(T.sem, T.mark("sa rot", i))

            def total(i):
                pe.wait_ge(A.sem, A.at("sa sq", i))
                if i == 5:
                    last = nc.tensor.matmul(MB[3][:, :], half_ones, SQ[:, i % 2, :], start=True, stop=True)
                else:
                    pe.wait_ge(A.sem, A.at("sa root"))
                    for c in range(NC):
                        at = c * AH + 2 * (i - 6)
                        last = nc.tensor.matmul(MB[3][:, at:at + 2], SQ[:, i % 2, ck(c)], half_ones[:, 0::AD],
                                                start=True, stop=True)
                last.then_inc(T.sem, T.mark("sa sum", i))

            def index_logits(qt):
                for h in range(IH):
                    n = (qt - 1) * IH + h
                    if n >= 2:
                        pe.wait_ge(A.sem, A.at("sa relu", n - 2))
                    nc.tensor.matmul(MB[n % 2][:, 0:(qt + 1) * P], AQI[:, h // 2, ck(qt)],
                                     AKI[:, h % 2, 0:(qt + 1) * P], start=True, stop=True
                                     ).then_inc(T.sem, T.mark("sa logit", n))

            for j in range(15):
                pe_tile(pe, "sa_in", j, h_tile, x_wait(pe, "sa_in") if j == 0 else None)
                if 1 <= j <= 5:
                    rot(j - 1)
                if j == 6:
                    pe.wait_ge(V.sem, V.at("sa rs", 4))
                    pe.wait_ge(A.sem, A.at("sa vw"))
                    for c in range(NC):
                        last = nc.tensor.transpose(MB[0][:, c * P:(c + 1) * P], AVW[:, ck(c)], ident)
                    last.then_inc(T.sem, T.mark("sa vt"))
                    pe.wait_ge(V.sem, V.at("sa vt"))
                    pe.wait_ge(V.sem, V.at("sa rope", 4))
                if j >= 7:
                    rot(j - 2)
                    total(j - 2)
                if j in LOGITS_AFTER:
                    index_logits(LOGITS_AFTER[j])
            rot(13)
            total(13)
            pe.wait_ge(G.sem, G.at("sa rope", 13))
            pe.wait_ge(V.sem, V.at("sa key"))
            pe.wait_ge(A.sem, A.at("sa relu", 3 * IH - 1))
            pe.wait_ge(A.sem, A.at("sa roots"))

            def logits(u):
                qt, h = UNITS[u]
                if u >= 3:
                    pe.wait_ge(V.sem, V.at("sa max", u - 3))
                nc.tensor.matmul(LB[u % 3][:, 0:(qt + 1) * P], AQ[:, h // 2, ck(qt)], AK[:, h % 2, 0:(qt + 1) * P],
                                 start=True, stop=True).then_inc(T.sem, T.mark("sa s", u))

            def flip(u):
                qt, h = UNITS[u]
                pe.wait_ge(A.sem, A.at("sa exp", u))
                if u >= 2:
                    pe.wait_ge(A.sem, A.at("sa pt", u - 2))
                for k in range(qt + 1):
                    last = nc.tensor.transpose(MB[u % 2][:, k * P:(k + 1) * P], APR[:, u % 3, k * P:(k + 1) * P], ident)
                last.then_inc(T.sem, T.mark("sa flip", u))

            def products(u):
                qt, h = UNITS[u]
                g = u // 8
                pe.wait_ge(A.sem, A.at("sa pt", u))
                if u % 8 == 0 and g >= 2:
                    pe.wait_ge(V.sem, V.at("sa ot", g - 2))
                for k in range(qt + 1):
                    last = nc.tensor.matmul(MB[2 + g % 2][:, u % 8 * AD:(u % 8 + 1) * AD], APT[:, u % 2, k * P:(k + 1) * P],
                                            AVT[:, k, 0:AD], start=k == 0, stop=k == qt)
                last.then_inc(T.sem, T.mark("sa pv", u))

            def back(g):
                pe.wait_ge(V.sem, V.at("sa ot", g))
                if g:
                    pe.wait_ge(A.sem, A.at("sa out", g - 1))
                for i in range(4):
                    last = nc.tensor.transpose(LB[3][:, i * P:(i + 1) * P], AOT[:, g % 2, i * P:(i + 1) * P], ident)
                last.then_inc(T.sem, T.mark("sa back", g))

            for u in range(64 + 6):
                if u < 64:
                    logits(u)
                if 0 <= u - 2 < 64:
                    flip(u - 2)
                if 0 <= u - 3 < 64:
                    products(u - 3)
                if u >= 13 and (u - 13) % 8 == 0:
                    back((u - 13) // 8)
            for j in range(8):
                pe_tile(pe, "sa_out", j, h_tile,
                        (lambda k: pe.wait_ge(G.sem, G.at("sa low", 7))) if j == 0 else None)

        def act_sa(act):
            act.dma_start(POS[:, :], a["pos"]).then_inc(pos_in, 16)
            act.wait_ge(V.sem, V.at("sa angles"))
            nc.scalar.activation(SIN[:, :], ANG[:, 0, :], ACT.Sin).then_inc(A.sem, A.mark())
            nc.scalar.activation(COS[:, :], ANG[:, 1, :], ACT.Sin).then_inc(A.sem, A.mark("sa sincos"))
            rope_of = {j: i for i, (j, _) in enumerate(ROPE)}

            def rotated(i):
                act.wait_ge(T.sem, T.at("sa rot", i))
                if i >= 7:
                    act.wait_ge(G.sem, G.at("sa rope", i - 2))
                nc.scalar.activation(ROT[:, i % 2, :], MB[2][:, :], ACT.Copy).then_inc(A.sem, A.mark("sa rotated", i))

            for j in range(15):
                bank = arrived(act, "sa_in", j)
                if j == 5:
                    nc.scalar.activation(AVW[:, :], bank[:, :], ACT.Copy).then_inc(A.sem, A.mark("sa vw"))
                    continue
                i = rope_of[j]
                if i >= 3:
                    if i - 3 < 5:
                        act.wait_ge(V.sem, V.at("sa rope", i - 3))
                    else:
                        act.wait_ge(G.sem, G.at("sa rope", i - 3))
                    act.wait_ge(T.sem, T.at("sa rot", i - 3))
                if i < 5:
                    nc.scalar.activation(RAW[:, i % 3, :], bank[:, :], ACT.Copy).then_inc(A.sem, A.mark("sa raw", i))
                else:
                    nc.scalar.activation(RAW[:, i % 3, :], bank[:, :], ACT.Copy,
                                         scale=vec("sa_k_norm" if i == 5 else "sa_q_norm")
                                         ).then_inc(A.sem, A.mark("sa raw", i))
                    if i >= 7:
                        act.wait_ge(T.sem, T.at("sa sum", i - 2))
                    nc.scalar.activation(SQ[:, i % 2, :], bank[:, :], ACT.Square).then_inc(A.sem, A.mark("sa sq", i))
                    if j >= 7:
                        rotated(i - 1)
                    if i == 6:
                        act.wait_ge(T.sem, T.at("sa sum", 5))
                        nc.scalar.activation(RN[:, 0, :], MB[3][:, :], ACT.Sqrt, bias=eps, scale=1.0 / AD
                                             ).then_inc(A.sem, A.mark("sa root"))
                if j in LOGITS_AFTER:
                    qt = LOGITS_AFTER[j]
                    w = (qt + 1) * P
                    for n in range((qt - 1) * IH, qt * IH):
                        act.wait_ge(T.sem, T.at("sa logit", n))
                        if n >= 8:
                            act.wait_ge(V.sem, V.at("sa score", n - 8))
                        nc.scalar.activation(RELS[n % 8][:, 0:w], MB[n % 2][:, 0:w], ACT.Relu
                                             ).then_inc(A.sem, A.mark("sa relu", n))
            rotated(13)
            act.wait_ge(T.sem, T.at("sa sum", 13))
            nc.scalar.activation(ARQ[:, 0, :], MB[3][:, 0:64], ACT.Sqrt, bias=eps, scale=1.0 / AD
                                 ).then_inc(A.sem, A.mark("sa roots"))

            def pt(u):
                act.wait_ge(T.sem, T.at("sa flip", u))
                if u >= 2:
                    act.wait_ge(T.sem, T.at("sa pv", u - 2))
                w = (UNITS[u][0] + 1) * P
                nc.scalar.activation(APT[:, u % 2, 0:w], MB[u % 2][:, 0:w], ACT.Copy).then_inc(A.sem, A.mark("sa pt", u))

            def out_tiles(g):
                act.wait_ge(T.sem, T.at("sa back", g))
                qt, hg = g // 2, g % 2
                nc.scalar.activation(AO[:, 4 * hg:4 * hg + 4, ck(qt)], four(LB[3]), ACT.Copy
                                     ).then_inc(A.sem, A.mark())
                nc.scalar.activation(HH[:, 4 * hg:4 * hg + 4, ck(qt)], four(LB[3]), ACT.Copy
                                     ).then_inc(A.sem, A.mark("sa out", g))

            for u in range(64 + 6):
                if 0 <= u - 2 < 64:
                    pt(u - 2)
                if u < 64:
                    w = (UNITS[u][0] + 1) * P
                    act.wait_ge(V.sem, V.at("sa negmax", u))
                    nc.scalar.activation(APR[:, u % 3, 0:w], APR[:, u % 3, 0:w], ACT.Exp, bias=ANM[:, u:u + 1],
                                         scale=ARQ[:, 1, u:u + 1], accum_out=ASM[:, u:u + 1]
                                         ).then_inc(A.sem, A.mark("sa exp", u))
                if u >= 13 and (u - 13) % 8 == 0:
                    out_tiles((u - 13) // 8)

        def halves(dst, x, y, op, *step):
            for half in range(2):
                r = slice(64 * half, 64 * half + 64)
                nc.vector.tensor_tensor(dst[r, half, :], x[r, :], y[r, :], op
                                        ).then_inc(V.sem, V.mark(*step) if half else V.mark())

        def dve_sa(dve):
            two_pi = 6.283185307179586
            c0, c1 = 6.28125, 0.0019350051879882812
            c2 = two_pi - c0 - c1
            magic = 12582912.0
            for t in (AKI, AK):
                for half in range(2):
                    nc.vector.memset(t[64 * (1 - half):64 * (2 - half), half, :], 0.0).then_inc(V.sem, V.mark())
            dve.wait_ge(pos_in, 16)
            chain(dve, V, nc.vector.tensor_copy(ANG[:, 0, :], POS[:, :]))
            chain(dve, V, nc.vector.tensor_scalar(ANG[:, 0, :], ANG[:, 0, :], cst("inv_freq", n=1), None, ALU.mult))
            chain(dve, V, nc.vector.tensor_scalar(ANG[:, 1, :], ANG[:, 0, :], 1.0 / two_pi, magic, ALU.mult, ALU.add))
            chain(dve, V, nc.vector.tensor_scalar(ANG[:, 1, :], ANG[:, 1, :], magic, None, ALU.subtract))
            for n, cc in enumerate((c0, c1, c2)):
                chain(dve, V, nc.vector.scalar_tensor_tensor(ANG[:, 0, :], ANG[:, 1, :], -cc, ANG[:, 0, :],
                                                             ALU.mult, ALU.add))
            pi = 3.1415925
            chain(dve, V, nc.vector.tensor_scalar(ANG[:, 1, :], ANG[:, 0, :], two_pi / 4, None, ALU.add))
            chain(dve, V, nc.vector.tensor_scalar(ANG[:, 2, :], ANG[:, 1, :], pi, -two_pi, ALU.is_gt, ALU.mult))
            chain(dve, V, nc.vector.tensor_tensor(ANG[:, 1, :], ANG[:, 1, :], ANG[:, 2, :], ALU.add))
            nc.vector.tensor_scalar(ANG[:, 0:2, :], ANG[:, 0:2, :], pi, -pi, ALU.min, ALU.max
                                    ).then_inc(V.sem, V.mark("sa angles"))
            dve.wait_ge(A.sem, A.at("sa sincos"))

            for i in range(5):
                dve.wait_ge(A.sem, A.at("sa raw", i))
                nc.vector.tensor_tensor(RTC[:, i % 2, :], RAW[:, i % 3, :], COS[:, :], ALU.mult).then_inc(V.sem, V.mark())
                dve.wait_ge(T.sem, T.at("sa rot", i))
                nc.vector.tensor_tensor(RTS[:, i % 2, :], SIN[:, :], MB[i % 2][:, :], ALU.mult
                                        ).then_inc(V.sem, V.mark("sa rs", i))
                dve.wait_ge(V.sem, V.at("sa rs", i))
                if i == 0:
                    halves(AKI, RTC[:, 0, :], RTS[:, 0, :], ALU.add, "sa rope", 0)
                else:
                    nc.vector.tensor_tensor(ROPE[i][1], RTC[:, i % 2, :], RTS[:, i % 2, :], ALU.add
                                            ).then_inc(V.sem, V.mark("sa rope", i))
            dve.wait_ge(T.sem, T.at("sa vt"))
            nc.vector.tensor_copy(AVT[:, :, :], MB[0][:, :].rearrange("p (c f) -> p c f", c=NC)[:, :, 0:AD + IH]
                                  ).then_inc(V.sem, V.mark("sa vt"))
            nc.vector.tensor_copy(AMB[:, 0, 0:P], cst("keep_lower")).then_inc(V.sem, V.mark("sa mask", 0))
            dve.wait_ge(V.sem, V.at("sa vt"))
            for qt in range(1, NC):
                w = (qt + 1) * P
                for h in range(IH):
                    n = (qt - 1) * IH + h
                    dve.wait_ge(A.sem, A.at("sa relu", n))
                    wi = AVT[:, qt, AD + h:AD + h + 1]
                    if h == 0:
                        ins = nc.vector.tensor_scalar(ASC[:, 0:w], RELS[n % 8][:, 0:w], wi, None, ALU.mult)
                    else:
                        dve.wait_ge(V.sem, V.at("sa score", n - 1))
                        ins = nc.vector.scalar_tensor_tensor(ASC[:, 0:w], RELS[n % 8][:, 0:w], wi, ASC[:, 0:w],
                                                             ALU.mult, ALU.add)
                    ins.then_inc(V.sem, V.mark("sa score", n))
                dve.wait_ge(V.sem, V.at("sa score", n))
                chain(dve, V, nc.vector.tensor_scalar(ASC[:, 0:w], ASC[:, 0:w], (IH * AD) ** -0.5, None, ALU.mult))
                chain(dve, V, nc.vector.tensor_tensor(ASC[:, qt * P:w], ASC[:, qt * P:w], cst("keep_lower"), ALU.add))
                for r in range(TOPK // 8):
                    src = AWK if r else ASC
                    chain(dve, V, nc.vector.max(AM8[:, :], src[:, 0:w]))
                    chain(dve, V, nc.vector.match_replace(AWK[:, 0:w], AM8[:, :], src[:, 0:w], -3.0e38))
                chain(dve, V, nc.vector.tensor_tensor(AMB[:, qt, 0:w], AWK[:, 0:w], ASC[:, 0:w], ALU.is_equal))
                nc.vector.tensor_scalar(AMB[:, qt, 0:w], AMB[:, qt, 0:w], NEG, None, ALU.mult
                                        ).then_inc(V.sem, V.mark("sa mask", qt))
                if qt == 1:
                    dve.wait_ge(A.sem, A.at("sa root"))
                    chain(dve, V, nc.vector.reciprocal(RN[:, 0, :], RN[:, 0, :]))
                    dve.wait_ge(G.sem, G.at("sa rope", 5))
                    halves(AK, KR, RN[:, 0, :], ALU.mult, "sa key")
            dve.wait_ge(A.sem, A.at("sa roots"))
            chain(dve, V, nc.vector.reciprocal(ARQ[:, 0, :], ARQ[:, 0, :]))
            chain(dve, V, nc.vector.tensor_scalar(ARQ[:, 1, :], ARQ[:, 0, :], AD ** -0.5, None, ALU.mult))
            chain(dve, V, nc.vector.tensor_scalar(ARQ[:, 2, :], ARQ[:, 1, :], -1.0, None, ALU.mult))

            def scale_out(g):
                dve.wait_ge(T.sem, T.at("sa pv", 8 * g + 7))
                dve.wait_ge(A.sem, A.at("sa exp", 8 * g + 7))
                if g >= 2:
                    dve.wait_ge(T.sem, T.at("sa back", g - 2))
                chain(dve, V, nc.vector.reciprocal(ARS[:, 8 * g:8 * g + 8], ASM[:, 8 * g:8 * g + 8]))
                nc.vector.tensor_tensor(AOT[:, g % 2, :].rearrange("p (h w) -> p h w", w=AD),
                                        heads(ARS[:, 8 * g:8 * g + 8], 8, AD),
                                        MB[2 + g % 2][:, :].rearrange("p (h w) -> p h w", w=AD), ALU.mult
                                        ).then_inc(V.sem, V.mark("sa ot", g))

            for u in range(64 + 5):
                if u < 64:
                    qt, h = UNITS[u]
                    w = (qt + 1) * P
                    dve.wait_ge(T.sem, T.at("sa s", u))
                    dve.wait_ge(V.sem, V.at("sa mask", qt))
                    if u >= 3:
                        dve.wait_ge(T.sem, T.at("sa flip", u - 3))
                    nc.vector.tensor_tensor_reduce(out=APR[:, u % 3, 0:w], in0=LB[u % 3][:, 0:w], in1=AMB[:, qt, 0:w],
                                                   scale=1.0, scalar=-3.0e38, op0=ALU.add, op1=ALU.max,
                                                   accum_out=AMX[:, u:u + 1]).then_inc(V.sem, V.mark("sa max", u))
                    dve.wait_ge(V.sem, V.at("sa max", u))
                    nc.vector.tensor_tensor(ANM[:, u:u + 1], AMX[:, u:u + 1], ARQ[:, 2, u:u + 1], ALU.mult
                                            ).then_inc(V.sem, V.mark("sa negmax", u))
                if u >= 11 and (u - 11) % 8 == 0:
                    scale_out((u - 11) // 8)
            residual(dve, "sa_out", lambda d: 1.0)

        def pool_sa(pool):
            def rope(i):
                pool.wait_ge(A.sem, A.at("sa raw", i))
                if i < 7:
                    pool.wait_ge(V.sem, V.at("sa rope", i - 2 if i == 6 else 3))
                nc.gpsimd.tensor_tensor(RTC[:, i % 2, :], RAW[:, i % 3, :], COS[:, :], ALU.mult).then_inc(G.sem, G.mark())
                pool.wait_ge(A.sem, A.at("sa rotated", i))
                chain(pool, G, nc.gpsimd.tensor_tensor(RTS[:, i % 2, :], SIN[:, :], ROT[:, i % 2, :], ALU.mult))
                nc.gpsimd.tensor_tensor(KR if i == 5 else ROPE[i][1], RTC[:, i % 2, :], RTS[:, i % 2, :], ALU.add
                                        ).then_inc(G.sem, G.mark("sa rope", i))

            mix_split(pool, "sa_in", 0, RING)
            pool_h_low(pool, "sa_in")
            mix_split(pool, "sa_in", RING, 10 - RING)
            for j in range(10, 15):
                rope(j - 5)
                mix_split(pool, "sa_in", j, 1)
            for i in range(10, 14):
                rope(i)
            mix_split(pool, "sa_out", 0, RING)
            for g in range(8):
                pool.wait_ge(A.sem, A.at("sa out", g))
                at = slice(4 * (g % 2), 4 * (g % 2) + 4)
                nc.gpsimd.tensor_tensor(HL[:, at, ck(g // 2)], AO[:, at, ck(g // 2)],
                                        HH[:, at, ck(g // 2)].bitcast(F32), ALU.subtract
                                        ).then_inc(G.sem, G.mark("sa low", g))
            mix_split(pool, "sa_out", RING)

        FREED["sa_in"] = lambda j: (A.sem, A.at("sa vw") if j == 5 else
                                    A.at("sa sq" if j > 5 else "sa raw", j if j < 5 else j - 1))

        block = ctx.enter_context(nc.Block())

        @block.sync
        def _(sp):
            sync_program(sp)

        @block.gpsimd
        def _(pool):
            pool_lru(pool)
            pool_gdn(pool)
            pool_ffn(pool, 0)
            pool_hy(pool)
            pool_ffn(pool, 1)
            pool_ffn(pool, 2)
            pool_sa(pool)
            pool_ffn(pool, 3)

        @block.scalar
        def _(act):
            act.dma_start(VEC[:, :], a["vec"]).then_inc(vec_in, 16)
            act.dma_start(CST[:, :], a["cst"]).then_inc(cst_in, 16)
            act.dma_start(X[:, :, :], a["x"]).then_inc(x_in, 16)
            act.dma_start(GW[:, :, :], a["gate_w"]).then_inc(gate_w_in, 16)
            act_ada(act)
            act_norm(act, 0)
            act_h_high(act, "lru_in", 0)
            act_lru(act)
            act_norm(act, 1)
            act_h_high(act, "gdn_in", 1)
            act_gdn(act)
            act_norm(act, 2)
            act_norm(act, 3, lambda: act_ffn_high(act, 3, 0))
            act_ffn(act, 0)
            act_norm(act, 4)
            act_h_high(act, "hy_in", 4)
            act_hy(act)
            act_norm(act, 5, lambda: act_ffn_high(act, 5, 1))
            act_ffn(act, 1)
            act_norm(act, 6, lambda: act_ffn_high(act, 6, 2))
            act_ffn(act, 2)
            act_norm(act, 7)
            act_h_high(act, "sa_in", 7)
            act_sa(act)
            act_norm(act, 8, lambda: act_ffn_high(act, 8, 3))
            act_ffn(act, 3)

        @block.vector
        def _(dve):
            dve_ada(dve)
            dve_norm(dve, 0, lambda d: GS[:, 0, d:d + 1], lambda d: COND[:, d:d + 1])
            dve_lru(dve)
            dve_norm(dve, 1, lambda d: GS[:, 1, d:d + 1], lambda d: COND[:, 24 + d:25 + d])
            dve_gdn(dve)
            dve_norm(dve, 2, lambda d: vec("final_g", d), dst=lambda d: X[:, d, :], sig=x_ready)
            dve_norm(dve, 3, lambda d: vec("ffn_norm", d))
            dve_ffn(dve, 0)
            dve_norm(dve, 4, lambda d: vec("mix_norm", d))
            dve_hy(dve)
            dve_norm(dve, 5, lambda d: vec("ffn_norm", 8 + d))
            dve_ffn(dve, 1)
            dve_norm(dve, 6, lambda d: vec("ffn_norm", 16 + d))
            dve_ffn(dve, 2)
            dve_norm(dve, 7, lambda d: vec("mix_norm", 8 + d))
            dve_sa(dve)
            dve_norm(dve, 8, lambda d: vec("ffn_norm", 24 + d))
            dve_ffn(dve, 3)

        @block.tensor
        def _(pe):
            pe.wait_ge(cst_in, 16)
            pe_norm(pe, 0)
            pe_ada(pe)
            pe_lru(pe)
            pe_norm(pe, 1)
            pe_gdn(pe)
            pe_norm(pe, 2)
            pe_norm(pe, 3)
            pe_ffn(pe, 0)
            pe_norm(pe, 4)
            pe_hy(pe)
            pe_norm(pe, 5)
            pe_ffn(pe, 1)
            pe_norm(pe, 6)
            pe_ffn(pe, 2)
            pe_norm(pe, 7)
            pe_sa(pe)
            pe_norm(pe, 8)
            pe_ffn(pe, 3)


def host_constants():
    import numpy as np
    cst = np.zeros((P, CONST_N), np.float32)

    def put(name, value):
        value = np.asarray(value, np.float32)
        cst[:, CONST_AT[name]:CONST_AT[name] + value.shape[1]] = value

    r = np.arange(P)
    put("ident", np.eye(P))
    put("ones", np.ones((P, P)))
    put("half_ones", (r[:, None] // 64) == (r[None, :] // 64))
    rot = np.zeros((P, P))
    for m in range(P):
        if m % 64 < 32:
            rot[m + 32, m] = -1.0
        else:
            rot[m - 32, m] = 1.0
    put("rotate", rot)
    put("keep_upper", np.where(r[:, None] <= r[None, :], 0.0, NEG))
    put("upper", r[:, None] <= r[None, :])
    put("keep_lower", np.where(r[:, None] >= r[None, :], 0.0, NEG))
    lev = [((r[:, None] >> l) == (r[None, :] >> l) + 1) & (((r[None, :] >> l) & 1) == 0) for l in range(LEVELS)]
    put("levels", np.concatenate(lev, 1))
    inv = np.float32(10000.0) ** (-np.arange(0, 64, 2, dtype=np.float32) / np.float32(64))
    put("inv_freq", inv[r % 32][:, None])
    put("eps", np.full((P, 1), EPS))
    put("one", np.ones((P, 1)))
    return cst


def kernel(**inputs):
    import numpy as np
    import concourse.bacc as bacc
    from concourse import mybir as mb
    from concourse.bass_utils import run_bass_kernel_spmd

    x = {k: np.asarray(v) for k, v in inputs.items()}

    def slabs(w, parts, k, per=1):
        out = np.zeros((len(parts) * per, P, k, P), w.dtype)
        w = w.reshape(per, k, P, w.shape[1])
        for t, runs in enumerate(parts):
            for c, n, at in runs:
                out[t * per:(t + 1) * per, :, :, at:at + n] = w[:, :, :, c:c + n].transpose(0, 2, 1, 3)
        return out.reshape(len(parts) * per, P, k * P)

    def tiles(first, n):
        return [[(first + P * t, P, 0)] for t in range(n)]

    arrays = {}
    ada = x["ada_w"].reshape(2, DT, P, 3, SLAB_K * P).transpose(0, 3, 1, 2, 4).reshape(6 * DT, P, SLAB_K * P)
    arrays["w_ada"] = np.ascontiguousarray(ada[0:2 * DT])
    arrays["w_ada2"] = np.ascontiguousarray(ada[2 * DT:])
    arrays["w_lru_in"] = slabs(x["lru_in_w"][0], tiles(0, 16), 8)
    arrays["w_lru_out"] = slabs(x["lru_out_w"][0], tiles(0, 8), 8)
    arrays["w_gdn_in"] = slabs(x["gdn_in_w"][0], [[(4096, 16, 0)]] + tiles(1024, 8) + tiles(0, 8)
                               + tiles(2048, 8) + tiles(3072, 8), 8)
    arrays["w_gdn_out"] = slabs(x["gdn_out_w"][0], tiles(0, 8), 8)
    for p in range(8):
        f, first, n = p // 2, PART[0] * (p % 2), PART[p % 2]
        gate = slabs(x["ffn_w_gate_2"][f // 2, f % 2], tiles(P * first, n), 8)
        up = slabs(x["ffn_w_up_2"][f // 2, f % 2], tiles(P * first, n), 8)
        arrays[f"w_up{p}"] = np.stack([gate, up], 1).reshape(2 * n, P, 8 * P)
        arrays[f"w_down{p}"] = slabs(x["ffn_w_down_2"][f // 2, f % 2][P * first:P * (first + n)],
                                     tiles(0, 8), n // 2, 2)
    arrays["w_hy_in"] = slabs(x["hy_w_in_2"][0], [[(2560, 16, 0), (5648, 4, 16 + 32), (5652, 4, 16 + 36 + 32)]] + tiles(1024, 12) + tiles(0, 8)
                              + tiles(2576, 4) + tiles(3088, 4) + tiles(3600, 8) + tiles(4624, 8), 8)
    arrays["w_hy_out"] = slabs(x["hy_w_out_2"][0], tiles(0, 8), 8, 2)
    arrays["w_sa_in"] = slabs(x["sa_w_in_2"][0], [[(1664, 64, 0), (1664, 64, 64)]] + tiles(1152, 4)
                              + [[(1088, 64, 0), (1728, 8, 64)]] + [[(1024, 64, 0), (1024, 64, 64)]]
                              + tiles(0, 8), 8)
    arrays["w_sa_out"] = slabs(x["sa_w_out_2"][0], tiles(0, 8), 8)
    arrays["gate_w"] = np.ascontiguousarray(
        x["lru_gate_w"][0].transpose(2, 0, 1, 3).reshape(P, 16, P))
    arrays["x"] = np.ascontiguousarray(x["x"][0].T.reshape(DT, P, S).transpose(1, 0, 2))
    arrays["pos"] = np.ascontiguousarray(np.broadcast_to(x["positions_2"], (P, S)))

    def cols(v):
        return v.reshape(-1, P).T

    v = np.zeros((P, VEC_N), np.float32)

    def put(name, value, rows=P, first=0):
        v[first:first + rows, VEC_AT[name]:VEC_AT[name] + value.shape[1]] = value

    put("norm_g", cols(x["norm_g"]))
    put("final_g", cols(x["final_g"]))
    put("ada_b", cols(x["ada_b"]))
    put("lru_conv_w", cols(x["lru_conv_w"]))
    put("lru_conv_b", cols(x["lru_conv_b"]))
    put("lru_gate_b", cols(x["lru_gate_b"]))
    put("lru_lambda", cols(x["lru_lambda"]))
    put("gdn_conv_w", cols(x["gdn_conv_w"]))
    put("gdn_onorm_g", cols(x["gdn_onorm_g"]))
    put("ffn_norm", cols(x["ffn_norm_2"]))
    put("mix_norm", cols(x["mix_norm_2"]))
    put("hy_conv_w", cols(x["hy_conv_w_2"]))
    put("hy_conv_b", cols(x["hy_conv_b_2"]))
    put("hy_ssd_norm", cols(x["hy_ssd_norm_2"]))
    put("hy_mlstm_norm", cols(x["hy_mlstm_norm_2"]))
    put("hy_d_skip", cols(np.repeat(x["hy_d_skip_2"][0], SP_)))
    put("sa_q_norm", np.tile(x["sa_q_norm_2"][0], 2)[:, None])
    put("sa_k_norm", np.tile(x["sa_k_norm_2"][0], 2)[:, None])
    put("gdn_a_log", x["gdn_a_log"].T, GH)
    put("gdn_dt_bias", x["gdn_dt_bias"].T, GH)
    put("hy_dt_bias", x["hy_dt_bias_2"].T, SH)
    put("hy_a_log", x["hy_a_log_2"].T, SH)
    put("hy_igate_bias", x["hy_igate_bias_2"].T, MH, 32)
    put("hy_fgate_bias", x["hy_fgate_bias_2"].T, MH, 32)
    put("c", cols(x["c"]))
    arrays["vec"] = v
    arrays["cst"] = host_constants()

    def build(table, final):
        nc = bacc.Bacc("TRN2", target_bir_lowering=False, num_devices=1)
        ins = {n: nc.dram_tensor(f"in_{n}", t.shape, mb.dt.from_np(t.dtype), kind="ExternalInput").ap()
               for n, t in arrays.items()}
        out = nc.dram_tensor("out_0", (P, DT, S), mb.dt.float32, kind="ExternalOutput").ap()
        bass_program(nc, ins, out, table, final)
        return nc

    table = {}
    build(table, False)
    nc = build(table, True)
    r = run_bass_kernel_spmd(nc, [{f"in_{n}": t for n, t in arrays.items()}], core_ids=[0])
    y = r.results[0]["out_0"]
    return np.ascontiguousarray(y.transpose(1, 0, 2).reshape(D, S).T)[None]
```
